# Optimizing a Trainium2 kernel written in Bass

```python
import math
import numpy as np
import jax
import jax.numpy as jnp
from jax import lax
import jax, jax.numpy as jnp

D_MODEL = 1024
BATCH = 1
SEQ = 512
DEPTH = 2

SSD_D_INNER = D_MODEL
SSD_HEADDIM = 64
SSD_HEADS = SSD_D_INNER // SSD_HEADDIM
SSD_GROUPS = 2
SSD_STATE = 128
SSD_CONV = 5
SSD_CHUNK = 128
MLSTM_D = D_MODEL
MLSTM_HEADS = 8
MLSTM_HEADDIM = MLSTM_D // MLSTM_HEADS
MLSTM_CHUNK = 128
GLA_HEADS = 4
GLA_DK = D_MODEL // 2
GLA_DV = D_MODEL
GLA_HEAD_DK = GLA_DK // GLA_HEADS
GLA_HEAD_DV = GLA_DV // GLA_HEADS
GLA_RANK = 16
GLA_TAU = 16.0
GLA_CHUNK = 64
FFN_DIM = 11 * D_MODEL // 4
FFN_CONV = 3
NORM_EPS = 1e-6

SSD_XBC = SSD_D_INNER + 2 * SSD_GROUPS * SSD_STATE
L0_SPLITS = (SSD_D_INNER, SSD_XBC, 2 * SSD_HEADS, MLSTM_D, MLSTM_D, MLSTM_D, MLSTM_D, 4 * MLSTM_HEADS)
L0_IN = sum(L0_SPLITS)
L0_MIX = SSD_D_INNER + MLSTM_D
L1_SPLITS = (GLA_DK, GLA_DK, GLA_DV, GLA_DV, 2 * GLA_RANK)
L1_IN = sum(L1_SPLITS)
N_EVEN_LAYERS = (DEPTH + 1) // 2
N_ODD_LAYERS = DEPTH // 2


def _split(u, sizes):
    return jnp.split(u, np.cumsum(sizes)[:-1].tolist(), axis=-1)

def _rev(t):
    return jnp.flip(t, axis=1)

def _lower_tri(n):
    return jnp.tril(jnp.ones((n, n), dtype=bool))

def _rmsnorm(x, g):
    xf = x.astype(jnp.float32)
    y = xf * lax.rsqrt(jnp.mean(xf * xf, axis=-1, keepdims=True) + NORM_EPS)
    return (y * g.astype(jnp.float32)).astype(x.dtype)

def _head_rmsnorm(x, g, n_heads):
    shp = x.shape
    xh = x.reshape(shp[:-1] + (n_heads, shp[-1] // n_heads))
    return _rmsnorm(xh, g.reshape(n_heads, -1)).reshape(shp)

def _dwconv(x, w, b):
    k = w.shape[0]
    y = lax.conv_general_dilated(x, w[:, None, :], window_strides=(1,), padding=[(k // 2, k // 2)],
                                 dimension_numbers=('NWC', 'WIO', 'NWC'), feature_group_count=x.shape[-1])
    return y + b

def _bidirectional(scan_fn, seq_fwd, seq_bwd, par_fwd=(), par_bwd=()):
    y_f = scan_fn(*seq_fwd, *par_fwd)
    y_b = scan_fn(*[_rev(t) for t in seq_bwd], *par_bwd)
    return y_f + _rev(y_b)

def _ssd_scan(x, dt, bm, cm, a):
    bsz, s, nh, p = x.shape
    g, n = bm.shape[2], bm.shape[3]
    e = nh // g
    l = SSD_CHUNK
    c = s // l
    dt = dt.astype(jnp.float32)
    xdt = (x * dt[..., None]).reshape(bsz, c, l, g, e, p)
    cs = jnp.cumsum((dt * a.astype(jnp.float32)).reshape(bsz, c, l, g, e), axis=2)
    bm = bm.reshape(bsz, c, l, g, n)
    cm = cm.reshape(bsz, c, l, g, n)
    cs_t = jnp.transpose(cs, (0, 3, 4, 1, 2))
    decay = jnp.exp(jnp.where(_lower_tri(l), cs_t[..., :, None] - cs_t[..., None, :], -jnp.inf))
    cb = jnp.einsum('bclgn,bcsgn->bgcls', cm, bm)
    y = jnp.einsum('bgecls,bcsgep->bclgep', cb[:, :, None] * decay, xdt)
    x_end = xdt * jnp.exp(cs[:, :, -1:] - cs)[..., None]
    states = jnp.einsum('bclgn,bclgep->cbgepn', bm, x_end)
    chunk_decay = jnp.exp(jnp.transpose(cs[:, :, -1], (1, 0, 2, 3)))

    def step(hs, inp):
        st, dec = inp
        return dec[..., None, None] * hs + st, hs

    _, h_prev = lax.scan(step, jnp.zeros(states.shape[1:], states.dtype), (states, chunk_decay))
    y = y + jnp.einsum('bclgn,cbgepn->bclgep', cm, h_prev) * jnp.exp(cs)[..., None]
    return y.reshape(bsz, s, nh, p)

def _mlstm_scan(q, k, v, ig, lf):
    bsz, s, nh, dk = q.shape
    dv = v.shape[-1]
    l = MLSTM_CHUNK
    c = s // l
    q = q.reshape(bsz, c, l, nh, dk)
    k = k.reshape(bsz, c, l, nh, dk)
    v = v.reshape(bsz, c, l, nh, dv)
    ig = ig.astype(jnp.float32).reshape(bsz, c, l, nh)
    fc = jnp.cumsum(lf.astype(jnp.float32).reshape(bsz, c, l, nh), axis=2)
    f_end = fc[:, :, -1]
    a = f_end[:, :, None] - fc + ig
    m_loc = jnp.max(a, axis=2)
    kw = k * jnp.exp(a - m_loc[:, :, None])[..., None]
    c_loc = jnp.einsum('bclhk,bclhv->cbhkv', kw, v)
    n_loc = jnp.transpose(jnp.sum(kw, axis=2), (1, 0, 2, 3))

    def step(carry, inp):
        c_st, n_st, m_st = carry
        c_l, n_l, m_l, f_l = inp
        m_new = jnp.maximum(f_l + m_st, m_l)
        s_old = jnp.exp(f_l + m_st - m_new)
        s_loc = jnp.exp(m_l - m_new)
        c_new = s_old[..., None, None] * c_st + s_loc[..., None, None] * c_l
        n_new = s_old[..., None] * n_st + s_loc[..., None] * n_l
        return (c_new, n_new, m_new), (c_st, n_st, m_st)

    init = (jnp.zeros(c_loc.shape[1:], c_loc.dtype), jnp.zeros(n_loc.shape[1:], n_loc.dtype),
            jnp.zeros((bsz, nh), jnp.float32))
    _, (c_st, n_st, m_st) = lax.scan(step, init, (c_loc, n_loc, jnp.transpose(m_loc, (1, 0, 2)),
                                                  jnp.transpose(f_end, (1, 0, 2))))
    fc_t = jnp.transpose(fc, (0, 3, 1, 2))
    ig_t = jnp.transpose(ig, (0, 3, 1, 2))
    dmat = jnp.where(_lower_tri(l), fc_t[..., :, None] - fc_t[..., None, :] + ig_t[..., None, :], -jnp.inf)
    m_inter = fc_t + jnp.transpose(m_st, (1, 2, 0))[..., None]
    m_t = jnp.maximum(m_inter, jnp.max(dmat, axis=-1))
    wmat = jnp.einsum('bclhk,bcshk->bhcls', q, k) * jnp.exp(dmat - m_t[..., None])
    s_inter = jnp.transpose(jnp.exp(m_inter - m_t), (0, 2, 3, 1))
    num = (jnp.einsum('bhcls,bcshv->bclhv', wmat, v)
           + s_inter[..., None] * jnp.einsum('bclhk,cbhkv->bclhv', q, c_st))
    den = (jnp.transpose(jnp.sum(wmat, axis=-1), (0, 2, 3, 1))
           + s_inter * jnp.einsum('bclhk,cbhk->bclh', q, n_st))
    floor = jnp.exp(-jnp.transpose(m_t, (0, 2, 3, 1)))
    h = num / jnp.maximum(jnp.abs(den), floor)[..., None]
    return h.reshape(bsz, s, nh, dv)

def _gla_scan(q, k, v, la):
    bsz, s, nh, dk = q.shape
    dv = v.shape[-1]
    l = GLA_CHUNK
    c = s // l
    q = q.reshape(bsz, c, l, nh, dk)
    k = k.reshape(bsz, c, l, nh, dk)
    v = v.reshape(bsz, c, l, nh, dv)
    bc = jnp.cumsum(la.astype(jnp.float32).reshape(bsz, c, l, nh, dk), axis=2)
    b_end = bc[:, :, -1:]
    q_in = q * jnp.exp(bc)
    att = jnp.einsum('bclhk,bcshk->bhcls', q_in, k * jnp.exp(-bc))
    att = jnp.where(_lower_tri(l), att, 0.0)
    o = jnp.einsum('bhcls,bcshv->bclhv', att, v)
    u = jnp.einsum('bclhk,bclhv->cbhkv', k * jnp.exp(b_end - bc), v)
    dec = jnp.exp(jnp.transpose(b_end[:, :, 0], (1, 0, 2, 3)))

    def step(st, inp):
        u_c, d_c = inp
        return d_c[..., None] * st + u_c, st

    _, s_prev = lax.scan(step, jnp.zeros(u.shape[1:], u.dtype), (u, dec))
    o = o + jnp.einsum('bclhk,cbhkv->bclhv', q_in, s_prev)
    return o.reshape(bsz, s, nh, dv)

def _ssd_mlstm_mixer(h, w_in, conv_w, conv_b, dt_bias, a_log, d_skip, ssd_norm, ig_bias, fg_bias, mlstm_norm, w_out):
    bsz, s, _ = h.shape
    z, xbc, dt_raw, q, k, v, o_pre, gates = _split(h @ w_in, L0_SPLITS)
    xbc = jax.nn.silu(_dwconv(xbc, conv_w, conv_b))
    xs, bm, cm = _split(xbc, (SSD_D_INNER, SSD_GROUPS * SSD_STATE, SSD_GROUPS * SSD_STATE))
    xs = xs.reshape(bsz, s, SSD_HEADS, SSD_HEADDIM)
    bm = bm.reshape(bsz, s, SSD_GROUPS, SSD_STATE)
    cm = cm.reshape(bsz, s, SSD_GROUPS, SSD_STATE)
    dt = jax.nn.softplus(dt_raw.reshape(bsz, s, 2, SSD_HEADS).astype(jnp.float32) + dt_bias)
    a = -jnp.exp(a_log.astype(jnp.float32))
    y = _bidirectional(_ssd_scan, (xs, dt[:, :, 0], bm, cm), (xs, dt[:, :, 1], bm, cm), (a[0],), (a[1],))
    y = y + d_skip[:, None] * xs
    y = _head_rmsnorm(y.reshape(bsz, s, SSD_D_INNER) * jax.nn.silu(z), ssd_norm, SSD_GROUPS)
    q = q.reshape(bsz, s, MLSTM_HEADS, MLSTM_HEADDIM)
    k = k.reshape(bsz, s, MLSTM_HEADS, MLSTM_HEADDIM) * MLSTM_HEADDIM ** -0.5
    v = v.reshape(bsz, s, MLSTM_HEADS, MLSTM_HEADDIM)
    gates = gates.reshape(bsz, s, 2, 2, MLSTM_HEADS).astype(jnp.float32)
    ig = gates[:, :, 0] + ig_bias
    lf = jax.nn.log_sigmoid(gates[:, :, 1] + fg_bias)
    hm = _bidirectional(_mlstm_scan, (q, k, v, ig[:, :, 0], lf[:, :, 0]), (q, k, v, ig[:, :, 1], lf[:, :, 1]))
    hm = jax.nn.sigmoid(o_pre) * hm.reshape(bsz, s, MLSTM_D)
    hm = _head_rmsnorm(hm, mlstm_norm, MLSTM_HEADS)
    return jnp.concatenate([y, hm], axis=-1) @ w_out

def _gla_mixer(h, w_in, gate_w2, gate_b, gla_norm, w_out):
    bsz, s, _ = h.shape
    q, k, v, r, g_lr = _split(h @ w_in, L1_SPLITS)
    q = q.reshape(bsz, s, GLA_HEADS, GLA_HEAD_DK) * GLA_HEAD_DK ** -0.5
    k = k.reshape(bsz, s, GLA_HEADS, GLA_HEAD_DK)
    v = v.reshape(bsz, s, GLA_HEADS, GLA_HEAD_DV)
    g_lr = g_lr.reshape(bsz, s, 2, GLA_RANK)
    logits = jnp.einsum('bsdr,drk->bsdk', g_lr, gate_w2) + gate_b
    la = (jax.nn.log_sigmoid(logits.astype(jnp.float32)) / GLA_TAU).reshape(bsz, s, 2, GLA_HEADS, GLA_HEAD_DK)
    o = _bidirectional(_gla_scan, (q, k, v, la[:, :, 0]), (q, k, v, la[:, :, 1]))
    o = _head_rmsnorm(o.reshape(bsz, s, GLA_DV), gla_norm, GLA_HEADS) * jax.nn.silu(r)
    return o @ w_out

def _conv_ffn(h, w_up, conv_w, conv_b, w_down):
    u = _dwconv(h @ w_up, conv_w, conv_b)
    gate, val = jnp.split(u, 2, axis=-1)
    return (jax.nn.gelu(gate, approximate=True) * val) @ w_down

def first_inputs(seed: int = 0) -> dict:
    key = jax.random.key(seed)
    keys = jax.random.split(key, 24)

    def nrm(i, shape, scale):
        return scale * jax.random.normal(keys[i], shape, jnp.float32)

    ne, no = N_EVEN_LAYERS, N_ODD_LAYERS
    dt0 = jnp.exp(jax.random.uniform(keys[5], (ne, 2, SSD_HEADS), jnp.float32, math.log(1e-3), math.log(1e-1)))
    return {
        'x': nrm(0, (BATCH, SEQ, D_MODEL), 1.0),
        'norm_g': 1.0 + nrm(1, (DEPTH, 4, D_MODEL), 0.05),
        'ab_w_in': nrm(2, (ne, D_MODEL, L0_IN), D_MODEL ** -0.5),
        'ab_conv_w': nrm(3, (ne, SSD_CONV, SSD_XBC), SSD_CONV ** -0.5),
        'ab_conv_b': nrm(4, (ne, SSD_XBC), 0.02),
        'ab_dt_bias': dt0 + jnp.log(-jnp.expm1(-dt0)),
        'ab_a_log': jnp.log(jax.random.uniform(keys[6], (ne, 2, SSD_HEADS), jnp.float32, 1.0, 16.0)),
        'ab_d_skip': 1.0 + nrm(7, (ne, SSD_HEADS), 0.1),
        'ab_ssd_norm': 1.0 + nrm(8, (ne, SSD_D_INNER), 0.05),
        'ab_ig_bias': nrm(9, (ne, 2, MLSTM_HEADS), 0.1),
        'ab_fg_bias': jnp.linspace(3.0, 6.0, MLSTM_HEADS, dtype=jnp.float32) + nrm(10, (ne, 2, MLSTM_HEADS), 0.1),
        'ab_mlstm_norm': 1.0 + nrm(11, (ne, MLSTM_D), 0.05),
        'ab_w_out': nrm(12, (ne, L0_MIX, D_MODEL), L0_MIX ** -0.5),
        'c_w_in': nrm(13, (no, D_MODEL, L1_IN), D_MODEL ** -0.5),
        'c_gate_w2': nrm(14, (no, 2, GLA_RANK, GLA_DK), GLA_RANK ** -0.5),
        'c_gate_b': nrm(15, (no, 2, GLA_DK), 0.1),
        'c_norm': 1.0 + nrm(16, (no, GLA_DV), 0.05),
        'c_w_out': nrm(17, (no, GLA_DV, D_MODEL), GLA_DV ** -0.5),
        'ffn_w_up': nrm(18, (DEPTH, D_MODEL, 2 * FFN_DIM), D_MODEL ** -0.5),
        'ffn_conv_w': nrm(19, (DEPTH, FFN_CONV, 2 * FFN_DIM), FFN_CONV ** -0.5),
        'ffn_conv_b': nrm(20, (DEPTH, 2 * FFN_DIM), 0.02),
        'ffn_w_down': nrm(21, (DEPTH, FFN_DIM, D_MODEL), FFN_DIM ** -0.5),
    }

def first_block(x, norm_g, ab_w_in, ab_conv_w, ab_conv_b, ab_dt_bias, ab_a_log, ab_d_skip, ab_ssd_norm,
              ab_ig_bias, ab_fg_bias, ab_mlstm_norm, ab_w_out, c_w_in, c_gate_w2, c_gate_b, c_norm, c_w_out,
              ffn_w_up, ffn_conv_w, ffn_conv_b, ffn_w_down):
    for i in range(DEPTH):
        j = i // 2
        h = _rmsnorm(x, norm_g[i, 0])
        if i % 2 == 0:
            h = _ssd_mlstm_mixer(h, ab_w_in[j], ab_conv_w[j], ab_conv_b[j], ab_dt_bias[j], ab_a_log[j],
                                 ab_d_skip[j], ab_ssd_norm[j], ab_ig_bias[j], ab_fg_bias[j], ab_mlstm_norm[j],
                                 ab_w_out[j])
        else:
            h = _gla_mixer(h, c_w_in[j], c_gate_w2[j], c_gate_b[j], c_norm[j], c_w_out[j])
        x = x + _rmsnorm(h, norm_g[i, 1])
        f = _conv_ffn(_rmsnorm(x, norm_g[i, 2]), ffn_w_up[i], ffn_conv_w[i], ffn_conv_b[i], ffn_w_down[i])
        x = x + _rmsnorm(f, norm_g[i, 3])
    return x


DEPTH_2 = 1

N_HEADS_A = 8
N_KV_HEADS_A = 2
HEAD_DIM_A = 64
IDX_HEADS = 8
IDX_DIM = 64
TOPK_MAX = 256
Q_BLOCK = 128
CONV_CH = 512
CONV_WIDTH = 31
N_MEM = 256
MEM_HEADS = 4
MEM_HEAD_DIM = 128
N_BRANCHES = 3
N_GROUPS = 4
EXPERTS_PER_GROUP = 8
N_EXPERTS = N_GROUPS * EXPERTS_PER_GROUP
TOP_K_INNER = 2
D_FF_EXPERT = 256

ROPE_THETA = 10000.0
EPS = 1e-6

SPLIT_SIZES = (
    N_HEADS_A * HEAD_DIM_A,
    N_KV_HEADS_A * HEAD_DIM_A,
    N_KV_HEADS_A * HEAD_DIM_A,
    IDX_HEADS * IDX_DIM,
    IDX_DIM,
    IDX_HEADS,
    2 * CONV_CH,
    MEM_HEADS * MEM_HEAD_DIM,
    N_BRANCHES * D_MODEL,
)
IN_COLS = sum(SPLIT_SIZES)


def rmsnorm(x, g):
    xf = x.astype(jnp.float32)
    y = xf * lax.rsqrt(jnp.mean(xf * xf, axis=-1, keepdims=True) + EPS)
    return (y * g.astype(jnp.float32)).astype(x.dtype)

def layernorm(x, g, b):
    xf = x.astype(jnp.float32)
    mu = jnp.mean(xf, axis=-1, keepdims=True)
    var = jnp.mean(jnp.square(xf - mu), axis=-1, keepdims=True)
    y = (xf - mu) * lax.rsqrt(var + EPS)
    return (y * g.astype(jnp.float32) + b.astype(jnp.float32)).astype(x.dtype)

def rope(x, pos):
    d = x.shape[-1]
    half = d // 2
    inv = ROPE_THETA ** (-jnp.arange(half, dtype=jnp.float32) / half)
    ang = pos.astype(jnp.float32)[:, None] * inv[None, :]
    cos = jnp.cos(ang)[None, :, None, :]
    sin = jnp.sin(ang)[None, :, None, :]
    xf = x.astype(jnp.float32)
    x1, x2 = xf[..., :half], xf[..., half:]
    out = jnp.concatenate([x1 * cos - x2 * sin, x2 * cos + x1 * sin], axis=-1)
    return out.astype(x.dtype)

def dsa_attention(q, k, v, q_idx, k_idx, w_idx, topk):
    B, S = q.shape[0], q.shape[1]
    G = N_HEADS_A // N_KV_HEADS_A
    n_blocks = S // Q_BLOCK
    key_pos = jnp.arange(S)
    w_idx = w_idx.astype(jnp.float32) * (IDX_HEADS ** -0.5)
    scale = HEAD_DIM_A ** -0.5

    def block(i):
        start = i * Q_BLOCK
        qb = lax.dynamic_slice_in_dim(q, start, Q_BLOCK, axis=1)
        qib = lax.dynamic_slice_in_dim(q_idx, start, Q_BLOCK, axis=1)
        wib = lax.dynamic_slice_in_dim(w_idx, start, Q_BLOCK, axis=1)
        tpos = start + jnp.arange(Q_BLOCK)
        logits = jnp.einsum('bqhd,bsd->bqhs', qib, k_idx,
                            preferred_element_type=jnp.float32) * (IDX_DIM ** -0.5)
        score = jnp.einsum('bqh,bqhs->bqs', wib, jax.nn.relu(logits))
        causal = key_pos[None, :] <= tpos[:, None]
        score = jnp.where(causal[None], score, -jnp.inf)
        _, sel = lax.top_k(score, topk)
        valid = sel <= tpos[None, :, None]
        kg = jax.vmap(lambda kk, ii: kk[ii])(k, sel)
        vg = jax.vmap(lambda vv, ii: vv[ii])(v, sel)
        qg = qb.reshape(B, Q_BLOCK, N_KV_HEADS_A, G, HEAD_DIM_A)
        s = jnp.einsum('bqhgd,bqkhd->bqhgk', qg, kg,
                       preferred_element_type=jnp.float32) * scale
        s = jnp.where(valid[:, :, None, None, :], s, -jnp.inf)
        p = jax.nn.softmax(s, axis=-1)
        o = jnp.einsum('bqhgk,bqkhd->bqhgd', p.astype(vg.dtype), vg)
        return o.reshape(B, Q_BLOCK, N_HEADS_A * HEAD_DIM_A)

    out = lax.map(block, jnp.arange(n_blocks))
    return jnp.moveaxis(out, 0, 1).reshape(B, S, N_HEADS_A * HEAD_DIM_A)

def conformer_conv(conv_in, conv_w, conv_b, ln_g, ln_b):
    a, gte = jnp.split(conv_in, 2, axis=-1)
    u = a * jax.nn.sigmoid(gte)
    y = lax.conv_general_dilated(
        u, conv_w, window_strides=(1,), padding=[(CONV_WIDTH - 1, 0)],
        dimension_numbers=('NWC', 'WIO', 'NWC'), feature_group_count=CONV_CH)
    y = y + conv_b
    return jax.nn.silu(layernorm(y, ln_g, ln_b))

def memory_attention(q_m, mem, g_mem, w_mem_kv, g_qm, g_km):
    B, S = q_m.shape[0], q_m.shape[1]
    M = mem.shape[1]
    kv = jnp.einsum('bmd,dc->bmc', rmsnorm(mem, g_mem), w_mem_kv)
    k_m, v_m = jnp.split(kv, 2, axis=-1)
    k_m = rmsnorm(k_m.reshape(B, M, MEM_HEADS, MEM_HEAD_DIM), g_km)
    v_m = v_m.reshape(B, M, MEM_HEADS, MEM_HEAD_DIM)
    q = rmsnorm(q_m.reshape(B, S, MEM_HEADS, MEM_HEAD_DIM), g_qm)
    s = jnp.einsum('bshd,bmhd->bhsm', q, k_m,
                   preferred_element_type=jnp.float32) * (MEM_HEAD_DIM ** -0.5)
    p = jax.nn.softmax(s, axis=-1)
    o = jnp.einsum('bhsm,bmhd->bshd', p.astype(v_m.dtype), v_m)
    return o.reshape(B, S, MEM_HEADS * MEM_HEAD_DIM)

def hier_moe(h, w_rg, b_rg, w_re, b_re, w_up, w_down):
    T = h.shape[0]
    g_logits = (h @ w_rg + b_rg).astype(jnp.float32)
    p_g = jax.nn.softmax(g_logits, axis=-1)
    g_sel = jnp.argmax(g_logits, axis=-1)
    p_sel = jnp.take_along_axis(p_g, g_sel[:, None], axis=1)
    e_logits = (h @ w_re + b_re).astype(jnp.float32).reshape(T, N_GROUPS, EXPERTS_PER_GROUP)
    e_in = jnp.take_along_axis(e_logits, g_sel[:, None, None], axis=1)[:, 0]
    top_v, top_i = lax.top_k(e_in, TOP_K_INNER)
    w2 = jax.nn.softmax(top_v, axis=-1) * p_sel
    expert_id = g_sel[:, None] * EXPERTS_PER_GROUP + top_i
    combine = jnp.sum(jax.nn.one_hot(expert_id, N_EXPERTS, dtype=jnp.float32)
                      * w2[..., None], axis=1).astype(h.dtype)
    out = jnp.zeros_like(h)
    for n in range(N_EXPERTS):
        a, b = jnp.split(h @ w_up[n], 2, axis=-1)
        out = out + combine[:, n:n + 1] * ((jax.nn.silu(a) * b) @ w_down[n])
    return out

def second_inputs(seed: int = 0) -> dict:
    key = jax.random.key(seed)
    ks = jax.random.split(key, 28)
    f32 = jnp.float32
    L = DEPTH_2

    def nrm(k, shape, fan_in):
        return jax.random.normal(k, shape, f32) * (fan_in ** -0.5)

    def gain(k, shape):
        return 1.0 + 0.05 * jax.random.normal(k, shape, f32)

    def small(k, shape, s):
        return s * jax.random.normal(k, shape, f32)

    return {
        "x": jax.random.normal(ks[0], (BATCH, SEQ, D_MODEL), f32),
        "mem": jax.random.normal(ks[1], (BATCH, N_MEM, D_MODEL), f32),
        "g_mix": gain(ks[2], (L, D_MODEL)),
        "w_in": nrm(ks[3], (L, D_MODEL, IN_COLS), D_MODEL),
        "b_gate": small(ks[4], (L, N_BRANCHES * D_MODEL), 0.02),
        "g_qa": gain(ks[5], (L, HEAD_DIM_A)),
        "g_ka": gain(ks[6], (L, HEAD_DIM_A)),
        "g_idx_k": gain(ks[7], (L, IDX_DIM)),
        "conv_w": nrm(ks[8], (L, CONV_WIDTH, 1, CONV_CH), CONV_WIDTH),
        "conv_b": small(ks[9], (L, CONV_CH), 0.02),
        "ln_g": gain(ks[10], (L, CONV_CH)),
        "ln_b": small(ks[11], (L, CONV_CH), 0.02),
        "g_mem": gain(ks[12], (L, D_MODEL)),
        "w_mem_kv": nrm(ks[13], (L, D_MODEL, 2 * MEM_HEADS * MEM_HEAD_DIM), D_MODEL),
        "g_qm": gain(ks[14], (L, MEM_HEAD_DIM)),
        "g_km": gain(ks[15], (L, MEM_HEAD_DIM)),
        "w_br_a": nrm(ks[16], (L, N_HEADS_A * HEAD_DIM_A, D_MODEL), N_HEADS_A * HEAD_DIM_A),
        "w_br_b": nrm(ks[17], (L, CONV_CH, D_MODEL), CONV_CH),
        "w_br_m": nrm(ks[18], (L, MEM_HEADS * MEM_HEAD_DIM, D_MODEL), MEM_HEADS * MEM_HEAD_DIM),
        "w_o": nrm(ks[19], (L, D_MODEL, D_MODEL), D_MODEL),
        "g_ffn": gain(ks[20], (L, D_MODEL)),
        "w_rg": nrm(ks[21], (L, D_MODEL, N_GROUPS), D_MODEL),
        "b_rg": small(ks[22], (L, N_GROUPS), 0.01),
        "w_re": nrm(ks[23], (L, D_MODEL, N_EXPERTS), D_MODEL),
        "b_re": small(ks[24], (L, N_EXPERTS), 0.01),
        "w_up": nrm(ks[25], (L, N_EXPERTS, D_MODEL, 2 * D_FF_EXPERT), D_MODEL),
        "w_down": nrm(ks[26], (L, N_EXPERTS, D_FF_EXPERT, D_MODEL), D_FF_EXPERT),
    }

def second_block(x, mem, g_mix, w_in, b_gate, g_qa, g_ka, g_idx_k, conv_w, conv_b, ln_g, ln_b,
              g_mem, w_mem_kv, g_qm, g_km, w_br_a, w_br_b, w_br_m, w_o, g_ffn,
              w_rg, b_rg, w_re, b_re, w_up, w_down):
    B, S, D = x.shape
    topk = min(TOPK_MAX, S // 4)
    pos = jnp.arange(S, dtype=jnp.int32)
    split_points = []
    acc = 0
    for sz in SPLIT_SIZES[:-1]:
        acc += sz
        split_points.append(acc)

    for l in range(DEPTH_2):
        h = rmsnorm(x, g_mix[l])
        proj = jnp.einsum('bsd,dc->bsc', h, w_in[l])
        q_a, k_a, v_a, q_i, k_i, w_i, conv_in, q_m, gate_logits = jnp.split(
            proj, split_points, axis=-1)

        q_a = rope(rmsnorm(q_a.reshape(B, S, N_HEADS_A, HEAD_DIM_A), g_qa[l]), pos)
        k_a = rope(rmsnorm(k_a.reshape(B, S, N_KV_HEADS_A, HEAD_DIM_A), g_ka[l]), pos)
        v_a = v_a.reshape(B, S, N_KV_HEADS_A, HEAD_DIM_A)
        q_i = rope(q_i.reshape(B, S, IDX_HEADS, IDX_DIM), pos)
        k_i = rope(rmsnorm(k_i, g_idx_k[l])[:, :, None, :], pos)[:, :, 0, :]
        o_a = dsa_attention(q_a, k_a, v_a, q_i, k_i, w_i, topk)

        o_b = conformer_conv(conv_in, conv_w[l], conv_b[l], ln_g[l], ln_b[l])

        o_m = memory_attention(q_m, mem, g_mem[l], w_mem_kv[l], g_qm[l], g_km[l])

        gates = jax.nn.sigmoid((gate_logits + b_gate[l]).astype(jnp.float32)).astype(x.dtype)
        gates = gates.reshape(B, S, N_BRANCHES, D)
        merged = (gates[:, :, 0] * (o_a @ w_br_a[l])
                  + gates[:, :, 1] * (o_b @ w_br_b[l])
                  + gates[:, :, 2] * (o_m @ w_br_m[l]))
        x = x + merged @ w_o[l]

        h2 = rmsnorm(x, g_ffn[l]).reshape(B * S, D)
        moe = hier_moe(h2, w_rg[l], b_rg[l], w_re[l], b_re[l], w_up[l], w_down[l])
        x = x + moe.reshape(B, S, D)
    return x


def setup_inputs(seed=0):
    out = dict(first_inputs(seed))
    for name, value in second_inputs(seed + 1).items():
        if name != "x":
            out[name + "_2"] = value
    return out


def reference(
    x, norm_g, ab_w_in, ab_conv_w, ab_conv_b, ab_dt_bias, ab_a_log, ab_d_skip, ab_ssd_norm,
    ab_ig_bias, ab_fg_bias, ab_mlstm_norm, ab_w_out, c_w_in, c_gate_w2, c_gate_b, c_norm,
    c_w_out, ffn_w_up, ffn_conv_w, ffn_conv_b, ffn_w_down, mem_2, g_mix_2, w_in_2, b_gate_2,
    g_qa_2, g_ka_2, g_idx_k_2, conv_w_2, conv_b_2, ln_g_2, ln_b_2, g_mem_2, w_mem_kv_2, g_qm_2,
    g_km_2, w_br_a_2, w_br_b_2, w_br_m_2, w_o_2, g_ffn_2, w_rg_2, b_rg_2, w_re_2, b_re_2,
    w_up_2, w_down_2,
):
    x = first_block(
        x, norm_g, ab_w_in, ab_conv_w, ab_conv_b, ab_dt_bias, ab_a_log, ab_d_skip, ab_ssd_norm,
        ab_ig_bias, ab_fg_bias, ab_mlstm_norm, ab_w_out, c_w_in, c_gate_w2, c_gate_b, c_norm,
        c_w_out, ffn_w_up, ffn_conv_w, ffn_conv_b, ffn_w_down,
    )
    return second_block(
        x, mem_2, g_mix_2, w_in_2, b_gate_2, g_qa_2, g_ka_2, g_idx_k_2, conv_w_2, conv_b_2,
        ln_g_2, ln_b_2, g_mem_2, w_mem_kv_2, g_qm_2, g_km_2, w_br_a_2, w_br_b_2, w_br_m_2,
        w_o_2, g_ffn_2, w_rg_2, b_rg_2, w_re_2, b_re_2, w_up_2, w_down_2,
    )


_drawn_inputs = setup_inputs


def setup_inputs(seed=0):
    import zlib

    import numpy as np

    out = dict(_drawn_inputs(seed))
    spreads = {}
    factors = {'ab_ig_bias': 4.478,
     'g_mix_2': 3.355,
     'b_gate_2': 8.0,
     'g_qa_2': 7.997,
     'g_ka_2': 8.0,
     'g_idx_k_2': 6.44,
     'conv_b_2': 21.535,
     'ln_g_2': 13.498,
     'ln_b_2': 35.763,
     'g_mem_2': 8.0,
     'g_qm_2': 8.0,
     'g_km_2': 8.0,
     'b_rg_2': 64.0,
     'b_re_2': 54.226,
     'g_ffn_2': 5.93}
    for name, (base, spread) in spreads.items():
        noise = np.random.default_rng([zlib.crc32(name.encode()), seed]).standard_normal(out[name].shape)
        drawn = base * np.exp(spread * noise) if base else spread * noise
        out[name] = jnp.asarray(drawn.astype(out[name].dtype))
    for name, factor in factors.items():
        out[name] = (out[name] * factor).astype(out[name].dtype)
    return out
```

```python
from contextlib import ExitStack

import numpy as np

import concourse.bass as bass
from concourse import mybir

F32 = mybir.dt.float32
U32 = mybir.dt.uint32
I32 = mybir.dt.int32
ALU = mybir.AluOpType
ACT = mybir.ActivationFunctionType
AX = mybir.AxisListType

P = 128
T = 512
NT = T // P
D = 1024
KD = D // P
BANK = 512
NBANKS = 8
EPS = 1e-6
BIG = 1e30

SSD_H, SSD_P, SSD_N, SSD_TAPS = 16, 64, 128, 5
SSD_X = D + 2 * 2 * SSD_N
XT = SSD_X // P
PAD = SSD_TAPS // 2
ML_H, ML_D = 8, 128
Z0 = 0
XBC0 = Z0 + D
DT0 = XBC0 + SSD_X
Q0 = DT0 + 2 * SSD_H
K0 = Q0 + D
V0 = K0 + D
O0 = V0 + D
G0 = O0 + D
GLA_H, GLA_DK, GLA_DV, GLA_RANK, GLA_TAU, GLA_L = 4, 128, 256, 16, 16.0, 64
GC = T // GLA_L
FFN = 11 * D // 4
FT = FFN // P
HD = 64
NQ, NKV, NIDX = 8, 2, 8
TOPK = T // 4
CONV_C, CONV_W = 512, 31
CT = CONV_C // P
MEM, MH, MD = 256, 4, 128
MT = MEM // P
NE, EPG, NG, EF = 32, 8, 4, 256
QA0 = 0
KA0 = QA0 + NQ * HD
VA0 = KA0 + NKV * HD
QI0 = VA0 + NKV * HD
KI0 = QI0 + NIDX * HD
WI0 = KI0 + HD
CI0 = WI0 + NIDX
QM0 = CI0 + 2 * CONV_C
GT0 = QM0 + MH * MD
ATT = CI0


class Signal:

    def __init__(self, sem):
        self.sem, self.base = sem, 0

    def __call__(self, n):
        return self.sem, self.base + n

    def close(self, n):
        self.base += n


class Kernel:
    pass


def row(ap):
    return ap.rearrange("(o n) -> o n", o=1)


def everywhere(ap, n):
    return row(ap).to_broadcast([P, n])


def spread(ap, shape):
    return ap.to_broadcast(shape)


def open_kernel(nc, ctx, A):
    k = Kernel()
    k.nc, k.A = nc, A

    seen = {}

    def sb(name, shape, dt=F32, to=ctx):
        seen[name] = seen.get(name, 0) + 1
        name = name if seen[name] == 1 else f"{name}_{seen[name]}"
        return to.enter_context(nc.sbuf_tensor(name, shape, dt))

    def signal(name):
        return Signal(ctx.enter_context(nc.semaphore(name)))

    k.new_count = signal
    k.ps = ctx.enter_context(nc.psum_tensor("ps", [P, NBANKS, BANK], F32))
    k.x = sb("x_tm", [P, NT, D])
    k.h = sb("h_cm", [P, KD, T])
    k.ring = sb("ring", [P, 2, KD * BANK])
    k.ident = sb("ident", [P, P])
    k.ones = sb("ones", [P, P])
    k.tri = [sb("tri_fwd", [P, P]), sb("tri_bwd", [P, P])]
    k.pcol = sb("pcol", [P, 7, P])
    k.brow = sb("brow", [P, 640])
    k.gpost = sb("gpost", [P, D])
    k.stat = sb("stat", [P, 4, 64])
    k.loaded = [signal("w_loaded0"), signal("w_loaded1")]
    k.asked, k.taken, k.next_slot = [0, 0], [0, 0], 0
    k.up_loaded = [signal("up_loaded0"), signal("up_loaded1")]
    k.param_loaded = signal("param_loaded")
    k.acc_ready = signal("acc_ready")
    k.acc_free = signal("acc_free")
    k.mean_ready = signal("mean_ready")
    k.root_ready = signal("root_ready")
    k.norm_ready = signal("norm_ready")
    k.chunk_used = signal("chunk_used")
    k.pa = signal("step_pa")
    k.pb = signal("step_pb")
    k.pc = signal("step_pc")
    k.va = signal("step_va")
    k.vb = signal("step_vb")
    k.vc = signal("step_vc")
    k.vd = signal("step_vd")
    k.da = signal("step_da")
    k.sa = signal("step_sa")
    k.sb = signal("step_sb")
    k.ga = signal("step_ga")
    k.alloc = sb
    return k


def load_weights(k, sp, w, width=None):
    s = sum(k.asked) % 2
    tiles, cols = w.shape[0] // P, w.shape[1]
    dst = k.ring[:, s, 0:tiles * cols].rearrange("p (t n) -> p t n", t=tiles)
    sp.dma_start(dst, w.rearrange("(t p) n -> p t n", p=P)).then_inc(k.loaded[s].sem, 16)
    k.asked[s] += 1


def take_weights(k, pe, tiles, cols):
    s = sum(k.taken) % 2
    k.taken[s] += 1
    pe.wait_ge(k.loaded[s].sem, 16 * k.taken[s])
    return k.ring[:, s, 0:tiles * cols].rearrange("p (t n) -> p t n", t=tiles)



def setup(k, first):
    nc, A = k.nc, k.A
    rows = k.h[:, :, :].rearrange("p a b -> p (a b)")[:, 0:7 * P].rearrange("p (g c) -> p g c", g=7)

    def chunks(ap):
        return ap.rearrange("(r c) -> r c", c=P)

    plan = []
    for n, (i, j) in enumerate(((0, 0), (0, 2), (1, 0), (1, 2))):
        plan.append((0, 8 * n, chunks(A["norm_g"][i, j])))
    plan.append((0, 32, A["ab_conv_w"][0].rearrange("t (r c) -> (t r) c", c=P)))
    plan.append((0, 92, chunks(A["ab_conv_b"][0])))
    plan.append((0, 104, chunks(A["ab_ssd_norm"][0])))
    plan.append((0, 112, chunks(A["ab_mlstm_norm"][0])))
    for i in range(2):
        plan.append((1 + 2 * i, 0, A["ffn_conv_w"][i, 0:2].rearrange("t (r c) -> (t r) c", c=P)))
        plan.append((2 + 2 * i, 0, chunks(A["ffn_conv_w"][i, 2])))
        plan.append((2 + 2 * i, 2 * FT, chunks(A["ffn_conv_b"][i])))
    plan.append((5, 0, chunks(A["c_norm"][0])))
    plan.append((5, 8, A["c_gate_b"][0].rearrange("d (r c) -> (d r) c", c=P)))
    for n, name in enumerate(("g_mix_2", "g_ffn_2", "g_mem_2")):
        plan.append((5, 16 + 8 * n, chunks(A[name][0])))
    for n, name in enumerate(("conv_b_2", "ln_g_2", "ln_b_2")):
        plan.append((5, 40 + 4 * n, chunks(A[name][0])))
    plan.append((6, 0, A["conv_w_2"][0].rearrange("t o (r c) -> (t o r) c", c=P)))
    used = [max(r + ap.shape[0] for g, r, ap in plan if g == n) for n in range(7)]

    broad = [("ab_dt_bias", "a h -> (a h)"), ("ab_fg_bias", "a h -> (a h)"), ("ab_ig_bias", "a h -> (a h)"),
             ("ab_a_log", "a h -> (a h)"), ("ab_d_skip", None), ("g_qa_2", None), ("g_ka_2", None),
             ("g_idx_k_2", None), ("g_qm_2", None), ("g_km_2", None), ("b_rg_2", None), ("b_re_2", None)]
    k.b, at, bplan = {}, 0, []
    for name, how in broad:
        ap = A[name][0] if how is None else A[name][0].rearrange(how)
        n = ap.shape[0]
        if name == "b_rg_2":
            k.router_bias_at = at
        k.b[name] = k.brow[:, at:at + n]
        bplan.append((k.brow[:, at:at + n], everywhere(ap, n)))
        at += n

    with nc.Block(no_gpsimd_drain=True) as block:
        @block.sync
        def _(sp):
            sp.dma_start(k.x[:, :, :], A["x"].rearrange("o (t p) d -> p (o t) d", p=P)).then_inc(k.param_loaded.sem, 16)
            for g, r, ap in plan:
                sp.dma_start(rows[r:r + ap.shape[0], g, :], ap).then_inc(k.param_loaded.sem, 16)
            for dst, src in bplan:
                sp.dma_start(dst, src).then_inc(k.param_loaded.sem, 16)
            for w in first:
                load_weights(k, sp, w)
            sp.wait_ge(*k.param_loaded(16 * (1 + len(plan) + len(bplan))))

        @block.gpsimd
        def _(pool):
            nc.gpsimd.memset(k.ones[:, :], 1.0)
            pool.drain()
            nc.gpsimd.affine_select(out=k.ident[:, :], in_=k.ones[:, :], compare_op=ALU.is_equal, fill=0.0, base=0,
                                    pattern=[[1, P]], channel_multiplier=-1)
            nc.gpsimd.affine_select(out=k.tri[0][:, :], in_=k.ones[:, :], compare_op=ALU.is_ge, fill=0.0, base=0,
                                    pattern=[[1, P]], channel_multiplier=-1)
            nc.gpsimd.affine_select(out=k.tri[1][:, :], in_=k.ones[:, :], compare_op=ALU.is_ge, fill=0.0, base=0,
                                    pattern=[[-1, P]], channel_multiplier=1)
            pool.drain()
    k.param_loaded.close(16 * (1 + len(plan) + len(bplan)))

    with nc.Block(no_gpsimd_drain=True) as block:
        @block.tensor
        def _(pe):
            for g in range(7):
                nc.tensor.transpose(k.ps[:, g, 0:used[g]], rows[0:used[g], g, :],
                                    k.ident[0:used[g], 0:used[g]]).then_inc(k.acc_ready.sem, 1)

        @block.scalar
        def _(act):
            for g in range(7):
                act.wait_ge(*k.acc_ready(g + 1))
                nc.scalar.copy(k.pcol[:, g, 0:used[g]], k.ps[:, g, 0:used[g]])
    k.acc_ready.close(7)



def norm_to_cm(k, src, gain, dst, xn, tiles=NT, after=()):
    nc = k.nc
    ms, root, rstd = (k.stat[:, n, 0:tiles] for n in range(3))
    width = tiles * P

    with nc.Block(no_gpsimd_drain=True) as block:
        @block.sync
        def _(sp):
            for w in after:
                if callable(w):
                    w(sp)
                else:
                    load_weights(k, sp, w)

        @block.vector
        def _(dve):
            for t in range(tiles):
                nc.vector.tensor_tensor_reduce(out=xn[:, t, :], in0=src[:, t, :], in1=src[:, t, :], scale=1.0, scalar=0.0,
                                               op0=ALU.mult, op1=ALU.add, accum_out=ms[:, t:t + 1])
            dve.drain()
            nc.vector.tensor_scalar(ms, ms, 1.0 / D, EPS, ALU.mult, ALU.add).then_inc(k.mean_ready.sem, 1)
            dve.wait_ge(*k.root_ready(1))
            nc.vector.reciprocal(rstd, root)
            dve.drain()
            for t in range(tiles):
                nc.vector.tensor_scalar(xn[:, t, :], src[:, t, :], rstd[:, t:t + 1], None, ALU.mult).then_inc(k.norm_ready.sem, 1)
            for c in range(1, KD, 2):
                dve.wait_ge(*k.acc_ready(c + 1))
                nc.vector.tensor_scalar(dst[:, c, 0:width], k.ps[:, c, 0:width], gain[:, c:c + 1], None, ALU.mult)

        @block.scalar
        def _(act):
            act.wait_ge(*k.mean_ready(1))
            nc.scalar.activation(root, ms, ACT.Sqrt).then_inc(k.root_ready.sem, 1)
            for c in range(0, KD, 2):
                act.wait_ge(*k.acc_ready(c + 1))
                nc.scalar.activation(dst[:, c, 0:width], k.ps[:, c, 0:width], ACT.Copy, scale=gain[:, c:c + 1])

        @block.tensor
        def _(pe):
            pe.wait_ge(*k.norm_ready(tiles))
            for c in range(KD):
                for t in range(tiles):
                    last = nc.tensor.transpose(k.ps[:, c, t * P:(t + 1) * P], xn[:, t, c * P:(c + 1) * P], k.ident[:, :])
                last.then_inc(k.acc_ready.sem, 1)
    k.mean_ready.close(1)
    k.root_ready.close(1)
    k.norm_ready.close(tiles)
    k.acc_ready.close(KD)


def project(k, jobs, src=None, tiles=NT, after=(), cold=False, vector=None):
    nc = k.nc
    src = k.h if src is None else src
    width = tiles * P
    accs = []
    for j, (w, layout, _) in enumerate(jobs):
        accs += [(j, n) for n in range(tiles if layout == "tm" else -(-w.shape[1] // P))]
    last_of = {j: a for a, (j, _) in enumerate(accs)}

    def bank(a):
        j, _ = accs[a]
        cols = jobs[j][0].shape[1]
        if jobs[j][1] == "tm":
            return k.ps[:, a % NBANKS, 0:cols]
        return k.ps[0:min(cols - accs[a][1] * P, P), a % NBANKS, 0:width]

    with nc.Block(no_gpsimd_drain=True) as block:
        @block.sync
        def _(sp):
            for job in jobs[:2] if cold else ():
                load_weights(k, sp, job[0])
            ahead = [(j, job[0]) for j, job in enumerate(jobs)][2:] + [(len(jobs) + n, w) for n, w in enumerate(after)]
            for j, w in ahead:
                sp.wait_ge(*k.acc_ready(last_of[j - 2] + 1))
                load_weights(k, sp, w)

        @block.tensor
        def _(pe):
            for a, (j, n) in enumerate(accs):
                cols = jobs[j][0].shape[1]
                if n == 0:
                    w = take_weights(k, pe, KD, cols)
                if a >= NBANKS:
                    pe.wait_ge(*k.acc_free(a - NBANKS + 1))
                for c in range(KD):
                    if jobs[j][1] == "tm":
                        last = nc.tensor.matmul(bank(a), src[:, c, n * P:(n + 1) * P], w[:, c, :], start=(c == 0), stop=(c == KD - 1))
                    else:
                        last = nc.tensor.matmul(bank(a), w[:, c, n * P:min((n + 1) * P, cols)], src[:, c, 0:width],
                                                start=(c == 0), stop=(c == KD - 1))
                last.then_inc(k.acc_ready.sem, 1)

        @block.scalar
        def _(act):
            for a, (j, n) in enumerate(accs):
                act.wait_ge(*k.acc_ready(a + 1))
                dst, scale = jobs[j][2](n, bank(a))
                b = bank(a)
                if len(dst.shape) == 3:
                    b = b.rearrange("p (a b) -> p a b", a=dst.shape[1])
                nc.scalar.activation(dst, b, ACT.Copy, scale=scale).then_inc(k.acc_free.sem, 1)

        @block.vector
        def _(dve):
            if vector is not None:
                vector(dve)
    k.acc_ready.close(len(accs))
    k.acc_free.close(len(accs))


def out_chunks(w, tiles):
    return [w[r * P:min(r + 4, tiles) * P, :] for r in range(0, tiles, 4)]


def project_out(k, lhs, tiles, w, gain, after=(), scratch=None):
    nc = k.nc
    chunks = out_chunks(w, tiles)
    ss, ms, root, rstd = (k.stat[:, n, 0:NT] for n in range(4))

    def whole(t):
        return k.ps[:, 2 * t:2 * t + 2, :].rearrange("p a b -> p (a b)")

    with nc.Block(no_gpsimd_drain=True) as block:
        @block.sync
        def _(sp):
            if gain is not None:
                sp.dma_start(k.gpost[:, :], everywhere(gain, D)).then_inc(k.param_loaded.sem, 16)
            for c in range(2, len(chunks)):
                sp.wait_ge(*k.chunk_used(c - 1))
                load_weights(k, sp, chunks[c])
            for n, nxt in enumerate(after):
                sp.wait_ge(*k.chunk_used(len(chunks)))
                load_weights(k, sp, nxt)

        @block.tensor
        def _(pe):
            for c, chunk in enumerate(chunks):
                n = chunk.shape[0] // P
                wt = take_weights(k, pe, n, D)
                for t in range(NT):
                    for half in range(2):
                        for r in range(n):
                            kt = 4 * c + r
                            last = nc.tensor.matmul(k.ps[:, 2 * t + half, :], lhs(kt)[:, t * P:(t + 1) * P],
                                                    wt[:, r, half * BANK:(half + 1) * BANK],
                                                    start=(kt == 0), stop=(kt == tiles - 1), skip_group_check=True)
                last.then_inc(k.chunk_used.sem, 1)

        @block.scalar
        def _(act):
            if gain is None:
                return
            act.wait_ge(*k.chunk_used(len(chunks)))
            for t in range(NT):
                nc.scalar.activation(scratch[:, t, :], whole(t), ACT.Square, accum_out=ss[:, t:t + 1]).then_inc(k.mean_ready.sem, 1)
            act.wait_ge(*k.root_ready(1))
            nc.scalar.activation(root, ms, ACT.Sqrt).then_inc(k.mean_ready.sem, 1)

        @block.vector
        def _(dve):
            if gain is None:
                dve.wait_ge(*k.chunk_used(len(chunks)))
                for t in range(NT):
                    nc.vector.tensor_tensor(k.x[:, t, :], k.x[:, t, :], whole(t), ALU.add)
                return
            dve.wait_ge(*k.mean_ready(NT))
            nc.vector.tensor_scalar(ms, ss, 1.0 / D, EPS, ALU.mult, ALU.add).then_inc(k.root_ready.sem, 1)
            dve.wait_ge(*k.mean_ready(NT + 1))
            nc.vector.reciprocal(rstd, root)
            dve.wait_ge(*k.param_loaded(16))
            dve.drain()
            for t in range(NT):
                nc.vector.scalar_tensor_tensor(out=scratch[:, t, :], in0=whole(t), scalar=rstd[:, t:t + 1], in1=k.gpost[:, :],
                                               op0=ALU.mult, op1=ALU.mult)
            dve.drain()
            for t in range(NT):
                nc.vector.tensor_tensor(k.x[:, t, :], k.x[:, t, :], scratch[:, t, :], ALU.add)
    k.chunk_used.close(len(chunks))
    if gain is not None:
        k.param_loaded.close(16)
        k.mean_ready.close(NT + 1)
        k.root_ready.close(1)



DIRS = (0, 1)
GW = SSD_H + ML_H


def decays(k, g, small):
    nc = k.nc
    nd = 2 * SSD_H
    n = nd + 2 * ML_H
    pre, neg, ex, s, s2, poly = (g.work[:, i, :, :] for i in range(6))

    def to(ap):
        return ap.rearrange("p (o n) -> p o n", o=1).to_broadcast([P, NT, ap.shape[1]])

    with nc.Block(no_gpsimd_drain=True) as block:
        @block.vector
        def _(dve):
            nc.vector.tensor_tensor(pre[:, :, 0:nd], small[:, :, 0:nd], to(k.b["ab_dt_bias"]), ALU.add)
            nc.vector.tensor_tensor(pre[:, :, nd:n], small[:, :, nd + 2 * ML_H:nd + 4 * ML_H], to(k.b["ab_fg_bias"]), ALU.add)
            nc.vector.tensor_tensor(g.ig[:, :, :], small[:, :, nd:nd + 2 * ML_H], to(k.b["ab_ig_bias"]), ALU.add)
            dve.drain()
            nc.vector.tensor_scalar(pre[:, :, nd:n], pre[:, :, nd:n], -1.0, None, ALU.mult)
            dve.drain()
            nc.vector.scalar_tensor_tensor(out=neg, in0=pre, scalar=-1.0, in1=pre, op0=ALU.mult, op1=ALU.min).then_inc(k.va.sem, 1)
            dve.wait_ge(*k.sa(1))
            nc.vector.tensor_scalar(s, ex, 2.0, None, ALU.add)
            dve.drain()
            nc.vector.reciprocal(s2, s)
            dve.drain()
            nc.vector.tensor_tensor(s, ex, s2, ALU.mult)
            dve.drain()
            nc.vector.tensor_tensor(s2, s, s, ALU.mult)
            dve.drain()
            nc.vector.tensor_scalar(poly, s2, 1.0 / 17.0, None, ALU.mult)
            for m in (15, 13, 11, 9, 7, 5, 3):
                dve.drain()
                nc.vector.scalar_tensor_tensor(out=poly, in0=poly, scalar=1.0 / m, in1=s2, op0=ALU.add, op1=ALU.mult)
            dve.drain()
            nc.vector.scalar_tensor_tensor(out=poly, in0=poly, scalar=1.0, in1=s, op0=ALU.add, op1=ALU.mult)
            dve.drain()
            nc.vector.tensor_scalar(s, pre, 0.0, None, ALU.max)
            dve.drain()
            nc.vector.scalar_tensor_tensor(out=s, in0=poly, scalar=2.0, in1=s, op0=ALU.mult, op1=ALU.add)
            dve.drain()
            nc.vector.tensor_copy(g.dt[:, :, :], s[:, :, 0:nd])
            dve.wait_ge(*k.sa(2))
            for d in DIRS:
                nc.vector.scalar_tensor_tensor(out=g.ld[:, :, d * GW:d * GW + SSD_H], in0=s[:, :, d * SSD_H:(d + 1) * SSD_H], scalar=-1.0,
                                               in1=to(g.ea[:, d * SSD_H:(d + 1) * SSD_H]), op0=ALU.mult, op1=ALU.mult)
                last = nc.vector.tensor_scalar(g.ld[:, :, d * GW + SSD_H:(d + 1) * GW], s[:, :, nd + d * ML_H:nd + (d + 1) * ML_H],
                                               -1.0, None, ALU.mult)
            dve.drain()
            nc.vector.memset(poly, 0.0).then_inc(k.va.sem, 1)
            dve.wait_ge(*k.acc_ready(1))
            cps = k.ps[:, 0, 0:NT * 4 * GW].rearrange("p (c n) -> p c n", c=NT)
            nc.vector.tensor_copy(g.cum[:, :, :], cps[:, :, 0:2 * GW])
            nc.vector.tensor_copy(g.tot[:, :, :], cps[:, :, 2 * GW:4 * GW])
            dve.drain()
            for d in DIRS:
                nc.vector.tensor_tensor(g.wend[:, :, d * SSD_H:(d + 1) * SSD_H], g.tot[:, :, d * GW:d * GW + SSD_H],
                                        g.cum[:, :, d * GW:d * GW + SSD_H], ALU.subtract)
                nc.vector.tensor_tensor(g.u[:, d, :, :], g.ig[:, :, d * ML_H:(d + 1) * ML_H],
                                        g.cum[:, :, d * GW + SSD_H:(d + 1) * GW], ALU.subtract)
                nc.vector.tensor_copy(g.dec[:, :, d * SSD_H:(d + 1) * SSD_H], g.tot[:, :, d * GW:d * GW + SSD_H])
            dve.drain()
            nc.vector.memset(poly, 0.0).then_inc(k.va.sem, 1)
            dve.wait_ge(*k.sa(3))
            nc.vector.tensor_tensor(g.wend[:, :, :], g.wend[:, :, :], g.dt[:, :, :], ALU.mult)

        @block.scalar
        def _(act):
            act.wait_ge(*k.va(1))
            nc.scalar.activation(ex, neg, ACT.Exp).then_inc(k.sa.sem, 1)
            nc.scalar.activation(g.ea[:, :], k.b["ab_a_log"], ACT.Exp).then_inc(k.sa.sem, 1)
            act.wait_ge(*k.va(3))
            nc.scalar.activation(g.dec[:, :, :], g.dec[:, :, :], ACT.Exp)
            nc.scalar.activation(g.wend[:, :, :], g.wend[:, :, :], ACT.Exp).then_inc(k.sa.sem, 1)

        @block.tensor
        def _(pe):
            pe.wait_ge(*k.va(2))
            for c in range(NT):
                at = c * 4 * GW
                for d in DIRS:
                    nc.tensor.matmul(k.ps[:, 0, at + d * GW:at + (d + 1) * GW], k.tri[d][:, :], g.ld[:, c, d * GW:(d + 1) * GW],
                                     start=True, stop=True, skip_group_check=True)
                last = nc.tensor.matmul(k.ps[:, 0, at + 2 * GW:at + 4 * GW], k.ones[:, :], g.ld[:, c, :],
                                        start=True, stop=True, skip_group_check=True)
            last.then_inc(k.acc_ready.sem, 1)
    k.va.close(3)
    k.sa.close(3)
    k.acc_ready.close(1)



def ssd_conv(k, raw, out):
    nc = k.nc
    tap, bias = k.pcol[:, 0, 32:92], k.pcol[:, 0, 92:104]
    with nc.Block(no_gpsimd_drain=True) as block:
        @block.vector
        def _(dve):
            for first in range(0, XT, 4):
                tiles = range(first, first + 4)
                for j in tiles:
                    nc.vector.tensor_scalar(out[:, j, :], raw[:, j, 0:T], tap[:, j:j + 1], bias[:, j:j + 1], ALU.mult, ALU.add)
                dve.drain()
                for i in range(1, SSD_TAPS):
                    for j in tiles:
                        last = nc.vector.scalar_tensor_tensor(out=out[:, j, :], in0=raw[:, j, i:i + T], scalar=tap[:, i * XT + j:i * XT + j + 1],
                                                              in1=out[:, j, :], op0=ALU.mult, op1=ALU.add)
                    if i < SSD_TAPS - 1:
                        dve.drain()
                last.then_inc(k.va.sem, 1)

        @block.scalar
        def _(act):
            for j in range(XT):
                act.wait_ge(*k.va(j // 4 + 1))
                nc.scalar.activation(out[:, j, :], out[:, j, :], ACT.Silu)
    k.va.close(XT // 4)


def ssd_turn(k, xbc, x_tm, b_tm, cb):
    nc = k.nc
    with nc.Block(no_gpsimd_drain=True) as block:
        @block.tensor
        def _(pe):
            for c in range(NT):
                if c >= 2:
                    pe.wait_ge(*k.sa(c - 1))
                b = 3 * (c % 2)
                for j in range(10):
                    last = nc.tensor.transpose(k.ps[:, b + j // 4, (j % 4) * P:(j % 4 + 1) * P], xbc[:, j, c * P:(c + 1) * P], k.ident[:, :])
                last.then_inc(k.acc_ready.sem, 1)
            for grp in range(2):
                for c in range(NT):
                    last = nc.tensor.matmul(k.ps[:, 6 + grp, c * P:(c + 1) * P], xbc[:, 8 + grp, c * P:(c + 1) * P],
                                            xbc[:, 10 + grp, c * P:(c + 1) * P], start=True, stop=True, skip_group_check=True)
                last.then_inc(k.acc_ready.sem, 1)

        @block.scalar
        def _(act):
            for c in range(NT):
                b = 3 * (c % 2)
                act.wait_ge(*k.acc_ready(c + 1))
                nc.scalar.copy(b_tm[:, c, :], k.ps[:, b + 2, 0:2 * P])
                nc.scalar.copy(x_tm[:, c, :], k.ps[:, b:b + 2, :].rearrange("p a b -> p (a b)")).then_inc(k.sa.sem, 1)

        @block.vector
        def _(dve):
            for grp in range(2):
                dve.wait_ge(*k.acc_ready(NT + grp + 1))
                for d in DIRS:
                    nc.vector.tensor_tensor(cb[:, d, grp, :].rearrange("p (c l) -> p c l", c=NT),
                                            k.ps[:, 6 + grp, :].rearrange("p (c l) -> p c l", c=NT),
                                            k.tri[d][:, :].rearrange("p (o l) -> p o l", o=1).to_broadcast([P, NT, P]), ALU.mult)
    k.sa.close(NT)
    k.acc_ready.close(NT + 2)


def ssd_states(k, g, x_tm, b_tm, hst, xw):
    nc = k.nc
    steps = [(0, c) for c in range(NT - 1)] + [(1, c) for c in range(NT - 1, 0, -1)]
    with nc.Block(no_gpsimd_drain=True) as block:
        @block.vector
        def _(dve):
            nc.vector.memset(hst[:, 0, 0, :], 0.0)
            nc.vector.memset(hst[:, 1, NT - 1, :], 0.0)

            def weigh(n):
                d, c = steps[n]
                if n >= 2:
                    dve.wait_ge(*k.acc_ready(n - 1))
                nc.vector.tensor_tensor(xw[:, n % 2, :].rearrange("p (h e) -> p h e", h=SSD_H),
                                        x_tm[:, c, :].rearrange("p (h e) -> p h e", h=SSD_H),
                                        g.wend[:, c, d * SSD_H:(d + 1) * SSD_H].rearrange("p (h o) -> p h o", o=1).to_broadcast([P, SSD_H, SSD_P]),
                                        ALU.mult).then_inc(k.va.sem, 1)
            weigh(0)
            weigh(1)
            for n, (d, c) in enumerate(steps):
                nxt = c + 1 if d == 0 else c - 1
                dec = g.dec[:, c, d * SSD_H:(d + 1) * SSD_H].rearrange("p (h o) -> p h o", o=1).to_broadcast([P, SSD_H, SSD_P])
                dve.drain()
                nc.vector.tensor_tensor(hst[:, d, nxt, :].rearrange("p (h e) -> p h e", h=SSD_H),
                                        hst[:, d, c, :].rearrange("p (h e) -> p h e", h=SSD_H), dec, ALU.mult)
                dve.wait_ge(*k.acc_ready(n + 1))
                dve.drain()
                b = 2 * (n % 4)
                nc.vector.tensor_tensor(hst[:, d, nxt, :], hst[:, d, nxt, :], k.ps[:, b:b + 2, :].rearrange("p a b -> p (a b)"),
                                        ALU.add).then_inc(k.vb.sem, 1)
                if n + 2 < len(steps):
                    weigh(n + 2)

        @block.tensor
        def _(pe):
            for n, (d, c) in enumerate(steps):
                pe.wait_ge(*k.va(n + 1))
                if n >= 4:
                    pe.wait_ge(*k.vb(n - 3))
                for grp in range(2):
                    last = nc.tensor.matmul(k.ps[:, 2 * (n % 4) + grp, :], b_tm[:, c, grp * P:(grp + 1) * P],
                                            xw[:, n % 2, grp * BANK:(grp + 1) * BANK], start=True, stop=True)
                last.then_inc(k.acc_ready.sem, 1)
    k.va.close(len(steps))
    k.vb.close(len(steps))
    k.acc_ready.close(len(steps))


def ssd_mix(k, g, xbc, x_tm, cb, hst, y_tm, buf):
    nc = k.nc
    units = [(h, d) for h in range(SSD_H) for d in DIRS]
    arg, gg, w, ec, ce = buf
    half = SSD_H // 2

    def col(h, d):
        return d * GW + h

    with nc.Block(no_gpsimd_drain=True) as block:
        @block.tensor
        def _(pe):
            def sums(n):
                h, d = units[n]
                if n >= 2:
                    pe.wait_ge(*k.sa(n - 1))
                for c in range(NT):
                    last = nc.tensor.matmul(k.ps[:, 4 + n % 2, c * P:(c + 1) * P], spread(g.ld[:, c, col(h, d):col(h, d) + 1], [P, P]),
                                            k.tri[d][:, :], start=True, stop=True, skip_group_check=True)
                last.then_inc(k.pa.sem, 1)

            def mix(h):
                if h == half:
                    pe.wait_ge(*k.vc(1))
                pe.wait_ge(*k.vb(2 * h + 2))
                pe.wait_ge(*k.ga(2 * h + 2))
                at = h * SSD_P
                for c in range(NT):
                    out = k.ps[:, c, (h % half) * SSD_P:(h % half + 1) * SSD_P]
                    tok = slice(c * P, (c + 1) * P)
                    for d in DIRS:
                        nc.tensor.matmul(out, w[:, d, tok], x_tm[:, c, at:at + SSD_P], start=(d == 0), stop=False, skip_group_check=True)
                    for d in DIRS:
                        last = nc.tensor.matmul(out, ce[:, d, tok], hst[:, d, c, at:at + SSD_P], start=False, stop=(d == 1), skip_group_check=True)
                last.then_inc(k.pb.sem, 1)

            sums(0)
            sums(1)
            for h in range(SSD_H):
                if h + 1 < SSD_H:
                    sums(2 * h + 2)
                    sums(2 * h + 3)
                mix(h)

        @block.vector
        def _(dve):
            def args(n):
                h, d = units[n]
                dve.wait_ge(*k.pa(n + 1))
                if n >= 2:
                    dve.wait_ge(*k.sb(n - 1))
                for c in range(NT):
                    tok = slice(c * P, (c + 1) * P)
                    last = nc.vector.tensor_scalar(arg[:, n % 2, tok], k.ps[:, 4 + n % 2, tok], g.cum[:, c, col(h, d):col(h, d) + 1], 0.0,
                                                   ALU.subtract, ALU.min)
                last.then_inc(k.va.sem, 1)

            def weights(n):
                h, d = units[n]
                dve.wait_ge(*k.sb(n + 1))
                if n >= 2:
                    dve.wait_ge(*k.pb(n // 2))
                for c in range(NT):
                    tok = slice(c * P, (c + 1) * P)
                    last = nc.vector.scalar_tensor_tensor(out=w[:, d, tok], in0=gg[:, n % 2, tok], scalar=g.dt[:, c, d * SSD_H + h:d * SSD_H + h + 1],
                                                          in1=cb[:, d, h // half, tok], op0=ALU.mult, op1=ALU.mult)
                last.then_inc(k.vb.sem, 1)

            def read_out(part):
                dve.wait_ge(*k.pb(half * (part + 1)))
                for c in range(NT):
                    last = nc.vector.tensor_copy(y_tm[:, c, part * BANK:(part + 1) * BANK], k.ps[:, c, :])
                last.then_inc(k.vc.sem, 1)

            args(0)
            for n in range(len(units)):
                if n + 1 < len(units):
                    args(n + 1)
                if n == 2 * half:
                    read_out(0)
                weights(n)
            read_out(1)

        @block.scalar
        def _(act):
            for n, (h, d) in enumerate(units):
                act.wait_ge(*k.va(n + 1))
                if n >= 2:
                    act.wait_ge(*k.ga(n - 1))
                nc.scalar.activation(ec[:, n % 2, :], k.ps[:, 4 + n % 2, :], ACT.Exp).then_inc(k.sa.sem, 1)
                if n >= 2:
                    act.wait_ge(*k.vb(n - 1))
                nc.scalar.activation(gg[:, n % 2, :], arg[:, n % 2, :], ACT.Exp).then_inc(k.sb.sem, 1)

        @block.gpsimd
        def _(pool):
            for n, (h, d) in enumerate(units):
                pool.wait_ge(*k.sa(n + 1))
                if n >= 2:
                    pool.wait_ge(*k.pb(n // 2))
                nc.gpsimd.tensor_tensor(ce[:, d, :], xbc[:, 10 + h // half, :], ec[:, n % 2, :], ALU.mult).then_inc(k.ga.sem, 1)
            pool.drain()
    n = len(units)
    k.pa.close(n)
    k.pb.close(SSD_H)
    k.va.close(n)
    k.vb.close(n)
    k.vc.close(2)
    k.sa.close(n)
    k.sb.close(n)
    k.ga.close(n)


def ssd_finish(k, y_tm, x_tm, z_tm, ycm, work, after=()):
    nc = k.nc
    G = 2
    W = D // G
    ms, root, rstd = (k.stat[:, n, 0:NT * G].rearrange("p (t g) -> p t g", g=G) for n in range(3))
    gain = k.pcol[:, 0, 104:112]
    skip = k.b["ab_d_skip"].rearrange("p (h o) -> p h o", o=1).to_broadcast([P, SSD_H, SSD_P])
    with nc.Block(no_gpsimd_drain=True) as block:
        @block.sync
        def _(sp):
            for w in after:
                load_weights(k, sp, w)

        @block.scalar
        def _(act):
            for t in range(NT):
                nc.scalar.activation(z_tm[:, t, :], z_tm[:, t, :], ACT.Silu).then_inc(k.sa.sem, 1)
            act.wait_ge(*k.mean_ready(1))
            nc.scalar.activation(root, ms, ACT.Sqrt).then_inc(k.root_ready.sem, 1)
            for c in range(KD):
                act.wait_ge(*k.acc_ready(c + 1))
                nc.scalar.activation(ycm[:, c, :], k.ps[:, c, :], ACT.Copy, scale=gain[:, c:c + 1])

        @block.vector
        def _(dve):
            for t in range(NT):
                nc.vector.tensor_tensor(work[:, t, :].rearrange("p (h e) -> p h e", h=SSD_H), x_tm[:, t, :].rearrange("p (h e) -> p h e", h=SSD_H),
                                        skip, ALU.mult)
            dve.drain()
            for t in range(NT):
                nc.vector.tensor_tensor(y_tm[:, t, :], y_tm[:, t, :], work[:, t, :], ALU.add)
            dve.drain()
            for t in range(NT):
                dve.wait_ge(*k.sa(t + 1))
                nc.vector.tensor_tensor(y_tm[:, t, :], y_tm[:, t, :], z_tm[:, t, :], ALU.mult)
            dve.drain()
            for t in range(NT):
                for grp in range(G):
                    part = y_tm[:, t, grp * W:(grp + 1) * W]
                    nc.vector.tensor_tensor_reduce(out=work[:, t, grp * W:(grp + 1) * W], in0=part, in1=part, scale=1.0, scalar=0.0,
                                                   op0=ALU.mult, op1=ALU.add, accum_out=ms[:, t, grp:grp + 1])
            dve.drain()
            nc.vector.tensor_scalar(ms, ms, 1.0 / W, EPS, ALU.mult, ALU.add).then_inc(k.mean_ready.sem, 1)
            dve.wait_ge(*k.root_ready(1))
            nc.vector.reciprocal(rstd, root)
            dve.drain()
            for t in range(NT):
                for grp in range(G):
                    nc.vector.tensor_scalar(work[:, t, grp * W:(grp + 1) * W], y_tm[:, t, grp * W:(grp + 1) * W], rstd[:, t, grp:grp + 1],
                                            None, ALU.mult).then_inc(k.norm_ready.sem, 1)

        @block.tensor
        def _(pe):
            pe.wait_ge(*k.norm_ready(NT * G))
            for c in range(KD):
                for t in range(NT):
                    last = nc.tensor.transpose(k.ps[:, c, t * P:(t + 1) * P], work[:, t, c * P:(c + 1) * P], k.ident[:, :])
                last.then_inc(k.acc_ready.sem, 1)
    k.sa.close(NT)
    k.mean_ready.close(1)
    k.root_ready.close(1)
    k.norm_ready.close(NT * G)
    k.acc_ready.close(KD)



MW = ML_D + 1


def mlstm_gates(k, g, r):
    nc = k.nc
    H = ML_H
    u_row, cm, ms_row, tot, mx, so = r.u_row, r.cm, r.ms_row, r.tot, r.mx, r.so

    def at_chunks(ap):
        return ap.rearrange("h d (c l) -> h d c l", c=NT)

    def each(ap):
        return ap.rearrange("h d (c o) -> h d c o", o=1).to_broadcast([H, 2, NT, P])

    with nc.Block(no_gpsimd_drain=True) as block:
        @block.gpsimd
        def _(pool):
            nc.gpsimd.memset(r.restart[:, :, :], 0.0)
            pool.drain()
            for c in range(NT):
                nc.gpsimd.memset(r.restart[:, 0, c * P:c * P + 1], -3e38)
                nc.gpsimd.memset(r.restart[:, 1, c * P + P - 1:c * P + P], -3e38)
            pool.drain()
            nc.gpsimd.memset(ms_row[:, :, :], 0.0).then_inc(k.ga.sem, 1)
            pool.drain()

        @block.tensor
        def _(pe):
            for d in DIRS:
                for c in range(NT):
                    last = nc.tensor.transpose(k.ps[0:H, d, c * P:(c + 1) * P], g.u[:, d, c, :], k.ident[:, :])
            last.then_inc(k.acc_ready.sem, 1)
            for d in DIRS:
                for c in range(NT):
                    last = nc.tensor.matmul(k.ps[0:H, 2, 4 * d + c:4 * d + c + 1], g.ld[:, c, d * GW + SSD_H:(d + 1) * GW], k.ones[:, 0:1],
                                            start=True, stop=True, skip_group_check=True)
            last.then_inc(k.acc_ready.sem, 1)
            pe.wait_ge(*k.vb(1))
            for d in DIRS:
                for c in range(NT):
                    last = nc.tensor.transpose(k.ps[:, 3, (d * NT + c) * H:(d * NT + c + 1) * H], r.nm[:, d, c * P:(c + 1) * P], k.ident[0:H, 0:H])
            last.then_inc(k.acc_ready.sem, 1)
            pe.wait_ge(*k.sa(1))
            for d in DIRS:
                for c in range(NT):
                    last = nc.tensor.transpose(k.ps[:, 4, (d * NT + c) * H:(d * NT + c + 1) * H], r.ew_row[:, d, c * P:(c + 1) * P], k.ident[0:H, 0:H])
            pe.wait_ge(*k.vc(1))
            nc.tensor.matmul(k.ps[:, 5, 0:2 * H * 2 * NT], k.ones[0:H, :], r.diag[:, :], start=True, stop=True).then_inc(k.acc_ready.sem, 1)

        @block.vector
        def _(dve):
            dve.wait_ge(*k.acc_ready(1))
            nc.vector.tensor_copy(u_row[:, :, :], k.ps[0:H, 0:2, :])
            dve.wait_ge(*k.acc_ready(2))
            nc.vector.tensor_copy(tot[:, :, :], k.ps[0:H, 2, 0:8].rearrange("h (d c) -> h d c", d=2))
            dve.wait_ge(*k.ga(1))
            dve.drain()
            nc.vector.tensor_tensor_scan(cm[:, 0, :], r.restart[:, 0, :], u_row[:, 0, :], 0.0, ALU.add, ALU.max)
            nc.vector.tensor_tensor_scan(cm[:, 1, :][:, ::-1], r.restart[:, 1, :][:, ::-1], u_row[:, 1, :][:, ::-1], 0.0, ALU.add, ALU.max)
            dve.drain()
            nc.vector.tensor_copy(r.umax[:, 0, :], at_chunks(cm[:, :, :])[:, 0, :, P - 1])
            nc.vector.tensor_copy(r.umax[:, 1, :], at_chunks(cm[:, :, :])[:, 1, :, 0])
            dve.drain()
            for n in range(NT):
                for d in DIRS:
                    c = n if d == 0 else NT - 1 - n
                    nc.vector.tensor_tensor(mx[:, d, c:c + 1], ms_row[:, d, c:c + 1], r.umax[:, d, c:c + 1], ALU.max)
                dve.drain()
                if n < NT - 1:
                    for d in DIRS:
                        c = n if d == 0 else NT - 1 - n
                        nxt = c + 1 if d == 0 else c - 1
                        nc.vector.tensor_tensor(ms_row[:, d, nxt:nxt + 1], mx[:, d, c:c + 1], tot[:, d, c:c + 1], ALU.add)
                    dve.drain()
            nc.vector.tensor_tensor(at_chunks(r.nm[:, :, :]), at_chunks(cm[:, :, :]), each(ms_row[:, :, :]), ALU.max)
            nc.vector.tensor_tensor(so[:, 0, :, :], ms_row[:, :, :], mx[:, :, :], ALU.subtract)
            nc.vector.tensor_tensor(so[:, 1, :, :], r.umax[:, :, :], mx[:, :, :], ALU.subtract)
            dve.drain()
            nc.vector.tensor_tensor(at_chunks(r.si[:, :, :]), each(ms_row[:, :, :]), at_chunks(r.nm[:, :, :]), ALU.subtract)
            nc.vector.tensor_tensor(at_chunks(r.ew_row[:, :, :]), at_chunks(u_row[:, :, :]), each(r.umax[:, :, :]), ALU.subtract)
            nc.vector.tensor_scalar(r.nm[:, :, :], r.nm[:, :, :], -1.0, None, ALU.mult)
            dve.drain()
            nc.vector.memset(r.bar[:, 0:1], 0.0).then_inc(k.vb.sem, 1)
            dve.wait_ge(*k.sa(2))
            nc.vector.tensor_tensor(r.diag[:, :].rearrange("h (n q) -> h n q", n=H), spread(so[:, :, :, :].rearrange("h s d c -> h (s d c)").rearrange("h (o q) -> h o q", o=1), [H, H, 4 * NT]),
                                    spread(k.ident[0:H, 0:H].rearrange("h (n o) -> h n o", o=1), [H, H, 4 * NT]), ALU.mult).then_inc(k.vc.sem, 1)
            dve.wait_ge(*k.acc_ready(3))
            for d in DIRS:
                nc.vector.tensor_tensor(r.floor[:, d, :, :], k.ps[:, 3, d * NT * H:(d + 1) * NT * H].rearrange("p (c h) -> p c h", c=NT),
                                        g.cum[:, :, d * GW + SSD_H:(d + 1) * GW], ALU.subtract)
            dve.drain()
            nc.vector.memset(r.bar[:, 1:2], 0.0).then_inc(k.vc.sem, 1)
            dve.wait_ge(*k.acc_ready(4))
            nc.vector.tensor_copy(r.ew[:, :, :, :].rearrange("p d c h -> p (d c h)"), k.ps[:, 4, 0:2 * NT * H])
            spr = k.ps[:, 5, 0:H * 4 * NT].rearrange("p (h s d c) -> p h s d c", h=H, s=2, d=2)
            for d in DIRS:
                nc.vector.tensor_copy(r.sold[:, d, :, :].rearrange("p c h -> p h c"), spr[:, :, 0, d, :])
                nc.vector.tensor_copy(r.sloc[:, d, :, :].rearrange("p c h -> p h c"), spr[:, :, 1, d, :])

        @block.scalar
        def _(act):
            act.wait_ge(*k.vb(1))
            nc.scalar.activation(r.ew_row[:, :, :], r.ew_row[:, :, :], ACT.Exp).then_inc(k.sa.sem, 1)
            nc.scalar.activation(so[:, :, :, :], so[:, :, :, :], ACT.Exp).then_inc(k.sa.sem, 1)
            nc.scalar.activation(r.si[:, :, :], r.si[:, :, :], ACT.Exp)
            act.wait_ge(*k.vc(2))
            nc.scalar.activation(r.floor[:, :, :, :], r.floor[:, :, :, :], ACT.Exp)
    k.ga.close(1)
    k.acc_ready.close(4)
    k.vb.close(1)
    k.vc.close(2)
    k.sa.close(2)


def mlstm_states(k, r, k_cm, v, cst, kw):
    nc = k.nc
    H = ML_H
    steps = [(0, c) for c in range(NT - 1)] + [(1, c) for c in range(NT - 1, 0, -1)]

    def bank(h):
        return k.ps[:, 4 + h // 2, (h % 2) * 256:(h % 2) * 256 + MW]

    def banks():
        return k.ps[:, 4:8, :].rearrange("p b (e w) -> p (b e) w", e=2)[:, :, 0:MW]

    def per_head(ap):
        return ap.rearrange("p (h o) -> p h o", o=1).to_broadcast([P, H, MW])

    with nc.Block(no_gpsimd_drain=True) as block:
        @block.tensor
        def _(pe):
            def turn(n):
                d, c = steps[n]
                if n >= 2:
                    pe.wait_ge(*k.va(n - 1))
                for h in range(H):
                    last = nc.tensor.transpose(k.ps[:, 2 * (n % 2) + h // 4, (h % 4) * P:(h % 4 + 1) * P], k_cm[:, h, c * P:(c + 1) * P], k.ident[:, :])
                last.then_inc(k.pa.sem, 1)

            turn(0)
            for n, (d, c) in enumerate(steps):
                if n + 1 < len(steps):
                    turn(n + 1)
                pe.wait_ge(*k.va(n + 1))
                if n >= 1:
                    pe.wait_ge(*k.vb(n))
                for h in range(H):
                    last = nc.tensor.matmul(bank(h), kw[:, n % 2, h * P:(h + 1) * P], v[:, c, h, :], start=True, stop=True, skip_group_check=True)
                last.then_inc(k.pb.sem, 1)

        @block.vector
        def _(dve):
            nc.vector.memset(cst[:, 0, 0, :, :], 0.0)
            nc.vector.memset(cst[:, 1, NT - 1, :, :], 0.0)
            dve.drain()

            def weigh(n):
                d, c = steps[n]
                dve.wait_ge(*k.pa(n + 1))
                if n >= 2:
                    dve.wait_ge(*k.pb(n - 1))
                b = 2 * (n % 2)
                nc.vector.tensor_tensor(kw[:, n % 2, :].rearrange("p (h e) -> p h e", h=H), k.ps[:, b:b + 2, :].rearrange("p b (h e) -> p (b h) e", e=P),
                                        r.ew[:, d, c, :].rearrange("p (h o) -> p h o", o=1).to_broadcast([P, H, P]), ALU.mult).then_inc(k.va.sem, 1)

            weigh(0)
            for n, (d, c) in enumerate(steps):
                if n + 1 < len(steps):
                    weigh(n + 1)
                nxt = c + 1 if d == 0 else c - 1
                dve.wait_ge(*k.pb(n + 1))
                nc.vector.tensor_tensor(r.own[:, :, :], banks(), per_head(r.sloc[:, d, c, :]), ALU.mult).then_inc(k.vb.sem, 1)
                nc.vector.tensor_tensor(cst[:, d, nxt, :, :], cst[:, d, c, :, :], per_head(r.sold[:, d, c, :]), ALU.mult)
                dve.drain()
                nc.vector.tensor_tensor(cst[:, d, nxt, :, :], cst[:, d, nxt, :, :], r.own[:, :, :], ALU.add)
                dve.drain()
    n = len(steps)
    for s in (k.pa, k.pb, k.va, k.vb):
        s.close(n)


def mlstm_mix(k, g, r, q_cm, k_cm, v, cst, hm, buf):
    nc = k.nc
    H = ML_H
    units = [(h, d) for h in range(H) for d in DIRS]
    arg, gg, w, qs, qk = (buf[:, n, :, :] for n in range(5))
    NUM, SUMS, SI, QK = 0, 4, 5, 6

    def num(c, d):
        return k.ps[:, NUM + c, d * 256:d * 256 + MW]

    with nc.Block(no_gpsimd_drain=True) as block:
        @block.tensor
        def _(pe):
            def scores(h):
                if h >= 1:
                    pe.wait_ge(*k.vc(h))
                for c in range(NT):
                    tok = slice(c * P, (c + 1) * P)
                    last = nc.tensor.matmul(k.ps[:, QK, tok], k_cm[:, h, tok], q_cm[:, h, tok], start=True, stop=True, skip_group_check=True)
                last.then_inc(k.pc.sem, 1)

            def rows(n):
                h, d = units[n]
                if n >= 1:
                    pe.wait_ge(*k.va(n))
                pick = spread(k.ident[0:H, h:h + 1], [H, P])
                nc.tensor.matmul(k.ps[:, SUMS, :], pick, r.nm[:, d, :], start=True, stop=True)
                if n >= 1:
                    pe.wait_ge(*k.vd(n))
                nc.tensor.matmul(k.ps[:, SI, :], pick, r.si[:, d, :], start=True, stop=True).then_inc(k.pa.sem, 1)

            def mix(n):
                h, d = units[n]
                pe.wait_ge(*k.vb(n + 1))
                pe.wait_ge(*k.vd(n + 1))
                if h >= 1:
                    pe.wait_ge(*k.da(h))
                for c in range(NT):
                    tok = slice(c * P, (c + 1) * P)
                    nc.tensor.matmul(num(c, d), w[:, d, tok], v[:, c, h, :], start=True, stop=False, skip_group_check=True)
                    last = nc.tensor.matmul(num(c, d), qs[:, d, tok], cst[:, d, c, h, :], start=False, stop=True, skip_group_check=True)
                last.then_inc(k.pb.sem, 1)

            scores(0)
            rows(0)
            for n, (h, d) in enumerate(units):
                if n + 1 < len(units):
                    if d == 1:
                        scores(h + 1)
                    rows(n + 1)
                mix(n)

        @block.vector
        def _(dve):
            def prepare(n):
                h, d = units[n]
                if d == 0:
                    dve.wait_ge(*k.pc(h + 1))
                    for e in DIRS:
                        last = nc.vector.tensor_tensor(qk[:, e, :].rearrange("p (c l) -> p c l", c=NT), k.ps[:, QK, :].rearrange("p (c l) -> p c l", c=NT),
                                                       spread(k.tri[e][:, :].rearrange("p (o l) -> p o l", o=1), [P, NT, P]), ALU.mult)
                    last.then_inc(k.vc.sem, 1)
                dve.wait_ge(*k.pa(n + 1))
                if n >= 2:
                    dve.wait_ge(*k.sa(n - 1))
                for c in range(NT):
                    tok = slice(c * P, (c + 1) * P)
                    last = nc.vector.tensor_scalar(arg[:, n % 2, tok], k.ps[:, SUMS, tok], g.u[:, d, c, h:h + 1], 0.0, ALU.add, ALU.min)
                last.then_inc(k.va.sem, 1)
                if n >= 2:
                    dve.wait_ge(*k.pb(n - 1))
                nc.vector.tensor_tensor(qs[:, d, :], q_cm[:, h, :], k.ps[:, SI, :], ALU.mult).then_inc(k.vd.sem, 1)

            def weights(n):
                h, d = units[n]
                dve.wait_ge(*k.sa(n + 1))
                if d == 0:
                    dve.drain()
                nc.vector.tensor_tensor(w[:, d, :], gg[:, n % 2, :], qk[:, d, :], ALU.mult).then_inc(k.vb.sem, 1)

            def read_out(h):
                dve.wait_ge(*k.sb(h + 1))
                nc.vector.tensor_tensor(r.den[:, :, :], r.den[:, :, :], r.floor[:, :, :, h].rearrange("p d c -> p c d"), ALU.max)
                dve.drain()
                nc.vector.reciprocal(r.rden[:, :, :], r.den[:, :, :])
                dve.drain()
                at = slice(h * ML_D, (h + 1) * ML_D)
                for c in range(NT):
                    nc.vector.tensor_scalar(hm[:, c, at], num(c, 0)[:, 0:ML_D], r.rden[:, c, 0:1], None, ALU.mult)
                dve.drain()
                for c in range(NT):
                    last = nc.vector.scalar_tensor_tensor(out=hm[:, c, at], in0=num(c, 1)[:, 0:ML_D], scalar=r.rden[:, c, 1:2], in1=hm[:, c, at],
                                                          op0=ALU.mult, op1=ALU.add)
                last.then_inc(k.da.sem, 1)

            prepare(0)
            for n, (h, d) in enumerate(units):
                weights(n)
                if n + 1 < len(units):
                    if d == 1:
                        dve.drain()
                    prepare(n + 1)
                if d == 1:
                    read_out(h)

        @block.scalar
        def _(act):
            for n, (h, d) in enumerate(units):
                act.wait_ge(*k.va(n + 1))
                if n >= 2:
                    act.wait_ge(*k.vb(n - 1))
                nc.scalar.activation(gg[:, n % 2, :], arg[:, n % 2, :], ACT.Exp).then_inc(k.sa.sem, 1)
                if d == 1:
                    act.wait_ge(*k.pb(n + 1))
                    if h >= 1:
                        act.wait_ge(*k.da(h))
                    nc.scalar.activation(r.den[:, :, :], k.ps[:, NUM:NUM + NT, :].rearrange("p c (d w) -> p c d w", d=2)[:, :, :, ML_D],
                                         ACT.Abs).then_inc(k.sb.sem, 1)
    n = len(units)
    for s in (k.pa, k.pb, k.va, k.vb, k.vd, k.sa):
        s.close(n)
    for s in (k.pc, k.vc, k.da, k.sb):
        s.close(H)


def gated_norm(k, y_tm, o_tm, heads, gain, dst, work, gate, first_gate, after=()):
    nc = k.nc
    W = D // heads
    ms, root, rstd = (k.stat[:, n, 0:NT * heads].rearrange("p (t h) -> p t h", h=heads) for n in range(3))

    def per_head(ap):
        return ap.rearrange("p t (h e) -> p t h e", h=heads)

    with nc.Block(no_gpsimd_drain=True) as block:
        @block.sync
        def _(sp):
            for w in after:
                load_weights(k, sp, w)

        @block.scalar
        def _(act):
            for t in range(NT):
                nc.scalar.activation(o_tm[:, t, :], o_tm[:, t, :], gate).then_inc(k.sa.sem, 1)
            act.wait_ge(*k.mean_ready(1))
            nc.scalar.activation(root, ms, ACT.Sqrt).then_inc(k.root_ready.sem, 1)
            for c in range(KD):
                act.wait_ge(*k.acc_ready(c + 1))
                nc.scalar.activation(dst[:, c, :], k.ps[:, c, :], ACT.Copy, scale=gain[:, c:c + 1])

        @block.vector
        def _(dve):
            if first_gate:
                for t in range(NT):
                    dve.wait_ge(*k.sa(t + 1))
                    nc.vector.tensor_tensor(y_tm[:, t, :], y_tm[:, t, :], o_tm[:, t, :], ALU.mult)
                dve.drain()
            for t in range(NT):
                nc.vector.tensor_tensor(work[:, t, :], y_tm[:, t, :], y_tm[:, t, :], ALU.mult)
            dve.drain()
            nc.vector.tensor_reduce(ms, per_head(work[:, :, :]), AX.X, ALU.add)
            dve.drain()
            nc.vector.tensor_scalar(ms, ms, 1.0 / W, EPS, ALU.mult, ALU.add).then_inc(k.mean_ready.sem, 1)
            dve.wait_ge(*k.root_ready(1))
            nc.vector.reciprocal(rstd, root)
            dve.drain()
            for t in range(NT):
                last = nc.vector.tensor_tensor(work[:, t, :].rearrange("p (h e) -> p h e", h=heads), y_tm[:, t, :].rearrange("p (h e) -> p h e", h=heads),
                                               spread(rstd[:, t, :].rearrange("p (h o) -> p h o", o=1), [P, heads, W]), ALU.mult)
                if first_gate:
                    last.then_inc(k.norm_ready.sem, 1)
            if not first_gate:
                dve.drain()
                for t in range(NT):
                    dve.wait_ge(*k.sa(t + 1))
                    nc.vector.tensor_tensor(work[:, t, :], work[:, t, :], o_tm[:, t, :], ALU.mult).then_inc(k.norm_ready.sem, 1)

        @block.tensor
        def _(pe):
            pe.wait_ge(*k.norm_ready(NT))
            for c in range(KD):
                for t in range(NT):
                    last = nc.tensor.transpose(k.ps[:, c, t * P:(t + 1) * P], work[:, t, c * P:(c + 1) * P], k.ident[:, :])
                last.then_inc(k.acc_ready.sem, 1)
    k.sa.close(NT)
    k.mean_ready.close(1)
    k.root_ready.close(1)
    k.norm_ready.close(NT)
    k.acc_ready.close(KD)


def layer0_mixer(k, after):
    nc, A, sb = k.nc, k.A, k.alloc
    w = A["ab_w_in"][0]

    def cols(at, n):
        return w[:, at:at + n]

    def into_tm(dst, at, n):
        return lambda t, b: (dst[:, t, at:at + n], 1.0)

    def into_cm(dst, tile, scale=1.0):
        return lambda j, b: (dst[:, tile + j, 0:T], scale)

    with ExitStack() as layer:
        z = sb("z_tm", [P, NT, D], to=layer)
        ycm = z[:, :, :].rearrange("p a b -> p (a b)").rearrange("p (k t) -> p k t", k=KD)
        g = Kernel()
        g.small = sb("g_small", [P, NT, 64], to=layer)
        g.dt = sb("g_dt", [P, NT, 32], to=layer)
        g.ig = sb("g_ig", [P, NT, 16], to=layer)
        g.ea = sb("g_ea", [P, 32], to=layer)
        g.ld = sb("g_ld", [P, NT, 2 * GW], to=layer)
        g.cum = sb("g_cum", [P, NT, 2 * GW], to=layer)
        g.tot = sb("g_tot", [P, NT, 2 * GW], to=layer)
        g.wend = sb("g_wend", [P, NT, 32], to=layer)
        g.dec = sb("g_dec", [P, NT, 32], to=layer)
        g.u = sb("g_u", [P, 2, NT, ML_H], to=layer)
        mjobs = [(cols(Q0 + n * BANK, BANK), "cm") for n in range(2)] + [(cols(K0 + n * BANK, BANK), "cm") for n in range(2)] \
            + [(cols(V0 + n * BANK, BANK), "tm") for n in range(2)]
        with ExitStack() as c:
            x_tm = sb("x_heads", [P, NT, D], to=c)
            xbc = sb("xbc", [P, XT, T], to=c)
            with ExitStack() as e:
                raw = sb("xbc_raw", [P, XT, T + 2 * PAD], to=e)
                g.work = sb("g_work", [P, 6, NT, 48], to=e)
                with nc.Block(no_gpsimd_drain=True) as block:
                    @block.vector
                    def _(dve):
                        nc.vector.memset(raw[:, :, 0:PAD], 0.0)
                        nc.vector.memset(raw[:, :, T + PAD:T + 2 * PAD], 0.0)
                jobs = [(cols(Z0 + n * BANK, BANK), "tm", into_tm(z, n * BANK, BANK)) for n in range(2)]
                for n in range(3):
                    jobs.append((cols(XBC0 + n * BANK, BANK), "cm", (lambda n: lambda j, b: (raw[:, 4 * n + j, PAD:PAD + T], 1.0))(n)))
                jobs.append((cols(DT0, 32), "tm", into_tm(g.small, 0, 32)))
                jobs.append((cols(G0, 32), "tm", into_tm(g.small, 32, 32)))
                project(k, jobs, after=[mjobs[0][0], mjobs[1][0]])
                decays(k, g, g.small[:, :, :])
                ssd_conv(k, raw, xbc)
            b_tm = sb("b_tm", [P, NT, 256], to=c)
            cb = sb("cb", [P, 2, 2, T], to=c)
            hst = sb("hst", [P, 2, NT, D], to=c)
            ssd_turn(k, xbc, x_tm, b_tm, cb)
            with ExitStack() as e:
                xw = sb("xw", [P, 2, D], to=e)
                ssd_states(k, g, x_tm, b_tm, hst, xw)
            with ExitStack() as e:
                ce = sb("ssd_ce", [P, 2, T], to=e)
                buf = [xbc[:, 2 * n:2 * n + 2, :] for n in range(4)] + [ce[:, :, :]]
                y_tm = k.ytmp
                ssd_mix(k, g, xbc, x_tm, cb, hst, y_tm, buf)
            ssd_finish(k, y_tm, x_tm, z, ycm, hst[:, 0, :, :])
        with ExitStack() as c:
            q_cm = sb("q_cm", [P, ML_H, T], to=c)
            k_cm = sb("k_cm", [P, ML_H, T], to=c)
            v = sb("v_ext", [P, NT, ML_H, MW], to=c)
            r = Kernel()
            r.nm, r.si = (sb("r_" + name, [ML_H, 2, T], to=c) for name in ("nm", "si"))
            r.ms_row, r.tot, r.mx, r.umax = (sb("r_" + name, [ML_H, 2, NT], to=c) for name in ("ms_row", "tot", "mx", "umax"))
            r.so = sb("r_so", [ML_H, 2, 2, NT], to=c)
            r.diag = sb("r_diag", [ML_H, ML_H * 4 * NT], to=c)
            r.bar = sb("r_bar", [P, 2], to=c)
            r.floor, r.ew, r.sold, r.sloc = (sb("r_" + name, [P, 2, NT, ML_H], to=c) for name in ("floor", "ew", "sold", "sloc"))
            r.den = sb("r_den", [P, NT, 2], to=c)
            r.rden = sb("r_rden", [P, NT, 2], to=c)
            with nc.Block(no_gpsimd_drain=True) as block:
                @block.vector
                def _(dve):
                    nc.vector.memset(v[:, :, :, ML_D:MW], 1.0)
            outs = [into_cm(q_cm, 0), into_cm(q_cm, 4), into_cm(k_cm, 0, ML_D ** -0.5), into_cm(k_cm, 4, ML_D ** -0.5)]
            outs += [(lambda n: lambda t, b: (v[:, t, 4 * n:4 * n + 4, 0:ML_D], 1.0))(n) for n in range(2)]
            project(k, [(*j, f) for j, f in zip(mjobs, outs)])
            with ExitStack() as e:
                r.u_row, r.cm, r.ew_row, r.restart = (sb("r_" + name, [ML_H, 2, T], to=e) for name in ("u_row", "cm", "ew_row", "restart"))
                mlstm_gates(k, g, r)
            cst = sb("cst", [P, 2, NT, ML_H, MW], to=c)
            idle = k.ring[:, :, :].rearrange("p s n -> p (s n)")
            r.own = idle[:, 2 * D:2 * D + ML_H * MW].rearrange("p (h w) -> p h w", h=ML_H)
            mlstm_states(k, r, k_cm, v, cst, idle[:, 0:2 * D].rearrange("p (s n) -> p s n", s=2))
            hm = k.ytmp
            mlstm_mix(k, g, r, q_cm, k_cm, v, cst, hm, idle[:, 0:10 * T].rearrange("p (a s n) -> p a s n", a=5, s=2))

            def as_tm(ap):
                return ap.rearrange("p a b -> p (a b)").rearrange("p (t n) -> p t n", t=NT)

            o, work = as_tm(k_cm[:, :, :]), as_tm(q_cm[:, :, :])
            wo = out_chunks(A["ab_w_out"][0], 16)
            project(k, [(cols(O0 + n * BANK, BANK), "tm", into_tm(o, n * BANK, BANK)) for n in range(2)], after=wo[:2], cold=True)
            gated_norm(k, hm, o, ML_H, k.pcol[:, 0, 112:120], k.h, work, ACT.Sigmoid, True)
            project_out(k, lambda n: ycm[:, n, :] if n < KD else k.h[:, n - KD, :], 16, A["ab_w_out"][0], A["norm_g"][0, 1], after=after,
                        scratch=work)



def up_slot(k, s):
    return k.ring[:, (k.parity + s) % 2, 0:KD * 2 * P].rearrange("p (t h n) -> p t h n", t=KD, h=2)


def load_up(k, sp, w, s, at):
    wt = w.rearrange("(t p) n -> p t n", p=P)
    for half in range(2):
        sp.dma_start(up_slot(k, s)[:, :, half, :], wt[:, :, bass.ds(at + half * FFN, P)]).then_inc(k.up_loaded[s].sem, 16)


def ffn_up(k, layer, g_cm, ybuf, down):
    nc = k.nc
    w = k.A["ffn_w_up"][layer]
    PAIRS = FT // 2
    tap0, tap1 = k.pcol[:, 1 + 2 * layer, 0:2 * FT], k.pcol[:, 1 + 2 * layer, 2 * FT:4 * FT]
    tap2, bias = k.pcol[:, 2 + 2 * layer, 0:2 * FT], k.pcol[:, 2 + 2 * layer, 2 * FT:4 * FT]

    def column(cols, i, s, half):
        return cols[:, bass.ds(2 * i + (s + half * FT), 1)]

    def bank(s, half):
        return k.ps[:, 2 * s + half, :]

    with nc.Block(no_gpsimd_drain=True) as block:
        @block.sync
        def _(sp):
            with sp.Fori(1, PAIRS) as i:
                for s in range(2):
                    sem, base = k.pa(0)
                    sp.wait_ge(sem, 2 * i + (base + s - 1))
                    load_up(k, sp, w, s, i * (2 * P) + s * P)
            sp.wait_ge(*k.pa(FT))
            for chunk in down:
                load_weights(k, sp, chunk)

        @block.tensor
        def _(pe):
            with pe.Fori(0, PAIRS) as i:
                for s in range(2):
                    sem, base = k.up_loaded[s](0)
                    pe.wait_ge(sem, 32 * i + (base + 32))
                    sem, base = k.vb(0)
                    pe.wait_ge(sem, 2 * i + (base + s + 1))
                    for half in range(2):
                        for c in range(KD):
                            last = nc.tensor.matmul(bank(s, half), up_slot(k, s)[:, c, half, :], k.h[:, c, :], start=(c == 0), stop=(c == KD - 1))
                    last.then_inc(k.pa.sem, 1)

        @block.scalar
        def _(act):
            with act.Fori(0, PAIRS) as i:
                for s in range(2):
                    sem, base = k.pa(0)
                    act.wait_ge(sem, 2 * i + (base + s + 1))
                    for half in range(2):
                        last = nc.scalar.activation(ybuf[:, s, half, :], bank(s, half), ACT.Identity, bias=column(bias, i, s, half),
                                                    scale=column(tap1, i, s, half))
                    last.then_inc(k.sa.sem, 1)
                    sem, base = k.va(0)
                    act.wait_ge(sem, 2 * i + (base + s + 1))
                    nc.scalar.activation(ybuf[:, s, 0, :], ybuf[:, s, 0, :], ACT.Gelu_apprx_tanh).then_inc(k.sb.sem, 1)

        @block.vector
        def _(dve):
            nc.vector.sem_inc(k.vb.sem, 2)
            with dve.Fori(0, PAIRS) as i:
                for s in range(2):
                    sem, base = k.sa(0)
                    dve.wait_ge(sem, 2 * i + (base + s + 1))
                    for half in range(2):
                        nc.vector.scalar_tensor_tensor(out=ybuf[:, s, half, 1:T], in0=bank(s, half)[:, 0:T - 1], scalar=column(tap0, i, s, half),
                                                       in1=ybuf[:, s, half, 1:T], op0=ALU.mult, op1=ALU.add)
                    dve.drain()
                    for half in range(2):
                        last = nc.vector.scalar_tensor_tensor(out=ybuf[:, s, half, 0:T - 1], in0=bank(s, half)[:, 1:T], scalar=column(tap2, i, s, half),
                                                              in1=ybuf[:, s, half, 0:T - 1], op0=ALU.mult, op1=ALU.add)
                    last.then_inc(k.va.sem, 1)
                    dve.drain()
                    sem, base = k.sb(0)
                    dve.wait_ge(sem, 2 * i + (base + s + 1))
                    nc.vector.tensor_tensor(g_cm[:, bass.ds(2 * i + s, 1), :].rearrange("p o t -> p (o t)"), ybuf[:, s, 0, :], ybuf[:, s, 1, :],
                                            ALU.mult).then_inc(k.vb.sem, 1)
    k.pa.close(FT)
    k.sa.close(FT)
    k.sb.close(FT)
    k.va.close(FT)
    k.vb.close(FT + 2)
    for s in range(2):
        k.up_loaded[s].close(32 * PAIRS)


def ffn(k, layer, gain, after):
    with ExitStack() as c:
        g_cm = k.alloc("ffn_g", [P, FT, T], to=c)
        ybuf = k.alloc("ffn_y", [P, 2, 2, T], to=c)
        k.parity = sum(k.asked) % 2

        def first(sp):
            for s in range(2):
                load_up(k, sp, k.A["ffn_w_up"][layer], s, s * P)
        norm_to_cm(k, k.x, k.pcol[:, 0, 16 * layer + 8:16 * layer + 16], k.h, k.ytmp, after=[first])
        down = out_chunks(k.A["ffn_w_down"][layer], FT)
        ffn_up(k, layer, g_cm, ybuf, down[:2])
        project_out(k, lambda n: g_cm[:, n, :], FT, k.A["ffn_w_down"][layer], gain, after=after, scratch=k.ytmp)



def gla_decay(k, glr, w2, bc, restart):
    nc = k.nc
    H = GLA_H
    bias = k.pcol[:, 5, 8:16]
    neg, low = bc.neg, bc.low

    def flat(ap, d):
        return ap[:, d * H:(d + 1) * H, :].rearrange("p a b -> p (a b)")

    with nc.Block(no_gpsimd_drain=True) as block:
        @block.gpsimd
        def _(pool):
            nc.gpsimd.memset(restart[:, :, :], 1.0)
            pool.drain()
            for d, at in ((0, 0), (1, GLA_L - 1)):
                nc.gpsimd.memset(restart[:, d, :].rearrange("p (c l) -> p c l", l=GLA_L)[:, :, at:at + 1], 0.0)
            pool.drain()
            nc.gpsimd.memset(bc.bar[:, 0:1], 0.0).then_inc(k.ga.sem, 1)
            pool.drain()

        @block.tensor
        def _(pe):
            for d in range(2):
                for h in range(H):
                    last = nc.tensor.matmul(k.ps[:, d * H + h, :], w2[:, d, h * P:(h + 1) * P], glr[:, d, :], start=True, stop=True)
                last.then_inc(k.pa.sem, 1)

        @block.scalar
        def _(act):
            for d in range(2):
                act.wait_ge(*k.pa(d + 1))
                for h in range(H):
                    last = nc.scalar.activation(bc.z[:, d * H + h, :], k.ps[:, d * H + h, :], ACT.Identity, bias=bias[:, d * H + h:d * H + h + 1])
                last.then_inc(k.sa.sem, 1)
            for d in range(2):
                act.wait_ge(*k.va(d + 1))
                nc.scalar.activation(flat(neg, d), flat(neg, d), ACT.Exp)
            act.drain()
            for d in range(2):
                nc.scalar.activation(flat(neg, d), flat(neg, d), ACT.Ln, bias=k.ones[:, 0:1]).then_inc(k.sb.sem, 1)

        @block.vector
        def _(dve):
            for d in range(2):
                dve.wait_ge(*k.sa(d + 1))
                nc.vector.scalar_tensor_tensor(out=flat(neg, d), in0=flat(bc.z, d), scalar=-1.0, in1=flat(bc.z, d), op0=ALU.mult, op1=ALU.min)\
                    .then_inc(k.va.sem, 1)
            dve.wait_ge(*k.ga(1))
            for d in range(2):
                dve.wait_ge(*k.sb(d + 1))
                nc.vector.scalar_tensor_tensor(out=flat(low, d), in0=flat(bc.z, d), scalar=0.0, in1=flat(neg, d), op0=ALU.min, op1=ALU.subtract)
                dve.drain()
                for h in range(H):
                    n = d * H + h
                    way = slice(None) if d == 0 else slice(None, None, -1)
                    nc.vector.tensor_tensor_scan(bc.sum[:, n, :][:, way], restart[:, d, :][:, way], low[:, n, :][:, way], 0.0, ALU.mult, ALU.add)
    k.ga.close(1)
    k.pa.close(2)
    k.sa.close(2)
    k.sb.close(2)
    k.va.close(2)


def gla_scale(k, bc, q_cm, k_cm, q_in, kd, kw, dec):
    nc = k.nc
    H = GLA_H
    S = 1.0 / GLA_TAU
    tiles = [(d, h) for d in range(2) for h in range(H)]

    def chunks(ap):
        return ap.rearrange("p (c l) -> p c l", l=GLA_L)

    with nc.Block(no_gpsimd_drain=True) as block:
        @block.scalar
        def _(act):
            for n, (d, h) in enumerate(tiles):
                nc.scalar.activation(q_in[:, n, :], bc[:, n, :], ACT.Exp, scale=S)
                nc.scalar.activation(kd[:, n, :], bc[:, n, :], ACT.Exp, scale=-S)
                end = chunks(bc[:, n, :])[:, :, GLA_L - 1 if d == 0 else 0]
                nc.scalar.activation(dec[:, n, :], end, ACT.Exp, scale=S)
                act.wait_ge(*k.va(n + 1))
                nc.scalar.activation(kw[:, n, :], kw[:, n, :], ACT.Exp, scale=S).then_inc(k.sa.sem, 1)

        @block.vector
        def _(dve):
            for n, (d, h) in enumerate(tiles):
                at = GLA_L - 1 if d == 0 else 0
                end = chunks(bc[:, n, :])[:, :, at:at + 1]
                nc.vector.tensor_tensor(chunks(kw[:, n, :]), spread(end, [P, GC, GLA_L]), chunks(bc[:, n, :]), ALU.subtract).then_inc(k.va.sem, 1)
            for n, (d, h) in enumerate(tiles):
                dve.wait_ge(*k.sa(n + 1))
                nc.vector.tensor_tensor(q_in[:, n, :], q_in[:, n, :], q_cm[:, h, :], ALU.mult)
                nc.vector.tensor_tensor(kd[:, n, :], kd[:, n, :], k_cm[:, h, :], ALU.mult)
                nc.vector.tensor_tensor(kw[:, n, :], kw[:, n, :], k_cm[:, h, :], ALU.mult)
    k.va.close(len(tiles))
    k.sa.close(len(tiles))


def gla_mix(k, q_in, kd, kw, dec, v, o, st, att, kwt, mask):
    nc = k.nc
    H = GLA_H
    W = GLA_DV
    steps = []
    for n in range(GC - 1):
        steps += [(0, n), (1, GC - 1 - n)]

    def tile(d, h):
        return d * H + h

    with nc.Block(no_gpsimd_drain=True) as block:
        @block.gpsimd
        def _(pool):
            for d in range(2):
                nc.gpsimd.tensor_copy(mask.f[:, d, :], k.tri[d][:, :])
            pool.drain()
            nc.gpsimd.memset(mask.f[0:GLA_L, 0, GLA_L:P], 0.0)
            pool.drain()
            nc.gpsimd.memset(mask.f[GLA_L:P, 1, 0:GLA_L], 0.0)
            pool.drain()
            nc.gpsimd.memset(att[:, :, :, :], 0.0)
            nc.gpsimd.memset(st[:, 0, 0, :], 0.0)
            nc.gpsimd.memset(st[:, 1, GC - 1, :], 0.0)
            pool.drain()
            nc.gpsimd.tensor_copy(mask.u[:, :, :], mask.f[:, :, :]).then_inc(k.ga.sem, 1)
            pool.drain()

        @block.tensor
        def _(pe):
            def scores(h):
                for d in range(2):
                    n = tile(d, h)
                    u = 2 * h + d
                    if h >= 1:
                        pe.wait_ge(*k.sa(u - 1))
                    for t in range(NT):
                        last = nc.tensor.transpose(k.ps[:, d, t * P:(t + 1) * P], kw[:, n, t * P:(t + 1) * P], k.ident[:, :])
                    last.then_inc(k.pa.sem, 1)
                    if h >= 1:
                        pe.wait_ge(*k.va(u - 1))
                    for t in range(NT):
                        tok = slice(t * P, (t + 1) * P)
                        last = nc.tensor.matmul(k.ps[:, 2 + d, tok], kd[:, n, tok], q_in[:, n, tok], start=True, stop=True, skip_group_check=True)
                    last.then_inc(k.pb.sem, 1)

            def states(h):
                pe.wait_ge(*k.sa(2 * h + 2))
                for m, (d, c) in enumerate(steps):
                    at = h * len(steps) + m
                    if at >= 2:
                        pe.wait_ge(*k.vb(at - 1))
                    rows = slice((c % 2) * GLA_L, (c % 2 + 1) * GLA_L)
                    nc.tensor.matmul(k.ps[:, 4 + m % 2, 0:W], kwt[rows, h % 2, d, (c // 2) * P:(c // 2 + 1) * P], v[rows, c // 2, h * W:(h + 1) * W],
                                     start=True, stop=True).then_inc(k.pc.sem, 1)

            def outputs(h):
                pe.wait_ge(*k.va(2 * h + 2))
                pe.wait_ge(*k.vb((h + 1) * len(steps)))
                if h >= 1:
                    pe.wait_ge(*k.acc_free(2 * h))
                for t in range(NT):
                    out = k.ps[:, 6 + t // 2, (t % 2) * W:(t % 2 + 1) * W]
                    for d in range(2):
                        nc.tensor.matmul(out, att[:, 2 * (h % 2) + d, t, :], v[:, t, h * W:(h + 1) * W], start=(d == 0), stop=False, skip_group_check=True)
                    for c in (2 * t, 2 * t + 1):
                        half = out[(c % 2) * GLA_L:(c % 2 + 1) * GLA_L, :]
                        for d in range(2):
                            last = nc.tensor.matmul(half, q_in[:, tile(d, h), c * GLA_L:(c + 1) * GLA_L], st[:, d, c, :],
                                                    start=False, stop=True, skip_group_check=True)
                    if t % 2 == 1:
                        last.then_inc(k.acc_ready.sem, 1)

            scores(0)
            for h in range(H):
                states(h)
                if h + 1 < H:
                    scores(h + 1)
                outputs(h)

        @block.scalar
        def _(act):
            def read_o(h):
                for b in range(2):
                    act.wait_ge(*k.acc_ready(2 * h + b + 1))
                    nc.scalar.copy(o[:, 2 * b:2 * b + 2, h * W:(h + 1) * W], k.ps[:, 6 + b, :].rearrange("p (t w) -> p t w", t=2)).then_inc(k.acc_free.sem, 1)

            for h in range(H):
                for d in range(2):
                    u = 2 * h + d
                    act.wait_ge(*k.pa(u + 1))
                    if h >= 2:
                        act.wait_ge(*k.pc((h - 1) * len(steps)))
                    nc.scalar.copy(kwt[:, h % 2, d, :], k.ps[:, d, :]).then_inc(k.sa.sem, 1)
                if h >= 1:
                    read_o(h - 1)
            read_o(H - 1)

        @block.vector
        def _(dve):
            dve.wait_ge(*k.ga(1))

            def masked(h):
                for d in range(2):
                    u = 2 * h + d
                    dve.wait_ge(*k.pb(u + 1))
                    if h >= 2:
                        dve.wait_ge(*k.acc_ready(2 * (h - 1)))
                    nc.vector.copy_predicated(att[:, 2 * (h % 2) + d, :, :], spread(mask.u[:, d, :].rearrange("p (o l) -> p o l", o=1), [P, NT, P]),
                                              k.ps[:, 2 + d, :].rearrange("p (t l) -> p t l", t=NT)).then_inc(k.va.sem, 1)

            masked(0)
            for h in range(H):
                if h >= 1:
                    dve.wait_ge(*k.acc_ready(2 * h))
                for m, (d, c) in enumerate(steps):
                    nxt = c + 1 if d == 0 else c - 1
                    dve.wait_ge(*k.pc(h * len(steps) + m + 1))
                    dve.drain()
                    nc.vector.scalar_tensor_tensor(out=st[:, d, nxt, :], in0=st[:, d, c, :], scalar=dec[:, tile(d, h), c:c + 1],
                                                   in1=k.ps[:, 4 + m % 2, 0:W], op0=ALU.mult, op1=ALU.add).then_inc(k.vb.sem, 1)
                if h + 1 < H:
                    masked(h + 1)
    k.ga.close(1)
    k.pa.close(2 * H)
    k.pb.close(2 * H)
    k.pc.close(H * len(steps))
    k.sa.close(2 * H)
    k.va.close(2 * H)
    k.vb.close(H * len(steps))
    k.acc_ready.close(2 * H)
    k.acc_free.close(2 * H)


GLA_R0 = 3 * D
GLA_JOBS = (0, BANK, D, D + BANK, 2 * D, 2 * D + BANK, GLA_R0, GLA_R0 + GLA_RANK)


def gla_weights(k):
    w = k.A["c_w_in"][0]
    return [w[:, at:at + (BANK if at < GLA_R0 else GLA_RANK)] for at in GLA_JOBS]


def layer1_mixer(k, after):
    nc, A, sb = k.nc, k.A, k.alloc
    with ExitStack() as c:
        qk = sb("gla_qk", [P, 2 * GLA_H, T], to=c)
        q_cm, k_cm = qk[:, 0:GLA_H, :], qk[:, GLA_H:2 * GLA_H, :]
        v = sb("gla_v", [P, NT, D], to=c)
        r = sb("gla_r", [P, NT, D], to=c)
        dec = sb("gla_dec", [P, 2 * GLA_H, GC], to=c)
        q_in = sb("gla_q_in", [P, 2 * GLA_H, T], to=c)
        kd = sb("gla_kd", [P, 2 * GLA_H, T], to=c)
        kw = sb("gla_kw", [P, 2 * GLA_H, T], to=c)
        early = c.enter_context(ExitStack())
        glr = sb("gla_lr", [GLA_RANK, 2, T], to=early)
        w2 = sb("gla_w2", [GLA_RANK, 2, GLA_H * P], to=early)
        restart = sb("gla_restart", [P, 2, T], to=early)
        bc = Kernel()
        bc.bar = sb("gla_bar", [P, 1], to=early)
        bc.z, bc.neg, bc.low = q_in, kd, kw
        bc.sum = k.ytmp[:, :, :].rearrange("p a b -> p (a b)").rearrange("p (n t) -> p n t", t=T)
        outs = [lambda j, b: (q_cm[:, j, :], GLA_DK ** -0.5), lambda j, b: (k_cm[:, j, :], 1.0)]
        for dst in (v, r):
            outs += [(lambda dst, n: lambda t, b: (dst[:, t, n * BANK:(n + 1) * BANK], 1.0))(dst, n) for n in range(2)]
        outs += [(lambda d: lambda j, b: (glr[:, d, :], 1.0))(d) for d in range(2)]
        kinds = ["cm", "cm", "tm", "tm", "tm", "tm", "cm", "cm"]
        wo = out_chunks(A["c_w_out"][0], KD)

        with nc.Block(no_gpsimd_drain=True) as block:
            @block.sync
            def _(sp):
                sp.dma_start(w2[:, :, :], A["c_gate_w2"][0].rearrange("d r n -> r d n")).then_inc(k.param_loaded.sem, 16)
                sp.wait_ge(*k.param_loaded(16))
        k.param_loaded.close(16)
        project(k, list(zip(gla_weights(k), kinds, outs)), after=wo[:2])
        gla_decay(k, glr, w2, bc, restart)
        early.close()
        gla_scale(k, bc.sum, q_cm, k_cm, q_in, kd, kw, dec)
        with ExitStack() as e:
            att = sb("gla_att", [P, 4, NT, P], to=e)
            kwt = sb("gla_kwt", [P, 2, 2, T], to=e)
            mask = Kernel()
            mask.f = sb("gla_mask", [P, 2, P], to=e)
            mask.u = sb("gla_mask_u", [P, 2, P], U32, to=e)
            st = qk[:, :, :].rearrange("p a b -> p (a b)").rearrange("p (d c w) -> p d c w", d=2, c=GC)
            gla_mix(k, q_in, kd, kw, dec, v, k.ytmp, st, att, kwt, mask)
        work = kd[:, :, :].rearrange("p a b -> p (a b)").rearrange("p (t n) -> p t n", t=NT)
        gated_norm(k, k.ytmp, r, GLA_H, k.pcol[:, 5, 0:8], k.h, work, ACT.Silu, False)
        project_out(k, lambda n: k.h[:, n, :], KD, A["c_w_out"][0], A["norm_g"][1, 1], after=after, scratch=k.ytmp)



def turn(k, src, dst, tiles):
    nc = k.nc
    with nc.Block(no_gpsimd_drain=True) as block:
        @block.tensor
        def _(pe):
            for c in range(tiles):
                for t in range(NT):
                    last = nc.tensor.transpose(k.ps[:, c % NBANKS, t * P:(t + 1) * P], src[:, t, c * P:(c + 1) * P], k.ident[:, :])
                last.then_inc(k.pa.sem, 1)

        @block.scalar
        def _(act):
            for c in range(0, tiles, 2):
                act.wait_ge(*k.pa(c + 1))
                nc.scalar.copy(dst[:, c, :], k.ps[:, c, :])

        @block.vector
        def _(dve):
            for c in range(1, tiles, 2):
                dve.wait_ge(*k.pa(c + 1))
                nc.vector.tensor_copy(dst[:, c, :], k.ps[:, c, :])
    k.pa.close(tiles)


def head_norm_tm(k, src, dst, tiles, heads, width, gain, sq):
    nc = k.nc
    ms, root, rstd = (k.stat[:, n, 0:tiles * heads].rearrange("p (t h) -> p t h", h=heads) for n in range(3))

    def per_head(ap):
        return ap.rearrange("p (h e) -> p h e", h=heads)

    with nc.Block(no_gpsimd_drain=True) as block:
        @block.vector
        def _(dve):
            for t in range(tiles):
                nc.vector.tensor_tensor(sq[:, t, 0:heads * width], src[:, t, 0:heads * width], src[:, t, 0:heads * width], ALU.mult)
            dve.drain()
            for t in range(tiles):
                nc.vector.tensor_reduce(ms[:, t, :], per_head(sq[:, t, 0:heads * width]), AX.X, ALU.add)
            dve.drain()
            nc.vector.tensor_scalar(ms, ms, 1.0 / width, EPS, ALU.mult, ALU.add).then_inc(k.mean_ready.sem, 1)
            dve.wait_ge(*k.root_ready(1))
            nc.vector.reciprocal(rstd, root)
            dve.drain()
            for t in range(tiles):
                nc.vector.tensor_tensor(per_head(dst[:, t, 0:heads * width]), per_head(src[:, t, 0:heads * width]),
                                        spread(rstd[:, t, :].rearrange("p (h o) -> p h o", o=1), [P, heads, width]), ALU.mult)
            dve.drain()
            for t in range(tiles):
                nc.vector.tensor_tensor(per_head(dst[:, t, 0:heads * width]), per_head(dst[:, t, 0:heads * width]),
                                        spread(gain.rearrange("p (o e) -> p o e", o=1), [P, heads, width]), ALU.mult)

        @block.scalar
        def _(act):
            act.wait_ge(*k.mean_ready(1))
            nc.scalar.activation(root, ms, ACT.Sqrt).then_inc(k.root_ready.sem, 1)
    k.mean_ready.close(1)
    k.root_ready.close(1)


def attend(k, heads, query, key, keys_of, bias, value, width, scale, o, buf):
    nc = k.nc
    units = [(t, h) for t in range(NT) for h in range(heads)]
    s, p, pt = buf
    top, ntop, total, rtotal = (k.stat[:, n, 0:NT * heads].rearrange("p (t h) -> p t h", h=heads) for n in range(4))

    with nc.Block(no_gpsimd_drain=True) as block:
        @block.tensor
        def _(pe):
            def scores(n):
                t, h = units[n]
                if n >= 2:
                    pe.wait_ge(*k.va(n - 1))
                nc.tensor.matmul(k.ps[:, n % 2, 0:keys_of(t)], query(t, h), key(h, keys_of(t)), start=True, stop=True).then_inc(k.pa.sem, 1)

            def turned(n):
                t, h = units[n]
                pe.wait_ge(*k.sa(n + 1))
                if n >= 2:
                    pe.wait_ge(*k.sb(n - 1))
                for b in range(keys_of(t) // P):
                    last = nc.tensor.transpose(k.ps[:, 2 + n % 2, b * P:(b + 1) * P], p[:, n % 2, b * P:(b + 1) * P], k.ident[:, :])
                last.then_inc(k.pb.sem, 1)

            def values(n):
                t, h = units[n]
                pe.wait_ge(*k.sb(n + 1))
                if h == 0 and t >= 2:
                    pe.wait_ge(*k.vb(t - 1))
                nb = keys_of(t) // P
                for b in range(nb):
                    last = nc.tensor.matmul(k.ps[:, 4 + t % 2, h * width:(h + 1) * width], pt[:, n % 2, b * P:(b + 1) * P], value(h, b),
                                            start=(b == 0), stop=(b == nb - 1), skip_group_check=True)
                last.then_inc(k.pc.sem, 1)

            scores(0)
            for n in range(len(units)):
                if n + 1 < len(units):
                    scores(n + 1)
                if n >= 1:
                    turned(n - 1)
                if n >= 2:
                    values(n - 2)
            turned(len(units) - 1)
            values(len(units) - 2)
            values(len(units) - 1)

        @block.vector
        def _(dve):
            def largest(n):
                t, h = units[n]
                ps = k.ps[:, n % 2, 0:keys_of(t)]
                dve.wait_ge(*k.pa(n + 1))
                if n >= 2:
                    dve.wait_ge(*k.sa(n - 1))
                if bias is None:
                    nc.vector.tensor_copy(s[:, n % 2, 0:keys_of(t)], ps)
                else:
                    nc.vector.tensor_tensor(s[:, n % 2, 0:keys_of(t)], ps, bias(t, keys_of(t)), ALU.add)
                dve.drain()
                nc.vector.tensor_reduce(top[:, t, h:h + 1], s[:, n % 2, 0:keys_of(t)], AX.X, ALU.max)
                dve.drain()
                nc.vector.tensor_scalar(ntop[:, t, h:h + 1], top[:, t, h:h + 1], -scale, None, ALU.mult).then_inc(k.va.sem, 1)

            def read_out(t):
                dve.wait_ge(*k.sa((t + 1) * heads))
                nc.vector.reciprocal(rtotal[:, t, :], total[:, t, :])
                dve.wait_ge(*k.pc((t + 1) * heads))
                dve.drain()
                nc.vector.tensor_tensor(o[:, t, :].rearrange("p (h e) -> p h e", h=heads), k.ps[:, 4 + t % 2, 0:heads * width].rearrange("p (h e) -> p h e", h=heads),
                                        spread(rtotal[:, t, :].rearrange("p (h o) -> p h o", o=1), [P, heads, width]), ALU.mult).then_inc(k.vb.sem, 1)

            for n, (t, h) in enumerate(units):
                largest(n)
                if h == 2 and t >= 1:
                    read_out(t - 1)
            read_out(NT - 1)

        @block.scalar
        def _(act):
            def out(n):
                t, h = units[n]
                act.wait_ge(*k.pb(n + 1))
                if n >= 2:
                    act.wait_ge(*k.pc(n - 1))
                nc.scalar.copy(pt[:, n % 2, 0:keys_of(t)], k.ps[:, 2 + n % 2, 0:keys_of(t)]).then_inc(k.sb.sem, 1)

            for n, (t, h) in enumerate(units):
                act.wait_ge(*k.va(n + 1))
                if n >= 2:
                    act.wait_ge(*k.pb(n - 1))
                nc.scalar.activation(p[:, n % 2, 0:keys_of(t)], s[:, n % 2, 0:keys_of(t)], ACT.Exp, bias=ntop[:, t, h:h + 1], scale=scale,
                                     accum_out=total[:, t, h:h + 1]).then_inc(k.sa.sem, 1)
                if n >= 1:
                    out(n - 1)
            out(len(units) - 1)
    n = len(units)
    for sg in (k.pa, k.pb, k.pc, k.va, k.sa, k.sb):
        sg.close(n)
    k.vb.close(NT)



QK_HEADS = NQ + NKV
ROT = QK_HEADS + NIDX + 1


def rope(k, att, rot, tab, tmp):
    nc = k.nc
    half = HD // 2
    parts = [(0, QK_HEADS, QA0), (QK_HEADS, NIDX + 1, QI0)]
    with nc.Block(no_gpsimd_drain=True) as block:
        @block.vector
        def _(dve):
            for t in range(NT):
                for h0, n, at in parts:
                    x = att[:, t, at:at + n * HD].rearrange("p (h s e) -> p h s e", h=n, s=2)
                    y = rot[:, t, h0 * HD:(h0 + n) * HD].rearrange("p (h s e) -> p h s e", h=n, s=2)
                    cos, sin = (spread(tab[:, t, f * half:(f + 1) * half].rearrange("p (o e) -> p o e", o=1), [P, n, half]) for f in range(2))
                    nc.vector.tensor_tensor(y[:, :, 0, :], x[:, :, 0, :], cos, ALU.mult)
                    nc.vector.tensor_tensor(y[:, :, 1, :], x[:, :, 1, :], cos, ALU.mult)
                    nc.vector.tensor_tensor(tmp[:, 0, h0:h0 + n, :], x[:, :, 1, :], sin, ALU.mult)
                    nc.vector.tensor_tensor(tmp[:, 1, h0:h0 + n, :], x[:, :, 0, :], sin, ALU.mult)
                dve.drain()
                for h0, n, at in parts:
                    y = rot[:, t, h0 * HD:(h0 + n) * HD].rearrange("p (h s e) -> p h s e", h=n, s=2)
                    nc.vector.tensor_tensor(y[:, :, 0, :], y[:, :, 0, :], tmp[:, 0, h0:h0 + n, :], ALU.subtract)
                    nc.vector.tensor_tensor(y[:, :, 1, :], y[:, :, 1, :], tmp[:, 1, h0:h0 + n, :], ALU.add)
                dve.drain()


PAIR_K, PAIR_QI, PAIR_KI = NQ // 2, NQ // 2 + NKV, NQ // 2 + NKV + NIDX // 2
PAIRS = PAIR_KI + 1


def turn_heads(k, rot, cm, twice):
    nc = k.nc
    doubled = [(PAIR_K, NQ), (PAIR_K + 1, NQ + 1), (PAIR_KI, QK_HEADS + NIDX)]
    with nc.Block(no_gpsimd_drain=True) as block:
        @block.vector
        def _(dve):
            for n, (_, h) in enumerate(doubled):
                for half in range(2):
                    last = nc.vector.tensor_copy(twice[:, n, :, half * HD:(half + 1) * HD], rot[:, :, h * HD:(h + 1) * HD])
            last.then_inc(k.va.sem, 1)
            for c in range(1, PAIRS, 2):
                dve.wait_ge(*k.pa(c + 1))
                nc.vector.tensor_copy(cm[:, c, :], k.ps[:, c % NBANKS, :]).then_inc(k.vb.sem, 1)

        @block.tensor
        def _(pe):
            pe.wait_ge(*k.va(1))
            for c in range(PAIRS):
                if c >= NBANKS:
                    if c % 2:
                        pe.wait_ge(*k.vb((c - NBANKS) // 2 + 1))
                    else:
                        pe.wait_ge(*k.sa((c - NBANKS) // 2 + 1))
                found = [n for n, (pair, _) in enumerate(doubled) if pair == c]
                for t in range(NT):
                    if found:
                        src = twice[:, found[0], t, :]
                    else:
                        h = 2 * c if c < PAIR_K else QK_HEADS + 2 * (c - PAIR_QI)
                        src = rot[:, t, h * HD:(h + 2) * HD]
                    last = nc.tensor.transpose(k.ps[:, c % NBANKS, t * P:(t + 1) * P], src, k.ident[:, :])
                last.then_inc(k.pa.sem, 1)

        @block.scalar
        def _(act):
            for c in range(0, PAIRS, 2):
                act.wait_ge(*k.pa(c + 1))
                nc.scalar.copy(cm[:, c, :], k.ps[:, c % NBANKS, :]).then_inc(k.sa.sem, 1)
    k.va.close(1)
    k.pa.close(PAIRS)
    k.vb.close(PAIRS // 2)
    k.sa.close((PAIRS + 1) // 2)


def index_scores(k, cm, w_idx, score, relu):
    nc = k.nc
    units = [(t, h) for t in range(1, NT) for h in range(NIDX)]
    with nc.Block(no_gpsimd_drain=True) as block:
        @block.tensor
        def _(pe):
            for n, (t, h) in enumerate(units):
                rows = slice((h % 2) * HD, (h % 2 + 1) * HD)
                if n >= 4:
                    pe.wait_ge(*k.sa(n - 3))
                nc.tensor.matmul(k.ps[:, n % 4, 0:(t + 1) * P], cm[rows, PAIR_QI + h // 2, t * P:(t + 1) * P], cm[rows, PAIR_KI, 0:(t + 1) * P],
                                 start=True, stop=True).then_inc(k.pa.sem, 1)

        @block.scalar
        def _(act):
            for n, (t, h) in enumerate(units):
                act.wait_ge(*k.pa(n + 1))
                if n >= 4:
                    act.wait_ge(*k.va(n - 3))
                nc.scalar.activation(relu[:, n % 4, 0:(t + 1) * P], k.ps[:, n % 4, 0:(t + 1) * P], ACT.Relu, scale=HD ** -0.5).then_inc(k.sa.sem, 1)

        @block.vector
        def _(dve):
            nc.vector.tensor_scalar(w_idx, w_idx, NIDX ** -0.5, None, ALU.mult)
            dve.drain()
            for n, (t, h) in enumerate(units):
                dve.wait_ge(*k.sa(n + 1))
                out, r, w = score[:, t, 0:(t + 1) * P], relu[:, n % 4, 0:(t + 1) * P], w_idx[:, t, h:h + 1]
                if h == 0:
                    nc.vector.tensor_scalar(out, r, w, None, ALU.mult).then_inc(k.va.sem, 1)
                else:
                    dve.drain()
                    nc.vector.scalar_tensor_tensor(out=out, in0=r, scalar=w, in1=out, op0=ALU.mult, op1=ALU.add).then_inc(k.va.sem, 1)

        @block.gpsimd
        def _(pool):
            for t in range(1, NT):
                pool.wait_ge(*k.va(t * NIDX))
                nc.gpsimd.affine_select(out=score[:, t, t * P:(t + 1) * P], in_=score[:, t, t * P:(t + 1) * P], compare_op=ALU.is_ge, fill=-BIG, base=0,
                                        pattern=[[-1, P]], channel_multiplier=1)
            pool.drain()
    n = len(units)
    k.pa.close(n)
    k.sa.close(n)
    k.va.close(n)


TAKEN = -3e38


def choose(k, dve, score, eight):
    nc = k.nc
    tiles = range(1, NT)
    for step in range(TOPK // 8):
        for t in tiles:
            nc.vector.max(eight[:, t, :], score[:, t, 0:(t + 1) * P])
        dve.drain()
        for t in tiles:
            nc.vector.match_replace(score[:, t, 0:(t + 1) * P], eight[:, t, :], score[:, t, 0:(t + 1) * P], TAKEN)
        dve.drain()
    for t in tiles:
        nc.vector.tensor_scalar(score[:, t, 0:(t + 1) * P], score[:, t, 0:(t + 1) * P], -2 * BIG, BIG, ALU.is_lt, ALU.mult)
    nc.vector.tensor_scalar(score[:, 0, 0:P], k.tri[1][:, :], BIG, None, ALU.mult)
    dve.drain()
    for t in range(NT):
        nc.vector.tensor_scalar(score[:, t, 0:(t + 1) * P], score[:, t, 0:(t + 1) * P], -BIG, None, ALU.add)



def conv_gate(k, u, gate):
    nc = k.nc
    with nc.Block(no_gpsimd_drain=True) as block:
        @block.scalar
        def _(act):
            nc.scalar.activation(gate[:, :, :], gate[:, :, :], ACT.Sigmoid).then_inc(k.sa.sem, 1)

        @block.vector
        def _(dve):
            nc.vector.memset(u[:, :, 0:CONV_W - 1], 0.0)
            dve.wait_ge(*k.sa(1))
            for j in range(CT):
                nc.vector.tensor_tensor(u[:, j, CONV_W - 1:], u[:, j, CONV_W - 1:], gate[:, j, :], ALU.mult)
    k.sa.close(1)


def conv_taps(k, dve, u, y):
    nc = k.nc
    tap, bias = k.pcol[:, 6, :], k.pcol[:, 5, 40:44]
    for j in range(CT):
        nc.vector.tensor_scalar(y[:, j, :], u[:, j, 0:T], tap[:, j:j + 1], bias[:, j:j + 1], ALU.mult, ALU.add)
    for i in range(1, CONV_W):
        dve.drain()
        for j in range(CT):
            nc.vector.scalar_tensor_tensor(out=y[:, j, :], in0=u[:, j, i:i + T], scalar=tap[:, i * CT + j:i * CT + j + 1], in1=y[:, j, :],
                                           op0=ALU.mult, op1=ALU.add)


def conv_norm(k, y, ob, y_tm, sq):
    nc = k.nc
    gain, shift = k.pcol[:, 5, 44:48], k.pcol[:, 5, 48:52]
    mean, var, root, rstd = (k.stat[:, n, 0:NT] for n in range(4))
    with nc.Block(no_gpsimd_drain=True) as block:
        @block.tensor
        def _(pe):
            for t in range(NT):
                for j in range(CT):
                    last = nc.tensor.transpose(k.ps[:, t, j * P:(j + 1) * P], y[:, j, t * P:(t + 1) * P], k.ident[:, :])
                last.then_inc(k.pa.sem, 1)
            pe.wait_ge(*k.va(1))
            for j in range(CT):
                for t in range(NT):
                    last = nc.tensor.transpose(k.ps[:, 4 + j, t * P:(t + 1) * P], y_tm[:, t, j * P:(j + 1) * P], k.ident[:, :])
                last.then_inc(k.pb.sem, 1)

        @block.vector
        def _(dve):
            for t in range(NT):
                dve.wait_ge(*k.pa(t + 1))
                nc.vector.tensor_reduce(mean[:, t:t + 1], k.ps[:, t, :], AX.X, ALU.add)
            dve.drain()
            nc.vector.tensor_scalar(mean, mean, 1.0 / CONV_C, None, ALU.mult)
            dve.drain()
            for t in range(NT):
                nc.vector.tensor_scalar(y_tm[:, t, :], k.ps[:, t, :], mean[:, t:t + 1], None, ALU.subtract)
            dve.drain()
            for t in range(NT):
                nc.vector.tensor_tensor_reduce(out=sq[:, t, :], in0=y_tm[:, t, :], in1=y_tm[:, t, :], scale=1.0, scalar=0.0, op0=ALU.mult, op1=ALU.add,
                                               accum_out=var[:, t:t + 1])
            dve.drain()
            nc.vector.tensor_scalar(var, var, 1.0 / CONV_C, EPS, ALU.mult, ALU.add).then_inc(k.mean_ready.sem, 1)
            dve.wait_ge(*k.root_ready(1))
            nc.vector.reciprocal(rstd, root)
            dve.drain()
            for t in range(NT):
                last = nc.vector.tensor_scalar(y_tm[:, t, :], y_tm[:, t, :], rstd[:, t:t + 1], None, ALU.mult)
            last.then_inc(k.va.sem, 1)

        @block.scalar
        def _(act):
            act.wait_ge(*k.mean_ready(1))
            nc.scalar.activation(root, var, ACT.Sqrt).then_inc(k.root_ready.sem, 1)
            for j in range(CT):
                act.wait_ge(*k.pb(j + 1))
                nc.scalar.activation(ob[:, j, :], k.ps[:, 4 + j, :], ACT.Silu, bias=shift[:, j:j + 1], scale=gain[:, j:j + 1])
    k.pa.close(NT)
    k.pb.close(CT)
    k.va.close(1)
    k.mean_ready.close(1)
    k.root_ready.close(1)



def merge(k, branches, weights, gates, bgate, m, tmp, after):
    nc = k.nc
    NB = len(branches)
    with nc.Block(no_gpsimd_drain=True) as block:
        @block.sync
        def _(sp):
            sp.wait_ge(*k.acc_ready(NT))
            load_weights(k, sp, weights[2])
            sp.wait_ge(*k.acc_ready(2 * NT))
            load_weights(k, sp, after[0])
            sp.wait_ge(*k.acc_ready(3 * NT))
            load_weights(k, sp, after[1])

        @block.tensor
        def _(pe):
            for b in range(NB):
                w = take_weights(k, pe, CT, D)
                for t in range(NT):
                    n = b * NT + t
                    if n >= 4:
                        pe.wait_ge(*k.acc_free(n - 3))
                    for half in range(2):
                        for c in range(CT):
                            last = nc.tensor.matmul(k.ps[:, 2 * (n % 4) + half, :], branches[b][:, c, t * P:(t + 1) * P], w[:, c, half * BANK:(half + 1) * BANK],
                                                    start=(c == 0), stop=(c == CT - 1))
                    last.then_inc(k.acc_ready.sem, 1)

        @block.vector
        def _(dve):
            for b in range(NB):
                for t in range(NT):
                    g = gates[:, t, b * D:(b + 1) * D]
                    nc.vector.tensor_tensor(g, g, bgate[:, b * D:(b + 1) * D], ALU.add).then_inc(k.va.sem, 1)
            for b in range(NB):
                for t in range(NT):
                    n = b * NT + t
                    dve.wait_ge(*k.sa(n + 1))
                    dve.wait_ge(*k.acc_ready(n + 1))
                    acc = k.ps[:, 2 * (n % 4):2 * (n % 4) + 2, :].rearrange("p a b -> p (a b)")
                    dst = m[:, t, :] if b == 0 else tmp[:, n % 2, :]
                    nc.vector.tensor_tensor(dst, gates[:, t, b * D:(b + 1) * D], acc, ALU.mult).then_inc(k.acc_free.sem, 1)
                    dve.drain()
                    if b > 0:
                        nc.vector.tensor_tensor(m[:, t, :], m[:, t, :], tmp[:, n % 2, :], ALU.add)
                        dve.drain()

        @block.scalar
        def _(act):
            for n in range(NB * NT):
                act.wait_ge(*k.va(n + 1))
                g = gates[:, n % NT, (n // NT) * D:(n // NT + 1) * D]
                nc.scalar.activation(g, g, ACT.Sigmoid).then_inc(k.sa.sem, 1)
    k.acc_ready.close(NB * NT)
    k.acc_free.close(NB * NT)
    k.va.close(NB * NT)
    k.sa.close(NB * NT)


def block2_weights(k):
    w = k.A["w_in_2"][0]
    cuts = [(QA0, BANK), (QA0 + BANK, BANK), (QA0 + 2 * BANK, ATT - 2 * BANK), (CI0, BANK), (CI0 + BANK, BANK), (QM0, BANK)]
    return [w[:, at:at + n] for at, n in cuts]


def mixers2(k, after):
    nc, A, sb = k.nc, k.A, k.alloc
    w = A["w_in_2"][0]

    def into_tm(dst, at, n):
        return lambda t, b: (dst[:, t, at:at + n], 1.0)

    with ExitStack() as c:
        km_cm = sb("km_cm", [P, MH, MEM], to=c)
        vm = sb("vm_tm", [P, MT, MH * MD], to=c)
        qm = sb("qm_tm", [P, NT, MH * MD], to=c)
        u = sb("conv_u", [P, CT, T + CONV_W - 1], to=c)
        gate = sb("conv_gate", [P, CT, T], to=c)
        cm = sb("heads_cm", [P, PAIRS, T], to=c)
        va = sb("va_tm", [P, NT, NKV * HD], to=c)
        widx = sb("widx", [P, NT, NIDX], to=c)
        score = sb("score", [P, NT, T], to=c)
        eight = sb("eight", [P, NT, 8], to=c)
        with ExitStack() as e:
            mem = sb("mem_tm", [P, MT, D], to=e)
            mcm = sb("mem_cm", [P, KD, MEM], to=e)
            kvw = [A["w_mem_kv_2"][0][:, n * BANK:(n + 1) * BANK] for n in range(2)]
            with nc.Block(no_gpsimd_drain=True) as block:
                @block.sync
                def _(sp):
                    sp.dma_start(mem[:, :, :], A["mem_2"].rearrange("o (t p) d -> p (o t) d", p=P)).then_inc(k.param_loaded.sem, 16)
                    sp.wait_ge(*k.param_loaded(16))
            k.param_loaded.close(16)
            norm_to_cm(k, mem, k.pcol[:, 5, 32:40], mcm, k.ytmp, tiles=MT, after=kvw)
            km = k.ytmp
            proj = block2_weights(k)
            project(k, [(kvw[0], "tm", into_tm(km, 0, BANK)), (kvw[1], "tm", into_tm(vm, 0, BANK))], src=mcm, tiles=MT, after=proj[:2])
            head_norm_tm(k, km, km, MT, MH, MD, k.b["g_km_2"], mem)
            with nc.Block(no_gpsimd_drain=True) as block:
                @block.tensor
                def _(pe):
                    for h in range(MH):
                        for t in range(MT):
                            last = nc.tensor.transpose(k.ps[:, h, t * P:(t + 1) * P], km[:, t, h * MD:(h + 1) * MD], k.ident[:, :])
                        last.then_inc(k.pa.sem, 1)

                @block.scalar
                def _(act):
                    for h in range(MH):
                        act.wait_ge(*k.pa(h + 1))
                        nc.scalar.copy(km_cm[:, h, :], k.ps[:, h, 0:MEM])
            k.pa.close(MH)
        norm_to_cm(k, k.x, k.pcol[:, 5, 16:24], k.h, k.ytmp)
        gw = [w[:, GT0 + n * BANK:GT0 + (n + 1) * BANK] for n in range(6)]
        with ExitStack() as e:
            att = sb("att_tm", [P, NT, ATT], to=e)
            rot = sb("rot_tm", [P, NT, ROT * HD], to=e)
            tab = sb("rope_tab", [P, NT, HD], to=e)
            outs = [into_tm(att, 0, BANK), into_tm(att, BANK, BANK), into_tm(att, 2 * BANK, ATT - 2 * BANK),
                    lambda j, b: (u[:, j, CONV_W - 1:], 1.0), lambda j, b: (gate[:, j, :], 1.0), into_tm(qm, 0, BANK)]
            kinds = ["tm", "tm", "tm", "cm", "cm", "tm"]
            project(k, list(zip(proj, kinds, outs)), after=gw[:2])
            with nc.Block(no_gpsimd_drain=True) as block:
                @block.sync
                def _(sp):
                    sp.dma_start(tab[:, :, :], A["rope_table"].rearrange("(t p) e -> p t e", p=P)).then_inc(k.param_loaded.sem, 16)
                    sp.wait_ge(*k.param_loaded(16))

                @block.scalar
                def _(act):
                    nc.scalar.copy(va[:, :, :], att[:, :, VA0:VA0 + NKV * HD])
                    nc.scalar.copy(widx[:, :, :], att[:, :, WI0:WI0 + NIDX])
            k.param_loaded.close(16)
            head_norm_tm(k, att, att, NT, NQ, HD, k.b["g_qa_2"], rot)
            head_norm_tm(k, att[:, :, KA0:KA0 + NKV * HD], att[:, :, KA0:KA0 + NKV * HD], NT, NKV, HD, k.b["g_ka_2"], rot)
            head_norm_tm(k, att[:, :, KI0:KI0 + HD], att[:, :, KI0:KI0 + HD], NT, 1, HD, k.b["g_idx_k_2"], rot)
            rope(k, att, rot, tab, k.ytmp[:, 0:2, 0:ROT * HD // 2].rearrange("p s (h e) -> p s h e", h=ROT))
            twice = k.ytmp[:, 0:2, :].rearrange("p a b -> p (a b)")[:, 0:3 * NT * P].rearrange("p (n t e) -> p n t e", n=3, t=NT)
            turn_heads(k, rot, cm, twice)
        conv_gate(k, u, gate)
        index_scores(k, cm, widx[:, :, :], score, k.ytmp[:, :, 0:T])
        head_norm_tm(k, qm, qm, NT, MH, MD, k.b["g_qm_2"], k.ytmp)
        gates = sb("gates_tm", [P, NT, 3 * D], to=c)

        def meanwhile(dve):
            choose(k, dve, score, eight)
            conv_taps(k, dve, u, gate)
        brw = [A[n][0] for n in ("w_br_a_2", "w_br_b_2", "w_br_m_2")]
        project(k, [(gw[n], "tm", into_tm(gates, n * BANK, BANK)) for n in range(6)], after=brw[:2], vector=meanwhile)
        scratch = k.ytmp[:, :, :].rearrange("p a b -> p (a b)")
        halves = [scratch[:, n * 2 * D:(n + 1) * 2 * D].rearrange("p (t n) -> p t n", t=NT) for n in range(2)]
        conv_norm(k, gate, gate, *halves)
        spare = [scratch[:, n * D:(n + 1) * D].rearrange("p (s n) -> p s n", s=2) for n in range(3)]
        o_tm, oa, om = u[:, :, 0:T], cm[:, 0:CT, :], qm
        attend(k, NQ, lambda t, h: cm[(h % 2) * HD:(h % 2 + 1) * HD, h // 2, t * P:(t + 1) * P],
               lambda h, n: cm[(h % 2) * HD:(h % 2 + 1) * HD, PAIR_K + h // (NQ // NKV), 0:n], lambda t: (t + 1) * P,
               lambda t, n: score[:, t, 0:n], lambda h, b: va[:, b, (h // (NQ // NKV)) * HD:(h // (NQ // NKV) + 1) * HD], HD, HD ** -0.5, o_tm, spare)
        turn(k, o_tm, oa, CT)
        qm_cm = score
        turn(k, qm, qm_cm, CT)
        attend(k, MH, lambda t, h: qm_cm[:, h, t * P:(t + 1) * P], lambda h, n: km_cm[:, h, 0:n], lambda t: MEM, None,
               lambda h, b: vm[:, b, h * MD:(h + 1) * MD], MD, MD ** -0.5, o_tm, spare)
        turn(k, o_tm, om, CT)
        wo = out_chunks(A["w_o_2"][0], KD)
        bgate = cm[:, CT:CT + 3 * D // T, :].rearrange("p a b -> p (a b)")
        products = u[:, :, :].rearrange("p a b -> p (a b)")[:, 0:2 * D].rearrange("p (n d) -> p n d", n=2)
        with nc.Block(no_gpsimd_drain=True) as block:
            @block.sync
            def _(sp):
                sp.dma_start(bgate, everywhere(A["b_gate_2"][0], 3 * D)).then_inc(k.param_loaded.sem, 16)
                sp.wait_ge(*k.param_loaded(16))
        k.param_loaded.close(16)
        merge(k, [oa, gate, om], brw, gates, bgate, k.ytmp, products, wo)
        turn(k, k.ytmp, k.h, KD)
        project_out(k, lambda n: k.h[:, n, :], KD, A["w_o_2"][0], None, after=after)



def route(k, wr, r, rows, rows_dram):
    nc = k.nc
    n = NG + NE
    lg, ex, oneg, m1, m2, one1, one2, tmp, desc = r.lg, r.ex, r.oneg, r.m1, r.m2, r.one1, r.one2, r.tmp, r.desc

    def each(ap, w):
        return spread(ap, [P, NT, w])

    with nc.Block(no_gpsimd_drain=True) as block:
        @block.sync
        def _(sp):
            sp.dma_start(rows_dram.rearrange("(t p) d -> p t d", p=P), rows).then_inc(k.param_loaded.sem, 16)
            sp.wait_ge(*k.param_loaded(16))

        @block.gpsimd
        def _(pool):
            for e in range(NE):
                nc.gpsimd.memset(desc[:, e:e + 1], float(NE - e))
            pool.drain()
            nc.gpsimd.memset(r.bar[:, 0:1], 0.0).then_inc(k.ga.sem, 1)
            pool.drain()

        @block.tensor
        def _(pe):
            for t in range(NT):
                for c in range(KD):
                    last = nc.tensor.matmul(k.ps[:, 0, t * n:(t + 1) * n], k.h[:, c, t * P:(t + 1) * P], wr[:, c, :], start=(c == 0), stop=(c == KD - 1),
                                            skip_group_check=True)
            last.then_inc(k.pa.sem, 1)

        @block.vector
        def _(dve):
            def first(out, values, top, w, fall):
                nc.vector.tensor_tensor(out, values, each(top, w), ALU.is_equal)
                dve.drain()
                nc.vector.tensor_tensor(out, out, spread(fall.rearrange("p (o e) -> p o e", o=1), [P, NT, w]), ALU.mult)
                dve.drain()
                nc.vector.tensor_reduce(tmp[:, :, 0:1], out, AX.X, ALU.max)
                dve.drain()
                nc.vector.tensor_tensor(out, out, each(tmp[:, :, 0:1], w), ALU.is_equal)
                dve.drain()

            dve.wait_ge(*k.pa(1))
            dve.wait_ge(*k.ga(1))
            bias = k.brow[:, r.bias_at:r.bias_at + n]
            nc.vector.tensor_tensor(lg[:, :, :], k.ps[:, 0, 0:NT * n].rearrange("p (t e) -> p t e", t=NT),
                                    spread(bias.rearrange("p (o e) -> p o e", o=1), [P, NT, n]), ALU.add)
            dve.drain()
            gl, el = lg[:, :, 0:NG], lg[:, :, NG:n]
            nc.vector.tensor_reduce(m1[:, :, :], gl, AX.X, ALU.max)
            dve.drain()
            nc.vector.tensor_tensor(ex[:, :, 0:NG], gl, each(m1[:, :, :], NG), ALU.subtract).then_inc(k.va.sem, 1)
            first(oneg[:, :, :], gl, m1[:, :, :], NG, desc[:, 0:NG])
            per = "p t (g e) -> p t g e"
            for t in range(NT):
                nc.vector.tensor_tensor(el[:, t, :].rearrange("p (g e) -> p g e", g=NG), el[:, t, :].rearrange("p (g e) -> p g e", g=NG),
                                        spread(oneg[:, t, :].rearrange("p (g o) -> p g o", o=1), [P, NG, EPG]), ALU.mult)
            dve.drain()
            nc.vector.tensor_scalar(oneg[:, :, :], oneg[:, :, :], -1.0, BIG, ALU.add, ALU.mult)
            dve.drain()
            for t in range(NT):
                nc.vector.tensor_tensor(el[:, t, :].rearrange("p (g e) -> p g e", g=NG), el[:, t, :].rearrange("p (g e) -> p g e", g=NG),
                                        spread(oneg[:, t, :].rearrange("p (g o) -> p g o", o=1), [P, NG, EPG]), ALU.add)
            dve.drain()
            nc.vector.tensor_reduce(m1[:, :, :], el, AX.X, ALU.max)
            dve.drain()
            first(one1[:, :, :], el, m1[:, :, :], NE, desc[:, :])
            nc.vector.scalar_tensor_tensor(out=el, in0=one1[:, :, :], scalar=-4 * BIG, in1=el, op0=ALU.mult, op1=ALU.add)
            dve.drain()
            nc.vector.tensor_reduce(m2[:, :, :], el, AX.X, ALU.max)
            dve.drain()
            first(one2[:, :, :], el, m2[:, :, :], NE, desc[:, :])
            nc.vector.tensor_tensor(m2[:, :, :], m2[:, :, :], m1[:, :, :], ALU.subtract).then_inc(k.va.sem, 1)
            dve.wait_ge(*k.sa(2))
            nc.vector.tensor_reduce(tmp[:, :, 0:1], ex[:, :, 0:NG], AX.X, ALU.add)
            nc.vector.tensor_scalar(tmp[:, :, 1:2], m2[:, :, :], 1.0, None, ALU.add)
            dve.drain()
            nc.vector.tensor_tensor(tmp[:, :, 0:1], tmp[:, :, 0:1], tmp[:, :, 1:2], ALU.mult)
            dve.drain()
            nc.vector.reciprocal(m1[:, :, :], tmp[:, :, 0:1])
            dve.drain()
            nc.vector.tensor_tensor(m2[:, :, :], m2[:, :, :], m1[:, :, :], ALU.mult)
            nc.vector.tensor_tensor(r.both[:, :, :], one1[:, :, :], one2[:, :, :], ALU.add)

        @block.scalar
        def _(act):
            act.wait_ge(*k.va(1))
            nc.scalar.activation(ex[:, :, 0:NG], ex[:, :, 0:NG], ACT.Exp).then_inc(k.sa.sem, 1)
            act.wait_ge(*k.va(2))
            nc.scalar.activation(m2[:, :, :], m2[:, :, :], ACT.Exp).then_inc(k.sa.sem, 1)
    k.ga.close(1)
    k.pa.close(1)
    k.va.close(2)
    k.sa.close(2)
    k.param_loaded.close(16)


SLOTS = 2 * T
NB = 2 * -(-((SLOTS + NE * (P - 1)) // P) // 2)
FTE = EF // P


def place(k, r):
    nc = k.nc
    with nc.Block(no_gpsimd_drain=True) as block:
        @block.tensor
        def _(pe):
            ps = k.ps[:, 0, :]
            for t in range(NT):
                for before in range(t):
                    nc.tensor.matmul(ps[:, t * NE:(t + 1) * NE], k.ones[:, :], r.both[:, before, :], start=(before == 0), stop=False, skip_group_check=True)
                nc.tensor.matmul(ps[:, t * NE:(t + 1) * NE], k.tri[0][:, :], r.both[:, t, :], start=(t == 0), stop=True, skip_group_check=True)
            for t in range(NT):
                nc.tensor.matmul(ps[:, NT * NE:(NT + 1) * NE], k.ones[:, :], r.both[:, t, :], start=(t == 0), stop=(t == NT - 1), skip_group_check=True)
            nc.tensor.matmul(ps[:, (NT + 1) * NE:(NT + 1) * NE + 1], k.tri[0][:, :], k.ones[:, 0:1], start=True, stop=True,
                             skip_group_check=True).then_inc(k.pa.sem, 1)
            pe.wait_ge(*k.va(1))
            for n in range(2 * NT):
                last = nc.tensor.matmul(k.ps[:, 1, 0:NB], r.is_slot[:, n, :], r.is_block[:, n, :], start=(n == 0), stop=(n == 2 * NT - 1))
            last.then_inc(k.pb.sem, 1)

        @block.vector
        def _(dve):
            ps = k.ps[:, 0, :]
            upto = ps[:, 0:NT * NE].rearrange("p (t e) -> p t e", t=NT)
            count = ps[:, NT * NE:(NT + 1) * NE]
            nc.vector.tensor_tensor_scan(r.iota[:, :], k.ones[:, :], k.ones[:, :], 0.0, ALU.mult, ALU.add)
            dve.drain()
            nc.vector.tensor_scalar(r.iota[:, :], r.iota[:, :], -1.0, None, ALU.add)
            dve.wait_ge(*k.pa(1))
            nc.vector.tensor_scalar(r.blocks[:, :], count, 0.0, None, ALU.is_gt)
            for n in range(1, T // P):
                dve.drain()
                nc.vector.scalar_tensor_tensor(out=r.blocks[:, :], in0=count, scalar=float(n * P), in1=r.blocks[:, :], op0=ALU.is_gt, op1=ALU.add)
            dve.drain()
            nc.vector.tensor_tensor_scan(r.end[:, :], k.ones[:, 0:NE], r.blocks[:, :], 0.0, ALU.mult, ALU.add)
            dve.drain()
            nc.vector.tensor_tensor(r.start[:, :], r.end[:, :], r.blocks[:, :], ALU.subtract)
            dve.drain()
            for s, one in enumerate((r.one1, r.one2)):
                nc.vector.tensor_tensor(r.pick[:, 2 * s, :, :], one[:, :, :], upto, ALU.mult)
                nc.vector.tensor_tensor(r.pick[:, 2 * s + 1, :, :], one[:, :, :], spread(r.start.rearrange("p (o e) -> p o e", o=1), [P, NT, NE]), ALU.mult)
            dve.drain()
            nc.vector.tensor_reduce(r.picked[:, :, :, :], r.pick[:, :, :, :], AX.X, ALU.add)
            dve.drain()
            rank = [r.picked[:, 2 * s, :, 0] for s in range(2)]
            first = [r.picked[:, 2 * s + 1, :, 0] for s in range(2)]
            for s in range(2):
                sl = slice(s * NT, (s + 1) * NT)
                nc.vector.tensor_scalar(r.rank[:, sl], rank[s], -1.0, None, ALU.add)
                nc.vector.tensor_copy(r.block[:, sl], first[s])
            dve.drain()
            nc.vector.scalar_tensor_tensor(out=r.row_f[:, :], in0=r.block[:, :], scalar=float(P), in1=r.rank[:, :], op0=ALU.mult, op1=ALU.add)
            nc.vector.tensor_scalar(r.full[:, :], r.rank[:, :], float(P), None, ALU.is_ge)
            for n in range(2, T // P):
                dve.drain()
                nc.vector.scalar_tensor_tensor(out=r.full[:, :], in0=r.rank[:, :], scalar=float(n * P), in1=r.full[:, :], op0=ALU.is_ge, op1=ALU.add)
            dve.drain()
            nc.vector.tensor_tensor(r.block[:, :], r.block[:, :], r.full[:, :], ALU.add)
            nc.vector.scalar_tensor_tensor(out=r.rank[:, :], in0=r.full[:, :], scalar=-float(P), in1=r.rank[:, :], op0=ALU.mult, op1=ALU.add)
            nc.vector.tensor_copy(r.row[:, :], r.row_f[:, :])
            for t in range(NT):
                nc.vector.tensor_scalar(r.token_id[:, t:t + 1], ps[:, (NT + 1) * NE:(NT + 1) * NE + 1], float(t * P - 1), None, ALU.add)
            dve.drain()
            for n in range(2 * NT):
                nc.vector.tensor_scalar(r.is_slot[:, n, :], r.iota[:, :], r.rank[:, n:n + 1], None, ALU.is_equal)
                nc.vector.tensor_scalar(r.is_block[:, n, :], r.iota[:, 0:NB], r.block[:, n:n + 1], r.token_id[:, n % NT:n % NT + 1], ALU.is_equal, ALU.mult)
            dve.drain()
            nc.vector.tensor_tensor(r.ended[:, :, :], spread(r.end.rearrange("p (o e) -> p o e", o=1), [P, NB, NE]),
                                    spread(r.iota[:, 0:NB].rearrange("p (b o) -> p b o", o=1), [P, NB, NE]), ALU.is_le).then_inc(k.va.sem, 1)
            dve.drain()
            nc.vector.tensor_reduce(r.expert_f[:, :, :], r.ended[:, :, :], AX.X, ALU.add)
            dve.drain()
            nc.vector.tensor_scalar(r.expert[:, :], r.expert_f[:, :, 0], float(NE - 1), None, ALU.min)
            dve.wait_ge(*k.pb(1))
            nc.vector.tensor_copy(r.token[:, :], k.ps[:, 1, 0:NB])
    k.pa.close(1)
    k.va.close(1)
    k.pb.close(1)


def at_block(n, times=1, more=0):
    if isinstance(n, tuple):
        return n[0] * (2 * times) + (n[1] * times + more)
    return n * times + more


def experts(k, r, rows_dram, y_dram, up, dn, gain, e):
    nc, A = k.nc, k.A
    wu = A["w_up_2"][0].rearrange("e (t p) n -> e p t n", p=P)
    wd = A["w_down_2"][0].rearrange("e (t p) n -> e p t n", p=P)
    XB, UB, HB, YB = 0, 2, 4, 5

    def side(n):
        return n[1] % 2 if isinstance(n, tuple) else n % 2

    def early(n, before):
        return not isinstance(n, tuple) and n < before

    def pair(n, per):
        return n[0] * per + (n[1] // 2 + 1) * per if isinstance(n, tuple) else (n // 2 + 1) * per

    def each_block(engine, step):
        step(0)
        step(1)
        with engine.Fori(1, NB // 2 - 1) as i:
            step((i, 0))
            step((i, 1))
        step(NB - 2)
        step(NB - 1)

    def later(n, d):
        return (n[0], n[1] + d) if isinstance(n, tuple) else n + d

    def inside(n, d):
        return isinstance(n, tuple) or 0 <= n + d < NB

    with nc.Block(no_gpsimd_drain=True) as block:
        @block.sync
        def _(sp):
            def expert_of(n):
                at = at_block(n)
                one = r.expert[0:1, bass.ds(at, 1)] if isinstance(n, tuple) else r.expert[0:1, at:at + 1]
                return nc.sync.value_load(one, min_val=0, max_val=NE - 1)

            def load_up(n, expert):
                sp.dma_start(up[side(n)], wu[bass.ds(expert, 1)].rearrange("o p t n -> p (o t) n")).then_inc(e.up_loaded[side(n)], 16)

            def load_down(n, expert):
                sp.dma_start(dn[side(n)], wd[bass.ds(expert, 1)].rearrange("o p t n -> p (o t) n")).then_inc(e.down_loaded[side(n)], 16)

            def store(n):
                sp.wait_ge(e.y_ready, at_block(n, 1, 1))
                sp.dma_start(y_dram[bass.ds(at_block(n, P), P), :] if isinstance(n, tuple) else y_dram[n * P:(n + 1) * P, :],
                             e.y[:, side(n), :]).then_inc(e.y_stored[side(n)], 16)

            def step(n):
                if inside(n, 2):
                    expert = expert_of(later(n, 2))
                    sp.wait_ge(e.up_done, at_block(n, 1, 1))
                    load_up(later(n, 2), expert)
                if inside(n, -1):
                    if inside(n, 1):
                        expert = expert_of(later(n, 1))
                        sp.wait_ge(e.down_done, at_block(n))
                        load_down(later(n, 1), expert)
                    store(later(n, -1))

            for n in range(2):
                expert = expert_of(n)
                load_up(n, expert)
                load_down(n, expert)
            each_block(sp, step)
            store(NB - 1)
            for s in range(2):
                sp.wait_ge(e.y_stored[s], 16 * NB // 2)

        @block.gpsimd
        def _(pool):
            def step(n):
                s = side(n)
                if not early(n, 2):
                    pool.wait_ge(e.turned, at_block(n, 1, -1))
                nc.gpsimd.tensor_copy(e.slot_token[:, s:s + 1], r.token[:, bass.ds(at_block(n), 1)] if isinstance(n, tuple) else r.token[:, n:n + 1])
                pool.drain()
                nc.gpsimd.indirect_dma_start(e.rows[:, s, :], None, rows_dram, bass.IndirectOffsetOnAxis(ap=e.slot_token[:, s:s + 1], axis=0))\
                    .then_inc(e.gathered[s], 16)

            each_block(pool, step)
            for s in range(2):
                pool.wait_ge(e.gathered[s], 16 * NB // 2)
            pool.drain()

        @block.tensor
        def _(pe):
            def turn_rows(n):
                s = side(n)
                pe.wait_ge(e.gathered[s], pair(n, 16))
                if not early(n, 1):
                    pe.wait_ge(e.x_ready, at_block(n))
                for c in range(KD):
                    last = nc.tensor.transpose(k.ps[:, XB + c // NT, (c % NT) * P:(c % NT + 1) * P], e.rows[:, s, c * P:(c + 1) * P], k.ident[:, :])
                last.then_inc(e.turned, 1)

            def first(n):
                s = side(n)
                pe.wait_ge(e.x_ready, at_block(n, 1, 1))
                pe.wait_ge(e.up_loaded[s], pair(n, 16))
                if not early(n, 2):
                    pe.wait_ge(e.hidden, at_block(n, 1, -1))
                for c in range(KD):
                    last = nc.tensor.matmul(k.ps[:, UB + s, :], e.x[:, s, c, :], up[s][:, c, :], start=(c == 0), stop=(c == KD - 1))
                last.then_inc(e.up_done, 1)

            def turn_hidden(n):
                s = side(n)
                pe.wait_ge(e.hidden, at_block(n, 1, 1))
                if not early(n, 1):
                    pe.wait_ge(e.hid_ready, at_block(n))
                for j in range(FTE):
                    last = nc.tensor.transpose(k.ps[:, HB, j * P:(j + 1) * P], e.hid[:, s, j * P:(j + 1) * P], k.ident[:, :])
                last.then_inc(e.hid_turned, 1)

            def second(n):
                s = side(n)
                pe.wait_ge(e.hid_ready, at_block(n, 1, 1))
                pe.wait_ge(e.down_loaded[s], pair(n, 16))
                if not early(n, 1):
                    pe.wait_ge(e.y_ready, at_block(n))
                for half in range(2):
                    for j in range(FTE):
                        last = nc.tensor.matmul(k.ps[:, YB + half, :], e.hid_cm[:, s, j, :], dn[s][:, j, half * BANK:(half + 1) * BANK],
                                                start=(j == 0), stop=(j == FTE - 1))
                last.then_inc(e.down_done, 1)

            def step(n):
                if inside(n, 1):
                    first(later(n, 1))
                turn_hidden(n)
                if inside(n, 2):
                    turn_rows(later(n, 2))
                second(n)

            turn_rows(0)
            first(0)
            turn_rows(1)
            each_block(pe, step)

        @block.scalar
        def _(act):
            def silu(n):
                s = side(n)
                act.wait_ge(e.up_done, at_block(n, 1, 1))
                if not early(n, 2):
                    act.wait_ge(e.hidden, at_block(n, 1, -1))
                nc.scalar.activation(e.silu[:, s, :], k.ps[:, UB + s, 0:EF], ACT.Silu).then_inc(e.silu_ready, 1)

            def step(n):
                s = side(n)
                if inside(n, 1):
                    silu(later(n, 1))
                act.wait_ge(e.hid_turned, at_block(n, 1, 1))
                if not early(n, 2):
                    act.wait_ge(e.down_done, at_block(n, 1, -1))
                nc.scalar.copy(e.hid_cm[:, s, :, :], k.ps[:, HB, 0:EF].rearrange("p (j m) -> p j m", j=FTE)).then_inc(e.hid_ready, 1)
                act.wait_ge(e.down_done, at_block(n, 1, 1))
                if not early(n, 2):
                    act.wait_ge(e.y_stored[s], at_block_pairs(n))
                for half in range(2):
                    last = nc.scalar.copy(e.y[:, s, half * BANK:(half + 1) * BANK], k.ps[:, YB + half, :])
                last.then_inc(e.y_ready, 1)

            def at_block_pairs(n):
                return n[0] * 16 + 16 * (n[1] // 2) if isinstance(n, tuple) else 16 * (n // 2)

            silu(0)
            each_block(act, step)

        @block.vector
        def _(dve):
            def columns(n):
                s = side(n)
                dve.wait_ge(e.turned, at_block(n, 1, 1))
                if not early(n, 2):
                    dve.wait_ge(e.up_done, at_block(n, 1, -1))
                for half in range(2):
                    c = slice(half * NT, (half + 1) * NT)
                    last = nc.vector.tensor_tensor(e.x[:, s, c, :], k.ps[:, XB + half, :].rearrange("p (c m) -> p c m", c=NT),
                                                   spread(gain[:, c].rearrange("p (c o) -> p c o", o=1), [P, NT, P]), ALU.mult)
                last.then_inc(e.x_ready, 1)

            def gated(n):
                s = side(n)
                dve.wait_ge(e.silu_ready, at_block(n, 1, 1))
                if not early(n, 2):
                    dve.wait_ge(e.hid_turned, at_block(n, 1, -1))
                nc.vector.tensor_tensor(e.hid[:, s, :], e.silu[:, s, :], k.ps[:, UB + s, EF:2 * EF], ALU.mult).then_inc(e.hidden, 1)

            def step(n):
                if inside(n, 1):
                    gated(later(n, 1))
                if inside(n, 2):
                    columns(later(n, 2))

            columns(0)
            gated(0)
            columns(1)
            each_block(dve, step)


def combine(k, r, y_dram, picked, out):
    nc = k.nc
    tiles = out.rearrange("o (t p) d -> p (o t) d", p=P)
    with nc.Block(no_gpsimd_drain=True) as block:
        @block.gpsimd
        def _(pool):
            for n in range(2 * NT):
                at = (n % 2) * NT + n // 2
                nc.gpsimd.indirect_dma_start(picked[:, n, :], None, y_dram, bass.IndirectOffsetOnAxis(ap=r.row[:, at:at + 1], axis=0))\
                    .then_inc(r.row_picked[n % 2], 16)
            for s in range(2):
                pool.wait_ge(r.row_picked[s], 16 * NT)
            pool.drain()

        @block.vector
        def _(dve):
            for t in range(NT):
                for s, share in enumerate((r.m1, r.m2)):
                    dve.wait_ge(r.row_picked[s], 16 * NT)
                    last = nc.vector.scalar_tensor_tensor(out=k.x[:, t, :], in0=picked[:, 2 * t + s, :], scalar=share[:, t, 0:1], in1=k.x[:, t, :],
                                                          op0=ALU.mult, op1=ALU.add)
                    dve.drain()
                nc.vector.sem_inc(k.va.sem, 1)

        @block.sync
        def _(sp):
            for t in range(NT):
                sp.wait_ge(*k.va(t + 1))
                sp.dma_start(tiles[:, t, :], k.x[:, t, :]).then_inc(k.param_loaded.sem, 16)
            sp.wait_ge(*k.param_loaded(16 * NT))


def moe(k, out):
    nc, A, sb = k.nc, k.A, k.alloc
    with ExitStack() as c:
        wr = sb("router", [P, KD, NG + NE], to=c)
        r = Kernel()
        r.bias_at = k.router_bias_at
        r.lg, r.ex, r.oneg, r.m1, r.m2, r.one1, r.one2, r.tmp, r.both = (
            sb("moe_" + name, [P, NT, w], to=c) for name, w in (("logits", NG + NE), ("ex", NG), ("group", NG), ("share1", 1), ("share2", 1),
                                                                ("one1", NE), ("one2", NE), ("tmp", 2), ("both", NE)))
        r.desc = sb("moe_desc", [P, NE], to=c)
        r.bar = sb("moe_bar", [P, 1], to=c)
        r.iota = sb("moe_iota", [P, P], to=c)
        r.blocks, r.end, r.start = (sb("moe_" + name, [P, NE], to=c) for name in ("blocks", "block_end", "block_start"))
        r.pick = sb("moe_pick", [P, 4, NT, NE], to=c)
        r.picked = sb("moe_picked", [P, 4, NT, 1], to=c)
        r.rank, r.block, r.full, r.row_f = (sb("moe_" + name, [P, 2 * NT], to=c) for name in ("rank", "block", "full", "row_f"))
        r.row = sb("moe_row", [P, 2 * NT], I32, to=c)
        r.token_id = sb("moe_token_id", [P, NT], to=c)
        r.is_slot = sb("moe_is_slot", [P, 2 * NT, P], to=c)
        r.is_block = sb("moe_is_block", [P, 2 * NT, NB], to=c)
        r.ended = sb("moe_ended", [P, NB, NE], to=c)
        r.expert_f = sb("moe_expert_f", [P, NB, 1], to=c)
        r.expert = sb("moe_expert", [P, NB], I32, to=c)
        r.token = sb("moe_token", [P, NB], I32, to=c)
        r.row_picked = [k.new_count(f"row_picked{s}").sem for s in range(2)]
        e = Kernel()
        e.rows = sb("expert_rows", [P, 2, D], to=c)
        e.x = sb("expert_x", [P, 2, KD, P], to=c)
        e.silu = sb("expert_silu", [P, 2, EF], to=c)
        e.hid = sb("expert_hid", [P, 2, EF], to=c)
        e.hid_cm = sb("expert_hid_cm", [P, 2, FTE, P], to=c)
        e.y = sb("expert_y", [P, 2, D], to=c)
        e.slot_token = sb("expert_slot_token", [P, 2], I32, to=c)
        e.up_loaded, e.down_loaded, e.gathered, e.y_stored = (
            [k.new_count(f"{name}{s}").sem for s in range(2)] for name in ("expert_up_loaded", "expert_down_loaded", "rows_gathered", "y_stored"))
        e.turned, e.x_ready, e.up_done, e.silu_ready, e.hidden, e.hid_turned, e.hid_ready, e.down_done, e.y_ready = (
            k.new_count(name).sem for name in ("rows_turned", "x_ready", "up_done", "silu_ready", "hidden_ready", "hidden_turned", "hidden_cm_ready",
                                               "down_done", "y_ready"))
        down = sb("moe_down", [P, 2, FTE, D], to=c)
        up = [k.ring[:, s, :].rearrange("p (t n) -> p t n", t=KD) for s in range(2)]
        dn = [down[:, s, :, :] for s in range(2)]
        rows_dram = nc.dram_tensor("normalised_rows", (T, D), F32, kind="Internal").ap()
        y_dram = nc.dram_tensor("expert_results", (NB * P, D), F32, kind="Internal").ap()
        gain = k.pcol[:, 5, 24:32]

        def first(sp):
            sp.dma_start(wr[:, :, 0:NG], A["w_rg_2"][0].rearrange("(t p) n -> p t n", p=P)).then_inc(k.param_loaded.sem, 16)
            sp.dma_start(wr[:, :, NG:], A["w_re_2"][0].rearrange("(t p) n -> p t n", p=P)).then_inc(k.param_loaded.sem, 16)
            sp.wait_ge(*k.param_loaded(32))
        norm_to_cm(k, k.x, gain, k.h, k.ytmp, after=[first])
        k.param_loaded.close(32)
        route(k, wr, r, k.ytmp[:, :, :], rows_dram)
        place(k, r)
        experts(k, r, rows_dram, y_dram, up, dn, gain, e)
        picked = k.ring[:, :, :].rearrange("p s n -> p (s n)").rearrange("p (n d) -> p n d", n=2 * NT)
        combine(k, r, y_dram, picked, out)




def build(nc, A, out):
    with ExitStack() as ctx:
        k = open_kernel(nc, ctx, A)
        k.ytmp = k.alloc("y_tmp", [P, NT, D])
        w = A["ab_w_in"][0]
        setup(k, [w[:, 0:BANK], w[:, BANK:2 * BANK]])
        norm_to_cm(k, k.x, k.pcol[:, 0, 0:8], k.h, k.ytmp)
        layer0_mixer(k, [])
        ffn(k, 0, A["norm_g"][0, 3], [])
        norm_to_cm(k, k.x, k.pcol[:, 0, 16:24], k.h, k.ytmp, after=gla_weights(k)[:2])
        layer1_mixer(k, [])
        ffn(k, 1, A["norm_g"][1, 3], [])
        mixers2(k, [])
        moe(k, out)


def constants():
    half = HD // 2
    inv = np.float32(10000.0) ** (-np.arange(half, dtype=np.float32) / np.float32(half))
    angle = np.arange(T, dtype=np.float32)[:, None] * inv[None, :]
    return {"rope_table": np.concatenate([np.cos(angle), np.sin(angle)], axis=1).astype(np.float32)}


_OUT = ((1, T, D), "float32")


def kernel(**inputs):
    import concourse.bacc as _bacc
    from concourse.bass_utils import run_bass_kernel_spmd as _run

    nc = _bacc.Bacc("TRN2", target_bir_lowering=False, num_devices=1)
    arrays, handles = {}, {}
    for name, value in {**inputs, **constants()}.items():
        a = np.ascontiguousarray(value)
        arrays[f"in_{name}"] = a
        handles[name] = nc.dram_tensor(f"in_{name}", a.shape, mybir.dt.from_np(a.dtype), kind="ExternalInput").ap()
    out = nc.dram_tensor("out", _OUT[0], F32, kind="ExternalOutput").ap()
    build(nc, handles, out)
    r = _run(nc, [arrays], core_ids=[0])
    return r.results[0]["out"]
```

```python
from contextlib import ExitStack

import numpy as np

import concourse.bass as bass
from concourse import mybir

F32 = mybir.dt.float32
F32R = mybir.dt.float32r
U32 = mybir.dt.uint32
I32 = mybir.dt.int32
ALU = mybir.AluOpType
ACT = mybir.ActivationFunctionType
AX = mybir.AxisListType

P = 128
T = 512
NT = T // P
D = 1024
KD = D // P
BANK = 512
NBANKS = 8
EPS = 1e-6
BIG = 1e30

SSD_H, SSD_P, SSD_N, SSD_TAPS = 16, 64, 128, 5
SSD_X = D + 2 * 2 * SSD_N
XT = SSD_X // P
PAD = SSD_TAPS // 2
ML_H, ML_D = 8, 128
Z0 = 0
XBC0 = Z0 + D
DT0 = XBC0 + SSD_X
Q0 = DT0 + 2 * SSD_H
K0 = Q0 + D
V0 = K0 + D
O0 = V0 + D
G0 = O0 + D
GLA_H, GLA_DK, GLA_DV, GLA_RANK, GLA_TAU, GLA_L = 4, 128, 256, 16, 16.0, 64
GC = T // GLA_L
FFN = 11 * D // 4
FT = FFN // P
HD = 64
NQ, NKV, NIDX = 8, 2, 8
TOPK = T // 4
CONV_C, CONV_W = 512, 31
CT = CONV_C // P
MEM, MH, MD = 256, 4, 128
MT = MEM // P
NE, EPG, NG, EF = 32, 8, 4, 256
QA0 = 0
KA0 = QA0 + NQ * HD
VA0 = KA0 + NKV * HD
QI0 = VA0 + NKV * HD
KI0 = QI0 + NIDX * HD
WI0 = KI0 + HD
CI0 = WI0 + NIDX
QM0 = CI0 + 2 * CONV_C
GT0 = QM0 + MH * MD
ATT = CI0


class Signal:

    def __init__(self, sem):
        self.sem, self.base = sem, 0

    def __call__(self, n):
        return self.sem, self.base + n

    def close(self, n):
        self.base += n


class Kernel:
    pass


def row(ap):
    return ap.rearrange("(o n) -> o n", o=1)


def everywhere(ap, n):
    return row(ap).to_broadcast([P, n])


def spread(ap, shape):
    return ap.to_broadcast(shape)


def open_kernel(nc, ctx, A):
    k = Kernel()
    k.nc, k.A = nc, A

    seen = {}

    def sb(name, shape, dt=F32, to=ctx):
        seen[name] = seen.get(name, 0) + 1
        name = name if seen[name] == 1 else f"{name}_{seen[name]}"
        return to.enter_context(nc.sbuf_tensor(name, shape, dt))

    def signal(name):
        return Signal(ctx.enter_context(nc.semaphore(name)))

    k.new_count = signal
    k.ps = ctx.enter_context(nc.psum_tensor("ps", [P, NBANKS, BANK], F32))
    k.x = sb("x_tm", [P, NT, D])
    k.h = sb("h_cm", [P, KD, T])
    k.ring = sb("ring", [P, 2, KD * BANK])
    k.ident = sb("ident", [P, P])
    k.ones = sb("ones", [P, P])
    k.tri = [sb("tri_fwd", [P, P]), sb("tri_bwd", [P, P])]
    k.pcol = sb("pcol", [P, 7, P])
    k.brow = sb("brow", [P, 640])
    k.gpost = sb("gpost", [P, D])
    k.stat = sb("stat", [P, 4, 64])
    k.eps = sb("eps", [P, 1])
    k.loaded = [signal("w_loaded0"), signal("w_loaded1")]
    k.asked, k.taken, k.next_slot = [0, 0], [0, 0], 0
    k.up_loaded = [signal("up_loaded0"), signal("up_loaded1")]
    k.param_loaded = signal("param_loaded")
    k.weights_loaded = signal("small_weights_loaded")
    k.acc_ready = signal("acc_ready")
    k.acc_free = signal("acc_free")
    k.mean_ready = signal("mean_ready")
    k.root_ready = signal("root_ready")
    k.norm_ready = signal("norm_ready")
    k.x_ready = signal("x_ready")
    k.result_ready = signal("result_ready")
    k.w_hi_ready, k.w_lo_ready, k.h_hi_ready, k.h_lo_ready, k.products = (
        signal(name) for name in ("w_hi_ready", "w_lo_ready", "h_hi_ready", "h_lo_ready", "products"))
    k.pa = signal("step_pa")
    k.pb = signal("step_pb")
    k.pc = signal("step_pc")
    k.va = signal("step_va")
    k.vb = signal("step_vb")
    k.vc = signal("step_vc")
    k.vd = signal("step_vd")
    k.da = signal("step_da")
    k.sa = signal("step_sa")
    k.sb = signal("step_sb")
    k.ga = signal("step_ga")
    k.alloc = sb
    return k


def load_weights(k, sp, w, width=None):
    s = sum(k.asked) % 2
    tiles, cols = w.shape[0] // P, w.shape[1]
    dst = k.ring[:, s, 0:tiles * cols].rearrange("p (t n) -> p t n", t=tiles)
    sp.dma_start(dst, w.rearrange("(t p) n -> p t n", p=P)).then_inc(k.loaded[s].sem, 16)
    k.asked[s] += 1


def take_weights(k, pe, tiles, cols):
    s = sum(k.taken) % 2
    k.taken[s] += 1
    pe.wait_ge(k.loaded[s].sem, 16 * k.taken[s])
    return k.ring[:, s, 0:tiles * cols].rearrange("p (t n) -> p t n", t=tiles)



def setup(k, first):
    nc, A = k.nc, k.A
    rows = k.h[:, :, :].rearrange("p a b -> p (a b)")[:, 0:7 * P].rearrange("p (g c) -> p g c", g=7)

    def chunks(ap):
        return ap.rearrange("(r c) -> r c", c=P)

    plan = []
    for n, (i, j) in enumerate(((0, 0), (0, 2), (1, 0), (1, 2))):
        plan.append((0, 8 * n, chunks(A["norm_g"][i, j])))
    plan.append((0, 32, A["ab_conv_w"][0].rearrange("t (r c) -> (t r) c", c=P)))
    plan.append((0, 92, chunks(A["ab_conv_b"][0])))
    plan.append((0, 104, chunks(A["ab_ssd_norm"][0])))
    plan.append((0, 112, chunks(A["ab_mlstm_norm"][0])))
    for i in range(2):
        plan.append((1 + 2 * i, 0, A["ffn_conv_w"][i, 0:2].rearrange("t (r c) -> (t r) c", c=P)))
        plan.append((2 + 2 * i, 0, chunks(A["ffn_conv_w"][i, 2])))
        plan.append((2 + 2 * i, 2 * FT, chunks(A["ffn_conv_b"][i])))
    plan.append((5, 0, chunks(A["c_norm"][0])))
    plan.append((5, 8, A["c_gate_b"][0].rearrange("d (r c) -> (d r) c", c=P)))
    for n, name in enumerate(("g_mix_2", "g_ffn_2", "g_mem_2")):
        plan.append((5, 16 + 8 * n, chunks(A[name][0])))
    for n, name in enumerate(("conv_b_2", "ln_g_2", "ln_b_2")):
        plan.append((5, 40 + 4 * n, chunks(A[name][0])))
    plan.append((6, 0, A["conv_w_2"][0].rearrange("t o (r c) -> (t o r) c", c=P)))
    used = [max(r + ap.shape[0] for g, r, ap in plan if g == n) for n in range(7)]

    broad = [("ab_dt_bias", "a h -> (a h)"), ("ab_fg_bias", "a h -> (a h)"), ("ab_ig_bias", "a h -> (a h)"),
             ("ab_a_log", "a h -> (a h)"), ("ab_d_skip", None), ("g_qa_2", None), ("g_ka_2", None),
             ("g_idx_k_2", None), ("g_qm_2", None), ("g_km_2", None), ("b_rg_2", None), ("b_re_2", None)]
    k.b, at, bplan = {}, 0, []
    for name, how in broad:
        ap = A[name][0] if how is None else A[name][0].rearrange(how)
        n = ap.shape[0]
        if name == "b_rg_2":
            k.router_bias_at = at
        k.b[name] = k.brow[:, at:at + n]
        bplan.append((k.brow[:, at:at + n], everywhere(ap, n)))
        at += n

    with nc.Block(no_gpsimd_drain=True) as block:
        @block.sync
        def _(sp):
            sp.dma_start(k.x[:, :, :], A["x"].rearrange("o (t p) d -> p (o t) d", p=P)).then_inc(k.param_loaded.sem, 16)
            for g, r, ap in plan:
                sp.dma_start(rows[r:r + ap.shape[0], g, :], ap).then_inc(k.param_loaded.sem, 16)
            for dst, src in bplan:
                sp.dma_start(dst, src).then_inc(k.param_loaded.sem, 16)
            for w in first:
                load_weights(k, sp, w)
            sp.wait_ge(*k.param_loaded(16 * (1 + len(plan) + len(bplan))))

        @block.gpsimd
        def _(pool):
            nc.gpsimd.memset(k.ones[:, :], 1.0)
            nc.gpsimd.memset(k.eps[:, :], EPS)
            pool.drain()
            nc.gpsimd.affine_select(out=k.ident[:, :], in_=k.ones[:, :], compare_op=ALU.is_equal, fill=0.0, base=0,
                                    pattern=[[1, P]], channel_multiplier=-1)
            nc.gpsimd.affine_select(out=k.tri[0][:, :], in_=k.ones[:, :], compare_op=ALU.is_ge, fill=0.0, base=0,
                                    pattern=[[1, P]], channel_multiplier=-1)
            nc.gpsimd.affine_select(out=k.tri[1][:, :], in_=k.ones[:, :], compare_op=ALU.is_ge, fill=0.0, base=0,
                                    pattern=[[-1, P]], channel_multiplier=1)
            pool.drain()
    k.param_loaded.close(16 * (1 + len(plan) + len(bplan)))

    with nc.Block(no_gpsimd_drain=True) as block:
        @block.tensor
        def _(pe):
            for g in range(7):
                nc.tensor.transpose(k.ps[:, g, 0:used[g]], rows[0:used[g], g, :],
                                    k.ident[0:used[g], 0:used[g]]).then_inc(k.acc_ready.sem, 1)

        @block.scalar
        def _(act):
            for g in range(7):
                act.wait_ge(*k.acc_ready(g + 1))
                nc.scalar.copy(k.pcol[:, g, 0:used[g]], k.ps[:, g, 0:used[g]])
    k.acc_ready.close(7)



def norm_to_cm(k, src, gain, dst, xn, tiles=NT, after=()):
    nc = k.nc
    ms, root, rstd = (k.stat[:, n, 0:tiles] for n in range(3))
    width = tiles * P
    pair = isinstance(dst, tuple)

    with nc.Block(no_gpsimd_drain=True) as block:
        @block.sync
        def _(sp):
            for w in after:
                if callable(w):
                    w(sp)
                else:
                    load_weights(k, sp, w)

        @block.vector
        def _(dve):
            for t in range(tiles):
                nc.vector.tensor_tensor_reduce(out=xn[:, t, :], in0=src[:, t, :], in1=src[:, t, :], scale=1.0, scalar=0.0,
                                               op0=ALU.mult, op1=ALU.add, accum_out=ms[:, t:t + 1])
            dve.drain()
            nc.vector.tensor_scalar(ms, ms, 1.0 / D, EPS, ALU.mult, ALU.add).then_inc(k.mean_ready.sem, 1)
            dve.wait_ge(*k.root_ready(1))
            nc.vector.reciprocal(rstd, root)
            dve.drain()
            for t in range(tiles):
                nc.vector.tensor_scalar(xn[:, t, :], src[:, t, :], rstd[:, t:t + 1], None, ALU.mult).then_inc(k.norm_ready.sem, 1)
            for c in range(KD if pair else 0):
                dve.wait_ge(*k.h_hi_ready(c + 1))
                nc.vector.scalar_tensor_tensor(out=dst[1][:, c, 0:width], in0=k.ps[:, c, 0:width], scalar=gain[:, c:c + 1],
                                               in1=dst[0][:, c, 0:width].bitcast(F32), op0=ALU.mult, op1=ALU.subtract)
            for c in () if pair else range(1, KD, 2):
                dve.wait_ge(*k.acc_ready(c + 1))
                nc.vector.tensor_scalar(dst[:, c, 0:width], k.ps[:, c, 0:width], gain[:, c:c + 1], None, ALU.mult)

        @block.scalar
        def _(act):
            act.wait_ge(*k.mean_ready(1))
            nc.scalar.activation(root, ms, ACT.Sqrt).then_inc(k.root_ready.sem, 1)
            for c in range(KD if pair else 0):
                act.wait_ge(*k.acc_ready(c + 1))
                nc.scalar.activation(dst[0][:, c, 0:width], k.ps[:, c, 0:width], ACT.Copy, scale=gain[:, c:c + 1]).then_inc(k.h_hi_ready.sem, 1)
            for c in () if pair else range(0, KD, 2):
                act.wait_ge(*k.acc_ready(c + 1))
                nc.scalar.activation(dst[:, c, 0:width], k.ps[:, c, 0:width], ACT.Copy, scale=gain[:, c:c + 1])

        @block.tensor
        def _(pe):
            pe.wait_ge(*k.norm_ready(tiles))
            for c in range(KD):
                for t in range(tiles):
                    last = nc.tensor.transpose(k.ps[:, c, t * P:(t + 1) * P], xn[:, t, c * P:(c + 1) * P], k.ident[:, :])
                last.then_inc(k.acc_ready.sem, 1)
    k.mean_ready.close(1)
    k.root_ready.close(1)
    k.norm_ready.close(tiles)
    k.acc_ready.close(KD)
    if pair:
        k.h_hi_ready.close(KD)



def rest(engine, lo, whole, hi):
    return engine.tensor_tensor(lo, whole, hi.bitcast(F32), ALU.subtract)


def product(nc, out, left, right, start, stop, **more):
    nc.tensor.matmul(out, left[0], right[0], start=start, stop=False, **more)
    nc.tensor.matmul(out, left[0], right[1], start=False, stop=False, **more)
    return nc.tensor.matmul(out, left[1], right[0], start=False, stop=stop, **more)


PIECES = 3
PER_CM = KD // 2


def project(k, jobs, src=None, tiles=NT, after=(), cold=False, vector=None, split=True, depth=PIECES):
    nc = k.nc
    src = k.h if src is None else src
    width = tiles * P

    def is_split(j):
        return split and jobs[j][0].shape[1] >= 2 * P

    accs, groups, pieces = [], [], []
    ends = {}
    piece_end, chunk_pieces = [], {}
    for j, (w, layout, _) in enumerate(jobs):
        first, cols = len(accs), w.shape[1]
        count = tiles if layout == "tm" else -(-cols // P)
        accs += [(j, n) for n in range(count)]
        if not is_split(j):
            for n in range(count):
                groups.append((j, n, range(KD), None))
                ends[first + n] = len(groups)
        elif layout == "tm":
            for c in range(KD):
                for n in range(count):
                    groups.append((j, n, (c,), len(pieces)))
                    ends[first + n] = len(groups)
                pieces.append((j, slice(c, c + 1), slice(0, cols)))
                piece_end.append(len(groups))
        else:
            for n in range(count):
                for c in range(0, KD, PER_CM):
                    groups.append((j, n, range(c, c + PER_CM), len(pieces)))
                    pieces.append((j, slice(c, c + PER_CM), slice(n * P, (n + 1) * P)))
                    piece_end.append(len(groups))
                ends[first + n] = len(groups)
        ends["chunk", j] = len(groups)
        chunk_pieces[j] = len(pieces)
    acc_of = {acc: a for a, acc in enumerate(accs)}
    landed = []
    for j in range(len(jobs)):
        s = sum(k.taken) % 2
        k.taken[s] += 1
        landed.append((s, 16 * k.taken[s]))

    def bank(a):
        j, n = accs[a]
        cols = jobs[j][0].shape[1]
        if jobs[j][1] == "tm":
            return k.ps[:, a % NBANKS, 0:cols]
        return k.ps[0:min(cols - n * P, P), a % NBANKS, 0:width]

    def chunk(j):
        cols = jobs[j][0].shape[1]
        return k.ring[:, landed[j][0], 0:KD * cols].rearrange("p (t n) -> p t n", t=KD)

    def part(buffer, p):
        j, rows, cols = pieces[p]
        t, n = rows.stop - rows.start, cols.stop - cols.start
        return buffer[:, p % depth, 0:t * n].rearrange("p (t n) -> p t n", t=t)

    with ExitStack() as own:
        if pieces:
            h_hi, h_lo = (k.alloc("h_" + name, [P, KD, width], F32R, own) for name in ("hi", "lo"))
            w_hi, w_lo = (k.alloc("w_" + name, [P, depth, BANK], F32R, own) for name in ("hi", "lo"))
        block = own.enter_context(nc.Block(no_gpsimd_drain=True))

        @block.sync
        def _(sp):
            for job in jobs[:2] if cold else ():
                load_weights(k, sp, job[0])
            ahead = [(j, job[0]) for j, job in enumerate(jobs)][2:] + [(len(jobs) + n, w) for n, w in enumerate(after)]
            for j, w in ahead:
                if is_split(j - 2):
                    sp.wait_ge(*k.w_lo_ready(chunk_pieces[j - 2]))
                else:
                    sp.wait_ge(*k.products(ends["chunk", j - 2]))
                load_weights(k, sp, w)

        @block.tensor
        def _(pe):
            turned = 0
            for j, n, rows, p in groups:
                a = acc_of[j, n]
                if p is None:
                    if n == 0:
                        pe.wait_ge(k.loaded[landed[j][0]].sem, landed[j][1])
                elif p == 0 or piece_end[p - 1] == groups.index((j, n, rows, p)):
                    pe.wait_ge(*k.w_lo_ready(p + 1))
                if rows[0] == 0 and a >= NBANKS:
                    pe.wait_ge(*k.acc_free(a - NBANKS + 1))
                for c in rows:
                    start, stop = c == 0, c == KD - 1
                    if p is None:
                        w = chunk(j)
                        left, right = src[:, c, n * P:(n + 1) * P], w[:, c, :]
                        if jobs[j][1] == "cm":
                            left, right = w[:, c, n * P:min((n + 1) * P, w.shape[2])], src[:, c, 0:width]
                        last = nc.tensor.matmul(bank(a), left, right, start=start, stop=stop)
                        continue
                    if c >= turned:
                        turned = c + 1
                        pe.wait_ge(*k.h_lo_ready(turned))
                    weights = [part(w, p)[:, c - rows[0], :] for w in (w_hi, w_lo)]
                    if jobs[j][1] == "tm":
                        last = product(nc, bank(a), [h[:, c, n * P:(n + 1) * P] for h in (h_hi, h_lo)], weights, start, stop)
                    else:
                        last = product(nc, bank(a), weights, [h[:, c, :] for h in (h_hi, h_lo)], start, stop)
                last.then_inc(k.products.sem, 1)

        @block.scalar
        def _(act):
            done = 0

            def read_out(a):
                act.wait_ge(*k.products(ends[a]))
                j, n = accs[a]
                dst, scale = jobs[j][2](n, bank(a))
                b = bank(a)
                if len(dst.shape) == 3:
                    b = b.rearrange("p (a b) -> p a b", a=dst.shape[1])
                nc.scalar.activation(dst, b, ACT.Copy, scale=scale).then_inc(k.acc_free.sem, 1)

            inputs = 0
            for p, (j, rows, cols) in enumerate(pieces):
                if p == 0 or pieces[p - 1][0] != j:
                    act.wait_ge(k.loaded[landed[j][0]].sem, landed[j][1])
                if p >= depth:
                    act.wait_ge(*k.products(piece_end[p - depth]))
                nc.scalar.copy(part(w_hi, p), chunk(j)[:, rows, cols]).then_inc(k.w_hi_ready.sem, 1)
                while inputs < min(KD, rows.stop if p == 0 else KD if p >= depth - 1 else inputs + PER_CM):
                    nc.scalar.copy(h_hi[:, inputs, :], src[:, inputs, 0:width]).then_inc(k.h_hi_ready.sem, 1)
                    inputs += 1
                while p >= depth and ends[done] <= piece_end[p - depth]:
                    read_out(done)
                    done += 1
            for a in range(done, len(accs)):
                read_out(a)

        @block.vector
        def _(dve):
            for c in range(KD if pieces else 0):
                dve.wait_ge(*k.h_hi_ready(c + 1))
                rest(nc.vector, h_lo[:, c, :], src[:, c, 0:width], h_hi[:, c, :]).then_inc(k.h_lo_ready.sem, 1)
            if vector is not None:
                vector(dve)

        @block.gpsimd
        def _(pool):
            for p, (j, rows, cols) in enumerate(pieces):
                pool.wait_ge(*k.w_hi_ready(p + 1))
                rest(nc.gpsimd, part(w_lo, p), chunk(j)[:, rows, cols], part(w_hi, p)).then_inc(k.w_lo_ready.sem, 1)
            pool.drain()
    k.products.close(len(groups))
    k.acc_free.close(len(accs))
    k.w_hi_ready.close(len(pieces))
    k.w_lo_ready.close(len(pieces))
    if pieces:
        k.h_hi_ready.close(KD)
        k.h_lo_ready.close(KD)


def out_chunks(w, tiles):
    return [w[r * P:min(r + 4, tiles) * P, :] for r in range(0, tiles, 4)]


def project_out(k, lhs, tiles, w, gain, next_gain, after=(), scratch=None):
    nc = k.nc
    chunks = out_chunks(w, tiles)
    ss, root, ss2, root2 = (k.stat[:, n, 0:NT] for n in range(4))
    bulk = tiles - 2
    landed = []
    for _ in chunks:
        s = sum(k.taken) % 2
        k.taken[s] += 1
        landed.append((s, 16 * k.taken[s]))

    def whole(t):
        return k.ps[:, 2 * t:2 * t + 2, :].rearrange("p a b -> p (a b)")

    def weights(n):
        return k.ring[:, landed[n // 4][0], (n % 4) * D:(n % 4 + 1) * D]

    def steps(lead, middle, trail):
        for t in range(NT + 2):
            if t < NT:
                lead(t)
            if 1 <= t <= NT:
                middle(t - 1)
            if t >= 2:
                trail(t - 2)

    def turned_half(t, half):
        c = slice(half * NT, (half + 1) * NT)
        return k.h[:, c, t * P:(t + 1) * P], k.ps[:, 2 * t + half, :].rearrange("p (c m) -> p c m", c=NT)

    with ExitStack() as own:
        w_hi, w_lo = (k.alloc("wo_" + name, [P, PIECES, D], F32R, own) for name in ("hi", "lo"))
        l_hi, l_lo = (k.alloc("lhs_" + name, [P, PIECES, T], F32R, own) for name in ("hi", "lo"))
        gnext = k.alloc("next_gain", [P, D], F32, own)
        squares = k.alloc("squares", [P, D], F32, own)
        block = own.enter_context(nc.Block(no_gpsimd_drain=True))

        @block.sync
        def _(sp):
            sp.dma_start(gnext[:, :], everywhere(next_gain, D)).then_inc(k.param_loaded.sem, 16)
            if gain is not None:
                sp.dma_start(k.gpost[:, :], everywhere(gain, D)).then_inc(k.param_loaded.sem, 16)
            for c in range(2, len(chunks)):
                sp.wait_ge(*k.w_lo_ready(4 * (c - 1)))
                load_weights(k, sp, chunks[c])
            for nxt in after:
                sp.wait_ge(*k.w_lo_ready(tiles))
                if callable(nxt):
                    nxt(sp)
                else:
                    load_weights(k, sp, nxt)

        @block.tensor
        def _(pe):
            def tile(n, t):
                for half in range(2):
                    last = product(nc, k.ps[:, 2 * t + half, :], [h[:, n % PIECES, t * P:(t + 1) * P] for h in (l_hi, l_lo)],
                                   [h[:, n % PIECES, half * BANK:(half + 1) * BANK] for h in (w_hi, w_lo)], n == 0, n == tiles - 1,
                                   skip_group_check=True)
                return last

            for n in range(tiles):
                pe.wait_ge(*k.w_lo_ready(n + 1))
                pe.wait_ge(*k.h_lo_ready(n + 1))
                if n < bulk:
                    for t in range(NT):
                        last = tile(n, t)
                    last.then_inc(k.products.sem, 1)
            for t in range(NT):
                for n in range(bulk, tiles):
                    last = tile(n, t)
                last.then_inc(k.products.sem, 1)
            for t in range(NT):
                pe.wait_ge(*k.norm_ready(t + 1))
                for c in range(KD):
                    last = nc.tensor.transpose(k.ps[:, 2 * t + c // NT, (c % NT) * P:(c % NT + 1) * P], scratch[:, t, c * P:(c + 1) * P], k.ident[:, :])
                last.then_inc(k.acc_ready.sem, 1)

        @block.scalar
        def _(act):
            for n in range(tiles):
                if n % 4 == 0:
                    act.wait_ge(k.loaded[landed[n // 4][0]].sem, landed[n // 4][1])
                if n >= PIECES:
                    act.wait_ge(*k.products(n - PIECES + 1))
                nc.scalar.copy(w_hi[:, n % PIECES, :], weights(n)).then_inc(k.w_hi_ready.sem, 1)
                nc.scalar.copy(l_hi[:, n % PIECES, :], lhs(n)).then_inc(k.h_hi_ready.sem, 1)

            def root_of(t, values, total, out, signal):
                nc.scalar.activation(squares[:, :], values, ACT.Square, accum_out=total[:, t:t + 1])
                act.drain()
                nc.scalar.activation(out[:, t:t + 1], total[:, t:t + 1], ACT.Sqrt, bias=k.eps[:, 0:1], scale=1.0 / D).then_inc(signal.sem, 1)

            def result(t):
                if gain is not None:
                    act.wait_ge(*k.products(bulk + t + 1))
                    root_of(t, whole(t), ss, root, k.root_ready)

            def norm(t):
                act.wait_ge(*k.x_ready(t + 1))
                root_of(t, k.x[:, t, :], ss2, root2, k.mean_ready)

            def read_out(t):
                act.wait_ge(*k.acc_ready(t + 1))
                nc.scalar.copy(*turned_half(t, 0))

            steps(result, norm, read_out)

        @block.gpsimd
        def _(pool):
            for n in range(tiles):
                pool.wait_ge(*k.w_hi_ready(n + 1))
                rest(nc.gpsimd, w_lo[:, n % PIECES, :], weights(n), w_hi[:, n % PIECES, :]).then_inc(k.w_lo_ready.sem, 1)
            for t in range(NT if gain is not None else 0):
                pool.wait_ge(*k.result_ready(t + 1))
                nc.gpsimd.tensor_tensor(k.x[:, t, :], k.x[:, t, :], scratch[:, t, :], ALU.add).then_inc(k.x_ready.sem, 1)
            pool.drain()

        @block.vector
        def _(dve):
            for n in range(tiles):
                dve.wait_ge(*k.h_hi_ready(n + 1))
                rest(nc.vector, l_lo[:, n % PIECES, :], lhs(n), l_hi[:, n % PIECES, :]).then_inc(k.h_lo_ready.sem, 1)
            dve.wait_ge(*k.param_loaded(32 if gain is not None else 16))

            def result(t):
                if gain is None:
                    dve.wait_ge(*k.products(bulk + t + 1))
                    nc.vector.tensor_tensor(k.x[:, t, :], k.x[:, t, :], whole(t), ALU.add).then_inc(k.x_ready.sem, 1)
                    return
                dve.wait_ge(*k.root_ready(t + 1))
                nc.vector.reciprocal(ss[:, t:t + 1], root[:, t:t + 1])
                dve.drain()
                nc.vector.scalar_tensor_tensor(out=scratch[:, t, :], in0=whole(t), scalar=ss[:, t:t + 1], in1=k.gpost[:, :],
                                               op0=ALU.mult, op1=ALU.mult).then_inc(k.result_ready.sem, 1)

            def norm(t):
                dve.wait_ge(*k.mean_ready(t + 1))
                nc.vector.reciprocal(ss2[:, t:t + 1], root2[:, t:t + 1])
                dve.drain()
                nc.vector.scalar_tensor_tensor(out=scratch[:, t, :], in0=k.x[:, t, :], scalar=ss2[:, t:t + 1], in1=gnext[:, :],
                                               op0=ALU.mult, op1=ALU.mult).then_inc(k.norm_ready.sem, 1)

            def read_out(t):
                dve.wait_ge(*k.acc_ready(t + 1))
                nc.vector.tensor_copy(*turned_half(t, 1))

            steps(result, norm, read_out)
    for signal in (k.w_hi_ready, k.w_lo_ready, k.h_hi_ready, k.h_lo_ready):
        signal.close(tiles)
    k.products.close(bulk + NT)
    for signal in (k.x_ready, k.mean_ready, k.norm_ready, k.acc_ready):
        signal.close(NT)
    k.param_loaded.close(32 if gain is not None else 16)
    if gain is not None:
        k.root_ready.close(NT)
        k.result_ready.close(NT)



DIRS = (0, 1)
GW = SSD_H + ML_H


def decays(k, g, small):
    nc = k.nc
    nd = 2 * SSD_H
    n = nd + 2 * ML_H
    pre, neg, ex, s, s2, poly = (g.work[:, i, :, :] for i in range(6))

    def to(ap):
        return ap.rearrange("p (o n) -> p o n", o=1).to_broadcast([P, NT, ap.shape[1]])

    with nc.Block(no_gpsimd_drain=True) as block:
        @block.vector
        def _(dve):
            nc.vector.tensor_tensor(pre[:, :, 0:nd], small[:, :, 0:nd], to(k.b["ab_dt_bias"]), ALU.add)
            nc.vector.tensor_tensor(pre[:, :, nd:n], small[:, :, nd + 2 * ML_H:nd + 4 * ML_H], to(k.b["ab_fg_bias"]), ALU.add)
            nc.vector.tensor_tensor(g.ig[:, :, :], small[:, :, nd:nd + 2 * ML_H], to(k.b["ab_ig_bias"]), ALU.add)
            dve.drain()
            nc.vector.tensor_scalar(pre[:, :, nd:n], pre[:, :, nd:n], -1.0, None, ALU.mult)
            dve.drain()
            nc.vector.scalar_tensor_tensor(out=neg, in0=pre, scalar=-1.0, in1=pre, op0=ALU.mult, op1=ALU.min).then_inc(k.va.sem, 1)
            dve.wait_ge(*k.sa(1))
            nc.vector.tensor_scalar(s, ex, 2.0, None, ALU.add)
            dve.drain()
            nc.vector.reciprocal(s2, s)
            dve.drain()
            nc.vector.tensor_tensor(s, ex, s2, ALU.mult)
            dve.drain()
            nc.vector.tensor_tensor(s2, s, s, ALU.mult)
            dve.drain()
            nc.vector.tensor_scalar(poly, s2, 1.0 / 17.0, None, ALU.mult)
            for m in (15, 13, 11, 9, 7, 5, 3):
                dve.drain()
                nc.vector.scalar_tensor_tensor(out=poly, in0=poly, scalar=1.0 / m, in1=s2, op0=ALU.add, op1=ALU.mult)
            dve.drain()
            nc.vector.scalar_tensor_tensor(out=poly, in0=poly, scalar=1.0, in1=s, op0=ALU.add, op1=ALU.mult)
            dve.drain()
            nc.vector.tensor_scalar(s, pre, 0.0, None, ALU.max)
            dve.drain()
            nc.vector.scalar_tensor_tensor(out=s, in0=poly, scalar=2.0, in1=s, op0=ALU.mult, op1=ALU.add)
            dve.drain()
            nc.vector.tensor_copy(g.dt[:, :, :], s[:, :, 0:nd])
            dve.wait_ge(*k.sa(2))
            for d in DIRS:
                nc.vector.scalar_tensor_tensor(out=g.ld[:, :, d * GW:d * GW + SSD_H], in0=s[:, :, d * SSD_H:(d + 1) * SSD_H], scalar=-1.0,
                                               in1=to(g.ea[:, d * SSD_H:(d + 1) * SSD_H]), op0=ALU.mult, op1=ALU.mult)
                last = nc.vector.tensor_scalar(g.ld[:, :, d * GW + SSD_H:(d + 1) * GW], s[:, :, nd + d * ML_H:nd + (d + 1) * ML_H],
                                               -1.0, None, ALU.mult)
            dve.drain()
            nc.vector.memset(poly, 0.0).then_inc(k.va.sem, 1)
            dve.wait_ge(*k.acc_ready(1))
            cps = k.ps[:, 0, 0:NT * 4 * GW].rearrange("p (c n) -> p c n", c=NT)
            nc.vector.tensor_copy(g.cum[:, :, :], cps[:, :, 0:2 * GW])
            nc.vector.tensor_copy(g.tot[:, :, :], cps[:, :, 2 * GW:4 * GW])
            dve.drain()
            for d in DIRS:
                nc.vector.tensor_tensor(g.wend[:, :, d * SSD_H:(d + 1) * SSD_H], g.tot[:, :, d * GW:d * GW + SSD_H],
                                        g.cum[:, :, d * GW:d * GW + SSD_H], ALU.subtract)
                nc.vector.tensor_tensor(g.u[:, d, :, :], g.ig[:, :, d * ML_H:(d + 1) * ML_H],
                                        g.cum[:, :, d * GW + SSD_H:(d + 1) * GW], ALU.subtract)
                nc.vector.tensor_copy(g.dec[:, :, d * SSD_H:(d + 1) * SSD_H], g.tot[:, :, d * GW:d * GW + SSD_H])
            dve.drain()
            nc.vector.memset(poly, 0.0).then_inc(k.va.sem, 1)
            dve.wait_ge(*k.sa(3))
            nc.vector.tensor_tensor(g.wend[:, :, :], g.wend[:, :, :], g.dt[:, :, :], ALU.mult)

        @block.scalar
        def _(act):
            act.wait_ge(*k.va(1))
            nc.scalar.activation(ex, neg, ACT.Exp).then_inc(k.sa.sem, 1)
            nc.scalar.activation(g.ea[:, :], k.b["ab_a_log"], ACT.Exp).then_inc(k.sa.sem, 1)
            act.wait_ge(*k.va(3))
            nc.scalar.activation(g.dec[:, :, :], g.dec[:, :, :], ACT.Exp)
            nc.scalar.activation(g.wend[:, :, :], g.wend[:, :, :], ACT.Exp).then_inc(k.sa.sem, 1)

        @block.tensor
        def _(pe):
            pe.wait_ge(*k.va(2))
            for c in range(NT):
                at = c * 4 * GW
                for d in DIRS:
                    nc.tensor.matmul(k.ps[:, 0, at + d * GW:at + (d + 1) * GW], k.tri[d][:, :], g.ld[:, c, d * GW:(d + 1) * GW],
                                     start=True, stop=True, skip_group_check=True)
                last = nc.tensor.matmul(k.ps[:, 0, at + 2 * GW:at + 4 * GW], k.ones[:, :], g.ld[:, c, :],
                                        start=True, stop=True, skip_group_check=True)
            last.then_inc(k.acc_ready.sem, 1)
    k.va.close(3)
    k.sa.close(3)
    k.acc_ready.close(1)



def ssd_conv(k, raw, out):
    nc = k.nc
    tap, bias = k.pcol[:, 0, 32:92], k.pcol[:, 0, 92:104]
    with nc.Block(no_gpsimd_drain=True) as block:
        @block.vector
        def _(dve):
            for first in range(0, XT, 4):
                tiles = range(first, first + 4)
                for j in tiles:
                    nc.vector.tensor_scalar(out[:, j, :], raw[:, j, 0:T], tap[:, j:j + 1], bias[:, j:j + 1], ALU.mult, ALU.add)
                dve.drain()
                for i in range(1, SSD_TAPS):
                    for j in tiles:
                        last = nc.vector.scalar_tensor_tensor(out=out[:, j, :], in0=raw[:, j, i:i + T], scalar=tap[:, i * XT + j:i * XT + j + 1],
                                                              in1=out[:, j, :], op0=ALU.mult, op1=ALU.add)
                    if i < SSD_TAPS - 1:
                        dve.drain()
                last.then_inc(k.va.sem, 1)

        @block.scalar
        def _(act):
            for j in range(XT):
                act.wait_ge(*k.va(j // 4 + 1))
                nc.scalar.activation(out[:, j, :], out[:, j, :], ACT.Silu)
    k.va.close(XT // 4)


def ssd_turn(k, xbc, x_tm, b_tm, cb):
    nc = k.nc
    with nc.Block(no_gpsimd_drain=True) as block:
        @block.tensor
        def _(pe):
            for c in range(NT):
                if c >= 2:
                    pe.wait_ge(*k.sa(c - 1))
                b = 3 * (c % 2)
                for j in range(10):
                    last = nc.tensor.transpose(k.ps[:, b + j // 4, (j % 4) * P:(j % 4 + 1) * P], xbc[:, j, c * P:(c + 1) * P], k.ident[:, :])
                last.then_inc(k.acc_ready.sem, 1)
            for grp in range(2):
                for c in range(NT):
                    last = nc.tensor.matmul(k.ps[:, 6 + grp, c * P:(c + 1) * P], xbc[:, 8 + grp, c * P:(c + 1) * P],
                                            xbc[:, 10 + grp, c * P:(c + 1) * P], start=True, stop=True, skip_group_check=True)
                last.then_inc(k.acc_ready.sem, 1)

        @block.scalar
        def _(act):
            for c in range(NT):
                b = 3 * (c % 2)
                act.wait_ge(*k.acc_ready(c + 1))
                nc.scalar.copy(b_tm[:, c, :], k.ps[:, b + 2, 0:2 * P])
                nc.scalar.copy(x_tm[:, c, :], k.ps[:, b:b + 2, :].rearrange("p a b -> p (a b)")).then_inc(k.sa.sem, 1)

        @block.vector
        def _(dve):
            for grp in range(2):
                dve.wait_ge(*k.acc_ready(NT + grp + 1))
                for d in DIRS:
                    nc.vector.tensor_tensor(cb[:, d, grp, :].rearrange("p (c l) -> p c l", c=NT),
                                            k.ps[:, 6 + grp, :].rearrange("p (c l) -> p c l", c=NT),
                                            k.tri[d][:, :].rearrange("p (o l) -> p o l", o=1).to_broadcast([P, NT, P]), ALU.mult)
    k.sa.close(NT)
    k.acc_ready.close(NT + 2)


def ssd_states(k, g, x_tm, b_tm, hst, xw):
    nc = k.nc
    steps = [(0, c) for c in range(NT - 1)] + [(1, c) for c in range(NT - 1, 0, -1)]
    with nc.Block(no_gpsimd_drain=True) as block:
        @block.vector
        def _(dve):
            nc.vector.memset(hst[:, 0, 0, :], 0.0)
            nc.vector.memset(hst[:, 1, NT - 1, :], 0.0)

            def weigh(n):
                d, c = steps[n]
                if n >= 2:
                    dve.wait_ge(*k.acc_ready(n - 1))
                nc.vector.tensor_tensor(xw[:, n % 2, :].rearrange("p (h e) -> p h e", h=SSD_H),
                                        x_tm[:, c, :].rearrange("p (h e) -> p h e", h=SSD_H),
                                        g.wend[:, c, d * SSD_H:(d + 1) * SSD_H].rearrange("p (h o) -> p h o", o=1).to_broadcast([P, SSD_H, SSD_P]),
                                        ALU.mult).then_inc(k.va.sem, 1)
            weigh(0)
            weigh(1)
            for n, (d, c) in enumerate(steps):
                nxt = c + 1 if d == 0 else c - 1
                dec = g.dec[:, c, d * SSD_H:(d + 1) * SSD_H].rearrange("p (h o) -> p h o", o=1).to_broadcast([P, SSD_H, SSD_P])
                dve.drain()
                nc.vector.tensor_tensor(hst[:, d, nxt, :].rearrange("p (h e) -> p h e", h=SSD_H),
                                        hst[:, d, c, :].rearrange("p (h e) -> p h e", h=SSD_H), dec, ALU.mult)
                dve.wait_ge(*k.acc_ready(n + 1))
                dve.drain()
                b = 2 * (n % 4)
                nc.vector.tensor_tensor(hst[:, d, nxt, :], hst[:, d, nxt, :], k.ps[:, b:b + 2, :].rearrange("p a b -> p (a b)"),
                                        ALU.add).then_inc(k.vb.sem, 1)
                if n + 2 < len(steps):
                    weigh(n + 2)

        @block.tensor
        def _(pe):
            for n, (d, c) in enumerate(steps):
                pe.wait_ge(*k.va(n + 1))
                if n >= 4:
                    pe.wait_ge(*k.vb(n - 3))
                for grp in range(2):
                    last = nc.tensor.matmul(k.ps[:, 2 * (n % 4) + grp, :], b_tm[:, c, grp * P:(grp + 1) * P],
                                            xw[:, n % 2, grp * BANK:(grp + 1) * BANK], start=True, stop=True)
                last.then_inc(k.acc_ready.sem, 1)
    k.va.close(len(steps))
    k.vb.close(len(steps))
    k.acc_ready.close(len(steps))


def ssd_mix(k, g, xbc, x_tm, cb, hst, y_tm, buf):
    nc = k.nc
    units = [(h, d) for h in range(SSD_H) for d in DIRS]
    arg, gg, w, ec, ce = buf
    half = SSD_H // 2

    def col(h, d):
        return d * GW + h

    with nc.Block(no_gpsimd_drain=True) as block:
        @block.tensor
        def _(pe):
            def sums(n):
                h, d = units[n]
                if n >= 4:
                    pe.wait_ge(*k.sa(n - 3))
                for c in range(NT):
                    last = nc.tensor.matmul(k.ps[:, 4 + n % 4, c * P:(c + 1) * P], spread(g.ld[:, c, col(h, d):col(h, d) + 1], [P, P]),
                                            k.tri[d][:, :], start=True, stop=True, skip_group_check=True)
                last.then_inc(k.pa.sem, 1)

            def mix(h):
                if h == half:
                    pe.wait_ge(*k.vc(1))
                pe.wait_ge(*k.vb(2 * h + 2))
                pe.wait_ge(*k.ga(2 * h + 2))
                at = h * SSD_P
                for c in range(NT):
                    out = k.ps[:, c, (h % half) * SSD_P:(h % half + 1) * SSD_P]
                    tok = slice(c * P, (c + 1) * P)
                    for d in DIRS:
                        nc.tensor.matmul(out, w[:, 2 * (h % 2) + d, tok], x_tm[:, c, at:at + SSD_P], start=(d == 0), stop=False, skip_group_check=True)
                    for d in DIRS:
                        last = nc.tensor.matmul(out, ce[:, 2 * (h % 2) + d, tok], hst[:, d, c, at:at + SSD_P], start=False, stop=(d == 1), skip_group_check=True)
                last.then_inc(k.pb.sem, 1)

            for n in range(4):
                sums(n)
            for h in range(SSD_H):
                for n in (2 * h + 4, 2 * h + 5):
                    if n < len(units):
                        sums(n)
                mix(h)

        @block.vector
        def _(dve):
            def args(n):
                h, d = units[n]
                dve.wait_ge(*k.pa(n + 1))
                if n >= 2:
                    dve.wait_ge(*k.sb(n - 1))
                for c in range(NT):
                    tok = slice(c * P, (c + 1) * P)
                    last = nc.vector.tensor_scalar(arg[:, n % 2, tok], k.ps[:, 4 + n % 4, tok], g.cum[:, c, col(h, d):col(h, d) + 1], 0.0,
                                                   ALU.subtract, ALU.min)
                last.then_inc(k.va.sem, 1)

            def weights(n):
                h, d = units[n]
                dve.wait_ge(*k.sb(n + 1))
                if n >= 4:
                    dve.wait_ge(*k.pb(n // 2 - 1))
                for c in range(NT):
                    tok = slice(c * P, (c + 1) * P)
                    last = nc.vector.scalar_tensor_tensor(out=w[:, n % 4, tok], in0=gg[:, n % 2, tok], scalar=g.dt[:, c, d * SSD_H + h:d * SSD_H + h + 1],
                                                          in1=cb[:, d, h // half, tok], op0=ALU.mult, op1=ALU.mult)
                last.then_inc(k.vb.sem, 1)

            def read_out(part):
                dve.wait_ge(*k.pb(half * (part + 1)))
                for c in range(NT):
                    last = nc.vector.tensor_copy(y_tm[:, c, part * BANK:(part + 1) * BANK], k.ps[:, c, :])
                last.then_inc(k.vc.sem, 1)

            args(0)
            for n in range(len(units)):
                if n + 1 < len(units):
                    args(n + 1)
                if n == 2 * half:
                    read_out(0)
                weights(n)
            read_out(1)

        @block.scalar
        def _(act):
            for n, (h, d) in enumerate(units):
                act.wait_ge(*k.va(n + 1))
                if n >= 2:
                    act.wait_ge(*k.ga(n - 1))
                nc.scalar.activation(ec[:, n % 2, :], k.ps[:, 4 + n % 4, :], ACT.Exp).then_inc(k.sa.sem, 1)
                if n >= 2:
                    act.wait_ge(*k.vb(n - 1))
                nc.scalar.activation(gg[:, n % 2, :], arg[:, n % 2, :], ACT.Exp).then_inc(k.sb.sem, 1)

        @block.gpsimd
        def _(pool):
            for n, (h, d) in enumerate(units):
                pool.wait_ge(*k.sa(n + 1))
                if n >= 4:
                    pool.wait_ge(*k.pb(n // 2 - 1))
                nc.gpsimd.tensor_tensor(ce[:, n % 4, :], xbc[:, 10 + h // half, :], ec[:, n % 2, :], ALU.mult).then_inc(k.ga.sem, 1)
            pool.drain()
    n = len(units)
    k.pa.close(n)
    k.pb.close(SSD_H)
    k.va.close(n)
    k.vb.close(n)
    k.vc.close(2)
    k.sa.close(n)
    k.sb.close(n)
    k.ga.close(n)


def ssd_finish(k, y_tm, x_tm, z_tm, ycm, work, after=()):
    nc = k.nc
    G = 2
    W = D // G
    ms, root, rstd = (k.stat[:, n, 0:NT * G].rearrange("p (t g) -> p t g", g=G) for n in range(3))
    gain = k.pcol[:, 0, 104:112]
    skip = k.b["ab_d_skip"].rearrange("p (h o) -> p h o", o=1).to_broadcast([P, SSD_H, SSD_P])
    with nc.Block(no_gpsimd_drain=True) as block:
        @block.sync
        def _(sp):
            for w in after:
                load_weights(k, sp, w)

        @block.scalar
        def _(act):
            for t in range(NT):
                nc.scalar.activation(z_tm[:, t, :], z_tm[:, t, :], ACT.Silu).then_inc(k.sa.sem, 1)
            act.wait_ge(*k.mean_ready(1))
            nc.scalar.activation(root, ms, ACT.Sqrt).then_inc(k.root_ready.sem, 1)
            for c in range(KD):
                act.wait_ge(*k.acc_ready(c + 1))
                nc.scalar.activation(ycm[:, c, :], k.ps[:, c, :], ACT.Copy, scale=gain[:, c:c + 1])

        @block.vector
        def _(dve):
            for t in range(NT):
                nc.vector.tensor_tensor(work[:, t, :].rearrange("p (h e) -> p h e", h=SSD_H), x_tm[:, t, :].rearrange("p (h e) -> p h e", h=SSD_H),
                                        skip, ALU.mult)
            dve.drain()
            for t in range(NT):
                nc.vector.tensor_tensor(y_tm[:, t, :], y_tm[:, t, :], work[:, t, :], ALU.add)
            dve.drain()
            for t in range(NT):
                dve.wait_ge(*k.sa(t + 1))
                nc.vector.tensor_tensor(y_tm[:, t, :], y_tm[:, t, :], z_tm[:, t, :], ALU.mult)
            dve.drain()
            for t in range(NT):
                for grp in range(G):
                    part = y_tm[:, t, grp * W:(grp + 1) * W]
                    nc.vector.tensor_tensor_reduce(out=work[:, t, grp * W:(grp + 1) * W], in0=part, in1=part, scale=1.0, scalar=0.0,
                                                   op0=ALU.mult, op1=ALU.add, accum_out=ms[:, t, grp:grp + 1])
            dve.drain()
            nc.vector.tensor_scalar(ms, ms, 1.0 / W, EPS, ALU.mult, ALU.add).then_inc(k.mean_ready.sem, 1)
            dve.wait_ge(*k.root_ready(1))
            nc.vector.reciprocal(rstd, root)
            dve.drain()
            for t in range(NT):
                for grp in range(G):
                    nc.vector.tensor_scalar(work[:, t, grp * W:(grp + 1) * W], y_tm[:, t, grp * W:(grp + 1) * W], rstd[:, t, grp:grp + 1],
                                            None, ALU.mult).then_inc(k.norm_ready.sem, 1)

        @block.tensor
        def _(pe):
            pe.wait_ge(*k.norm_ready(NT * G))
            for c in range(KD):
                for t in range(NT):
                    last = nc.tensor.transpose(k.ps[:, c, t * P:(t + 1) * P], work[:, t, c * P:(c + 1) * P], k.ident[:, :])
                last.then_inc(k.acc_ready.sem, 1)
    k.sa.close(NT)
    k.mean_ready.close(1)
    k.root_ready.close(1)
    k.norm_ready.close(NT * G)
    k.acc_ready.close(KD)



MW = ML_D + 1


def mlstm_gates(k, g, r):
    nc = k.nc
    H = ML_H
    u_row, cm, ms_row, tot, mx, so = r.u_row, r.cm, r.ms_row, r.tot, r.mx, r.so

    def at_chunks(ap):
        return ap.rearrange("h d (c l) -> h d c l", c=NT)

    def each(ap):
        return ap.rearrange("h d (c o) -> h d c o", o=1).to_broadcast([H, 2, NT, P])

    with nc.Block(no_gpsimd_drain=True) as block:
        @block.gpsimd
        def _(pool):
            nc.gpsimd.memset(r.restart[:, :, :], 0.0)
            pool.drain()
            for c in range(NT):
                nc.gpsimd.memset(r.restart[:, 0, c * P:c * P + 1], -3e38)
                nc.gpsimd.memset(r.restart[:, 1, c * P + P - 1:c * P + P], -3e38)
            pool.drain()
            nc.gpsimd.memset(ms_row[:, :, :], 0.0).then_inc(k.ga.sem, 1)
            pool.drain()

        @block.tensor
        def _(pe):
            for d in DIRS:
                for c in range(NT):
                    last = nc.tensor.transpose(k.ps[0:H, d, c * P:(c + 1) * P], g.u[:, d, c, :], k.ident[:, :])
            last.then_inc(k.acc_ready.sem, 1)
            for d in DIRS:
                for c in range(NT):
                    last = nc.tensor.matmul(k.ps[0:H, 2, 4 * d + c:4 * d + c + 1], g.ld[:, c, d * GW + SSD_H:(d + 1) * GW], k.ones[:, 0:1],
                                            start=True, stop=True, skip_group_check=True)
            last.then_inc(k.acc_ready.sem, 1)
            pe.wait_ge(*k.vb(1))
            for d in DIRS:
                for c in range(NT):
                    last = nc.tensor.transpose(k.ps[:, 3, (d * NT + c) * H:(d * NT + c + 1) * H], r.nm[:, d, c * P:(c + 1) * P], k.ident[0:H, 0:H])
            last.then_inc(k.acc_ready.sem, 1)
            pe.wait_ge(*k.sa(1))
            for d in DIRS:
                for c in range(NT):
                    last = nc.tensor.transpose(k.ps[:, 4, (d * NT + c) * H:(d * NT + c + 1) * H], r.ew_row[:, d, c * P:(c + 1) * P], k.ident[0:H, 0:H])
            pe.wait_ge(*k.vc(1))
            nc.tensor.matmul(k.ps[:, 5, 0:2 * H * 2 * NT], k.ones[0:H, :], r.diag[:, :], start=True, stop=True).then_inc(k.acc_ready.sem, 1)

        @block.vector
        def _(dve):
            dve.wait_ge(*k.acc_ready(1))
            nc.vector.tensor_copy(u_row[:, :, :], k.ps[0:H, 0:2, :])
            dve.wait_ge(*k.acc_ready(2))
            nc.vector.tensor_copy(tot[:, :, :], k.ps[0:H, 2, 0:8].rearrange("h (d c) -> h d c", d=2))
            dve.wait_ge(*k.ga(1))
            dve.drain()
            nc.vector.tensor_tensor_scan(cm[:, 0, :], r.restart[:, 0, :], u_row[:, 0, :], 0.0, ALU.add, ALU.max)
            nc.vector.tensor_tensor_scan(cm[:, 1, :][:, ::-1], r.restart[:, 1, :][:, ::-1], u_row[:, 1, :][:, ::-1], 0.0, ALU.add, ALU.max)
            dve.drain()
            nc.vector.tensor_copy(r.umax[:, 0, :], at_chunks(cm[:, :, :])[:, 0, :, P - 1])
            nc.vector.tensor_copy(r.umax[:, 1, :], at_chunks(cm[:, :, :])[:, 1, :, 0])
            dve.drain()
            for n in range(NT):
                for d in DIRS:
                    c = n if d == 0 else NT - 1 - n
                    nc.vector.tensor_tensor(mx[:, d, c:c + 1], ms_row[:, d, c:c + 1], r.umax[:, d, c:c + 1], ALU.max)
                dve.drain()
                if n < NT - 1:
                    for d in DIRS:
                        c = n if d == 0 else NT - 1 - n
                        nxt = c + 1 if d == 0 else c - 1
                        nc.vector.tensor_tensor(ms_row[:, d, nxt:nxt + 1], mx[:, d, c:c + 1], tot[:, d, c:c + 1], ALU.add)
                    dve.drain()
            nc.vector.tensor_tensor(at_chunks(r.nm[:, :, :]), at_chunks(cm[:, :, :]), each(ms_row[:, :, :]), ALU.max)
            nc.vector.tensor_tensor(so[:, 0, :, :], ms_row[:, :, :], mx[:, :, :], ALU.subtract)
            nc.vector.tensor_tensor(so[:, 1, :, :], r.umax[:, :, :], mx[:, :, :], ALU.subtract)
            dve.drain()
            nc.vector.tensor_tensor(at_chunks(r.si[:, :, :]), each(ms_row[:, :, :]), at_chunks(r.nm[:, :, :]), ALU.subtract)
            nc.vector.tensor_tensor(at_chunks(r.ew_row[:, :, :]), at_chunks(u_row[:, :, :]), each(r.umax[:, :, :]), ALU.subtract)
            nc.vector.tensor_scalar(r.nm[:, :, :], r.nm[:, :, :], -1.0, None, ALU.mult)
            dve.drain()
            nc.vector.memset(r.bar[:, 0:1], 0.0).then_inc(k.vb.sem, 1)
            dve.wait_ge(*k.sa(2))
            nc.vector.tensor_tensor(r.diag[:, :].rearrange("h (n q) -> h n q", n=H), spread(so[:, :, :, :].rearrange("h s d c -> h (s d c)").rearrange("h (o q) -> h o q", o=1), [H, H, 4 * NT]),
                                    spread(k.ident[0:H, 0:H].rearrange("h (n o) -> h n o", o=1), [H, H, 4 * NT]), ALU.mult).then_inc(k.vc.sem, 1)
            dve.wait_ge(*k.acc_ready(3))
            for d in DIRS:
                nc.vector.tensor_tensor(r.floor[:, d, :, :], k.ps[:, 3, d * NT * H:(d + 1) * NT * H].rearrange("p (c h) -> p c h", c=NT),
                                        g.cum[:, :, d * GW + SSD_H:(d + 1) * GW], ALU.subtract)
            dve.drain()
            nc.vector.memset(r.bar[:, 1:2], 0.0).then_inc(k.vc.sem, 1)
            dve.wait_ge(*k.acc_ready(4))
            nc.vector.tensor_copy(r.ew[:, :, :, :].rearrange("p d c h -> p (d c h)"), k.ps[:, 4, 0:2 * NT * H])
            spr = k.ps[:, 5, 0:H * 4 * NT].rearrange("p (h s d c) -> p h s d c", h=H, s=2, d=2)
            for d in DIRS:
                nc.vector.tensor_copy(r.sold[:, d, :, :].rearrange("p c h -> p h c"), spr[:, :, 0, d, :])
                nc.vector.tensor_copy(r.sloc[:, d, :, :].rearrange("p c h -> p h c"), spr[:, :, 1, d, :])

        @block.scalar
        def _(act):
            act.wait_ge(*k.vb(1))
            nc.scalar.activation(r.ew_row[:, :, :], r.ew_row[:, :, :], ACT.Exp).then_inc(k.sa.sem, 1)
            nc.scalar.activation(so[:, :, :, :], so[:, :, :, :], ACT.Exp).then_inc(k.sa.sem, 1)
            nc.scalar.activation(r.si[:, :, :], r.si[:, :, :], ACT.Exp)
            act.wait_ge(*k.vc(2))
            nc.scalar.activation(r.floor[:, :, :, :], r.floor[:, :, :, :], ACT.Exp)
    k.ga.close(1)
    k.acc_ready.close(4)
    k.vb.close(1)
    k.vc.close(2)
    k.sa.close(2)


def mlstm_states(k, r, k_cm, v, cst, kw):
    nc = k.nc
    H = ML_H
    steps = [(0, c) for c in range(NT - 1)] + [(1, c) for c in range(NT - 1, 0, -1)]

    def bank(h):
        return k.ps[:, 4 + h // 2, (h % 2) * 256:(h % 2) * 256 + MW]

    def banks():
        return k.ps[:, 4:8, :].rearrange("p b (e w) -> p (b e) w", e=2)[:, :, 0:MW]

    def per_head(ap):
        return ap.rearrange("p (h o) -> p h o", o=1).to_broadcast([P, H, MW])

    with nc.Block(no_gpsimd_drain=True) as block:
        @block.tensor
        def _(pe):
            def turn(n):
                d, c = steps[n]
                if n >= 2:
                    pe.wait_ge(*k.va(n - 1))
                for h in range(H):
                    last = nc.tensor.transpose(k.ps[:, 2 * (n % 2) + h // 4, (h % 4) * P:(h % 4 + 1) * P], k_cm[:, h, c * P:(c + 1) * P], k.ident[:, :])
                last.then_inc(k.pa.sem, 1)

            turn(0)
            for n, (d, c) in enumerate(steps):
                if n + 1 < len(steps):
                    turn(n + 1)
                pe.wait_ge(*k.va(n + 1))
                if n >= 1:
                    pe.wait_ge(*k.vb(n))
                for h in range(H):
                    last = nc.tensor.matmul(bank(h), kw[:, n % 2, h * P:(h + 1) * P], v[:, c, h, :], start=True, stop=True, skip_group_check=True)
                last.then_inc(k.pb.sem, 1)

        @block.vector
        def _(dve):
            nc.vector.memset(cst[:, 0, 0, :, :], 0.0)
            nc.vector.memset(cst[:, 1, NT - 1, :, :], 0.0)
            dve.drain()

            def weigh(n):
                d, c = steps[n]
                dve.wait_ge(*k.pa(n + 1))
                if n >= 2:
                    dve.wait_ge(*k.pb(n - 1))
                b = 2 * (n % 2)
                nc.vector.tensor_tensor(kw[:, n % 2, :].rearrange("p (h e) -> p h e", h=H), k.ps[:, b:b + 2, :].rearrange("p b (h e) -> p (b h) e", e=P),
                                        r.ew[:, d, c, :].rearrange("p (h o) -> p h o", o=1).to_broadcast([P, H, P]), ALU.mult).then_inc(k.va.sem, 1)

            weigh(0)
            for n, (d, c) in enumerate(steps):
                if n + 1 < len(steps):
                    weigh(n + 1)
                nxt = c + 1 if d == 0 else c - 1
                dve.wait_ge(*k.pb(n + 1))
                nc.vector.tensor_tensor(r.own[:, :, :], banks(), per_head(r.sloc[:, d, c, :]), ALU.mult).then_inc(k.vb.sem, 1)
                nc.vector.tensor_tensor(cst[:, d, nxt, :, :], cst[:, d, c, :, :], per_head(r.sold[:, d, c, :]), ALU.mult)
                dve.drain()
                nc.vector.tensor_tensor(cst[:, d, nxt, :, :], cst[:, d, nxt, :, :], r.own[:, :, :], ALU.add)
                dve.drain()
    n = len(steps)
    for s in (k.pa, k.pb, k.va, k.vb):
        s.close(n)


def mlstm_mix(k, g, r, q_cm, k_cm, v, cst, hm, buf):
    nc = k.nc
    H = ML_H
    units = [(h, d) for h in range(H) for d in DIRS]
    arg, gg, w, qs, qk = (buf[:, n, :, :] for n in range(5))
    NUM, SUMS, SI, QK = 0, 4, 5, 6

    def num(c, d):
        return k.ps[:, NUM + c, d * 256:d * 256 + MW]

    with nc.Block(no_gpsimd_drain=True) as block:
        @block.tensor
        def _(pe):
            def scores(h):
                if h >= 1:
                    pe.wait_ge(*k.vc(h))
                for c in range(NT):
                    tok = slice(c * P, (c + 1) * P)
                    last = nc.tensor.matmul(k.ps[:, QK, tok], k_cm[:, h, tok], q_cm[:, h, tok], start=True, stop=True, skip_group_check=True)
                last.then_inc(k.pc.sem, 1)

            def rows(n):
                h, d = units[n]
                if n >= 1:
                    pe.wait_ge(*k.va(n))
                pick = spread(k.ident[0:H, h:h + 1], [H, P])
                nc.tensor.matmul(k.ps[:, SUMS, :], pick, r.nm[:, d, :], start=True, stop=True)
                if n >= 1:
                    pe.wait_ge(*k.vd(n))
                nc.tensor.matmul(k.ps[:, SI, :], pick, r.si[:, d, :], start=True, stop=True).then_inc(k.pa.sem, 1)

            def mix(n):
                h, d = units[n]
                pe.wait_ge(*k.vb(n + 1))
                pe.wait_ge(*k.vd(n + 1))
                if h >= 1:
                    pe.wait_ge(*k.da(h))
                for c in range(NT):
                    tok = slice(c * P, (c + 1) * P)
                    nc.tensor.matmul(num(c, d), w[:, d, tok], v[:, c, h, :], start=True, stop=False, skip_group_check=True)
                    last = nc.tensor.matmul(num(c, d), qs[:, d, tok], cst[:, d, c, h, :], start=False, stop=True, skip_group_check=True)
                last.then_inc(k.pb.sem, 1)

            scores(0)
            rows(0)
            for n, (h, d) in enumerate(units):
                if n + 1 < len(units):
                    if d == 1:
                        scores(h + 1)
                    rows(n + 1)
                mix(n)

        @block.vector
        def _(dve):
            def prepare(n):
                h, d = units[n]
                if d == 0:
                    dve.wait_ge(*k.pc(h + 1))
                    for e in DIRS:
                        last = nc.vector.tensor_tensor(qk[:, e, :].rearrange("p (c l) -> p c l", c=NT), k.ps[:, QK, :].rearrange("p (c l) -> p c l", c=NT),
                                                       spread(k.tri[e][:, :].rearrange("p (o l) -> p o l", o=1), [P, NT, P]), ALU.mult)
                    last.then_inc(k.vc.sem, 1)
                dve.wait_ge(*k.pa(n + 1))
                if n >= 2:
                    dve.wait_ge(*k.sa(n - 1))
                for c in range(NT):
                    tok = slice(c * P, (c + 1) * P)
                    last = nc.vector.tensor_scalar(arg[:, n % 2, tok], k.ps[:, SUMS, tok], g.u[:, d, c, h:h + 1], 0.0, ALU.add, ALU.min)
                last.then_inc(k.va.sem, 1)
                if n >= 2:
                    dve.wait_ge(*k.pb(n - 1))
                nc.vector.tensor_tensor(qs[:, d, :], q_cm[:, h, :], k.ps[:, SI, :], ALU.mult).then_inc(k.vd.sem, 1)

            def weights(n):
                h, d = units[n]
                dve.wait_ge(*k.sa(n + 1))
                if d == 0:
                    dve.drain()
                nc.vector.tensor_tensor(w[:, d, :], gg[:, n % 2, :], qk[:, d, :], ALU.mult).then_inc(k.vb.sem, 1)

            def read_out(h):
                dve.wait_ge(*k.sb(h + 1))
                nc.vector.tensor_tensor(r.den[:, :, :], r.den[:, :, :], r.floor[:, :, :, h].rearrange("p d c -> p c d"), ALU.max)
                dve.drain()
                nc.vector.reciprocal(r.rden[:, :, :], r.den[:, :, :])
                dve.drain()
                at = slice(h * ML_D, (h + 1) * ML_D)
                for c in range(NT):
                    nc.vector.tensor_scalar(hm[:, c, at], num(c, 0)[:, 0:ML_D], r.rden[:, c, 0:1], None, ALU.mult)
                dve.drain()
                for c in range(NT):
                    last = nc.vector.scalar_tensor_tensor(out=hm[:, c, at], in0=num(c, 1)[:, 0:ML_D], scalar=r.rden[:, c, 1:2], in1=hm[:, c, at],
                                                          op0=ALU.mult, op1=ALU.add)
                last.then_inc(k.da.sem, 1)

            prepare(0)
            for n, (h, d) in enumerate(units):
                weights(n)
                if n + 1 < len(units):
                    if d == 1:
                        dve.drain()
                    prepare(n + 1)
                if d == 1:
                    read_out(h)

        @block.scalar
        def _(act):
            for n, (h, d) in enumerate(units):
                act.wait_ge(*k.va(n + 1))
                if n >= 2:
                    act.wait_ge(*k.vb(n - 1))
                nc.scalar.activation(gg[:, n % 2, :], arg[:, n % 2, :], ACT.Exp).then_inc(k.sa.sem, 1)
                if d == 1:
                    act.wait_ge(*k.pb(n + 1))
                    if h >= 1:
                        act.wait_ge(*k.da(h))
                    nc.scalar.activation(r.den[:, :, :], k.ps[:, NUM:NUM + NT, :].rearrange("p c (d w) -> p c d w", d=2)[:, :, :, ML_D],
                                         ACT.Abs).then_inc(k.sb.sem, 1)
    n = len(units)
    for s in (k.pa, k.pb, k.va, k.vb, k.vd, k.sa):
        s.close(n)
    for s in (k.pc, k.vc, k.da, k.sb):
        s.close(H)


def gated_norm(k, y_tm, o_tm, heads, gain, dst, work, gate, first_gate, after=()):
    nc = k.nc
    W = D // heads
    ms, root, rstd = (k.stat[:, n, 0:NT * heads].rearrange("p (t h) -> p t h", h=heads) for n in range(3))

    def per_head(ap):
        return ap.rearrange("p t (h e) -> p t h e", h=heads)

    with nc.Block(no_gpsimd_drain=True) as block:
        @block.sync
        def _(sp):
            for w in after:
                load_weights(k, sp, w)

        @block.scalar
        def _(act):
            for t in range(NT):
                nc.scalar.activation(o_tm[:, t, :], o_tm[:, t, :], gate).then_inc(k.sa.sem, 1)
            act.wait_ge(*k.mean_ready(1))
            nc.scalar.activation(root, ms, ACT.Sqrt).then_inc(k.root_ready.sem, 1)
            for c in range(KD):
                act.wait_ge(*k.acc_ready(c + 1))
                nc.scalar.activation(dst[:, c, :], k.ps[:, c, :], ACT.Copy, scale=gain[:, c:c + 1])

        @block.vector
        def _(dve):
            if first_gate:
                for t in range(NT):
                    dve.wait_ge(*k.sa(t + 1))
                    nc.vector.tensor_tensor(y_tm[:, t, :], y_tm[:, t, :], o_tm[:, t, :], ALU.mult)
                dve.drain()
            for t in range(NT):
                nc.vector.tensor_tensor(work[:, t, :], y_tm[:, t, :], y_tm[:, t, :], ALU.mult)
            dve.drain()
            nc.vector.tensor_reduce(ms, per_head(work[:, :, :]), AX.X, ALU.add)
            dve.drain()
            nc.vector.tensor_scalar(ms, ms, 1.0 / W, EPS, ALU.mult, ALU.add).then_inc(k.mean_ready.sem, 1)
            dve.wait_ge(*k.root_ready(1))
            nc.vector.reciprocal(rstd, root)
            dve.drain()
            for t in range(NT):
                last = nc.vector.tensor_tensor(work[:, t, :].rearrange("p (h e) -> p h e", h=heads), y_tm[:, t, :].rearrange("p (h e) -> p h e", h=heads),
                                               spread(rstd[:, t, :].rearrange("p (h o) -> p h o", o=1), [P, heads, W]), ALU.mult)
                if first_gate:
                    last.then_inc(k.norm_ready.sem, 1)
            if not first_gate:
                dve.drain()
                for t in range(NT):
                    dve.wait_ge(*k.sa(t + 1))
                    nc.vector.tensor_tensor(work[:, t, :], work[:, t, :], o_tm[:, t, :], ALU.mult).then_inc(k.norm_ready.sem, 1)

        @block.tensor
        def _(pe):
            pe.wait_ge(*k.norm_ready(NT))
            for c in range(KD):
                for t in range(NT):
                    last = nc.tensor.transpose(k.ps[:, c, t * P:(t + 1) * P], work[:, t, c * P:(c + 1) * P], k.ident[:, :])
                last.then_inc(k.acc_ready.sem, 1)
    k.sa.close(NT)
    k.mean_ready.close(1)
    k.root_ready.close(1)
    k.norm_ready.close(NT)
    k.acc_ready.close(KD)


def layer0_mixer(k, next_gain, after):
    nc, A, sb = k.nc, k.A, k.alloc
    w = A["ab_w_in"][0]

    def cols(at, n):
        return w[:, at:at + n]

    def into_tm(dst, at, n):
        return lambda t, b: (dst[:, t, at:at + n], 1.0)

    def into_cm(dst, tile, scale=1.0):
        return lambda j, b: (dst[:, tile + j, 0:T], scale)

    with ExitStack() as layer:
        z = sb("z_tm", [P, NT, D], to=layer)
        ycm = z[:, :, :].rearrange("p a b -> p (a b)").rearrange("p (k t) -> p k t", k=KD)
        g = Kernel()
        g.small = sb("g_small", [P, NT, 64], to=layer)
        g.dt = sb("g_dt", [P, NT, 32], to=layer)
        g.ig = sb("g_ig", [P, NT, 16], to=layer)
        g.ea = sb("g_ea", [P, 32], to=layer)
        g.ld = sb("g_ld", [P, NT, 2 * GW], to=layer)
        g.cum = sb("g_cum", [P, NT, 2 * GW], to=layer)
        g.tot = sb("g_tot", [P, NT, 2 * GW], to=layer)
        g.wend = sb("g_wend", [P, NT, 32], to=layer)
        g.dec = sb("g_dec", [P, NT, 32], to=layer)
        g.u = sb("g_u", [P, 2, NT, ML_H], to=layer)
        mjobs = [(cols(Q0 + n * BANK, BANK), "cm") for n in range(2)] + [(cols(K0 + n * BANK, BANK), "cm") for n in range(2)] \
            + [(cols(V0 + n * BANK, BANK), "tm") for n in range(2)]
        with ExitStack() as c:
            xbc = sb("xbc", [P, XT, T], to=c)
            with ExitStack() as e:
                raw = sb("xbc_raw", [P, XT, T + 2 * PAD], to=e)
                with nc.Block(no_gpsimd_drain=True) as block:
                    @block.vector
                    def _(dve):
                        nc.vector.memset(raw[:, :, 0:PAD], 0.0)
                        nc.vector.memset(raw[:, :, T + PAD:T + 2 * PAD], 0.0)
                jobs = [(cols(Z0 + n * BANK, BANK), "tm", into_tm(z, n * BANK, BANK)) for n in range(2)]
                for n in range(3):
                    jobs.append((cols(XBC0 + n * BANK, BANK), "cm", (lambda n: lambda j, b: (raw[:, 4 * n + j, PAD:PAD + T], 1.0))(n)))
                jobs.append((cols(DT0, 32), "tm", into_tm(g.small, 0, 32)))
                jobs.append((cols(G0, 32), "tm", into_tm(g.small, 32, 32)))
                project(k, jobs, after=[mjobs[0][0], mjobs[1][0]])
                g.work = sb("g_work", [P, 6, NT, 48], to=e)
                decays(k, g, g.small[:, :, :])
                ssd_conv(k, raw, xbc)
            x_tm = sb("x_heads", [P, NT, D], to=c)
            b_tm = sb("b_tm", [P, NT, 256], to=c)
            cb = sb("cb", [P, 2, 2, T], to=c)
            hst = sb("hst", [P, 2, NT, D], to=c)
            ssd_turn(k, xbc, x_tm, b_tm, cb)
            with ExitStack() as e:
                xw = sb("xw", [P, 2, D], to=e)
                ssd_states(k, g, x_tm, b_tm, hst, xw)
            with ExitStack() as e:
                ce = sb("ssd_ce", [P, 4, T], to=e)
                buf = [xbc[:, 0:2, :], xbc[:, 2:4, :], xbc[:, 4:8, :], xbc[:, 8:10, :], ce[:, :, :]]
                y_tm = k.ytmp
                ssd_mix(k, g, xbc, x_tm, cb, hst, y_tm, buf)
            ssd_finish(k, y_tm, x_tm, z, ycm, hst[:, 0, :, :])
        with ExitStack() as c:
            q_cm = sb("q_cm", [P, ML_H, T], to=c)
            k_cm = sb("k_cm", [P, ML_H, T], to=c)
            v = sb("v_ext", [P, NT, ML_H, MW], to=c)
            with nc.Block(no_gpsimd_drain=True) as block:
                @block.vector
                def _(dve):
                    nc.vector.memset(v[:, :, :, ML_D:MW], 1.0)
            outs = [into_cm(q_cm, 0), into_cm(q_cm, 4), into_cm(k_cm, 0, ML_D ** -0.5), into_cm(k_cm, 4, ML_D ** -0.5)]
            outs += [(lambda n: lambda t, b: (v[:, t, 4 * n:4 * n + 4, 0:ML_D], 1.0))(n) for n in range(2)]
            project(k, [(*j, f) for j, f in zip(mjobs, outs)])
            states = c.enter_context(ExitStack())
            r = Kernel()
            r.nm, r.si = (sb("r_" + name, [ML_H, 2, T], to=states) for name in ("nm", "si"))
            r.ms_row, r.tot, r.mx, r.umax = (sb("r_" + name, [ML_H, 2, NT], to=states) for name in ("ms_row", "tot", "mx", "umax"))
            r.so = sb("r_so", [ML_H, 2, 2, NT], to=states)
            r.diag = sb("r_diag", [ML_H, ML_H * 4 * NT], to=states)
            r.bar = sb("r_bar", [P, 2], to=states)
            r.floor, r.ew, r.sold, r.sloc = (sb("r_" + name, [P, 2, NT, ML_H], to=states) for name in ("floor", "ew", "sold", "sloc"))
            r.den = sb("r_den", [P, NT, 2], to=states)
            r.rden = sb("r_rden", [P, NT, 2], to=states)
            with ExitStack() as e:
                r.u_row, r.cm, r.ew_row, r.restart = (sb("r_" + name, [ML_H, 2, T], to=e) for name in ("u_row", "cm", "ew_row", "restart"))
                mlstm_gates(k, g, r)
            cst = sb("cst", [P, 2, NT, ML_H, MW], to=states)
            idle = k.ring[:, :, :].rearrange("p s n -> p (s n)")
            r.own = idle[:, 2 * D:2 * D + ML_H * MW].rearrange("p (h w) -> p h w", h=ML_H)
            mlstm_states(k, r, k_cm, v, cst, idle[:, 0:2 * D].rearrange("p (s n) -> p s n", s=2))
            hm = k.ytmp
            mlstm_mix(k, g, r, q_cm, k_cm, v, cst, hm, idle[:, 0:10 * T].rearrange("p (a s n) -> p a s n", a=5, s=2))

            def as_tm(ap):
                return ap.rearrange("p a b -> p (a b)").rearrange("p (t n) -> p t n", t=NT)

            states.close()
            o, work = as_tm(k_cm[:, :, :]), as_tm(q_cm[:, :, :])
            wo = out_chunks(A["ab_w_out"][0], 16)
            project(k, [(cols(O0 + n * BANK, BANK), "tm", into_tm(o, n * BANK, BANK)) for n in range(2)], after=wo[:2], cold=True)
            gated_norm(k, hm, o, ML_H, k.pcol[:, 0, 112:120], k.h, work, ACT.Sigmoid, True)
            project_out(k, lambda n: ycm[:, n, :] if n < KD else k.h[:, n - KD, :], 16, A["ab_w_out"][0], A["norm_g"][0, 1], next_gain, after=after,
                        scratch=work)



def up_slot(k, s):
    return k.ring[:, (k.parity + s) % 2, 0:KD * 2 * P].rearrange("p (t h n) -> p t h n", t=KD, h=2)


def load_up(k, sp, w, s, at):
    wt = w.rearrange("(t p) n -> p t n", p=P)
    for half in range(2):
        sp.dma_start(up_slot(k, s)[:, :, half, :], wt[:, :, bass.ds(at + half * FFN, P)]).then_inc(k.up_loaded[s].sem, 16)


def ffn_first(k, layer):
    def load(sp):
        k.parity = sum(k.asked) % 2
        for s in range(2):
            load_up(k, sp, k.A["ffn_w_up"][layer], s, s * P)
    return load


def ffn_up(k, layer, h_hi, h_lo, g_cm, ybuf, w_hi, w_lo, down):
    nc = k.nc
    w = k.A["ffn_w_up"][layer]
    TURNS = FT // 2
    tap0, tap1 = k.pcol[:, 1 + 2 * layer, 0:2 * FT], k.pcol[:, 1 + 2 * layer, 2 * FT:4 * FT]
    tap2, bias = k.pcol[:, 2 + 2 * layer, 0:2 * FT], k.pcol[:, 2 + 2 * layer, 2 * FT:4 * FT]

    def column(cols, i, s, half):
        at = 2 * i + (s + half * FT)
        return cols[:, at:at + 1] if isinstance(i, int) else cols[:, bass.ds(at, 1)]

    def bank(s, half):
        return k.ps[:, 2 * s + half, :]

    def wait(engine, signal, i, per, more):
        sem, base = signal(0)
        engine.wait_ge(sem, i * per + (base + more))

    with nc.Block(no_gpsimd_drain=True) as block:
        @block.sync
        def _(sp):
            with sp.Fori(1, TURNS) as i:
                for s in range(2):
                    wait(sp, k.w_lo_ready, i, 4, 2 * (s - 1))
                    load_up(k, sp, w, s, i * (2 * P) + s * P)
            sp.wait_ge(*k.w_lo_ready(2 * FT))
            for chunk in down:
                load_weights(k, sp, chunk)

        @block.tensor
        def _(pe):
            def turn(i):
                for s in range(2):
                    wait(pe, k.vb, i, 2, s + 1)
                    for half in range(2):
                        wait(pe, k.w_lo_ready, i, 4, 2 * s + half + 1)
                        for c in range(KD):
                            if isinstance(i, int) and s + half == 0:
                                pe.wait_ge(*k.h_lo_ready(c + 1))
                            last = product(nc, bank(s, half), [part[:, s, half, c, :] for part in (w_hi, w_lo)], [h[:, c, :] for h in (h_hi, h_lo)],
                                           c == 0, c == KD - 1)
                    last.then_inc(k.products.sem, 1)

            turn(0)
            with pe.Fori(1, TURNS) as i:
                turn(i)

        @block.scalar
        def _(act):
            def split(i, s):
                wait(act, k.up_loaded[s], i, 32, 32)
                for half in range(2):
                    nc.scalar.copy(w_hi[:, s, half, :, :], up_slot(k, s)[:, :, half, :]).then_inc(k.w_hi_ready.sem, 1)

            def finish(i, s, ahead):
                wait(act, k.products, i, 2, s + 1)
                for half in range(2):
                    last = nc.scalar.activation(ybuf[:, s, half, :], bank(s, half), ACT.Identity, bias=column(bias, i, s, half),
                                                scale=column(tap1, i, s, half))
                last.then_inc(k.sa.sem, 1)
                if ahead:
                    split(i + 1, s)
                wait(act, k.va, i, 2, s + 1)
                nc.scalar.activation(ybuf[:, s, 0, :], ybuf[:, s, 0, :], ACT.Gelu_apprx_tanh).then_inc(k.sb.sem, 1)

            split(0, 0)
            for c in range(KD):
                nc.scalar.copy(h_hi[:, c, :], k.h[:, c, :]).then_inc(k.h_hi_ready.sem, 1)
            split(0, 1)
            with act.Fori(0, TURNS - 1) as i:
                for s in range(2):
                    finish(i, s, True)
            for s in range(2):
                finish(TURNS - 1, s, False)

        @block.gpsimd
        def _(pool):
            with pool.Fori(0, TURNS) as i:
                for s in range(2):
                    for half in range(2):
                        wait(pool, k.w_hi_ready, i, 4, 2 * s + half + 1)
                        rest(nc.gpsimd, w_lo[:, s, half, :, :], up_slot(k, s)[:, :, half, :], w_hi[:, s, half, :, :]).then_inc(k.w_lo_ready.sem, 1)
            pool.drain()

        @block.vector
        def _(dve):
            nc.vector.sem_inc(k.vb.sem, 2)
            for c in range(KD):
                dve.wait_ge(*k.h_hi_ready(c + 1))
                rest(nc.vector, h_lo[:, c, :], k.h[:, c, :], h_hi[:, c, :]).then_inc(k.h_lo_ready.sem, 1)
            with dve.Fori(0, TURNS) as i:
                for s in range(2):
                    wait(dve, k.sa, i, 2, s + 1)
                    for half in range(2):
                        nc.vector.scalar_tensor_tensor(out=ybuf[:, s, half, 1:T], in0=bank(s, half)[:, 0:T - 1], scalar=column(tap0, i, s, half),
                                                       in1=ybuf[:, s, half, 1:T], op0=ALU.mult, op1=ALU.add)
                    dve.drain()
                    for half in range(2):
                        last = nc.vector.scalar_tensor_tensor(out=ybuf[:, s, half, 0:T - 1], in0=bank(s, half)[:, 1:T], scalar=column(tap2, i, s, half),
                                                              in1=ybuf[:, s, half, 0:T - 1], op0=ALU.mult, op1=ALU.add)
                    last.then_inc(k.va.sem, 1)
                    dve.drain()
                    wait(dve, k.sb, i, 2, s + 1)
                    nc.vector.tensor_tensor(g_cm[:, bass.ds(2 * i + s, 1), :].rearrange("p o t -> p (o t)"), ybuf[:, s, 0, :], ybuf[:, s, 1, :],
                                            ALU.mult).then_inc(k.vb.sem, 1)
    for signal in (k.products, k.sa, k.sb, k.va):
        signal.close(FT)
    k.vb.close(FT + 2)
    k.h_hi_ready.close(KD)
    k.h_lo_ready.close(KD)
    k.w_hi_ready.close(2 * FT)
    k.w_lo_ready.close(2 * FT)
    for s in range(2):
        k.up_loaded[s].close(32 * TURNS)


def ffn(k, layer, gain, next_gain, after):
    with ExitStack() as c:
        g_cm = k.alloc("ffn_g", [P, FT, T], to=c)
        down = out_chunks(k.A["ffn_w_down"][layer], FT)
        with ExitStack() as e:
            ybuf = k.ytmp[:, 0:2, :].rearrange("p s (h t) -> p s h t", h=2)
            h_hi, h_lo = (k.alloc("ffn_h_" + name, [P, KD, T], F32R, e) for name in ("hi", "lo"))
            w_hi, w_lo = (k.alloc("ffn_w_" + name, [P, 2, 2, KD, P], F32R, e) for name in ("hi", "lo"))
            ffn_up(k, layer, h_hi, h_lo, g_cm, ybuf, w_hi, w_lo, down[:2])
        project_out(k, lambda n: g_cm[:, n, :], FT, k.A["ffn_w_down"][layer], gain, next_gain, after=after, scratch=k.ytmp)



def gla_decay(k, glr, w2, bc, restart):
    nc = k.nc
    H = GLA_H
    bias = k.pcol[:, 5, 8:16]
    neg, low = bc.neg, bc.low

    def flat(ap, d):
        return ap[:, d * H:(d + 1) * H, :].rearrange("p a b -> p (a b)")

    with nc.Block(no_gpsimd_drain=True) as block:
        @block.gpsimd
        def _(pool):
            nc.gpsimd.memset(restart[:, :, :], 1.0)
            pool.drain()
            for d, at in ((0, 0), (1, GLA_L - 1)):
                nc.gpsimd.memset(restart[:, d, :].rearrange("p (c l) -> p c l", l=GLA_L)[:, :, at:at + 1], 0.0)
            pool.drain()
            nc.gpsimd.memset(bc.bar[:, 0:1], 0.0).then_inc(k.ga.sem, 1)
            pool.drain()

        @block.tensor
        def _(pe):
            for d in range(2):
                for h in range(H):
                    last = nc.tensor.matmul(k.ps[:, d * H + h, :], w2[:, d, h * P:(h + 1) * P], glr[:, d, :], start=True, stop=True)
                last.then_inc(k.pa.sem, 1)

        @block.scalar
        def _(act):
            for d in range(2):
                act.wait_ge(*k.pa(d + 1))
                for h in range(H):
                    last = nc.scalar.activation(bc.z[:, d * H + h, :], k.ps[:, d * H + h, :], ACT.Identity, bias=bias[:, d * H + h:d * H + h + 1])
                last.then_inc(k.sa.sem, 1)
            for d in range(2):
                act.wait_ge(*k.va(d + 1))
                nc.scalar.activation(flat(neg, d), flat(neg, d), ACT.Exp)
            act.drain()
            for d in range(2):
                nc.scalar.activation(flat(neg, d), flat(neg, d), ACT.Ln, bias=k.ones[:, 0:1]).then_inc(k.sb.sem, 1)

        @block.vector
        def _(dve):
            for d in range(2):
                dve.wait_ge(*k.sa(d + 1))
                nc.vector.scalar_tensor_tensor(out=flat(neg, d), in0=flat(bc.z, d), scalar=-1.0, in1=flat(bc.z, d), op0=ALU.mult, op1=ALU.min)\
                    .then_inc(k.va.sem, 1)
            dve.wait_ge(*k.ga(1))
            for d in range(2):
                dve.wait_ge(*k.sb(d + 1))
                nc.vector.scalar_tensor_tensor(out=flat(low, d), in0=flat(bc.z, d), scalar=0.0, in1=flat(neg, d), op0=ALU.min, op1=ALU.subtract)
                dve.drain()
                for h in range(H):
                    n = d * H + h
                    way = slice(None) if d == 0 else slice(None, None, -1)
                    nc.vector.tensor_tensor_scan(bc.sum[:, n, :][:, way], restart[:, d, :][:, way], low[:, n, :][:, way], 0.0, ALU.mult, ALU.add)
    k.ga.close(1)
    k.pa.close(2)
    k.sa.close(2)
    k.sb.close(2)
    k.va.close(2)


def gla_scale(k, bc, q_cm, k_cm, q_in, kd, kw, dec):
    nc = k.nc
    H = GLA_H
    S = 1.0 / GLA_TAU
    tiles = [(d, h) for d in range(2) for h in range(H)]

    def chunks(ap):
        return ap.rearrange("p (c l) -> p c l", l=GLA_L)

    with nc.Block(no_gpsimd_drain=True) as block:
        @block.scalar
        def _(act):
            for n, (d, h) in enumerate(tiles):
                nc.scalar.activation(q_in[:, n, :], bc[:, n, :], ACT.Exp, scale=S)
                nc.scalar.activation(kd[:, n, :], bc[:, n, :], ACT.Exp, scale=-S)
                end = chunks(bc[:, n, :])[:, :, GLA_L - 1 if d == 0 else 0]
                nc.scalar.activation(dec[:, n, :], end, ACT.Exp, scale=S)
                act.wait_ge(*k.va(n + 1))
                nc.scalar.activation(kw[:, n, :], kw[:, n, :], ACT.Exp, scale=S).then_inc(k.sa.sem, 1)

        @block.vector
        def _(dve):
            for n, (d, h) in enumerate(tiles):
                at = GLA_L - 1 if d == 0 else 0
                end = chunks(bc[:, n, :])[:, :, at:at + 1]
                nc.vector.tensor_tensor(chunks(kw[:, n, :]), spread(end, [P, GC, GLA_L]), chunks(bc[:, n, :]), ALU.subtract).then_inc(k.va.sem, 1)
            for n, (d, h) in enumerate(tiles):
                dve.wait_ge(*k.sa(n + 1))
                nc.vector.tensor_tensor(q_in[:, n, :], q_in[:, n, :], q_cm[:, h, :], ALU.mult)
                nc.vector.tensor_tensor(kd[:, n, :], kd[:, n, :], k_cm[:, h, :], ALU.mult)
                nc.vector.tensor_tensor(kw[:, n, :], kw[:, n, :], k_cm[:, h, :], ALU.mult)
    k.va.close(len(tiles))
    k.sa.close(len(tiles))


def gla_mix(k, q_in, kd, kw, dec, v, o, st, att, kwt, mask):
    nc = k.nc
    H = GLA_H
    W = GLA_DV
    steps = []
    for n in range(GC - 1):
        steps += [(0, n), (1, GC - 1 - n)]

    def tile(d, h):
        return d * H + h

    with nc.Block(no_gpsimd_drain=True) as block:
        @block.gpsimd
        def _(pool):
            for d in range(2):
                nc.gpsimd.tensor_copy(mask.f[:, d, :], k.tri[d][:, :])
            pool.drain()
            nc.gpsimd.memset(mask.f[0:GLA_L, 0, GLA_L:P], 0.0)
            pool.drain()
            nc.gpsimd.memset(mask.f[GLA_L:P, 1, 0:GLA_L], 0.0)
            pool.drain()
            nc.gpsimd.memset(att[:, :, :, :], 0.0)
            nc.gpsimd.memset(st[:, 0, 0, :], 0.0)
            nc.gpsimd.memset(st[:, 1, GC - 1, :], 0.0)
            pool.drain()
            nc.gpsimd.tensor_copy(mask.u[:, :, :], mask.f[:, :, :]).then_inc(k.ga.sem, 1)
            pool.drain()

        @block.tensor
        def _(pe):
            def scores(h):
                for d in range(2):
                    n = tile(d, h)
                    u = 2 * h + d
                    if h >= 1:
                        pe.wait_ge(*k.sa(u - 1))
                    for t in range(NT):
                        last = nc.tensor.transpose(k.ps[:, d, t * P:(t + 1) * P], kw[:, n, t * P:(t + 1) * P], k.ident[:, :])
                    last.then_inc(k.pa.sem, 1)
                    if h >= 1:
                        pe.wait_ge(*k.va(u - 1))
                    for t in range(NT):
                        tok = slice(t * P, (t + 1) * P)
                        last = nc.tensor.matmul(k.ps[:, 2 + d, tok], kd[:, n, tok], q_in[:, n, tok], start=True, stop=True, skip_group_check=True)
                    last.then_inc(k.pb.sem, 1)

            def states(h):
                pe.wait_ge(*k.sa(2 * h + 2))
                for m, (d, c) in enumerate(steps):
                    at = h * len(steps) + m
                    if at >= 2:
                        pe.wait_ge(*k.vb(at - 1))
                    rows = slice((c % 2) * GLA_L, (c % 2 + 1) * GLA_L)
                    nc.tensor.matmul(k.ps[:, 4 + m % 2, 0:W], kwt[rows, h % 2, d, (c // 2) * P:(c // 2 + 1) * P], v[rows, c // 2, h * W:(h + 1) * W],
                                     start=True, stop=True).then_inc(k.pc.sem, 1)

            def outputs(h):
                pe.wait_ge(*k.va(2 * h + 2))
                pe.wait_ge(*k.vb((h + 1) * len(steps)))
                if h >= 1:
                    pe.wait_ge(*k.acc_free(2 * h))
                for t in range(NT):
                    out = k.ps[:, 6 + t // 2, (t % 2) * W:(t % 2 + 1) * W]
                    for d in range(2):
                        nc.tensor.matmul(out, att[:, 2 * (h % 2) + d, t, :], v[:, t, h * W:(h + 1) * W], start=(d == 0), stop=False, skip_group_check=True)
                    for c in (2 * t, 2 * t + 1):
                        half = out[(c % 2) * GLA_L:(c % 2 + 1) * GLA_L, :]
                        for d in range(2):
                            last = nc.tensor.matmul(half, q_in[:, tile(d, h), c * GLA_L:(c + 1) * GLA_L], st[:, d, c, :],
                                                    start=False, stop=True, skip_group_check=True)
                    if t % 2 == 1:
                        last.then_inc(k.acc_ready.sem, 1)

            scores(0)
            for h in range(H):
                states(h)
                if h + 1 < H:
                    scores(h + 1)
                outputs(h)

        @block.scalar
        def _(act):
            def read_o(h):
                for b in range(2):
                    act.wait_ge(*k.acc_ready(2 * h + b + 1))
                    nc.scalar.copy(o[:, 2 * b:2 * b + 2, h * W:(h + 1) * W], k.ps[:, 6 + b, :].rearrange("p (t w) -> p t w", t=2)).then_inc(k.acc_free.sem, 1)

            for h in range(H):
                for d in range(2):
                    u = 2 * h + d
                    act.wait_ge(*k.pa(u + 1))
                    if h >= 2:
                        act.wait_ge(*k.pc((h - 1) * len(steps)))
                    nc.scalar.copy(kwt[:, h % 2, d, :], k.ps[:, d, :]).then_inc(k.sa.sem, 1)
                if h >= 1:
                    read_o(h - 1)
            read_o(H - 1)

        @block.vector
        def _(dve):
            dve.wait_ge(*k.ga(1))

            def masked(h):
                for d in range(2):
                    u = 2 * h + d
                    dve.wait_ge(*k.pb(u + 1))
                    if h >= 2:
                        dve.wait_ge(*k.acc_ready(2 * (h - 1)))
                    nc.vector.copy_predicated(att[:, 2 * (h % 2) + d, :, :], spread(mask.u[:, d, :].rearrange("p (o l) -> p o l", o=1), [P, NT, P]),
                                              k.ps[:, 2 + d, :].rearrange("p (t l) -> p t l", t=NT)).then_inc(k.va.sem, 1)

            masked(0)
            for h in range(H):
                if h >= 1:
                    dve.wait_ge(*k.acc_ready(2 * h))
                for m, (d, c) in enumerate(steps):
                    nxt = c + 1 if d == 0 else c - 1
                    dve.wait_ge(*k.pc(h * len(steps) + m + 1))
                    dve.drain()
                    nc.vector.scalar_tensor_tensor(out=st[:, d, nxt, :], in0=st[:, d, c, :], scalar=dec[:, tile(d, h), c:c + 1],
                                                   in1=k.ps[:, 4 + m % 2, 0:W], op0=ALU.mult, op1=ALU.add).then_inc(k.vb.sem, 1)
                if h + 1 < H:
                    masked(h + 1)
    k.ga.close(1)
    k.pa.close(2 * H)
    k.pb.close(2 * H)
    k.pc.close(H * len(steps))
    k.sa.close(2 * H)
    k.va.close(2 * H)
    k.vb.close(H * len(steps))
    k.acc_ready.close(2 * H)
    k.acc_free.close(2 * H)


GLA_R0 = 3 * D
GLA_JOBS = (0, BANK, D, D + BANK, 2 * D, 2 * D + BANK, GLA_R0, GLA_R0 + GLA_RANK)


def gla_weights(k):
    w = k.A["c_w_in"][0]
    return [w[:, at:at + (BANK if at < GLA_R0 else GLA_RANK)] for at in GLA_JOBS]


def layer1_mixer(k, next_gain, after):
    nc, A, sb = k.nc, k.A, k.alloc
    with ExitStack() as c:
        qk = sb("gla_qk", [P, 2 * GLA_H, T], to=c)
        q_cm, k_cm = qk[:, 0:GLA_H, :], qk[:, GLA_H:2 * GLA_H, :]
        v = sb("gla_v", [P, NT, D], to=c)
        r = sb("gla_r", [P, NT, D], to=c)
        dec = sb("gla_dec", [P, 2 * GLA_H, GC], to=c)
        glr = k.gpost[0:GLA_RANK, :].rearrange("p (d t) -> p d t", d=2)
        outs = [lambda j, b: (q_cm[:, j, :], GLA_DK ** -0.5), lambda j, b: (k_cm[:, j, :], 1.0)]
        for dst in (v, r):
            outs += [(lambda dst, n: lambda t, b: (dst[:, t, n * BANK:(n + 1) * BANK], 1.0))(dst, n) for n in range(2)]
        outs += [(lambda d: lambda j, b: (glr[:, d, :], 1.0))(d) for d in range(2)]
        kinds = ["cm", "cm", "tm", "tm", "tm", "tm", "cm", "cm"]
        wo = out_chunks(A["c_w_out"][0], KD)

        project(k, list(zip(gla_weights(k), kinds, outs)), after=wo[:2])
        scan = c.enter_context(ExitStack())
        q_in = sb("gla_q_in", [P, 2 * GLA_H, T], to=scan)
        kd = sb("gla_kd", [P, 2 * GLA_H, T], to=scan)
        kw = sb("gla_kw", [P, 2 * GLA_H, T], to=scan)
        early = c.enter_context(ExitStack())
        w2 = sb("gla_w2", [GLA_RANK, 2, GLA_H * P], to=early)
        restart = sb("gla_restart", [P, 2, T], to=early)
        bc = Kernel()
        bc.bar = sb("gla_bar", [P, 1], to=early)
        bc.z, bc.neg, bc.low = q_in, kd, kw
        bc.sum = k.ytmp[:, :, :].rearrange("p a b -> p (a b)").rearrange("p (n t) -> p n t", t=T)
        with nc.Block(no_gpsimd_drain=True) as block:
            @block.sync
            def _(sp):
                sp.dma_start(w2[:, :, :], A["c_gate_w2"][0].rearrange("d r n -> r d n")).then_inc(k.param_loaded.sem, 16)
                sp.wait_ge(*k.param_loaded(16))
        k.param_loaded.close(16)
        gla_decay(k, glr, w2, bc, restart)
        early.close()
        gla_scale(k, bc.sum, q_cm, k_cm, q_in, kd, kw, dec)
        with ExitStack() as e:
            att = sb("gla_att", [P, 4, NT, P], to=e)
            kwt = sb("gla_kwt", [P, 2, 2, T], to=e)
            mask = Kernel()
            mask.f = sb("gla_mask", [P, 2, P], to=e)
            mask.u = sb("gla_mask_u", [P, 2, P], U32, to=e)
            st = qk[:, :, :].rearrange("p a b -> p (a b)").rearrange("p (d c w) -> p d c w", d=2, c=GC)
            gla_mix(k, q_in, kd, kw, dec, v, k.ytmp, st, att, kwt, mask)
        work = kd[:, :, :].rearrange("p a b -> p (a b)").rearrange("p (t n) -> p t n", t=NT)
        gated_norm(k, k.ytmp, r, GLA_H, k.pcol[:, 5, 0:8], k.h, work, ACT.Silu, False)
        scan.close()
        project_out(k, lambda n: k.h[:, n, :], KD, A["c_w_out"][0], A["norm_g"][1, 1], next_gain, after=after, scratch=k.ytmp)



def turn(k, src, dst, tiles):
    nc = k.nc
    with nc.Block(no_gpsimd_drain=True) as block:
        @block.tensor
        def _(pe):
            for c in range(tiles):
                for t in range(NT):
                    last = nc.tensor.transpose(k.ps[:, c % NBANKS, t * P:(t + 1) * P], src[:, t, c * P:(c + 1) * P], k.ident[:, :])
                last.then_inc(k.pa.sem, 1)

        @block.scalar
        def _(act):
            for c in range(0, tiles, 2):
                act.wait_ge(*k.pa(c + 1))
                nc.scalar.copy(dst[:, c, :], k.ps[:, c, :])

        @block.vector
        def _(dve):
            for c in range(1, tiles, 2):
                dve.wait_ge(*k.pa(c + 1))
                nc.vector.tensor_copy(dst[:, c, :], k.ps[:, c, :])
    k.pa.close(tiles)


def head_norm_tm(k, src, dst, tiles, heads, width, gain, sq):
    nc = k.nc
    ms, root, rstd = (k.stat[:, n, 0:tiles * heads].rearrange("p (t h) -> p t h", h=heads) for n in range(3))

    def per_head(ap):
        return ap.rearrange("p (h e) -> p h e", h=heads)

    with nc.Block(no_gpsimd_drain=True) as block:
        @block.vector
        def _(dve):
            for t in range(tiles):
                nc.vector.tensor_tensor(sq[:, t, 0:heads * width], src[:, t, 0:heads * width], src[:, t, 0:heads * width], ALU.mult)
            dve.drain()
            for t in range(tiles):
                nc.vector.tensor_reduce(ms[:, t, :], per_head(sq[:, t, 0:heads * width]), AX.X, ALU.add)
            dve.drain()
            nc.vector.tensor_scalar(ms, ms, 1.0 / width, EPS, ALU.mult, ALU.add).then_inc(k.mean_ready.sem, 1)
            dve.wait_ge(*k.root_ready(1))
            nc.vector.reciprocal(rstd, root)
            dve.drain()
            for t in range(tiles):
                nc.vector.tensor_tensor(per_head(dst[:, t, 0:heads * width]), per_head(src[:, t, 0:heads * width]),
                                        spread(rstd[:, t, :].rearrange("p (h o) -> p h o", o=1), [P, heads, width]), ALU.mult)
            dve.drain()
            for t in range(tiles):
                nc.vector.tensor_tensor(per_head(dst[:, t, 0:heads * width]), per_head(dst[:, t, 0:heads * width]),
                                        spread(gain.rearrange("p (o e) -> p o e", o=1), [P, heads, width]), ALU.mult)

        @block.scalar
        def _(act):
            act.wait_ge(*k.mean_ready(1))
            nc.scalar.activation(root, ms, ACT.Sqrt).then_inc(k.root_ready.sem, 1)
    k.mean_ready.close(1)
    k.root_ready.close(1)


def attend(k, heads, query, key, keys_of, bias, value, width, scale, o, buf):
    nc = k.nc
    units = [(t, h) for t in range(NT) for h in range(heads)]
    s, p, pt = buf
    top, ntop, total, rtotal = (k.stat[:, n, 0:NT * heads].rearrange("p (t h) -> p t h", h=heads) for n in range(4))

    with nc.Block(no_gpsimd_drain=True) as block:
        @block.tensor
        def _(pe):
            def scores(n):
                t, h = units[n]
                if n >= 2:
                    pe.wait_ge(*k.va(n - 1))
                nc.tensor.matmul(k.ps[:, n % 2, 0:keys_of(t)], query(t, h), key(h, keys_of(t)), start=True, stop=True).then_inc(k.pa.sem, 1)

            def turned(n):
                t, h = units[n]
                pe.wait_ge(*k.sa(n + 1))
                if n >= 2:
                    pe.wait_ge(*k.sb(n - 1))
                for b in range(keys_of(t) // P):
                    last = nc.tensor.transpose(k.ps[:, 2 + n % 2, b * P:(b + 1) * P], p[:, n % 2, b * P:(b + 1) * P], k.ident[:, :])
                last.then_inc(k.pb.sem, 1)

            def values(n):
                t, h = units[n]
                pe.wait_ge(*k.sb(n + 1))
                if h == 0 and t >= 2:
                    pe.wait_ge(*k.vb(t - 1))
                nb = keys_of(t) // P
                for b in range(nb):
                    last = nc.tensor.matmul(k.ps[:, 4 + t % 2, h * width:(h + 1) * width], pt[:, n % 2, b * P:(b + 1) * P], value(h, b),
                                            start=(b == 0), stop=(b == nb - 1), skip_group_check=True)
                last.then_inc(k.pc.sem, 1)

            scores(0)
            for n in range(len(units)):
                if n + 1 < len(units):
                    scores(n + 1)
                if n >= 1:
                    turned(n - 1)
                if n >= 2:
                    values(n - 2)
            turned(len(units) - 1)
            values(len(units) - 2)
            values(len(units) - 1)

        @block.vector
        def _(dve):
            def largest(n):
                t, h = units[n]
                ps = k.ps[:, n % 2, 0:keys_of(t)]
                dve.wait_ge(*k.pa(n + 1))
                if n >= 2:
                    dve.wait_ge(*k.sa(n - 1))
                if bias is None:
                    nc.vector.tensor_copy(s[:, n % 2, 0:keys_of(t)], ps)
                else:
                    nc.vector.tensor_tensor(s[:, n % 2, 0:keys_of(t)], ps, bias(t, keys_of(t)), ALU.add)
                dve.drain()
                nc.vector.tensor_reduce(top[:, t, h:h + 1], s[:, n % 2, 0:keys_of(t)], AX.X, ALU.max)
                dve.drain()
                nc.vector.tensor_scalar(ntop[:, t, h:h + 1], top[:, t, h:h + 1], -scale, None, ALU.mult).then_inc(k.va.sem, 1)

            def read_out(t):
                dve.wait_ge(*k.sa((t + 1) * heads))
                nc.vector.reciprocal(rtotal[:, t, :], total[:, t, :])
                dve.wait_ge(*k.pc((t + 1) * heads))
                dve.drain()
                nc.vector.tensor_tensor(o[:, t, :].rearrange("p (h e) -> p h e", h=heads), k.ps[:, 4 + t % 2, 0:heads * width].rearrange("p (h e) -> p h e", h=heads),
                                        spread(rtotal[:, t, :].rearrange("p (h o) -> p h o", o=1), [P, heads, width]), ALU.mult).then_inc(k.vb.sem, 1)

            for n, (t, h) in enumerate(units):
                largest(n)
                if h == 2 and t >= 1:
                    read_out(t - 1)
            read_out(NT - 1)

        @block.scalar
        def _(act):
            def out(n):
                t, h = units[n]
                act.wait_ge(*k.pb(n + 1))
                if n >= 2:
                    act.wait_ge(*k.pc(n - 1))
                nc.scalar.copy(pt[:, n % 2, 0:keys_of(t)], k.ps[:, 2 + n % 2, 0:keys_of(t)]).then_inc(k.sb.sem, 1)

            for n, (t, h) in enumerate(units):
                act.wait_ge(*k.va(n + 1))
                if n >= 2:
                    act.wait_ge(*k.pb(n - 1))
                nc.scalar.activation(p[:, n % 2, 0:keys_of(t)], s[:, n % 2, 0:keys_of(t)], ACT.Exp, bias=ntop[:, t, h:h + 1], scale=scale,
                                     accum_out=total[:, t, h:h + 1]).then_inc(k.sa.sem, 1)
                if n >= 1:
                    out(n - 1)
            out(len(units) - 1)
    n = len(units)
    for sg in (k.pa, k.pb, k.pc, k.va, k.sa, k.sb):
        sg.close(n)
    k.vb.close(NT)



QK_HEADS = NQ + NKV
ROT = QK_HEADS + NIDX + 1


def rope(k, att, rot, tab, tmp):
    nc = k.nc
    half = HD // 2
    parts = [(0, QK_HEADS, QA0), (QK_HEADS, NIDX + 1, QI0)]
    with nc.Block(no_gpsimd_drain=True) as block:
        @block.vector
        def _(dve):
            for t in range(NT):
                for h0, n, at in parts:
                    x = att[:, t, at:at + n * HD].rearrange("p (h s e) -> p h s e", h=n, s=2)
                    y = rot[:, t, h0 * HD:(h0 + n) * HD].rearrange("p (h s e) -> p h s e", h=n, s=2)
                    cos, sin = (spread(tab[:, t, f * half:(f + 1) * half].rearrange("p (o e) -> p o e", o=1), [P, n, half]) for f in range(2))
                    nc.vector.tensor_tensor(y[:, :, 0, :], x[:, :, 0, :], cos, ALU.mult)
                    nc.vector.tensor_tensor(y[:, :, 1, :], x[:, :, 1, :], cos, ALU.mult)
                    nc.vector.tensor_tensor(tmp[:, 0, h0:h0 + n, :], x[:, :, 1, :], sin, ALU.mult)
                    nc.vector.tensor_tensor(tmp[:, 1, h0:h0 + n, :], x[:, :, 0, :], sin, ALU.mult)
                dve.drain()
                for h0, n, at in parts:
                    y = rot[:, t, h0 * HD:(h0 + n) * HD].rearrange("p (h s e) -> p h s e", h=n, s=2)
                    nc.vector.tensor_tensor(y[:, :, 0, :], y[:, :, 0, :], tmp[:, 0, h0:h0 + n, :], ALU.subtract)
                    nc.vector.tensor_tensor(y[:, :, 1, :], y[:, :, 1, :], tmp[:, 1, h0:h0 + n, :], ALU.add)
                dve.drain()


PAIR_K, PAIR_QI, PAIR_KI = NQ // 2, NQ // 2 + NKV, NQ // 2 + NKV + NIDX // 2
PAIRS = PAIR_KI + 1


def turn_heads(k, rot, cm, twice):
    nc = k.nc
    doubled = [(PAIR_K, NQ), (PAIR_K + 1, NQ + 1), (PAIR_KI, QK_HEADS + NIDX)]
    with nc.Block(no_gpsimd_drain=True) as block:
        @block.vector
        def _(dve):
            for n, (_, h) in enumerate(doubled):
                for half in range(2):
                    last = nc.vector.tensor_copy(twice[:, n, :, half * HD:(half + 1) * HD], rot[:, :, h * HD:(h + 1) * HD])
            last.then_inc(k.va.sem, 1)
            for c in range(1, PAIRS, 2):
                dve.wait_ge(*k.pa(c + 1))
                nc.vector.tensor_copy(cm[:, c, :], k.ps[:, c % NBANKS, :]).then_inc(k.vb.sem, 1)

        @block.tensor
        def _(pe):
            pe.wait_ge(*k.va(1))
            for c in range(PAIRS):
                if c >= NBANKS:
                    if c % 2:
                        pe.wait_ge(*k.vb((c - NBANKS) // 2 + 1))
                    else:
                        pe.wait_ge(*k.sa((c - NBANKS) // 2 + 1))
                found = [n for n, (pair, _) in enumerate(doubled) if pair == c]
                for t in range(NT):
                    if found:
                        src = twice[:, found[0], t, :]
                    else:
                        h = 2 * c if c < PAIR_K else QK_HEADS + 2 * (c - PAIR_QI)
                        src = rot[:, t, h * HD:(h + 2) * HD]
                    last = nc.tensor.transpose(k.ps[:, c % NBANKS, t * P:(t + 1) * P], src, k.ident[:, :])
                last.then_inc(k.pa.sem, 1)

        @block.scalar
        def _(act):
            for c in range(0, PAIRS, 2):
                act.wait_ge(*k.pa(c + 1))
                nc.scalar.copy(cm[:, c, :], k.ps[:, c % NBANKS, :]).then_inc(k.sa.sem, 1)
    k.va.close(1)
    k.pa.close(PAIRS)
    k.vb.close(PAIRS // 2)
    k.sa.close((PAIRS + 1) // 2)


def index_scores(k, cm, w_idx, score, relu):
    nc = k.nc
    units = [(t, h) for t in range(1, NT) for h in range(NIDX)]
    with nc.Block(no_gpsimd_drain=True) as block:
        @block.tensor
        def _(pe):
            for n, (t, h) in enumerate(units):
                rows = slice((h % 2) * HD, (h % 2 + 1) * HD)
                if n >= 4:
                    pe.wait_ge(*k.sa(n - 3))
                nc.tensor.matmul(k.ps[:, n % 4, 0:(t + 1) * P], cm[rows, PAIR_QI + h // 2, t * P:(t + 1) * P], cm[rows, PAIR_KI, 0:(t + 1) * P],
                                 start=True, stop=True).then_inc(k.pa.sem, 1)

        @block.scalar
        def _(act):
            for n, (t, h) in enumerate(units):
                act.wait_ge(*k.pa(n + 1))
                if n >= 4:
                    act.wait_ge(*k.va(n - 3))
                nc.scalar.activation(relu[:, n % 4, 0:(t + 1) * P], k.ps[:, n % 4, 0:(t + 1) * P], ACT.Relu, scale=HD ** -0.5).then_inc(k.sa.sem, 1)

        @block.vector
        def _(dve):
            nc.vector.tensor_scalar(w_idx, w_idx, NIDX ** -0.5, None, ALU.mult)
            dve.drain()
            for n, (t, h) in enumerate(units):
                dve.wait_ge(*k.sa(n + 1))
                out, r, w = score[:, t, 0:(t + 1) * P], relu[:, n % 4, 0:(t + 1) * P], w_idx[:, t, h:h + 1]
                if h == 0:
                    nc.vector.tensor_scalar(out, r, w, None, ALU.mult).then_inc(k.va.sem, 1)
                else:
                    dve.drain()
                    nc.vector.scalar_tensor_tensor(out=out, in0=r, scalar=w, in1=out, op0=ALU.mult, op1=ALU.add).then_inc(k.va.sem, 1)

        @block.gpsimd
        def _(pool):
            for t in range(1, NT):
                pool.wait_ge(*k.va(t * NIDX))
                nc.gpsimd.affine_select(out=score[:, t, t * P:(t + 1) * P], in_=score[:, t, t * P:(t + 1) * P], compare_op=ALU.is_ge, fill=-BIG, base=0,
                                        pattern=[[-1, P]], channel_multiplier=1)
            pool.drain()
    n = len(units)
    k.pa.close(n)
    k.sa.close(n)
    k.va.close(n)


TAKEN = -3e38


def choose(k, dve, score, eight):
    nc = k.nc
    tiles = range(1, NT)
    for step in range(TOPK // 8):
        for t in tiles:
            nc.vector.max(eight[:, t, :], score[:, t, 0:(t + 1) * P])
        dve.drain()
        for t in tiles:
            nc.vector.match_replace(score[:, t, 0:(t + 1) * P], eight[:, t, :], score[:, t, 0:(t + 1) * P], TAKEN)
        dve.drain()
    for t in tiles:
        nc.vector.tensor_scalar(score[:, t, 0:(t + 1) * P], score[:, t, 0:(t + 1) * P], -2 * BIG, BIG, ALU.is_lt, ALU.mult)
    nc.vector.tensor_scalar(score[:, 0, 0:P], k.tri[1][:, :], BIG, None, ALU.mult)
    dve.drain()
    for t in range(NT):
        nc.vector.tensor_scalar(score[:, t, 0:(t + 1) * P], score[:, t, 0:(t + 1) * P], -BIG, None, ALU.add)



def conv_gate(k, u, gate):
    nc = k.nc
    with nc.Block(no_gpsimd_drain=True) as block:
        @block.scalar
        def _(act):
            nc.scalar.activation(gate[:, :, :], gate[:, :, :], ACT.Sigmoid).then_inc(k.sa.sem, 1)

        @block.vector
        def _(dve):
            nc.vector.memset(u[:, :, 0:CONV_W - 1], 0.0)
            dve.wait_ge(*k.sa(1))
            for j in range(CT):
                nc.vector.tensor_tensor(u[:, j, CONV_W - 1:], u[:, j, CONV_W - 1:], gate[:, j, :], ALU.mult)
    k.sa.close(1)


def conv_taps(k, dve, u, y):
    nc = k.nc
    tap, bias = k.pcol[:, 6, :], k.pcol[:, 5, 40:44]
    for j in range(CT):
        nc.vector.tensor_scalar(y[:, j, :], u[:, j, 0:T], tap[:, j:j + 1], bias[:, j:j + 1], ALU.mult, ALU.add)
    for i in range(1, CONV_W):
        dve.drain()
        for j in range(CT):
            nc.vector.scalar_tensor_tensor(out=y[:, j, :], in0=u[:, j, i:i + T], scalar=tap[:, i * CT + j:i * CT + j + 1], in1=y[:, j, :],
                                           op0=ALU.mult, op1=ALU.add)


def conv_norm(k, y, ob, y_tm, sq):
    nc = k.nc
    gain, shift = k.pcol[:, 5, 44:48], k.pcol[:, 5, 48:52]
    mean, var, root, rstd = (k.stat[:, n, 0:NT] for n in range(4))
    with nc.Block(no_gpsimd_drain=True) as block:
        @block.tensor
        def _(pe):
            for t in range(NT):
                for j in range(CT):
                    last = nc.tensor.transpose(k.ps[:, t, j * P:(j + 1) * P], y[:, j, t * P:(t + 1) * P], k.ident[:, :])
                last.then_inc(k.pa.sem, 1)
            pe.wait_ge(*k.va(1))
            for j in range(CT):
                for t in range(NT):
                    last = nc.tensor.transpose(k.ps[:, 4 + j, t * P:(t + 1) * P], y_tm[:, t, j * P:(j + 1) * P], k.ident[:, :])
                last.then_inc(k.pb.sem, 1)

        @block.vector
        def _(dve):
            for t in range(NT):
                dve.wait_ge(*k.pa(t + 1))
                nc.vector.tensor_reduce(mean[:, t:t + 1], k.ps[:, t, :], AX.X, ALU.add)
            dve.drain()
            nc.vector.tensor_scalar(mean, mean, 1.0 / CONV_C, None, ALU.mult)
            dve.drain()
            for t in range(NT):
                nc.vector.tensor_scalar(y_tm[:, t, :], k.ps[:, t, :], mean[:, t:t + 1], None, ALU.subtract)
            dve.drain()
            for t in range(NT):
                nc.vector.tensor_tensor_reduce(out=sq[:, t, :], in0=y_tm[:, t, :], in1=y_tm[:, t, :], scale=1.0, scalar=0.0, op0=ALU.mult, op1=ALU.add,
                                               accum_out=var[:, t:t + 1])
            dve.drain()
            nc.vector.tensor_scalar(var, var, 1.0 / CONV_C, EPS, ALU.mult, ALU.add).then_inc(k.mean_ready.sem, 1)
            dve.wait_ge(*k.root_ready(1))
            nc.vector.reciprocal(rstd, root)
            dve.drain()
            for t in range(NT):
                last = nc.vector.tensor_scalar(y_tm[:, t, :], y_tm[:, t, :], rstd[:, t:t + 1], None, ALU.mult)
            last.then_inc(k.va.sem, 1)

        @block.scalar
        def _(act):
            act.wait_ge(*k.mean_ready(1))
            nc.scalar.activation(root, var, ACT.Sqrt).then_inc(k.root_ready.sem, 1)
            for j in range(CT):
                act.wait_ge(*k.pb(j + 1))
                nc.scalar.activation(ob[:, j, :], k.ps[:, 4 + j, :], ACT.Silu, bias=shift[:, j:j + 1], scale=gain[:, j:j + 1])
    k.pa.close(NT)
    k.pb.close(CT)
    k.va.close(1)
    k.mean_ready.close(1)
    k.root_ready.close(1)



def merge(k, branches, weights, gates, bgate, m, tmp, after):
    nc = k.nc
    NB = len(branches)
    with nc.Block(no_gpsimd_drain=True) as block:
        @block.sync
        def _(sp):
            sp.wait_ge(*k.acc_ready(NT))
            load_weights(k, sp, weights[2])
            sp.wait_ge(*k.acc_ready(2 * NT))
            load_weights(k, sp, after[0])
            sp.wait_ge(*k.acc_ready(3 * NT))
            load_weights(k, sp, after[1])

        @block.tensor
        def _(pe):
            for b in range(NB):
                w = take_weights(k, pe, CT, D)
                for t in range(NT):
                    n = b * NT + t
                    if n >= 4:
                        pe.wait_ge(*k.acc_free(n - 3))
                    for half in range(2):
                        for c in range(CT):
                            last = nc.tensor.matmul(k.ps[:, 2 * (n % 4) + half, :], branches[b][:, c, t * P:(t + 1) * P], w[:, c, half * BANK:(half + 1) * BANK],
                                                    start=(c == 0), stop=(c == CT - 1))
                    last.then_inc(k.acc_ready.sem, 1)

        @block.vector
        def _(dve):
            for b in range(NB):
                for t in range(NT):
                    g = gates[:, t, b * D:(b + 1) * D]
                    nc.vector.tensor_tensor(g, g, bgate[:, b * D:(b + 1) * D], ALU.add).then_inc(k.va.sem, 1)
            for b in range(NB):
                for t in range(NT):
                    n = b * NT + t
                    dve.wait_ge(*k.sa(n + 1))
                    dve.wait_ge(*k.acc_ready(n + 1))
                    acc = k.ps[:, 2 * (n % 4):2 * (n % 4) + 2, :].rearrange("p a b -> p (a b)")
                    dst = m[:, t, :] if b == 0 else tmp[:, n % 2, :]
                    nc.vector.tensor_tensor(dst, gates[:, t, b * D:(b + 1) * D], acc, ALU.mult).then_inc(k.acc_free.sem, 1)
                    dve.drain()
                    if b > 0:
                        nc.vector.tensor_tensor(m[:, t, :], m[:, t, :], tmp[:, n % 2, :], ALU.add)
                        dve.drain()

        @block.scalar
        def _(act):
            for n in range(NB * NT):
                act.wait_ge(*k.va(n + 1))
                g = gates[:, n % NT, (n // NT) * D:(n // NT + 1) * D]
                nc.scalar.activation(g, g, ACT.Sigmoid).then_inc(k.sa.sem, 1)
    k.acc_ready.close(NB * NT)
    k.acc_free.close(NB * NT)
    k.va.close(NB * NT)
    k.sa.close(NB * NT)


def block2_weights(k):
    w = k.A["w_in_2"][0]
    cuts = [(QA0, BANK), (QA0 + BANK, BANK), (QA0 + 2 * BANK, ATT - 2 * BANK), (CI0, BANK), (CI0 + BANK, BANK), (QM0, BANK)]
    return [w[:, at:at + n] for at, n in cuts]


def memory_weights(k):
    return [k.A["w_mem_kv_2"][0][:, n * BANK:(n + 1) * BANK] for n in range(2)]


def mixers2(k, next_gain, after):
    nc, A, sb = k.nc, k.A, k.alloc
    w = A["w_in_2"][0]

    def into_tm(dst, at, n):
        return lambda t, b: (dst[:, t, at:at + n], 1.0)

    with ExitStack() as c:
        km_cm = k.gpost[:, :].rearrange("p (h n) -> p h n", h=MH)
        vm = sb("vm_tm", [P, MT, MH * MD], to=c)
        qm = sb("qm_tm", [P, NT, MH * MD], to=c)
        u = sb("conv_u", [P, CT, T + CONV_W - 1], to=c)
        gate = sb("conv_gate", [P, CT, T], to=c)
        cm = sb("heads_cm", [P, PAIRS, T], to=c)
        va = sb("va_tm", [P, NT, NKV * HD], to=c)
        widx = sb("widx", [P, NT, NIDX], to=c)
        with ExitStack() as e:
            mem = sb("mem_tm", [P, MT, D], to=e)
            mcm = sb("mem_cm", [P, KD, MEM], to=e)
            kvw = memory_weights(k)
            with nc.Block(no_gpsimd_drain=True) as block:
                @block.sync
                def _(sp):
                    sp.dma_start(mem[:, :, :], A["mem_2"].rearrange("o (t p) d -> p (o t) d", p=P)).then_inc(k.param_loaded.sem, 16)
                    sp.wait_ge(*k.param_loaded(16))
            k.param_loaded.close(16)
            norm_to_cm(k, mem, k.pcol[:, 5, 32:40], mcm, k.ytmp, tiles=MT)
            km = k.ytmp
            proj = block2_weights(k)
            project(k, [(kvw[0], "tm", into_tm(km, 0, BANK)), (kvw[1], "tm", into_tm(vm, 0, BANK))], src=mcm, tiles=MT, after=proj[:2])
            head_norm_tm(k, km, km, MT, MH, MD, k.b["g_km_2"], mem)
            with nc.Block(no_gpsimd_drain=True) as block:
                @block.tensor
                def _(pe):
                    for h in range(MH):
                        for t in range(MT):
                            last = nc.tensor.transpose(k.ps[:, h, t * P:(t + 1) * P], km[:, t, h * MD:(h + 1) * MD], k.ident[:, :])
                        last.then_inc(k.pa.sem, 1)

                @block.scalar
                def _(act):
                    for h in range(MH):
                        act.wait_ge(*k.pa(h + 1))
                        nc.scalar.copy(km_cm[:, h, :], k.ps[:, h, 0:MEM])
            k.pa.close(MH)
        gw = [w[:, GT0 + n * BANK:GT0 + (n + 1) * BANK] for n in range(6)]
        with ExitStack() as e:
            att = sb("att_tm", [P, NT, ATT], to=e)
            outs = [into_tm(att, 0, BANK), into_tm(att, BANK, BANK), into_tm(att, 2 * BANK, ATT - 2 * BANK),
                    lambda j, b: (u[:, j, CONV_W - 1:], 1.0), lambda j, b: (gate[:, j, :], 1.0), into_tm(qm, 0, BANK)]
            kinds = ["tm", "tm", "tm", "cm", "cm", "tm"]
            project(k, list(zip(proj, kinds, outs)), after=gw[:2], depth=2)
            rot = sb("rot_tm", [P, NT, ROT * HD], to=e)
            tab = sb("rope_tab", [P, NT, HD], to=e)
            with nc.Block(no_gpsimd_drain=True) as block:
                @block.sync
                def _(sp):
                    sp.dma_start(tab[:, :, :], A["rope_table"].rearrange("(t p) e -> p t e", p=P)).then_inc(k.param_loaded.sem, 16)
                    sp.wait_ge(*k.param_loaded(16))

                @block.scalar
                def _(act):
                    nc.scalar.copy(va[:, :, :], att[:, :, VA0:VA0 + NKV * HD])
                    nc.scalar.copy(widx[:, :, :], att[:, :, WI0:WI0 + NIDX])
            k.param_loaded.close(16)
            head_norm_tm(k, att, att, NT, NQ, HD, k.b["g_qa_2"], rot)
            head_norm_tm(k, att[:, :, KA0:KA0 + NKV * HD], att[:, :, KA0:KA0 + NKV * HD], NT, NKV, HD, k.b["g_ka_2"], rot)
            head_norm_tm(k, att[:, :, KI0:KI0 + HD], att[:, :, KI0:KI0 + HD], NT, 1, HD, k.b["g_idx_k_2"], rot)
            rope(k, att, rot, tab, k.ytmp[:, 0:2, 0:ROT * HD // 2].rearrange("p s (h e) -> p s h e", h=ROT))
            twice = k.ytmp[:, 0:2, :].rearrange("p a b -> p (a b)")[:, 0:3 * NT * P].rearrange("p (n t e) -> p n t e", n=3, t=NT)
            turn_heads(k, rot, cm, twice)
        score = sb("score", [P, NT, T], to=c)
        eight = sb("eight", [P, NT, 8], to=c)
        conv_gate(k, u, gate)
        index_scores(k, cm, widx[:, :, :], score, k.ytmp[:, :, 0:T])
        head_norm_tm(k, qm, qm, NT, MH, MD, k.b["g_qm_2"], k.ytmp)
        gates = sb("gates_tm", [P, NT, 3 * D], to=c)

        def meanwhile(dve):
            choose(k, dve, score, eight)
            conv_taps(k, dve, u, gate)
        brw = [A[n][0] for n in ("w_br_a_2", "w_br_b_2", "w_br_m_2")]
        project(k, [(gw[n], "tm", into_tm(gates, n * BANK, BANK)) for n in range(6)], after=brw[:2], vector=meanwhile, split=False)
        scratch = k.ytmp[:, :, :].rearrange("p a b -> p (a b)")
        halves = [scratch[:, n * 2 * D:(n + 1) * 2 * D].rearrange("p (t n) -> p t n", t=NT) for n in range(2)]
        conv_norm(k, gate, gate, *halves)
        spare = [scratch[:, n * D:(n + 1) * D].rearrange("p (s n) -> p s n", s=2) for n in range(3)]
        o_tm, oa, om = u[:, :, 0:T], cm[:, 0:CT, :], qm
        attend(k, NQ, lambda t, h: cm[(h % 2) * HD:(h % 2 + 1) * HD, h // 2, t * P:(t + 1) * P],
               lambda h, n: cm[(h % 2) * HD:(h % 2 + 1) * HD, PAIR_K + h // (NQ // NKV), 0:n], lambda t: (t + 1) * P,
               lambda t, n: score[:, t, 0:n], lambda h, b: va[:, b, (h // (NQ // NKV)) * HD:(h // (NQ // NKV) + 1) * HD], HD, HD ** -0.5, o_tm, spare)
        turn(k, o_tm, oa, CT)
        qm_cm = score
        turn(k, qm, qm_cm, CT)
        attend(k, MH, lambda t, h: qm_cm[:, h, t * P:(t + 1) * P], lambda h, n: km_cm[:, h, 0:n], lambda t: MEM, None,
               lambda h, b: vm[:, b, h * MD:(h + 1) * MD], MD, MD ** -0.5, o_tm, spare)
        turn(k, o_tm, om, CT)
        wo = out_chunks(A["w_o_2"][0], KD)
        bgate = cm[:, CT:CT + 3 * D // T, :].rearrange("p a b -> p (a b)")
        products = u[:, :, :].rearrange("p a b -> p (a b)")[:, 0:2 * D].rearrange("p (n d) -> p n d", n=2)
        with nc.Block(no_gpsimd_drain=True) as block:
            @block.sync
            def _(sp):
                sp.dma_start(bgate, everywhere(A["b_gate_2"][0], 3 * D)).then_inc(k.param_loaded.sem, 16)
                sp.wait_ge(*k.param_loaded(16))
        k.param_loaded.close(16)
        merge(k, [oa, gate, om], brw, gates, bgate, k.ytmp, products, wo)
    turn(k, k.ytmp, k.h, KD)
    project_out(k, lambda n: k.h[:, n, :], KD, A["w_o_2"][0], None, next_gain, after=after, scratch=k.ytmp)



def route(k, wr, r, rows, rows_dram):
    nc = k.nc
    n = NG + NE
    lg, ex, oneg, m1, m2, one1, one2, tmp, desc = r.lg, r.ex, r.oneg, r.m1, r.m2, r.one1, r.one2, r.tmp, r.desc

    def each(ap, w):
        return spread(ap, [P, NT, w])

    with nc.Block(no_gpsimd_drain=True) as block:
        @block.sync
        def _(sp):
            sp.dma_start(wr[:, :, 0:NG], k.A["w_rg_2"][0].rearrange("(t p) n -> p t n", p=P)).then_inc(k.weights_loaded.sem, 16)
            sp.dma_start(wr[:, :, NG:], k.A["w_re_2"][0].rearrange("(t p) n -> p t n", p=P)).then_inc(k.weights_loaded.sem, 16)
            sp.dma_start(rows_dram.rearrange("(t p) d -> p t d", p=P), rows).then_inc(k.param_loaded.sem, 16)
            sp.wait_ge(*k.param_loaded(16))

        @block.gpsimd
        def _(pool):
            for e in range(NE):
                nc.gpsimd.memset(desc[:, e:e + 1], float(NE - e))
            pool.drain()
            nc.gpsimd.memset(r.bar[:, 0:1], 0.0).then_inc(k.ga.sem, 1)
            pool.drain()

        @block.tensor
        def _(pe):
            pe.wait_ge(*k.weights_loaded(32))
            for t in range(NT):
                for c in range(KD):
                    last = nc.tensor.matmul(k.ps[:, 0, t * n:(t + 1) * n], k.h[:, c, t * P:(t + 1) * P], wr[:, c, :], start=(c == 0), stop=(c == KD - 1),
                                            skip_group_check=True)
            last.then_inc(k.pa.sem, 1)

        @block.vector
        def _(dve):
            def first(out, values, top, w, fall):
                nc.vector.tensor_tensor(out, values, each(top, w), ALU.is_equal)
                dve.drain()
                nc.vector.tensor_tensor(out, out, spread(fall.rearrange("p (o e) -> p o e", o=1), [P, NT, w]), ALU.mult)
                dve.drain()
                nc.vector.tensor_reduce(tmp[:, :, 0:1], out, AX.X, ALU.max)
                dve.drain()
                nc.vector.tensor_tensor(out, out, each(tmp[:, :, 0:1], w), ALU.is_equal)
                dve.drain()

            dve.wait_ge(*k.pa(1))
            dve.wait_ge(*k.ga(1))
            bias = k.brow[:, r.bias_at:r.bias_at + n]
            nc.vector.tensor_tensor(lg[:, :, :], k.ps[:, 0, 0:NT * n].rearrange("p (t e) -> p t e", t=NT),
                                    spread(bias.rearrange("p (o e) -> p o e", o=1), [P, NT, n]), ALU.add)
            dve.drain()
            gl, el = lg[:, :, 0:NG], lg[:, :, NG:n]
            nc.vector.tensor_reduce(m1[:, :, :], gl, AX.X, ALU.max)
            dve.drain()
            nc.vector.tensor_tensor(ex[:, :, 0:NG], gl, each(m1[:, :, :], NG), ALU.subtract).then_inc(k.va.sem, 1)
            first(oneg[:, :, :], gl, m1[:, :, :], NG, desc[:, 0:NG])
            per = "p t (g e) -> p t g e"
            for t in range(NT):
                nc.vector.tensor_tensor(el[:, t, :].rearrange("p (g e) -> p g e", g=NG), el[:, t, :].rearrange("p (g e) -> p g e", g=NG),
                                        spread(oneg[:, t, :].rearrange("p (g o) -> p g o", o=1), [P, NG, EPG]), ALU.mult)
            dve.drain()
            nc.vector.tensor_scalar(oneg[:, :, :], oneg[:, :, :], -1.0, BIG, ALU.add, ALU.mult)
            dve.drain()
            for t in range(NT):
                nc.vector.tensor_tensor(el[:, t, :].rearrange("p (g e) -> p g e", g=NG), el[:, t, :].rearrange("p (g e) -> p g e", g=NG),
                                        spread(oneg[:, t, :].rearrange("p (g o) -> p g o", o=1), [P, NG, EPG]), ALU.add)
            dve.drain()
            nc.vector.tensor_reduce(m1[:, :, :], el, AX.X, ALU.max)
            dve.drain()
            first(one1[:, :, :], el, m1[:, :, :], NE, desc[:, :])
            nc.vector.scalar_tensor_tensor(out=el, in0=one1[:, :, :], scalar=-4 * BIG, in1=el, op0=ALU.mult, op1=ALU.add)
            dve.drain()
            nc.vector.tensor_reduce(m2[:, :, :], el, AX.X, ALU.max)
            dve.drain()
            first(one2[:, :, :], el, m2[:, :, :], NE, desc[:, :])
            nc.vector.tensor_tensor(m2[:, :, :], m2[:, :, :], m1[:, :, :], ALU.subtract).then_inc(k.va.sem, 1)
            dve.wait_ge(*k.sa(2))
            nc.vector.tensor_reduce(tmp[:, :, 0:1], ex[:, :, 0:NG], AX.X, ALU.add)
            nc.vector.tensor_scalar(tmp[:, :, 1:2], m2[:, :, :], 1.0, None, ALU.add)
            dve.drain()
            nc.vector.tensor_tensor(tmp[:, :, 0:1], tmp[:, :, 0:1], tmp[:, :, 1:2], ALU.mult)
            dve.drain()
            nc.vector.reciprocal(m1[:, :, :], tmp[:, :, 0:1])
            dve.drain()
            nc.vector.tensor_tensor(m2[:, :, :], m2[:, :, :], m1[:, :, :], ALU.mult)
            nc.vector.tensor_tensor(r.both[:, :, :], one1[:, :, :], one2[:, :, :], ALU.add)

        @block.scalar
        def _(act):
            act.wait_ge(*k.va(1))
            nc.scalar.activation(ex[:, :, 0:NG], ex[:, :, 0:NG], ACT.Exp).then_inc(k.sa.sem, 1)
            act.wait_ge(*k.va(2))
            nc.scalar.activation(m2[:, :, :], m2[:, :, :], ACT.Exp).then_inc(k.sa.sem, 1)
    k.ga.close(1)
    k.pa.close(1)
    k.va.close(2)
    k.sa.close(2)
    k.param_loaded.close(16)
    k.weights_loaded.close(32)


SLOTS = 2 * T
NB = 2 * -(-((SLOTS + NE * (P - 1)) // P) // 2)
FTE = EF // P


def place(k, r, zeros):
    nc = k.nc
    with nc.Block(no_gpsimd_drain=True) as block:
        @block.tensor
        def _(pe):
            ps = k.ps[:, 0, :]
            for t in range(NT):
                for before in range(t):
                    nc.tensor.matmul(ps[:, t * NE:(t + 1) * NE], k.ones[:, :], r.both[:, before, :], start=(before == 0), stop=False, skip_group_check=True)
                nc.tensor.matmul(ps[:, t * NE:(t + 1) * NE], k.tri[0][:, :], r.both[:, t, :], start=(t == 0), stop=True, skip_group_check=True)
            for t in range(NT):
                nc.tensor.matmul(ps[:, NT * NE:(NT + 1) * NE], k.ones[:, :], r.both[:, t, :], start=(t == 0), stop=(t == NT - 1), skip_group_check=True)
            nc.tensor.matmul(ps[:, (NT + 1) * NE:(NT + 1) * NE + 1], k.tri[0][:, :], k.ones[:, 0:1], start=True, stop=True,
                             skip_group_check=True).then_inc(k.pa.sem, 1)
            pe.wait_ge(*k.va(1))
            for n in range(2 * NT):
                last = nc.tensor.matmul(k.ps[:, 1, 0:NB], r.is_slot[:, n, :], r.is_block[:, n, :], start=(n == 0), stop=(n == 2 * NT - 1))
            last.then_inc(k.pb.sem, 1)

        @block.vector
        def _(dve):
            nc.vector.memset(zeros[:, :], 0.0)
            ps = k.ps[:, 0, :]
            upto = ps[:, 0:NT * NE].rearrange("p (t e) -> p t e", t=NT)
            count = ps[:, NT * NE:(NT + 1) * NE]
            nc.vector.tensor_tensor_scan(r.iota[:, :], k.ones[:, :], k.ones[:, :], 0.0, ALU.mult, ALU.add)
            dve.drain()
            nc.vector.tensor_scalar(r.iota[:, :], r.iota[:, :], -1.0, None, ALU.add)
            dve.wait_ge(*k.pa(1))
            nc.vector.tensor_scalar(r.blocks[:, :], count, 0.0, None, ALU.is_gt)
            for n in range(1, T // P):
                dve.drain()
                nc.vector.scalar_tensor_tensor(out=r.blocks[:, :], in0=count, scalar=float(n * P), in1=r.blocks[:, :], op0=ALU.is_gt, op1=ALU.add)
            dve.drain()
            nc.vector.tensor_tensor_scan(r.end[:, :], k.ones[:, 0:NE], r.blocks[:, :], 0.0, ALU.mult, ALU.add)
            dve.drain()
            nc.vector.tensor_tensor(r.start[:, :], r.end[:, :], r.blocks[:, :], ALU.subtract)
            dve.drain()
            for s, one in enumerate((r.one1, r.one2)):
                nc.vector.tensor_tensor(r.pick[:, 2 * s, :, :], one[:, :, :], upto, ALU.mult)
                nc.vector.tensor_tensor(r.pick[:, 2 * s + 1, :, :], one[:, :, :], spread(r.start.rearrange("p (o e) -> p o e", o=1), [P, NT, NE]), ALU.mult)
            dve.drain()
            nc.vector.tensor_reduce(r.picked[:, :, :, :], r.pick[:, :, :, :], AX.X, ALU.add)
            dve.drain()
            rank = [r.picked[:, 2 * s, :, 0] for s in range(2)]
            first = [r.picked[:, 2 * s + 1, :, 0] for s in range(2)]
            for s in range(2):
                sl = slice(s * NT, (s + 1) * NT)
                nc.vector.tensor_scalar(r.rank[:, sl], rank[s], -1.0, None, ALU.add)
                nc.vector.tensor_copy(r.block[:, sl], first[s])
            dve.drain()
            nc.vector.scalar_tensor_tensor(out=r.row_f[:, :], in0=r.block[:, :], scalar=float(P), in1=r.rank[:, :], op0=ALU.mult, op1=ALU.add)
            nc.vector.tensor_scalar(r.full[:, :], r.rank[:, :], float(P), None, ALU.is_ge)
            for n in range(2, T // P):
                dve.drain()
                nc.vector.scalar_tensor_tensor(out=r.full[:, :], in0=r.rank[:, :], scalar=float(n * P), in1=r.full[:, :], op0=ALU.is_ge, op1=ALU.add)
            dve.drain()
            nc.vector.tensor_tensor(r.block[:, :], r.block[:, :], r.full[:, :], ALU.add)
            nc.vector.scalar_tensor_tensor(out=r.rank[:, :], in0=r.full[:, :], scalar=-float(P), in1=r.rank[:, :], op0=ALU.mult, op1=ALU.add)
            nc.vector.tensor_copy(r.row[:, :], r.row_f[:, :])
            for t in range(NT):
                nc.vector.tensor_scalar(r.token_id[:, t:t + 1], ps[:, (NT + 1) * NE:(NT + 1) * NE + 1], float(t * P - 1), None, ALU.add)
            dve.drain()
            for n in range(2 * NT):
                nc.vector.tensor_scalar(r.is_slot[:, n, :], r.iota[:, :], r.rank[:, n:n + 1], None, ALU.is_equal)
                nc.vector.tensor_scalar(r.is_block[:, n, :], r.iota[:, 0:NB], r.block[:, n:n + 1], r.token_id[:, n % NT:n % NT + 1], ALU.is_equal, ALU.mult)
            dve.drain()
            nc.vector.tensor_tensor(r.ended[:, :, :], spread(r.end.rearrange("p (o e) -> p o e", o=1), [P, NB, NE]),
                                    spread(r.iota[:, 0:NB].rearrange("p (b o) -> p b o", o=1), [P, NB, NE]), ALU.is_le).then_inc(k.va.sem, 1)
            dve.drain()
            nc.vector.tensor_reduce(r.expert_f[:, :, :], r.ended[:, :, :], AX.X, ALU.add)
            dve.drain()
            nc.vector.tensor_scalar(r.pairs[:, :], r.iota[:, 0:NB // 2], 2.0, r.end[:, NE - 1:NE], ALU.mult, ALU.is_lt)
            dve.drain()
            nc.vector.tensor_reduce(r.count[:, :], r.pairs[:, 1:], AX.X, ALU.add)
            dve.drain()
            nc.vector.tensor_scalar(r.before_last[:, :], r.count[:, :], -1.0, None, ALU.add)
            nc.vector.tensor_scalar(r.expert[:, :], r.expert_f[:, :, 0], float(NE - 1), None, ALU.min)
            dve.wait_ge(*k.pb(1))
            nc.vector.tensor_copy(r.token[:, :], k.ps[:, 1, 0:NB])
    k.pa.close(1)
    k.va.close(1)
    k.pb.close(1)


def at_block(n, times=1, more=0):
    if isinstance(n, tuple):
        return n[0] * (2 * times) + (n[1] * times + more)
    return n * times + more


def experts(k, r, rows_dram, y_dram, up, dn, e):
    nc, A = k.nc, k.A
    wu = A["w_up_2"][0].rearrange("e (t p) n -> e p t n", p=P)
    wd = A["w_down_2"][0].rearrange("e (t p) n -> e p t n", p=P)
    XB, UB, HB, YB = 0, 2, 4, 5

    def side(n):
        return n[1] % 2 if isinstance(n, tuple) else n % 2

    def early(n, before):
        return not isinstance(n, tuple) and n < before

    def pair(n, per):
        return n[0] * per + (n[1] // 2 + 1) * per if isinstance(n, tuple) else (n // 2 + 1) * per

    def pair_before_last(queue):
        return queue.value_load(r.before_last[0:1, 0:1], min_val=0, max_val=NB // 2 - 2)

    def each_block(engine, before, step):
        step(0)
        step(1)
        with engine.Fori(1, NB // 2 - 1) as i:
            with engine.If(i <= before):
                step((i, 0, NB))
                step((i, 1, NB))
        step((before, 2, 4))
        step((before, 3, 4))

    def later(n, d):
        return (n[0], n[1] + d, n[2]) if isinstance(n, tuple) else n + d

    def inside(n, d):
        return n[1] + d < n[2] if isinstance(n, tuple) else n + d >= 0

    with nc.Block(no_gpsimd_drain=True) as block:
        @block.sync
        def _(sp):
            def expert_of(n):
                at = at_block(n)
                one = r.expert[0:1, bass.ds(at, 1)] if isinstance(n, tuple) else r.expert[0:1, at:at + 1]
                return nc.sync.value_load(one, min_val=0, max_val=NE - 1)

            def load_up(n, expert):
                sp.dma_start(up[side(n)], wu[bass.ds(expert, 1)].rearrange("o p t n -> p (o t) n")).then_inc(e.up_loaded[side(n)], 16)

            def load_down(n, expert):
                sp.dma_start(dn[side(n)], wd[bass.ds(expert, 1)].rearrange("o p t n -> p (o t) n")).then_inc(e.down_loaded[side(n)], 16)

            def of_last_pair(n):
                return isinstance(n, tuple) and n[1] >= 2 and n[2] == 4

            def store(n):
                sp.wait_ge(e.y_ready, at_block(n, 1, 1))
                sp.dma_start(y_dram[bass.ds(at_block(n, P), P), :] if isinstance(n, tuple) else y_dram[n * P:(n + 1) * P, :],
                             e.y[:, side(n), :]).then_inc(e.y_ended if of_last_pair(n) else e.y_stored[side(n)], 16)

            def step(n):
                if inside(n, 2):
                    expert = expert_of(later(n, 2))
                    sp.wait_ge(e.up_done, at_block(n, 1, 1))
                    load_up(later(n, 2), expert)
                if inside(n, -1):
                    if inside(n, 1):
                        expert = expert_of(later(n, 1))
                        sp.wait_ge(e.down_done, at_block(n))
                        load_down(later(n, 1), expert)
                    store(later(n, -1))

            for n in range(2):
                expert = expert_of(n)
                load_up(n, expert)
                load_down(n, expert)
            before = pair_before_last(nc.sync)
            with sp.Fori(0, NB // 2 - 1) as i:
                with sp.If(before < i):
                    sp.dma_start(y_dram[bass.ds(i * (2 * P) + 2 * P, 2 * P), :].rearrange("(s p) d -> p s d", p=P),
                                 e.zeros[:, :].rearrange("p (o d) -> p o d", o=1).to_broadcast([P, 2, D])).then_inc(e.y_zeroed, 16)
                with sp.If(i <= before):
                    sp.sem_inc(e.y_zeroed, 16)
            each_block(sp, before, step)
            store((before, 3, 4))
            sp.wait_ge(e.y_ended, 32)
            sp.wait_ge(e.y_zeroed, 16 * (NB // 2 - 1))

        @block.gpsimd
        def _(pool):
            def step(n):
                s = side(n)
                if not early(n, 2):
                    pool.wait_ge(e.turned, at_block(n, 1, -1))
                nc.gpsimd.tensor_copy(e.slot_token[:, s:s + 1], r.token[:, bass.ds(at_block(n), 1)] if isinstance(n, tuple) else r.token[:, n:n + 1])
                pool.drain()
                nc.gpsimd.indirect_dma_start(e.rows[:, s, :], None, rows_dram, bass.IndirectOffsetOnAxis(ap=e.slot_token[:, s:s + 1], axis=0))\
                    .then_inc(e.gathered[s], 16)

            each_block(pool, pair_before_last(nc.gpsimd), step)
            pool.drain()

        @block.tensor
        def _(pe):
            def turn_rows(n):
                s = side(n)
                pe.wait_ge(e.gathered[s], pair(n, 16))
                if not early(n, 1):
                    pe.wait_ge(e.x_ready, at_block(n))
                for c in range(KD):
                    last = nc.tensor.transpose(k.ps[:, XB + c // NT, (c % NT) * P:(c % NT + 1) * P], e.rows[:, s, c * P:(c + 1) * P], k.ident[:, :])
                last.then_inc(e.turned, 1)

            def first(n):
                s = side(n)
                pe.wait_ge(e.x_ready, at_block(n, 1, 1))
                pe.wait_ge(e.up_loaded[s], pair(n, 16))
                if not early(n, 2):
                    pe.wait_ge(e.hidden, at_block(n, 1, -1))
                for c in range(KD):
                    last = nc.tensor.matmul(k.ps[:, UB + s, :], e.x[:, s, c, :], up[s][:, c, :], start=(c == 0), stop=(c == KD - 1))
                last.then_inc(e.up_done, 1)

            def turn_hidden(n):
                s = side(n)
                pe.wait_ge(e.hidden, at_block(n, 1, 1))
                if not early(n, 1):
                    pe.wait_ge(e.hid_ready, at_block(n))
                for j in range(FTE):
                    last = nc.tensor.transpose(k.ps[:, HB, j * P:(j + 1) * P], e.hid[:, s, j * P:(j + 1) * P], k.ident[:, :])
                last.then_inc(e.hid_turned, 1)

            def second(n):
                s = side(n)
                pe.wait_ge(e.hid_ready, at_block(n, 1, 1))
                pe.wait_ge(e.down_loaded[s], pair(n, 16))
                if not early(n, 1):
                    pe.wait_ge(e.y_ready, at_block(n))
                for half in range(2):
                    for j in range(FTE):
                        last = nc.tensor.matmul(k.ps[:, YB + half, :], e.hid_cm[:, s, j, :], dn[s][:, j, half * BANK:(half + 1) * BANK],
                                                start=(j == 0), stop=(j == FTE - 1))
                last.then_inc(e.down_done, 1)

            def step(n):
                if inside(n, 1):
                    first(later(n, 1))
                turn_hidden(n)
                if inside(n, 2):
                    turn_rows(later(n, 2))
                second(n)

            turn_rows(0)
            first(0)
            turn_rows(1)
            each_block(pe, pair_before_last(nc.tensor), step)

        @block.scalar
        def _(act):
            def silu(n):
                s = side(n)
                act.wait_ge(e.up_done, at_block(n, 1, 1))
                if not early(n, 2):
                    act.wait_ge(e.hidden, at_block(n, 1, -1))
                nc.scalar.activation(e.silu[:, s, :], k.ps[:, UB + s, 0:EF], ACT.Silu).then_inc(e.silu_ready, 1)

            def step(n):
                s = side(n)
                if inside(n, 1):
                    silu(later(n, 1))
                act.wait_ge(e.hid_turned, at_block(n, 1, 1))
                if not early(n, 2):
                    act.wait_ge(e.down_done, at_block(n, 1, -1))
                nc.scalar.copy(e.hid_cm[:, s, :, :], k.ps[:, HB, 0:EF].rearrange("p (j m) -> p j m", j=FTE)).then_inc(e.hid_ready, 1)
                act.wait_ge(e.down_done, at_block(n, 1, 1))
                if not early(n, 2):
                    act.wait_ge(e.y_stored[s], at_block_pairs(n))
                for half in range(2):
                    last = nc.scalar.copy(e.y[:, s, half * BANK:(half + 1) * BANK], k.ps[:, YB + half, :])
                last.then_inc(e.y_ready, 1)

            def at_block_pairs(n):
                return n[0] * 16 + 16 * (n[1] // 2) if isinstance(n, tuple) else 16 * (n // 2)

            silu(0)
            each_block(act, pair_before_last(nc.scalar), step)

        @block.vector
        def _(dve):
            def columns(n):
                s = side(n)
                dve.wait_ge(e.turned, at_block(n, 1, 1))
                if not early(n, 2):
                    dve.wait_ge(e.up_done, at_block(n, 1, -1))
                for half in range(2):
                    c = slice(half * NT, (half + 1) * NT)
                    last = nc.vector.tensor_copy(e.x[:, s, c, :], k.ps[:, XB + half, :].rearrange("p (c m) -> p c m", c=NT))
                last.then_inc(e.x_ready, 1)

            def gated(n):
                s = side(n)
                dve.wait_ge(e.silu_ready, at_block(n, 1, 1))
                if not early(n, 2):
                    dve.wait_ge(e.hid_turned, at_block(n, 1, -1))
                nc.vector.tensor_tensor(e.hid[:, s, :], e.silu[:, s, :], k.ps[:, UB + s, EF:2 * EF], ALU.mult).then_inc(e.hidden, 1)

            def step(n):
                if inside(n, 1):
                    gated(later(n, 1))
                if inside(n, 2):
                    columns(later(n, 2))

            columns(0)
            gated(0)
            columns(1)
            each_block(dve, pair_before_last(nc.vector), step)


def combine(k, r, y_dram, picked, out):
    nc = k.nc
    tiles = out.rearrange("o (t p) d -> p (o t) d", p=P)
    with nc.Block(no_gpsimd_drain=True) as block:
        @block.gpsimd
        def _(pool):
            for n in range(2 * NT):
                at = (n % 2) * NT + n // 2
                nc.gpsimd.indirect_dma_start(picked[:, n, :], None, y_dram, bass.IndirectOffsetOnAxis(ap=r.row[:, at:at + 1], axis=0))\
                    .then_inc(r.row_picked[n % 2], 16)
            for s in range(2):
                pool.wait_ge(r.row_picked[s], 16 * NT)
            pool.drain()

        @block.vector
        def _(dve):
            for t in range(NT):
                for s, share in enumerate((r.m1, r.m2)):
                    dve.wait_ge(r.row_picked[s], 16 * NT)
                    last = nc.vector.scalar_tensor_tensor(out=k.x[:, t, :], in0=picked[:, 2 * t + s, :], scalar=share[:, t, 0:1], in1=k.x[:, t, :],
                                                          op0=ALU.mult, op1=ALU.add)
                    dve.drain()
                nc.vector.sem_inc(k.va.sem, 1)

        @block.sync
        def _(sp):
            for t in range(NT):
                sp.wait_ge(*k.va(t + 1))
                sp.dma_start(tiles[:, t, :], k.x[:, t, :]).then_inc(k.param_loaded.sem, 16)
            sp.wait_ge(*k.param_loaded(16 * NT))


def moe(k, out):
    nc, A, sb = k.nc, k.A, k.alloc
    with ExitStack() as c:
        wr = sb("router", [P, KD, NG + NE], to=c)
        r = Kernel()
        r.bias_at = k.router_bias_at
        r.lg, r.ex, r.oneg, r.m1, r.m2, r.one1, r.one2, r.tmp, r.both = (
            sb("moe_" + name, [P, NT, w], to=c) for name, w in (("logits", NG + NE), ("ex", NG), ("group", NG), ("share1", 1), ("share2", 1),
                                                                ("one1", NE), ("one2", NE), ("tmp", 2), ("both", NE)))
        r.desc = sb("moe_desc", [P, NE], to=c)
        r.bar = sb("moe_bar", [P, 1], to=c)
        r.iota = sb("moe_iota", [P, P], to=c)
        r.blocks, r.end, r.start = (sb("moe_" + name, [P, NE], to=c) for name in ("blocks", "block_end", "block_start"))
        r.pick = sb("moe_pick", [P, 4, NT, NE], to=c)
        r.picked = sb("moe_picked", [P, 4, NT, 1], to=c)
        r.rank, r.block, r.full, r.row_f = (sb("moe_" + name, [P, 2 * NT], to=c) for name in ("rank", "block", "full", "row_f"))
        r.row = sb("moe_row", [P, 2 * NT], I32, to=c)
        r.token_id = sb("moe_token_id", [P, NT], to=c)
        r.is_slot = sb("moe_is_slot", [P, 2 * NT, P], to=c)
        r.is_block = sb("moe_is_block", [P, 2 * NT, NB], to=c)
        r.ended = sb("moe_ended", [P, NB, NE], to=c)
        r.expert_f = sb("moe_expert_f", [P, NB, 1], to=c)
        r.expert = sb("moe_expert", [P, NB], I32, to=c)
        r.pairs = sb("moe_pairs", [P, NB // 2], to=c)
        r.count = sb("moe_count", [P, 1], to=c)
        r.before_last = sb("moe_before_last", [P, 1], I32, to=c)
        r.token = sb("moe_token", [P, NB], I32, to=c)
        r.row_picked = [k.new_count(f"row_picked{s}").sem for s in range(2)]
        e = Kernel()
        e.rows = sb("expert_rows", [P, 2, D], to=c)
        e.x = sb("expert_x", [P, 2, KD, P], to=c)
        e.silu = sb("expert_silu", [P, 2, EF], to=c)
        e.hid = sb("expert_hid", [P, 2, EF], to=c)
        e.hid_cm = sb("expert_hid_cm", [P, 2, FTE, P], to=c)
        e.zeros = sb("zeros", [P, D], to=c)
        e.y = sb("expert_y", [P, 2, D], to=c)
        e.slot_token = sb("expert_slot_token", [P, 2], I32, to=c)
        e.up_loaded, e.down_loaded, e.gathered, e.y_stored = (
            [k.new_count(f"{name}{s}").sem for s in range(2)] for name in ("expert_up_loaded", "expert_down_loaded", "rows_gathered", "y_stored"))
        e.y_zeroed, e.y_ended = (k.new_count(name).sem for name in ("y_zeroed", "y_ended"))
        e.turned, e.x_ready, e.up_done, e.silu_ready, e.hidden, e.hid_turned, e.hid_ready, e.down_done, e.y_ready = (
            k.new_count(name).sem for name in ("rows_turned", "columns_ready", "up_done", "silu_ready", "hidden_ready", "hidden_turned", "hidden_cm_ready",
                                               "down_done", "y_ready"))
        down = sb("moe_down", [P, 2, FTE, D], to=c)
        up = [k.ring[:, s, :].rearrange("p (t n) -> p t n", t=KD) for s in range(2)]
        dn = [down[:, s, :, :] for s in range(2)]
        rows_dram = nc.dram_tensor("normalised_rows", (T, D), F32, kind="Internal").ap()
        y_dram = nc.dram_tensor("expert_results", (NB * P, D), F32, kind="Internal").ap()
        route(k, wr, r, k.ytmp[:, :, :], rows_dram)
        place(k, r, e.zeros)
        experts(k, r, rows_dram, y_dram, up, dn, e)
        picked = k.ring[:, :, :].rearrange("p s n -> p (s n)").rearrange("p (n d) -> p n d", n=2 * NT)
        combine(k, r, y_dram, picked, out)




def build(nc, A, out):
    with ExitStack() as ctx:
        k = open_kernel(nc, ctx, A)
        k.ytmp = k.alloc("y_tmp", [P, NT, D])
        w = A["ab_w_in"][0]
        setup(k, [w[:, 0:BANK], w[:, BANK:2 * BANK]])
        norm_to_cm(k, k.x, k.pcol[:, 0, 0:8], k.h, k.ytmp)
        layer0_mixer(k, A["norm_g"][0, 2], [ffn_first(k, 0)])
        ffn(k, 0, A["norm_g"][0, 3], A["norm_g"][1, 0], gla_weights(k)[:2])
        layer1_mixer(k, A["norm_g"][1, 2], [ffn_first(k, 1)])
        ffn(k, 1, A["norm_g"][1, 3], A["g_mix_2"][0], memory_weights(k))
        mixers2(k, A["g_ffn_2"][0], [])
        moe(k, out)


def constants():
    half = HD // 2
    inv = np.float32(10000.0) ** (-np.arange(half, dtype=np.float32) / np.float32(half))
    angle = np.arange(T, dtype=np.float32)[:, None] * inv[None, :]
    return {"rope_table": np.concatenate([np.cos(angle), np.sin(angle)], axis=1).astype(np.float32)}


_OUT = ((1, T, D), "float32")


def kernel(**inputs):
    import concourse.bacc as _bacc
    from concourse.bass_utils import run_bass_kernel_spmd as _run

    nc = _bacc.Bacc("TRN2", target_bir_lowering=False, num_devices=1)
    arrays, handles = {}, {}
    for name, value in {**inputs, **constants()}.items():
        a = np.ascontiguousarray(value)
        arrays[f"in_{name}"] = a
        handles[name] = nc.dram_tensor(f"in_{name}", a.shape, mybir.dt.from_np(a.dtype), kind="ExternalInput").ap()
    out = nc.dram_tensor("out", _OUT[0], F32, kind="ExternalOutput").ap()
    build(nc, handles, out)
    r = _run(nc, [arrays], core_ids=[0])
    return r.results[0]["out"]
```

```python
from contextlib import ExitStack

import numpy as np

import concourse.bass as bass
from concourse import mybir

F32 = mybir.dt.float32
F32R = mybir.dt.float32r
U32 = mybir.dt.uint32
I32 = mybir.dt.int32
ALU = mybir.AluOpType
ACT = mybir.ActivationFunctionType
AX = mybir.AxisListType

P = 128
T = 512
NT = T // P
D = 1024
KD = D // P
BANK = 512
NBANKS = 8
EPS = 1e-6
BIG = 1e30

SSD_H, SSD_P, SSD_N, SSD_TAPS = 16, 64, 128, 5
SSD_X = D + 2 * 2 * SSD_N
XT = SSD_X // P
PAD = SSD_TAPS // 2
ML_H, ML_D = 8, 128
Z0 = 0
XBC0 = Z0 + D
DT0 = XBC0 + SSD_X
Q0 = DT0 + 2 * SSD_H
K0 = Q0 + D
V0 = K0 + D
O0 = V0 + D
G0 = O0 + D
GLA_H, GLA_DK, GLA_DV, GLA_RANK, GLA_TAU, GLA_L = 4, 128, 256, 16, 16.0, 64
GC = T // GLA_L
FFN = 11 * D // 4
FT = FFN // P
HD = 64
NQ, NKV, NIDX = 8, 2, 8
TOPK = T // 4
CONV_C, CONV_W = 512, 31
CT = CONV_C // P
MEM, MH, MD = 256, 4, 128
MT = MEM // P
NE, EPG, NG, EF = 32, 8, 4, 256
QA0 = 0
KA0 = QA0 + NQ * HD
VA0 = KA0 + NKV * HD
QI0 = VA0 + NKV * HD
KI0 = QI0 + NIDX * HD
WI0 = KI0 + HD
CI0 = WI0 + NIDX
QM0 = CI0 + 2 * CONV_C
GT0 = QM0 + MH * MD
ATT = CI0


class Signal:

    def __init__(self, sem):
        self.sem, self.base = sem, 0

    def __call__(self, n):
        return self.sem, self.base + n

    def close(self, n):
        self.base += n


class Kernel:
    pass


def row(ap):
    return ap.rearrange("(o n) -> o n", o=1)


def everywhere(ap, n):
    return row(ap).to_broadcast([P, n])


def spread(ap, shape):
    return ap.to_broadcast(shape)


def open_kernel(nc, ctx, A):
    k = Kernel()
    k.nc, k.A = nc, A

    seen = {}

    def sb(name, shape, dt=F32, to=ctx):
        seen[name] = seen.get(name, 0) + 1
        name = name if seen[name] == 1 else f"{name}_{seen[name]}"
        return to.enter_context(nc.sbuf_tensor(name, shape, dt))

    def signal(name):
        return Signal(ctx.enter_context(nc.semaphore(name)))

    k.new_count = signal
    k.ps = ctx.enter_context(nc.psum_tensor("ps", [P, NBANKS, BANK], F32))
    k.x = sb("x_tm", [P, NT, D])
    k.h = sb("h_cm", [P, KD, T])
    k.ring = sb("ring", [P, 2, KD * BANK])
    k.ident = sb("ident", [P, P])
    k.ones = sb("ones", [P, P])
    k.tri = [sb("tri_fwd", [P, P]), sb("tri_bwd", [P, P])]
    k.pcol = sb("pcol", [P, 7, P])
    k.brow = sb("brow", [P, 640])
    k.gpost = sb("gpost", [P, D])
    k.stat = sb("stat", [P, 4, 64])
    k.eps = sb("eps", [P, 1])
    k.loaded = [signal("w_loaded0"), signal("w_loaded1")]
    k.asked, k.taken, k.next_slot = [0, 0], [0, 0], 0
    k.up_loaded = [signal("up_loaded0"), signal("up_loaded1")]
    k.param_loaded = signal("param_loaded")
    k.weights_loaded = signal("small_weights_loaded")
    k.acc_ready = signal("acc_ready")
    k.acc_free = signal("acc_free")
    k.mean_ready = signal("mean_ready")
    k.root_ready = signal("root_ready")
    k.norm_ready = signal("norm_ready")
    k.x_ready = signal("x_ready")
    k.result_ready = signal("result_ready")
    k.w_hi_ready, k.w_lo_ready, k.h_hi_ready, k.h_lo_ready, k.products = (
        signal(name) for name in ("w_hi_ready", "w_lo_ready", "h_hi_ready", "h_lo_ready", "products"))
    k.pa = signal("step_pa")
    k.pb = signal("step_pb")
    k.pc = signal("step_pc")
    k.va = signal("step_va")
    k.vb = signal("step_vb")
    k.vc = signal("step_vc")
    k.vd = signal("step_vd")
    k.da = signal("step_da")
    k.sa = signal("step_sa")
    k.sb = signal("step_sb")
    k.ga = signal("step_ga")
    k.alloc = sb
    return k


def load_weights(k, sp, w, width=None):
    s = sum(k.asked) % 2
    tiles, cols = w.shape[0] // P, w.shape[1]
    dst = k.ring[:, s, 0:tiles * cols].rearrange("p (t n) -> p t n", t=tiles)
    sp.dma_start(dst, w.rearrange("(t p) n -> p t n", p=P)).then_inc(k.loaded[s].sem, 16)
    k.asked[s] += 1


def take_weights(k, pe, tiles, cols):
    s = sum(k.taken) % 2
    k.taken[s] += 1
    pe.wait_ge(k.loaded[s].sem, 16 * k.taken[s])
    return k.ring[:, s, 0:tiles * cols].rearrange("p (t n) -> p t n", t=tiles)



def setup(k, first, xn):
    nc, A = k.nc, k.A
    rows = k.h[:, :, :].rearrange("p a b -> p (a b)")[:, 0:7 * P].rearrange("p (g c) -> p g c", g=7)

    def chunks(ap):
        return ap.rearrange("(r c) -> r c", c=P)

    plan = []
    for n, (i, j) in enumerate(((0, 0), (0, 2), (1, 0), (1, 2))):
        plan.append((0, 8 * n, chunks(A["norm_g"][i, j])))
    plan.append((0, 32, A["ab_conv_w"][0].rearrange("t (r c) -> (t r) c", c=P)))
    plan.append((0, 92, chunks(A["ab_conv_b"][0])))
    plan.append((0, 104, chunks(A["ab_ssd_norm"][0])))
    plan.append((0, 112, chunks(A["ab_mlstm_norm"][0])))
    for i in range(2):
        plan.append((1 + 2 * i, 0, A["ffn_conv_w"][i, 0:2].rearrange("t (r c) -> (t r) c", c=P)))
        plan.append((2 + 2 * i, 0, chunks(A["ffn_conv_w"][i, 2])))
        plan.append((2 + 2 * i, 2 * FT, chunks(A["ffn_conv_b"][i])))
    plan.append((5, 0, chunks(A["c_norm"][0])))
    plan.append((5, 8, A["c_gate_b"][0].rearrange("d (r c) -> (d r) c", c=P)))
    for n, name in enumerate(("g_mix_2", "g_ffn_2", "g_mem_2")):
        plan.append((5, 16 + 8 * n, chunks(A[name][0])))
    for n, name in enumerate(("conv_b_2", "ln_g_2", "ln_b_2")):
        plan.append((5, 40 + 4 * n, chunks(A[name][0])))
    plan.append((6, 0, A["conv_w_2"][0].rearrange("t o (r c) -> (t o r) c", c=P)))
    used = [max(r + ap.shape[0] for g, r, ap in plan if g == n) for n in range(7)]

    broad = [("ab_dt_bias", "a h -> (a h)"), ("ab_fg_bias", "a h -> (a h)"), ("ab_ig_bias", "a h -> (a h)"),
             ("ab_a_log", "a h -> (a h)"), ("ab_d_skip", None), ("g_qa_2", None), ("g_ka_2", None),
             ("g_idx_k_2", None), ("g_qm_2", None), ("g_km_2", None), ("b_rg_2", None), ("b_re_2", None)]
    k.b, at, bplan = {}, 0, []
    for name, how in broad:
        ap = A[name][0] if how is None else A[name][0].rearrange(how)
        n = ap.shape[0]
        if name == "b_rg_2":
            k.router_bias_at = at
        k.b[name] = k.brow[:, at:at + n]
        bplan.append((k.brow[:, at:at + n], everywhere(ap, n)))
        at += n

    with nc.Block(no_gpsimd_drain=True) as block:
        @block.sync
        def _(sp):
            sp.dma_start(k.x[:, :, :], A["x"].rearrange("o (t p) d -> p (o t) d", p=P)).then_inc(k.weights_loaded.sem, 16)
            for g, r, ap in plan:
                sp.dma_start(rows[r:r + ap.shape[0], g, :], ap).then_inc(k.param_loaded.sem, 16)
            for dst, src in bplan:
                sp.dma_start(dst, src).then_inc(k.param_loaded.sem, 16)
            for w in first:
                load_weights(k, sp, w)
            sp.wait_ge(*k.param_loaded(16 * (len(plan) + len(bplan))))

        @block.vector
        def _(dve):
            dve.wait_ge(*k.weights_loaded(16))
            norm_rows(k, dve, k.x, xn, NT)

        @block.scalar
        def _(act):
            norm_root(k, act, NT)

        @block.gpsimd
        def _(pool):
            nc.gpsimd.memset(k.ones[:, :], 1.0)
            nc.gpsimd.memset(k.eps[:, :], EPS)
            pool.drain()
            nc.gpsimd.affine_select(out=k.ident[:, :], in_=k.ones[:, :], compare_op=ALU.is_equal, fill=0.0, base=0,
                                    pattern=[[1, P]], channel_multiplier=-1)
            nc.gpsimd.affine_select(out=k.tri[0][:, :], in_=k.ones[:, :], compare_op=ALU.is_ge, fill=0.0, base=0,
                                    pattern=[[1, P]], channel_multiplier=-1)
            nc.gpsimd.affine_select(out=k.tri[1][:, :], in_=k.ones[:, :], compare_op=ALU.is_ge, fill=0.0, base=0,
                                    pattern=[[-1, P]], channel_multiplier=1)
            pool.drain()
    k.param_loaded.close(16 * (len(plan) + len(bplan)))
    k.weights_loaded.close(16)
    close_norm(k, NT)

    with nc.Block(no_gpsimd_drain=True) as block:
        @block.tensor
        def _(pe):
            for g in range(7):
                nc.tensor.transpose(k.ps[:, g, 0:used[g]], rows[0:used[g], g, :],
                                    k.ident[0:used[g], 0:used[g]]).then_inc(k.acc_ready.sem, 1)

        @block.scalar
        def _(act):
            for g in range(7):
                act.wait_ge(*k.acc_ready(g + 1))
                nc.scalar.copy(k.pcol[:, g, 0:used[g]], k.ps[:, g, 0:used[g]])
    k.acc_ready.close(7)



def norm_rows(k, dve, src, xn, tiles):
    nc = k.nc
    ms, root, rstd = (k.stat[:, n, 0:tiles] for n in range(3))
    for t in range(tiles):
        nc.vector.tensor_tensor_reduce(out=xn[:, t, :], in0=src[:, t, :], in1=src[:, t, :], scale=1.0, scalar=0.0,
                                       op0=ALU.mult, op1=ALU.add, accum_out=ms[:, t:t + 1])
    dve.drain()
    nc.vector.tensor_scalar(ms, ms, 1.0 / D, EPS, ALU.mult, ALU.add).then_inc(k.mean_ready.sem, 1)
    dve.wait_ge(*k.root_ready(1))
    nc.vector.reciprocal(rstd, root)
    dve.drain()
    for t in range(tiles):
        nc.vector.tensor_scalar(xn[:, t, :], src[:, t, :], rstd[:, t:t + 1], None, ALU.mult).then_inc(k.norm_ready.sem, 1)


def norm_root(k, act, tiles):
    act.wait_ge(*k.mean_ready(1))
    k.nc.scalar.activation(k.stat[:, 1, 0:tiles], k.stat[:, 0, 0:tiles], ACT.Sqrt).then_inc(k.root_ready.sem, 1)


def norm_to_cm(k, src, gain, dst, xn, tiles=NT, rows_done=False):
    nc = k.nc
    width = tiles * P

    with nc.Block(no_gpsimd_drain=True) as block:
        @block.vector
        def _(dve):
            if not rows_done:
                norm_rows(k, dve, src, xn, tiles)
            for c in range(1, KD, 2):
                dve.wait_ge(*k.acc_ready(c + 1))
                nc.vector.tensor_scalar(dst[:, c, 0:width], k.ps[:, c, 0:width], gain[:, c:c + 1], None, ALU.mult)

        @block.scalar
        def _(act):
            if not rows_done:
                norm_root(k, act, tiles)
            for c in range(0, KD, 2):
                act.wait_ge(*k.acc_ready(c + 1))
                nc.scalar.activation(dst[:, c, 0:width], k.ps[:, c, 0:width], ACT.Copy, scale=gain[:, c:c + 1])

        @block.tensor
        def _(pe):
            if not rows_done:
                pe.wait_ge(*k.norm_ready(tiles))
            for c in range(KD):
                for t in range(tiles):
                    last = nc.tensor.transpose(k.ps[:, c, t * P:(t + 1) * P], xn[:, t, c * P:(c + 1) * P], k.ident[:, :])
                last.then_inc(k.acc_ready.sem, 1)
    if not rows_done:
        close_norm(k, tiles)
    k.acc_ready.close(KD)


def close_norm(k, tiles):
    k.mean_ready.close(1)
    k.root_ready.close(1)
    k.norm_ready.close(tiles)



def rest(engine, lo, whole, hi):
    return engine.tensor_tensor(lo, whole, hi.bitcast(F32), ALU.subtract)


def product(nc, out, left, right, start, stop, **more):
    nc.tensor.matmul(out, left[0], right[0], start=start, stop=False, **more)
    nc.tensor.matmul(out, left[0], right[1], start=False, stop=False, **more)
    return nc.tensor.matmul(out, left[1], right[0], start=False, stop=stop, **more)


PIECES = 3
PER_CM = KD // 2


def project(k, jobs, src=None, tiles=NT, after=(), cold=False, vector=None, scalar=None, load=None, split=True, depth=PIECES):
    nc = k.nc
    src = k.h if src is None else src
    width = tiles * P

    def is_split(j):
        return split and jobs[j][0].shape[1] >= 2 * P

    accs, groups, pieces = [], [], []
    ends = {}
    piece_end, chunk_pieces = [], {}
    for j, (w, layout, _) in enumerate(jobs):
        first, cols = len(accs), w.shape[1]
        count = tiles if layout == "tm" else -(-cols // P)
        accs += [(j, n) for n in range(count)]
        if not is_split(j):
            for n in range(count):
                groups.append((j, n, range(KD), None))
                ends[first + n] = len(groups)
        elif layout == "tm":
            for c in range(KD):
                for n in range(count):
                    groups.append((j, n, (c,), len(pieces)))
                    ends[first + n] = len(groups)
                pieces.append((j, slice(c, c + 1), slice(0, cols)))
                piece_end.append(len(groups))
        else:
            for n in range(count):
                for c in range(0, KD, PER_CM):
                    groups.append((j, n, range(c, c + PER_CM), len(pieces)))
                    pieces.append((j, slice(c, c + PER_CM), slice(n * P, (n + 1) * P)))
                    piece_end.append(len(groups))
                ends[first + n] = len(groups)
        ends["chunk", j] = len(groups)
        chunk_pieces[j] = len(pieces)
    acc_of = {acc: a for a, acc in enumerate(accs)}
    landed = []
    for j in range(len(jobs)):
        s = sum(k.taken) % 2
        k.taken[s] += 1
        landed.append((s, 16 * k.taken[s]))

    def bank(a):
        j, n = accs[a]
        cols = jobs[j][0].shape[1]
        if jobs[j][1] == "tm":
            return k.ps[:, a % NBANKS, 0:cols]
        return k.ps[0:min(cols - n * P, P), a % NBANKS, 0:width]

    def chunk(j):
        cols = jobs[j][0].shape[1]
        return k.ring[:, landed[j][0], 0:KD * cols].rearrange("p (t n) -> p t n", t=KD)

    def part(buffer, p):
        j, rows, cols = pieces[p]
        t, n = rows.stop - rows.start, cols.stop - cols.start
        return buffer[:, p % depth, 0:t * n].rearrange("p (t n) -> p t n", t=t)

    with ExitStack() as own:
        if pieces:
            h_hi, h_lo = (k.alloc("h_" + name, [P, KD, width], F32R, own) for name in ("hi", "lo"))
            w_hi, w_lo = (k.alloc("w_" + name, [P, depth, BANK], F32R, own) for name in ("hi", "lo"))
        block = own.enter_context(nc.Block(no_gpsimd_drain=True))

        @block.sync
        def _(sp):
            if load is not None:
                load(sp)
            for job in jobs[:2] if cold else ():
                load_weights(k, sp, job[0])
            ahead = [(j, job[0]) for j, job in enumerate(jobs)][2:] + [(len(jobs) + n, w) for n, w in enumerate(after)]
            for j, w in ahead:
                if is_split(j - 2):
                    sp.wait_ge(*k.w_lo_ready(chunk_pieces[j - 2]))
                else:
                    sp.wait_ge(*k.products(ends["chunk", j - 2]))
                load_weights(k, sp, w)

        @block.tensor
        def _(pe):
            ready, turned = 0, 0
            for j, n, rows, p in groups:
                a = acc_of[j, n]
                if p is None:
                    if n == 0:
                        pe.wait_ge(k.loaded[landed[j][0]].sem, landed[j][1])
                elif p >= ready:
                    ready = p + 1
                    pe.wait_ge(*k.w_lo_ready(ready))
                if rows[0] == 0 and a >= NBANKS:
                    pe.wait_ge(*k.acc_free(a - NBANKS + 1))
                for c in rows:
                    start, stop = c == 0, c == KD - 1
                    if p is None:
                        w = chunk(j)
                        left, right = src[:, c, n * P:(n + 1) * P], w[:, c, :]
                        if jobs[j][1] == "cm":
                            left, right = w[:, c, n * P:min((n + 1) * P, w.shape[2])], src[:, c, 0:width]
                        last = nc.tensor.matmul(bank(a), left, right, start=start, stop=stop)
                        continue
                    if c >= turned:
                        turned = c + 1
                        pe.wait_ge(*k.h_lo_ready(turned))
                    weights = [part(w, p)[:, c - rows[0], :] for w in (w_hi, w_lo)]
                    if jobs[j][1] == "tm":
                        last = product(nc, bank(a), [h[:, c, n * P:(n + 1) * P] for h in (h_hi, h_lo)], weights, start, stop)
                    else:
                        last = product(nc, bank(a), weights, [h[:, c, :] for h in (h_hi, h_lo)], start, stop)
                last.then_inc(k.products.sem, 1)

        @block.scalar
        def _(act):
            done = 0

            def read_out(a):
                act.wait_ge(*k.products(ends[a]))
                j, n = accs[a]
                dst, scale, *func = jobs[j][2](n, bank(a))
                b = bank(a)
                if len(dst.shape) == 3:
                    b = b.rearrange("p (a b) -> p a b", a=dst.shape[1])
                nc.scalar.activation(dst, b, func[0] if func else ACT.Copy, scale=scale).then_inc(k.acc_free.sem, 1)
                if scalar is not None and a in scalar:
                    scalar[a](act)

            inputs = 0
            for p, (j, rows, cols) in enumerate(pieces):
                if p == 0 or pieces[p - 1][0] != j:
                    while j >= 2 and not is_split(j - 2) and accs[done][0] <= j - 2:
                        read_out(done)
                        done += 1
                    act.wait_ge(k.loaded[landed[j][0]].sem, landed[j][1])
                if p >= depth:
                    act.wait_ge(*k.products(piece_end[p - depth]))
                nc.scalar.copy(part(w_hi, p), chunk(j)[:, rows, cols]).then_inc(k.w_hi_ready.sem, 1)
                while inputs < min(KD, rows.stop if p == 0 else KD if p >= depth - 1 else inputs + PER_CM):
                    nc.scalar.copy(h_hi[:, inputs, :], src[:, inputs, 0:width]).then_inc(k.h_hi_ready.sem, 1)
                    inputs += 1
                while p >= depth and ends[done] <= piece_end[p - depth]:
                    read_out(done)
                    done += 1
            for a in range(done, len(accs)):
                read_out(a)

        @block.vector
        def _(dve):
            for c in range(KD if pieces else 0):
                dve.wait_ge(*k.h_hi_ready(c + 1))
                rest(nc.vector, h_lo[:, c, :], src[:, c, 0:width], h_hi[:, c, :]).then_inc(k.h_lo_ready.sem, 1)
            if vector is not None:
                vector(dve)

        @block.gpsimd
        def _(pool):
            for p, (j, rows, cols) in enumerate(pieces):
                pool.wait_ge(*k.w_hi_ready(p + 1))
                rest(nc.gpsimd, part(w_lo, p), chunk(j)[:, rows, cols], part(w_hi, p)).then_inc(k.w_lo_ready.sem, 1)
            pool.drain()
    k.products.close(len(groups))
    k.acc_free.close(len(accs))
    k.w_hi_ready.close(len(pieces))
    k.w_lo_ready.close(len(pieces))
    if pieces:
        k.h_hi_ready.close(KD)
        k.h_lo_ready.close(KD)


def out_chunks(w, tiles):
    return [w[r * P:min(r + 4, tiles) * P, :] for r in range(0, tiles, 4)]


def project_out(k, lhs, tiles, w, gain, next_gain, after=(), scratch=None):
    nc = k.nc
    chunks = out_chunks(w, tiles)
    ss, root, ss2, root2 = (k.stat[:, n, 0:NT] for n in range(4))
    bulk = tiles - 2
    landed = []
    for _ in chunks:
        s = sum(k.taken) % 2
        k.taken[s] += 1
        landed.append((s, 16 * k.taken[s]))

    def whole(t):
        return k.ps[:, 2 * t:2 * t + 2, :].rearrange("p a b -> p (a b)")

    def weights(n):
        return k.ring[:, landed[n // 4][0], (n % 4) * D:(n % 4 + 1) * D]

    def steps(lead, middle, trail):
        for t in range(NT + 2):
            if t < NT:
                lead(t)
            if 1 <= t <= NT:
                middle(t - 1)
            if t >= 2:
                trail(t - 2)

    def turned_half(t, half):
        c = slice(half * NT, (half + 1) * NT)
        return k.h[:, c, t * P:(t + 1) * P], k.ps[:, 2 * t + half, :].rearrange("p (c m) -> p c m", c=NT)

    with ExitStack() as own:
        w_hi, w_lo = (k.alloc("wo_" + name, [P, PIECES, D], F32R, own) for name in ("hi", "lo"))
        l_hi, l_lo = (k.alloc("lhs_" + name, [P, PIECES, T], F32R, own) for name in ("hi", "lo"))
        gnext = k.alloc("next_gain", [P, D], F32, own)
        squares = k.alloc("squares", [P, D], F32, own)
        block = own.enter_context(nc.Block(no_gpsimd_drain=True))

        @block.sync
        def _(sp):
            sp.dma_start(gnext[:, :], everywhere(next_gain, D)).then_inc(k.param_loaded.sem, 16)
            if gain is not None:
                sp.dma_start(k.gpost[:, :], everywhere(gain, D)).then_inc(k.param_loaded.sem, 16)
            for c in range(2, len(chunks)):
                sp.wait_ge(*k.w_lo_ready(4 * (c - 1)))
                load_weights(k, sp, chunks[c])
            for nxt in after:
                sp.wait_ge(*k.w_lo_ready(tiles))
                if callable(nxt):
                    nxt(sp)
                else:
                    load_weights(k, sp, nxt)

        @block.tensor
        def _(pe):
            def tile(n, t):
                for half in range(2):
                    last = product(nc, k.ps[:, 2 * t + half, :], [h[:, n % PIECES, t * P:(t + 1) * P] for h in (l_hi, l_lo)],
                                   [h[:, n % PIECES, half * BANK:(half + 1) * BANK] for h in (w_hi, w_lo)], n == 0, n == tiles - 1,
                                   skip_group_check=True)
                return last

            for n in range(tiles):
                pe.wait_ge(*k.w_lo_ready(n + 1))
                pe.wait_ge(*k.h_lo_ready(n + 1))
                if n < bulk:
                    for t in range(NT):
                        last = tile(n, t)
                    last.then_inc(k.products.sem, 1)
            for t in range(NT):
                for n in range(bulk, tiles):
                    last = tile(n, t)
                last.then_inc(k.products.sem, 1)
            for t in range(NT):
                pe.wait_ge(*k.norm_ready(t + 1))
                for c in range(KD):
                    last = nc.tensor.transpose(k.ps[:, 2 * t + c // NT, (c % NT) * P:(c % NT + 1) * P], scratch[:, t, c * P:(c + 1) * P], k.ident[:, :])
                last.then_inc(k.acc_ready.sem, 1)

        @block.scalar
        def _(act):
            for n in range(tiles):
                if n % 4 == 0:
                    act.wait_ge(k.loaded[landed[n // 4][0]].sem, landed[n // 4][1])
                if n >= PIECES:
                    act.wait_ge(*k.products(n - PIECES + 1))
                nc.scalar.copy(w_hi[:, n % PIECES, :], weights(n)).then_inc(k.w_hi_ready.sem, 1)
                nc.scalar.copy(l_hi[:, n % PIECES, :], lhs(n)).then_inc(k.h_hi_ready.sem, 1)

            def root_of(t, values, total, out, signal):
                nc.scalar.activation(squares[:, :], values, ACT.Square, accum_out=total[:, t:t + 1])
                act.drain()
                nc.scalar.activation(out[:, t:t + 1], total[:, t:t + 1], ACT.Sqrt, bias=k.eps[:, 0:1], scale=1.0 / D).then_inc(signal.sem, 1)

            def result(t):
                if gain is not None:
                    act.wait_ge(*k.products(bulk + t + 1))
                    root_of(t, whole(t), ss, root, k.root_ready)

            def norm(t):
                act.wait_ge(*k.x_ready(t + 1))
                root_of(t, k.x[:, t, :], ss2, root2, k.mean_ready)

            def read_out(t):
                act.wait_ge(*k.acc_ready(t + 1))
                nc.scalar.copy(*turned_half(t, 0))

            steps(result, norm, read_out)

        @block.gpsimd
        def _(pool):
            for n in range(tiles):
                pool.wait_ge(*k.w_hi_ready(n + 1))
                rest(nc.gpsimd, w_lo[:, n % PIECES, :], weights(n), w_hi[:, n % PIECES, :]).then_inc(k.w_lo_ready.sem, 1)
            for t in range(NT if gain is not None else 0):
                pool.wait_ge(*k.result_ready(t + 1))
                nc.gpsimd.tensor_tensor(k.x[:, t, :], k.x[:, t, :], scratch[:, t, :], ALU.add).then_inc(k.x_ready.sem, 1)
            pool.drain()

        @block.vector
        def _(dve):
            for n in range(tiles):
                dve.wait_ge(*k.h_hi_ready(n + 1))
                rest(nc.vector, l_lo[:, n % PIECES, :], lhs(n), l_hi[:, n % PIECES, :]).then_inc(k.h_lo_ready.sem, 1)
            dve.wait_ge(*k.param_loaded(32 if gain is not None else 16))

            def result(t):
                if gain is None:
                    dve.wait_ge(*k.products(bulk + t + 1))
                    nc.vector.tensor_tensor(k.x[:, t, :], k.x[:, t, :], whole(t), ALU.add).then_inc(k.x_ready.sem, 1)
                    return
                dve.wait_ge(*k.root_ready(t + 1))
                nc.vector.reciprocal(ss[:, t:t + 1], root[:, t:t + 1])
                dve.drain()
                nc.vector.scalar_tensor_tensor(out=scratch[:, t, :], in0=whole(t), scalar=ss[:, t:t + 1], in1=k.gpost[:, :],
                                               op0=ALU.mult, op1=ALU.mult).then_inc(k.result_ready.sem, 1)

            def norm(t):
                dve.wait_ge(*k.mean_ready(t + 1))
                nc.vector.reciprocal(ss2[:, t:t + 1], root2[:, t:t + 1])
                dve.drain()
                nc.vector.scalar_tensor_tensor(out=scratch[:, t, :], in0=k.x[:, t, :], scalar=ss2[:, t:t + 1], in1=gnext[:, :],
                                               op0=ALU.mult, op1=ALU.mult).then_inc(k.norm_ready.sem, 1)

            def read_out(t):
                dve.wait_ge(*k.acc_ready(t + 1))
                nc.vector.tensor_copy(*turned_half(t, 1))

            steps(result, norm, read_out)
    for signal in (k.w_hi_ready, k.w_lo_ready, k.h_hi_ready, k.h_lo_ready):
        signal.close(tiles)
    k.products.close(bulk + NT)
    for signal in (k.x_ready, k.mean_ready, k.norm_ready, k.acc_ready):
        signal.close(NT)
    k.param_loaded.close(32 if gain is not None else 16)
    if gain is not None:
        k.root_ready.close(NT)
        k.result_ready.close(NT)



DIRS = (0, 1)
GW = SSD_H + ML_H


def decays(k, g, small, xbc):
    nc = k.nc
    nd = 2 * SSD_H
    n = nd + 2 * ML_H
    pre, neg, ex, s, s2, poly = (g.work[:, i, :, :] for i in range(6))

    def to(ap):
        return ap.rearrange("p (o n) -> p o n", o=1).to_broadcast([P, NT, ap.shape[1]])

    with nc.Block(no_gpsimd_drain=True) as block:
        @block.vector
        def _(dve):
            nc.vector.tensor_tensor(pre[:, :, 0:nd], small[:, :, 0:nd], to(k.b["ab_dt_bias"]), ALU.add)
            nc.vector.tensor_tensor(pre[:, :, nd:n], small[:, :, nd + 2 * ML_H:nd + 4 * ML_H], to(k.b["ab_fg_bias"]), ALU.add)
            nc.vector.tensor_tensor(g.ig[:, :, :], small[:, :, nd:nd + 2 * ML_H], to(k.b["ab_ig_bias"]), ALU.add)
            dve.drain()
            nc.vector.tensor_scalar(pre[:, :, nd:n], pre[:, :, nd:n], -1.0, None, ALU.mult)
            dve.drain()
            nc.vector.scalar_tensor_tensor(out=neg, in0=pre, scalar=-1.0, in1=pre, op0=ALU.mult, op1=ALU.min).then_inc(k.va.sem, 1)
            dve.wait_ge(*k.sa(1))
            nc.vector.tensor_scalar(s, ex, 2.0, None, ALU.add)
            dve.drain()
            nc.vector.reciprocal(s2, s)
            dve.drain()
            nc.vector.tensor_tensor(s, ex, s2, ALU.mult)
            dve.drain()
            nc.vector.tensor_tensor(s2, s, s, ALU.mult)
            dve.drain()
            nc.vector.tensor_scalar(poly, s2, 1.0 / 17.0, None, ALU.mult)
            for m in (15, 13, 11, 9, 7, 5, 3):
                dve.drain()
                nc.vector.scalar_tensor_tensor(out=poly, in0=poly, scalar=1.0 / m, in1=s2, op0=ALU.add, op1=ALU.mult)
            dve.drain()
            nc.vector.scalar_tensor_tensor(out=poly, in0=poly, scalar=1.0, in1=s, op0=ALU.add, op1=ALU.mult)
            dve.drain()
            nc.vector.tensor_scalar(s, pre, 0.0, None, ALU.max)
            dve.drain()
            nc.vector.scalar_tensor_tensor(out=s, in0=poly, scalar=2.0, in1=s, op0=ALU.mult, op1=ALU.add)
            dve.drain()
            nc.vector.tensor_copy(g.dt[:, :, :], s[:, :, 0:nd])
            dve.wait_ge(*k.sa(2))
            for d in DIRS:
                nc.vector.scalar_tensor_tensor(out=g.ld[:, :, d * GW:d * GW + SSD_H], in0=s[:, :, d * SSD_H:(d + 1) * SSD_H], scalar=-1.0,
                                               in1=to(g.ea[:, d * SSD_H:(d + 1) * SSD_H]), op0=ALU.mult, op1=ALU.mult)
                last = nc.vector.tensor_scalar(g.ld[:, :, d * GW + SSD_H:(d + 1) * GW], s[:, :, nd + d * ML_H:nd + (d + 1) * ML_H],
                                               -1.0, None, ALU.mult)
            dve.drain()
            nc.vector.memset(poly, 0.0).then_inc(k.va.sem, 1)
            dve.wait_ge(*k.acc_ready(1))
            cps = k.ps[:, 0, 0:NT * 4 * GW].rearrange("p (c n) -> p c n", c=NT)
            nc.vector.tensor_copy(g.cum[:, :, :], cps[:, :, 0:2 * GW])
            nc.vector.tensor_copy(g.tot[:, :, :], cps[:, :, 2 * GW:4 * GW])
            dve.drain()
            for d in DIRS:
                nc.vector.tensor_tensor(g.wend[:, :, d * SSD_H:(d + 1) * SSD_H], g.tot[:, :, d * GW:d * GW + SSD_H],
                                        g.cum[:, :, d * GW:d * GW + SSD_H], ALU.subtract)
                nc.vector.tensor_tensor(g.u[:, d, :, :], g.ig[:, :, d * ML_H:(d + 1) * ML_H],
                                        g.cum[:, :, d * GW + SSD_H:(d + 1) * GW], ALU.subtract)
                nc.vector.tensor_copy(g.dec[:, :, d * SSD_H:(d + 1) * SSD_H], g.tot[:, :, d * GW:d * GW + SSD_H])
            dve.drain()
            nc.vector.memset(poly, 0.0).then_inc(k.va.sem, 1)
            dve.wait_ge(*k.sa(3))
            nc.vector.tensor_tensor(g.wend[:, :, :], g.wend[:, :, :], g.dt[:, :, :], ALU.mult)

        @block.scalar
        def _(act):
            act.wait_ge(*k.va(1))
            nc.scalar.activation(ex, neg, ACT.Exp).then_inc(k.sa.sem, 1)
            nc.scalar.activation(g.ea[:, :], k.b["ab_a_log"], ACT.Exp).then_inc(k.sa.sem, 1)
            for j in range(0, XT, 4):
                nc.scalar.activation(xbc[:, j:j + 4, :], xbc[:, j:j + 4, :], ACT.Silu)
            act.wait_ge(*k.va(3))
            nc.scalar.activation(g.dec[:, :, :], g.dec[:, :, :], ACT.Exp)
            nc.scalar.activation(g.wend[:, :, :], g.wend[:, :, :], ACT.Exp).then_inc(k.sa.sem, 1)

        @block.tensor
        def _(pe):
            pe.wait_ge(*k.va(2))
            for c in range(NT):
                at = c * 4 * GW
                for d in DIRS:
                    nc.tensor.matmul(k.ps[:, 0, at + d * GW:at + (d + 1) * GW], k.tri[d][:, :], g.ld[:, c, d * GW:(d + 1) * GW],
                                     start=True, stop=True, skip_group_check=True)
                last = nc.tensor.matmul(k.ps[:, 0, at + 2 * GW:at + 4 * GW], k.ones[:, :], g.ld[:, c, :],
                                        start=True, stop=True, skip_group_check=True)
            last.then_inc(k.acc_ready.sem, 1)
    k.va.close(3)
    k.sa.close(3)
    k.acc_ready.close(1)



def ssd_taps(k, dve, raw, out, after):
    nc = k.nc
    tap, bias = k.pcol[:, 0, 32:92], k.pcol[:, 0, 92:104]
    for first in range(0, XT, 4):
        tiles = range(first, first + 4)
        dve.wait_ge(*k.acc_free(after[first // 4]))
        for j in tiles:
            nc.vector.tensor_scalar(out[:, j, :], raw[:, j, 0:T], tap[:, j:j + 1], bias[:, j:j + 1], ALU.mult, ALU.add)
        dve.drain()
        for i in range(1, SSD_TAPS):
            for j in tiles:
                nc.vector.scalar_tensor_tensor(out=out[:, j, :], in0=raw[:, j, i:i + T], scalar=tap[:, i * XT + j:i * XT + j + 1],
                                               in1=out[:, j, :], op0=ALU.mult, op1=ALU.add)
            dve.drain()


def ssd_turn(k, xbc, x_tm, b_tm, cb):
    nc = k.nc
    with nc.Block(no_gpsimd_drain=True) as block:
        @block.tensor
        def _(pe):
            for c in range(NT):
                if c >= 2:
                    pe.wait_ge(*k.sa(c - 1))
                b = 3 * (c % 2)
                for j in range(10):
                    last = nc.tensor.transpose(k.ps[:, b + j // 4, (j % 4) * P:(j % 4 + 1) * P], xbc[:, j, c * P:(c + 1) * P], k.ident[:, :])
                last.then_inc(k.acc_ready.sem, 1)
            for grp in range(2):
                for c in range(NT):
                    last = nc.tensor.matmul(k.ps[:, 6 + grp, c * P:(c + 1) * P], xbc[:, 8 + grp, c * P:(c + 1) * P],
                                            xbc[:, 10 + grp, c * P:(c + 1) * P], start=True, stop=True, skip_group_check=True)
                last.then_inc(k.acc_ready.sem, 1)

        @block.scalar
        def _(act):
            for c in range(NT):
                b = 3 * (c % 2)
                act.wait_ge(*k.acc_ready(c + 1))
                nc.scalar.copy(b_tm[:, c, :], k.ps[:, b + 2, 0:2 * P])
                nc.scalar.copy(x_tm[:, c, :], k.ps[:, b:b + 2, :].rearrange("p a b -> p (a b)")).then_inc(k.sa.sem, 1)

        @block.vector
        def _(dve):
            for grp in range(2):
                dve.wait_ge(*k.acc_ready(NT + grp + 1))
                for d in DIRS:
                    nc.vector.tensor_tensor(cb[:, d, grp, :].rearrange("p (c l) -> p c l", c=NT),
                                            k.ps[:, 6 + grp, :].rearrange("p (c l) -> p c l", c=NT),
                                            k.tri[d][:, :].rearrange("p (o l) -> p o l", o=1).to_broadcast([P, NT, P]), ALU.mult)
    k.sa.close(NT)
    k.acc_ready.close(NT + 2)


def ssd_states(k, g, x_tm, b_tm, hst, xw):
    nc = k.nc
    steps = [step for c in range(NT - 1) for step in ((0, c), (1, NT - 1 - c))]
    with nc.Block(no_gpsimd_drain=True) as block:
        @block.gpsimd
        def _(pool):
            for n, (d, c) in enumerate(steps):
                if n >= 2:
                    pool.wait_ge(*k.acc_ready(n - 1))
                nc.gpsimd.tensor_tensor(xw[:, n % 2, :].rearrange("p (h e) -> p h e", h=SSD_H),
                                        x_tm[:, c, :].rearrange("p (h e) -> p h e", h=SSD_H),
                                        g.wend[:, c, d * SSD_H:(d + 1) * SSD_H].rearrange("p (h o) -> p h o", o=1).to_broadcast([P, SSD_H, SSD_P]),
                                        ALU.mult).then_inc(k.va.sem, 1)
            pool.drain()

        @block.vector
        def _(dve):
            nc.vector.memset(hst[:, 0, 0, :], 0.0)
            nc.vector.memset(hst[:, 1, NT - 1, :], 0.0)

            for n, (d, c) in enumerate(steps):
                nxt = c + 1 if d == 0 else c - 1
                dec = g.dec[:, c, d * SSD_H:(d + 1) * SSD_H].rearrange("p (h o) -> p h o", o=1).to_broadcast([P, SSD_H, SSD_P])
                dve.drain()
                nc.vector.tensor_tensor(hst[:, d, nxt, :].rearrange("p (h e) -> p h e", h=SSD_H),
                                        hst[:, d, c, :].rearrange("p (h e) -> p h e", h=SSD_H), dec, ALU.mult)
                dve.wait_ge(*k.acc_ready(n + 1))
                dve.drain()
                b = 2 * (n % 4)
                nc.vector.tensor_tensor(hst[:, d, nxt, :], hst[:, d, nxt, :], k.ps[:, b:b + 2, :].rearrange("p a b -> p (a b)"),
                                        ALU.add).then_inc(k.vb.sem, 1)

        @block.tensor
        def _(pe):
            for n, (d, c) in enumerate(steps):
                pe.wait_ge(*k.va(n + 1))
                if n >= 4:
                    pe.wait_ge(*k.vb(n - 3))
                for grp in range(2):
                    last = nc.tensor.matmul(k.ps[:, 2 * (n % 4) + grp, :], b_tm[:, c, grp * P:(grp + 1) * P],
                                            xw[:, n % 2, grp * BANK:(grp + 1) * BANK], start=True, stop=True)
                last.then_inc(k.acc_ready.sem, 1)
    k.va.close(len(steps))
    k.vb.close(len(steps))
    k.acc_ready.close(len(steps))


def ssd_mix(k, g, xbc, x_tm, cb, hst, y_tm, buf):
    nc = k.nc
    units = [(h, d) for h in range(SSD_H) for d in DIRS]
    arg, gg, w, ec, ce = buf
    half = SSD_H // 2

    def col(h, d):
        return d * GW + h

    with nc.Block(no_gpsimd_drain=True) as block:
        @block.tensor
        def _(pe):
            def sums(n):
                h, d = units[n]
                if n >= 4:
                    pe.wait_ge(*k.sa(n - 3))
                for c in range(NT):
                    last = nc.tensor.matmul(k.ps[:, 4 + n % 4, c * P:(c + 1) * P], spread(g.ld[:, c, col(h, d):col(h, d) + 1], [P, P]),
                                            k.tri[d][:, :], start=True, stop=True, skip_group_check=True)
                last.then_inc(k.pa.sem, 1)

            def mix(h):
                if h == half:
                    pe.wait_ge(*k.vc(1))
                pe.wait_ge(*k.vb(2 * h + 2))
                pe.wait_ge(*k.ga(2 * h + 2))
                at = h * SSD_P
                for c in range(NT):
                    out = k.ps[:, c, (h % half) * SSD_P:(h % half + 1) * SSD_P]
                    tok = slice(c * P, (c + 1) * P)
                    for d in DIRS:
                        nc.tensor.matmul(out, w[:, 2 * (h % 2) + d, tok], x_tm[:, c, at:at + SSD_P], start=(d == 0), stop=False, skip_group_check=True)
                    for d in DIRS:
                        last = nc.tensor.matmul(out, ce[:, 2 * (h % 2) + d, tok], hst[:, d, c, at:at + SSD_P], start=False, stop=(d == 1), skip_group_check=True)
                last.then_inc(k.pb.sem, 1)

            for n in range(4):
                sums(n)
            for h in range(SSD_H):
                for n in (2 * h + 4, 2 * h + 5):
                    if n < len(units):
                        sums(n)
                mix(h)

        @block.vector
        def _(dve):
            def args(n):
                h, d = units[n]
                dve.wait_ge(*k.pa(n + 1))
                if n >= 2:
                    dve.wait_ge(*k.sb(n - 1))
                for c in range(NT):
                    tok = slice(c * P, (c + 1) * P)
                    last = nc.vector.tensor_scalar(arg[:, n % 2, tok], k.ps[:, 4 + n % 4, tok], g.cum[:, c, col(h, d):col(h, d) + 1], 0.0,
                                                   ALU.subtract, ALU.min)
                last.then_inc(k.va.sem, 1)

            def weights(n):
                h, d = units[n]
                dve.wait_ge(*k.sb(n + 1))
                if n >= 4:
                    dve.wait_ge(*k.pb(n // 2 - 1))
                for c in range(NT):
                    tok = slice(c * P, (c + 1) * P)
                    last = nc.vector.scalar_tensor_tensor(out=w[:, n % 4, tok], in0=gg[:, n % 2, tok], scalar=g.dt[:, c, d * SSD_H + h:d * SSD_H + h + 1],
                                                          in1=cb[:, d, h // half, tok], op0=ALU.mult, op1=ALU.mult)
                last.then_inc(k.vb.sem, 1)

            def read_out(part):
                dve.wait_ge(*k.pb(half * (part + 1)))
                for c in range(NT):
                    last = nc.vector.tensor_copy(y_tm[:, c, part * BANK:(part + 1) * BANK], k.ps[:, c, :])
                last.then_inc(k.vc.sem, 1)

            args(0)
            for n in range(len(units)):
                if n + 1 < len(units):
                    args(n + 1)
                if n == 2 * half:
                    read_out(0)
                weights(n)
            read_out(1)

        @block.scalar
        def _(act):
            for n, (h, d) in enumerate(units):
                act.wait_ge(*k.va(n + 1))
                if n >= 2:
                    act.wait_ge(*k.ga(n - 1))
                nc.scalar.activation(ec[:, n % 2, :], k.ps[:, 4 + n % 4, :], ACT.Exp).then_inc(k.sa.sem, 1)
                if n >= 2:
                    act.wait_ge(*k.vb(n - 1))
                nc.scalar.activation(gg[:, n % 2, :], arg[:, n % 2, :], ACT.Exp).then_inc(k.sb.sem, 1)

        @block.gpsimd
        def _(pool):
            for n, (h, d) in enumerate(units):
                pool.wait_ge(*k.sa(n + 1))
                if n >= 4:
                    pool.wait_ge(*k.pb(n // 2 - 1))
                nc.gpsimd.tensor_tensor(ce[:, n % 4, :], xbc[:, 10 + h // half, :], ec[:, n % 2, :], ALU.mult).then_inc(k.ga.sem, 1)
            pool.drain()
    n = len(units)
    k.pa.close(n)
    k.pb.close(SSD_H)
    k.va.close(n)
    k.vb.close(n)
    k.vc.close(2)
    k.sa.close(n)
    k.sb.close(n)
    k.ga.close(n)





MW = ML_D + 1


def mlstm_gates(k, g, r):
    nc = k.nc
    H = ML_H
    u_row, cm, ms_row, tot, mx, so = r.u_row, r.cm, r.ms_row, r.tot, r.mx, r.so

    def at_chunks(ap):
        return ap.rearrange("h d (c l) -> h d c l", c=NT)

    def each(ap):
        return ap.rearrange("h d (c o) -> h d c o", o=1).to_broadcast([H, 2, NT, P])

    with nc.Block(no_gpsimd_drain=True) as block:
        @block.gpsimd
        def _(pool):
            nc.gpsimd.memset(r.restart[:, :, :], 0.0)
            pool.drain()
            for c in range(NT):
                nc.gpsimd.memset(r.restart[:, 0, c * P:c * P + 1], -3e38)
                nc.gpsimd.memset(r.restart[:, 1, c * P + P - 1:c * P + P], -3e38)
            pool.drain()
            nc.gpsimd.memset(ms_row[:, :, :], 0.0).then_inc(k.ga.sem, 1)
            pool.drain()

        @block.tensor
        def _(pe):
            for d in DIRS:
                for c in range(NT):
                    last = nc.tensor.transpose(k.ps[0:H, d, c * P:(c + 1) * P], g.u[:, d, c, :], k.ident[:, :])
            last.then_inc(k.acc_ready.sem, 1)
            for d in DIRS:
                for c in range(NT):
                    last = nc.tensor.matmul(k.ps[0:H, 2, 4 * d + c:4 * d + c + 1], g.ld[:, c, d * GW + SSD_H:(d + 1) * GW], k.ones[:, 0:1],
                                            start=True, stop=True, skip_group_check=True)
            last.then_inc(k.acc_ready.sem, 1)
            pe.wait_ge(*k.vb(1))
            for d in DIRS:
                for c in range(NT):
                    last = nc.tensor.transpose(k.ps[:, 3, (d * NT + c) * H:(d * NT + c + 1) * H], r.nm[:, d, c * P:(c + 1) * P], k.ident[0:H, 0:H])
            last.then_inc(k.acc_ready.sem, 1)
            pe.wait_ge(*k.sa(1))
            for d in DIRS:
                for c in range(NT):
                    last = nc.tensor.transpose(k.ps[:, 4, (d * NT + c) * H:(d * NT + c + 1) * H], r.ew_row[:, d, c * P:(c + 1) * P], k.ident[0:H, 0:H])
            pe.wait_ge(*k.vc(1))
            nc.tensor.matmul(k.ps[:, 5, 0:2 * H * 2 * NT], k.ones[0:H, :], r.diag[:, :], start=True, stop=True).then_inc(k.acc_ready.sem, 1)

        @block.vector
        def _(dve):
            dve.wait_ge(*k.acc_ready(1))
            nc.vector.tensor_copy(u_row[:, :, :], k.ps[0:H, 0:2, :])
            dve.wait_ge(*k.acc_ready(2))
            nc.vector.tensor_copy(tot[:, :, :], k.ps[0:H, 2, 0:8].rearrange("h (d c) -> h d c", d=2))
            dve.wait_ge(*k.ga(1))
            dve.drain()
            nc.vector.tensor_tensor_scan(cm[:, 0, :], r.restart[:, 0, :], u_row[:, 0, :], 0.0, ALU.add, ALU.max)
            nc.vector.tensor_tensor_scan(cm[:, 1, :][:, ::-1], r.restart[:, 1, :][:, ::-1], u_row[:, 1, :][:, ::-1], 0.0, ALU.add, ALU.max)
            dve.drain()
            nc.vector.tensor_copy(r.umax[:, 0, :], at_chunks(cm[:, :, :])[:, 0, :, P - 1])
            nc.vector.tensor_copy(r.umax[:, 1, :], at_chunks(cm[:, :, :])[:, 1, :, 0])
            dve.drain()
            for n in range(NT):
                for d in DIRS:
                    c = n if d == 0 else NT - 1 - n
                    nc.vector.tensor_tensor(mx[:, d, c:c + 1], ms_row[:, d, c:c + 1], r.umax[:, d, c:c + 1], ALU.max)
                dve.drain()
                if n < NT - 1:
                    for d in DIRS:
                        c = n if d == 0 else NT - 1 - n
                        nxt = c + 1 if d == 0 else c - 1
                        nc.vector.tensor_tensor(ms_row[:, d, nxt:nxt + 1], mx[:, d, c:c + 1], tot[:, d, c:c + 1], ALU.add)
                    dve.drain()
            nc.vector.tensor_tensor(at_chunks(r.nm[:, :, :]), at_chunks(cm[:, :, :]), each(ms_row[:, :, :]), ALU.max)
            nc.vector.tensor_tensor(so[:, 0, :, :], ms_row[:, :, :], mx[:, :, :], ALU.subtract)
            nc.vector.tensor_tensor(so[:, 1, :, :], r.umax[:, :, :], mx[:, :, :], ALU.subtract)
            dve.drain()
            nc.vector.tensor_tensor(at_chunks(r.si[:, :, :]), each(ms_row[:, :, :]), at_chunks(r.nm[:, :, :]), ALU.subtract)
            nc.vector.tensor_tensor(at_chunks(r.ew_row[:, :, :]), at_chunks(u_row[:, :, :]), each(r.umax[:, :, :]), ALU.subtract)
            nc.vector.tensor_scalar(r.nm[:, :, :], r.nm[:, :, :], -1.0, None, ALU.mult)
            dve.drain()
            nc.vector.memset(r.bar[:, 0:1], 0.0).then_inc(k.vb.sem, 1)
            dve.wait_ge(*k.sa(2))
            nc.vector.tensor_tensor(r.diag[:, :].rearrange("h (n q) -> h n q", n=H), spread(so[:, :, :, :].rearrange("h s d c -> h (s d c)").rearrange("h (o q) -> h o q", o=1), [H, H, 4 * NT]),
                                    spread(k.ident[0:H, 0:H].rearrange("h (n o) -> h n o", o=1), [H, H, 4 * NT]), ALU.mult).then_inc(k.vc.sem, 1)
            dve.wait_ge(*k.acc_ready(3))
            for d in DIRS:
                nc.vector.tensor_tensor(r.floor[:, d, :, :], k.ps[:, 3, d * NT * H:(d + 1) * NT * H].rearrange("p (c h) -> p c h", c=NT),
                                        g.cum[:, :, d * GW + SSD_H:(d + 1) * GW], ALU.subtract)
            dve.drain()
            nc.vector.memset(r.bar[:, 1:2], 0.0).then_inc(k.vc.sem, 1)
            dve.wait_ge(*k.acc_ready(4))
            nc.vector.tensor_copy(r.ew[:, :, :, :].rearrange("p d c h -> p (d c h)"), k.ps[:, 4, 0:2 * NT * H])
            spr = k.ps[:, 5, 0:H * 4 * NT].rearrange("p (h s d c) -> p h s d c", h=H, s=2, d=2)
            for d in DIRS:
                nc.vector.tensor_copy(r.sold[:, d, :, :].rearrange("p c h -> p h c"), spr[:, :, 0, d, :])
                nc.vector.tensor_copy(r.sloc[:, d, :, :].rearrange("p c h -> p h c"), spr[:, :, 1, d, :])

        @block.scalar
        def _(act):
            act.wait_ge(*k.vb(1))
            nc.scalar.activation(r.ew_row[:, :, :], r.ew_row[:, :, :], ACT.Exp).then_inc(k.sa.sem, 1)
            nc.scalar.activation(so[:, :, :, :], so[:, :, :, :], ACT.Exp).then_inc(k.sa.sem, 1)
            nc.scalar.activation(r.si[:, :, :], r.si[:, :, :], ACT.Exp)
            act.wait_ge(*k.vc(2))
            nc.scalar.activation(r.floor[:, :, :, :], r.floor[:, :, :, :], ACT.Exp)
    k.ga.close(1)
    k.acc_ready.close(4)
    k.vb.close(1)
    k.vc.close(2)
    k.sa.close(2)


def mlstm_states(k, r, k_cm, v, cst, kw):
    nc = k.nc
    H = ML_H
    steps = [step for c in range(NT - 1) for step in ((0, c), (1, NT - 1 - c))]

    def bank(h):
        return k.ps[:, 4 + h // 2, (h % 2) * 256:(h % 2) * 256 + MW]

    def banks():
        return k.ps[:, 4:8, :].rearrange("p b (e w) -> p (b e) w", e=2)[:, :, 0:MW]

    def per_head(ap):
        return ap.rearrange("p (h o) -> p h o", o=1).to_broadcast([P, H, MW])

    with nc.Block(no_gpsimd_drain=True) as block:
        @block.tensor
        def _(pe):
            def turn(n):
                d, c = steps[n]
                if n >= 2:
                    pe.wait_ge(*k.va(n - 1))
                for h in range(H):
                    last = nc.tensor.transpose(k.ps[:, 2 * (n % 2) + h // 4, (h % 4) * P:(h % 4 + 1) * P], k_cm[:, h, c * P:(c + 1) * P], k.ident[:, :])
                last.then_inc(k.pa.sem, 1)

            turn(0)
            for n, (d, c) in enumerate(steps):
                if n + 1 < len(steps):
                    turn(n + 1)
                pe.wait_ge(*k.va(n + 1))
                if n >= 1:
                    pe.wait_ge(*k.vb(n))
                for h in range(H):
                    last = nc.tensor.matmul(bank(h), kw[:, n % 2, h * P:(h + 1) * P], v[:, c, h, :], start=True, stop=True, skip_group_check=True)
                last.then_inc(k.pb.sem, 1)

        @block.gpsimd
        def _(pool):
            nc.gpsimd.memset(cst[:, 0, 0, :, :], 0.0)
            nc.gpsimd.memset(cst[:, 1, NT - 1, :, :], 0.0)
            pool.drain()
            for n, (d, c) in enumerate(steps):
                nxt = c + 1 if d == 0 else c - 1
                if n >= 2:
                    pool.wait_ge(*k.vc(n - 1))
                nc.gpsimd.tensor_tensor(cst[:, d, nxt, :, :], cst[:, d, c, :, :], per_head(r.sold[:, d, c, :]), ALU.mult).then_inc(k.ga.sem, 1)
            pool.drain()

        @block.vector
        def _(dve):
            def weigh(n):
                d, c = steps[n]
                dve.wait_ge(*k.pa(n + 1))
                if n >= 2:
                    dve.wait_ge(*k.pb(n - 1))
                b = 2 * (n % 2)
                nc.vector.tensor_tensor(kw[:, n % 2, :].rearrange("p (h e) -> p h e", h=H), k.ps[:, b:b + 2, :].rearrange("p b (h e) -> p (b h) e", e=P),
                                        r.ew[:, d, c, :].rearrange("p (h o) -> p h o", o=1).to_broadcast([P, H, P]), ALU.mult).then_inc(k.va.sem, 1)

            weigh(0)
            for n, (d, c) in enumerate(steps):
                if n + 1 < len(steps):
                    weigh(n + 1)
                nxt = c + 1 if d == 0 else c - 1
                dve.wait_ge(*k.pb(n + 1))
                nc.vector.tensor_tensor(r.own[:, :, :], banks(), per_head(r.sloc[:, d, c, :]), ALU.mult).then_inc(k.vb.sem, 1)
                dve.wait_ge(*k.ga(n + 1))
                dve.drain()
                nc.vector.tensor_tensor(cst[:, d, nxt, :, :], cst[:, d, nxt, :, :], r.own[:, :, :], ALU.add).then_inc(k.vc.sem, 1)
                dve.drain()
    n = len(steps)
    for s in (k.pa, k.pb, k.va, k.vb, k.vc, k.ga):
        s.close(n)


def mlstm_mix(k, g, r, q_cm, k_cm, v, cst, hm, buf):
    nc = k.nc
    H = ML_H
    units = [(h, d) for h in range(H) for d in DIRS]
    arg, gg, w, qs, qk = (buf[:, n, :, :] for n in range(5))
    NUM, SUMS, SI, QK = 0, 4, 5, 6

    def num(c, d):
        return k.ps[:, NUM + c, d * 256:d * 256 + MW]

    with nc.Block(no_gpsimd_drain=True) as block:
        @block.tensor
        def _(pe):
            def scores(h):
                if h >= 1:
                    pe.wait_ge(*k.vc(h))
                for c in range(NT):
                    tok = slice(c * P, (c + 1) * P)
                    last = nc.tensor.matmul(k.ps[:, QK, tok], k_cm[:, h, tok], q_cm[:, h, tok], start=True, stop=True, skip_group_check=True)
                last.then_inc(k.pc.sem, 1)

            def rows(n):
                h, d = units[n]
                if n >= 1:
                    pe.wait_ge(*k.va(n))
                pick = spread(k.ident[0:H, h:h + 1], [H, P])
                nc.tensor.matmul(k.ps[:, SUMS, :], pick, r.nm[:, d, :], start=True, stop=True)
                if n >= 1:
                    pe.wait_ge(*k.vd(n))
                nc.tensor.matmul(k.ps[:, SI, :], pick, r.si[:, d, :], start=True, stop=True).then_inc(k.pa.sem, 1)

            def mix(n):
                h, d = units[n]
                pe.wait_ge(*k.vb(n + 1))
                pe.wait_ge(*k.vd(n + 1))
                if h >= 1:
                    pe.wait_ge(*k.da(h))
                for c in range(NT):
                    tok = slice(c * P, (c + 1) * P)
                    nc.tensor.matmul(num(c, d), w[:, d, tok], v[:, c, h, :], start=True, stop=False, skip_group_check=True)
                    last = nc.tensor.matmul(num(c, d), qs[:, d, tok], cst[:, d, c, h, :], start=False, stop=True, skip_group_check=True)
                last.then_inc(k.pb.sem, 1)

            scores(0)
            rows(0)
            for n, (h, d) in enumerate(units):
                if n + 1 < len(units):
                    if d == 1:
                        scores(h + 1)
                    rows(n + 1)
                mix(n)

        @block.vector
        def _(dve):
            def prepare(n):
                h, d = units[n]
                if d == 0:
                    dve.wait_ge(*k.pc(h + 1))
                    for e in DIRS:
                        last = nc.vector.tensor_tensor(qk[:, e, :].rearrange("p (c l) -> p c l", c=NT), k.ps[:, QK, :].rearrange("p (c l) -> p c l", c=NT),
                                                       spread(k.tri[e][:, :].rearrange("p (o l) -> p o l", o=1), [P, NT, P]), ALU.mult)
                    last.then_inc(k.vc.sem, 1)
                dve.wait_ge(*k.pa(n + 1))
                if n >= 2:
                    dve.wait_ge(*k.sa(n - 1))
                for c in range(NT):
                    tok = slice(c * P, (c + 1) * P)
                    last = nc.vector.tensor_scalar(arg[:, n % 2, tok], k.ps[:, SUMS, tok], g.u[:, d, c, h:h + 1], 0.0, ALU.add, ALU.min)
                last.then_inc(k.va.sem, 1)
                if n >= 2:
                    dve.wait_ge(*k.pb(n - 1))
                nc.vector.tensor_tensor(qs[:, d, :], q_cm[:, h, :], k.ps[:, SI, :], ALU.mult).then_inc(k.vd.sem, 1)

            def weights(n):
                h, d = units[n]
                dve.wait_ge(*k.sa(n + 1))
                if d == 0:
                    dve.drain()
                nc.vector.tensor_tensor(w[:, d, :], gg[:, n % 2, :], qk[:, d, :], ALU.mult).then_inc(k.vb.sem, 1)

            def read_out(h):
                dve.wait_ge(*k.sb(h + 1))
                nc.vector.tensor_tensor(r.den[:, :, :], r.den[:, :, :], r.floor[:, :, :, h].rearrange("p d c -> p c d"), ALU.max)
                dve.drain()
                nc.vector.reciprocal(r.rden[:, :, :], r.den[:, :, :])
                dve.drain()
                at = slice(h * ML_D, (h + 1) * ML_D)
                for c in range(NT):
                    nc.vector.tensor_scalar(hm[:, c, at], num(c, 0)[:, 0:ML_D], r.rden[:, c, 0:1], None, ALU.mult)
                dve.drain()
                for c in range(NT):
                    last = nc.vector.scalar_tensor_tensor(out=hm[:, c, at], in0=num(c, 1)[:, 0:ML_D], scalar=r.rden[:, c, 1:2], in1=hm[:, c, at],
                                                          op0=ALU.mult, op1=ALU.add)
                last.then_inc(k.da.sem, 1)

            prepare(0)
            for n, (h, d) in enumerate(units):
                weights(n)
                if n + 1 < len(units):
                    if d == 1:
                        dve.drain()
                    prepare(n + 1)
                if d == 1:
                    read_out(h)

        @block.scalar
        def _(act):
            for n, (h, d) in enumerate(units):
                act.wait_ge(*k.va(n + 1))
                if n >= 2:
                    act.wait_ge(*k.vb(n - 1))
                nc.scalar.activation(gg[:, n % 2, :], arg[:, n % 2, :], ACT.Exp).then_inc(k.sa.sem, 1)
                if d == 1:
                    act.wait_ge(*k.pb(n + 1))
                    if h >= 1:
                        act.wait_ge(*k.da(h))
                    nc.scalar.activation(r.den[:, :, :], k.ps[:, NUM:NUM + NT, :].rearrange("p c (d w) -> p c d w", d=2)[:, :, :, ML_D],
                                         ACT.Abs).then_inc(k.sb.sem, 1)
    n = len(units)
    for s in (k.pa, k.pb, k.va, k.vb, k.vd, k.sa):
        s.close(n)
    for s in (k.pc, k.vc, k.da, k.sb):
        s.close(H)


def gated_norm(k, y, o, heads, gain, dst, work, first_gate, skip=None, after=()):
    nc = k.nc
    W = D // heads
    few = heads <= 4
    ms, root, rstd = (k.stat[:, n, 0:NT * heads].rearrange("p (t h) -> p t h", h=heads) for n in range(3))

    def per_head(ap):
        return ap.rearrange("p (h e) -> p h e", h=heads)

    with nc.Block(no_gpsimd_drain=True) as block:
        @block.sync
        def _(sp):
            for w in after:
                load_weights(k, sp, w)

        @block.gpsimd
        def _(pool):
            for t in range(NT):
                if skip is not None:
                    x, factor = skip
                    factor = factor.rearrange("p (h o) -> p h o", o=1)
                    shape = [P, factor.shape[1], D // factor.shape[1]]
                    nc.gpsimd.tensor_tensor(work[:, t, :].rearrange("p (h e) -> p h e", h=shape[1]), x[:, t, :].rearrange("p (h e) -> p h e", h=shape[1]),
                                            spread(factor, shape), ALU.mult).then_inc(k.ga.sem, 1)
                elif first_gate:
                    nc.gpsimd.tensor_tensor(y[:, t, :], y[:, t, :], o[:, t, :], ALU.mult).then_inc(k.va.sem, 1)
                else:
                    pool.wait_ge(*k.vc(t + 1))
                    nc.gpsimd.tensor_tensor(work[:, t, :], work[:, t, :], o[:, t, :], ALU.mult).then_inc(k.norm_ready.sem, 1)
            pool.drain()

        @block.vector
        def _(dve):
            def total(t):
                if skip is not None:
                    dve.wait_ge(*k.ga(t + 1))
                    nc.vector.tensor_tensor(y[:, t, :], y[:, t, :], work[:, t, :], ALU.add)
                    dve.drain()
                    nc.vector.tensor_tensor(y[:, t, :], y[:, t, :], o[:, t, :], ALU.mult).then_inc(k.va.sem, 1)
                if not few:
                    dve.wait_ge(*k.sa(t + 1))
                    nc.vector.tensor_reduce(ms[:, t, :], per_head(work[:, t, :]), AX.X, ALU.add).then_inc(k.mean_ready.sem, 1)

            def norm(t):
                dve.wait_ge(*k.root_ready(t + 1))
                nc.vector.reciprocal(rstd[:, t, :], root[:, t, :])
                dve.drain()
                nc.vector.tensor_tensor(per_head(work[:, t, :]), per_head(y[:, t, :]), spread(rstd[:, t, :].rearrange("p (h o) -> p h o", o=1), [P, heads, W]),
                                        ALU.mult).then_inc((k.norm_ready if first_gate else k.vc).sem, 1)

            for t in range(NT):
                total(t)
                if t >= 1:
                    norm(t - 1)
            norm(NT - 1)
            dve.wait_ge(*k.acc_ready(1))
            for c in range(1, KD, 2):
                nc.vector.tensor_scalar(dst[:, c, :], k.ps[:, c, :], gain[:, c:c + 1], None, ALU.mult)

        @block.scalar
        def _(act):
            def roots(t):
                if not few:
                    act.wait_ge(*k.mean_ready(t + 1))
                nc.scalar.activation(root[:, t, :], ms[:, t, :], ACT.Sqrt, bias=k.eps[:, 0:1], scale=1.0 / W).then_inc(k.root_ready.sem, 1)

            for t in range(NT):
                if first_gate:
                    act.wait_ge(*k.va(t + 1))
                if few:
                    for h in range(heads):
                        at = slice(h * W, (h + 1) * W)
                        nc.scalar.activation(work[:, t, at], y[:, t, at], ACT.Square, accum_out=ms[:, t, h:h + 1])
                    act.drain()
                    roots(t)
                else:
                    nc.scalar.activation(work[:, t, :], y[:, t, :], ACT.Square).then_inc(k.sa.sem, 1)
                    if t >= 1:
                        roots(t - 1)
            if not few:
                roots(NT - 1)
            act.wait_ge(*k.acc_ready(1))
            for c in range(0, KD, 2):
                nc.scalar.activation(dst[:, c, :], k.ps[:, c, :], ACT.Copy, scale=gain[:, c:c + 1])

        @block.tensor
        def _(pe):
            for t in range(NT):
                pe.wait_ge(*k.norm_ready(t + 1))
                for c in range(KD):
                    last = nc.tensor.transpose(k.ps[:, c, t * P:(t + 1) * P], work[:, t, c * P:(c + 1) * P], k.ident[:, :])
            last.then_inc(k.acc_ready.sem, 1)
    if skip is not None:
        k.ga.close(NT)
    if first_gate:
        k.va.close(NT)
    else:
        k.vc.close(NT)
    if not few:
        k.sa.close(NT)
        k.mean_ready.close(NT)
    k.root_ready.close(NT)
    k.norm_ready.close(NT)
    k.acc_ready.close(1)


def layer0_mixer(k, next_gain, after):
    nc, A, sb = k.nc, k.A, k.alloc
    w = A["ab_w_in"][0]

    def cols(at, n):
        return w[:, at:at + n]

    def into_tm(dst, at, n):
        return lambda t, b: (dst[:, t, at:at + n], 1.0)

    def gate_tm(dst, at, gate):
        return lambda t, b: (dst[:, t, at:at + BANK], 1.0, gate)

    def into_cm(dst, tile, scale=1.0):
        return lambda j, b: (dst[:, tile + j, 0:T], scale)

    with ExitStack() as layer:
        z = sb("z_tm", [P, NT, D], to=layer)
        ycm = z[:, :, :].rearrange("p a b -> p (a b)").rearrange("p (k t) -> p k t", k=KD)
        g = Kernel()
        g.small = sb("g_small", [P, NT, 64], to=layer)
        g.dt = sb("g_dt", [P, NT, 32], to=layer)
        g.ig = sb("g_ig", [P, NT, 16], to=layer)
        g.ea = sb("g_ea", [P, 32], to=layer)
        g.ld = sb("g_ld", [P, NT, 2 * GW], to=layer)
        g.cum = sb("g_cum", [P, NT, 2 * GW], to=layer)
        g.tot = sb("g_tot", [P, NT, 2 * GW], to=layer)
        g.wend = sb("g_wend", [P, NT, 32], to=layer)
        g.dec = sb("g_dec", [P, NT, 32], to=layer)
        g.u = sb("g_u", [P, 2, NT, ML_H], to=layer)
        mjobs = [(cols(Q0 + n * BANK, BANK), "cm") for n in range(2)] + [(cols(K0 + n * BANK, BANK), "cm") for n in range(2)] \
            + [(cols(V0 + n * BANK, BANK), "tm") for n in range(2)]
        with ExitStack() as c:
            xbc = sb("xbc", [P, XT, T], to=c)
            with ExitStack() as e:
                raw = sb("xbc_raw", [P, XT, T + 2 * PAD], to=e)
                with nc.Block(no_gpsimd_drain=True) as block:
                    @block.vector
                    def _(dve):
                        nc.vector.memset(raw[:, :, 0:PAD], 0.0)
                        nc.vector.memset(raw[:, :, T + PAD:T + 2 * PAD], 0.0)
                x_jobs = [(cols(XBC0 + n * BANK, BANK), "cm", (lambda n: lambda j, b: (raw[:, 4 * n + j, PAD:PAD + T], 1.0))(n)) for n in range(3)]
                dt_job = (cols(DT0, 32), "tm", into_tm(g.small, 0, 32))
                gate_job = (cols(G0, 32), "tm", into_tm(g.small, 32, 32))
                jobs = [x_jobs[0], dt_job, x_jobs[1], gate_job, x_jobs[2]]
                jobs += [(cols(Z0 + n * BANK, BANK), "tm", gate_tm(z, n * BANK, ACT.Silu)) for n in range(2)]
                project(k, jobs, after=[mjobs[0][0], mjobs[1][0]], vector=lambda dve: ssd_taps(k, dve, raw, xbc, [NT * n for n in (1, 3, 5)]))
                g.work = sb("g_work", [P, 6, NT, 48], to=e)
                decays(k, g, g.small[:, :, :], xbc)
            x_tm = sb("x_heads", [P, NT, D], to=c)
            b_tm = sb("b_tm", [P, NT, 256], to=c)
            cb = sb("cb", [P, 2, 2, T], to=c)
            hst = sb("hst", [P, 2, NT, D], to=c)
            ssd_turn(k, xbc, x_tm, b_tm, cb)
            with ExitStack() as e:
                xw = sb("xw", [P, 2, D], to=e)
                ssd_states(k, g, x_tm, b_tm, hst, xw)
            with ExitStack() as e:
                ce = sb("ssd_ce", [P, 4, T], to=e)
                buf = [xbc[:, 0:2, :], xbc[:, 2:4, :], xbc[:, 4:8, :], xbc[:, 8:10, :], ce[:, :, :]]
                y_tm = k.ytmp
                ssd_mix(k, g, xbc, x_tm, cb, hst, y_tm, buf)
            gated_norm(k, y_tm, z, 2, k.pcol[:, 0, 104:112], ycm, hst[:, 0, :, :], True, skip=(x_tm, k.b["ab_d_skip"]))
        with ExitStack() as c:
            q_cm = sb("q_cm", [P, ML_H, T], to=c)
            k_cm = sb("k_cm", [P, ML_H, T], to=c)
            v = sb("v_ext", [P, NT, ML_H, MW], to=c)
            with nc.Block(no_gpsimd_drain=True) as block:
                @block.vector
                def _(dve):
                    nc.vector.memset(v[:, :, :, ML_D:MW], 1.0)
            outs = [into_cm(q_cm, 0), into_cm(q_cm, 4), into_cm(k_cm, 0, ML_D ** -0.5), into_cm(k_cm, 4, ML_D ** -0.5)]
            outs += [(lambda n: lambda t, b: (v[:, t, 4 * n:4 * n + 4, 0:ML_D], 1.0))(n) for n in range(2)]
            project(k, [(*j, f) for j, f in zip(mjobs, outs)])
            states = c.enter_context(ExitStack())
            r = Kernel()
            r.nm, r.si = (sb("r_" + name, [ML_H, 2, T], to=states) for name in ("nm", "si"))
            r.ms_row, r.tot, r.mx, r.umax = (sb("r_" + name, [ML_H, 2, NT], to=states) for name in ("ms_row", "tot", "mx", "umax"))
            r.so = sb("r_so", [ML_H, 2, 2, NT], to=states)
            r.diag = sb("r_diag", [ML_H, ML_H * 4 * NT], to=states)
            r.bar = sb("r_bar", [P, 2], to=states)
            r.floor, r.ew, r.sold, r.sloc = (sb("r_" + name, [P, 2, NT, ML_H], to=states) for name in ("floor", "ew", "sold", "sloc"))
            r.den = sb("r_den", [P, NT, 2], to=states)
            r.rden = sb("r_rden", [P, NT, 2], to=states)
            with ExitStack() as e:
                r.u_row, r.cm, r.ew_row, r.restart = (sb("r_" + name, [ML_H, 2, T], to=e) for name in ("u_row", "cm", "ew_row", "restart"))
                mlstm_gates(k, g, r)
            cst = sb("cst", [P, 2, NT, ML_H, MW], to=states)
            idle = k.ring[:, :, :].rearrange("p s n -> p (s n)")
            r.own = idle[:, 2 * D:2 * D + ML_H * MW].rearrange("p (h w) -> p h w", h=ML_H)
            mlstm_states(k, r, k_cm, v, cst, idle[:, 0:2 * D].rearrange("p (s n) -> p s n", s=2))
            hm = k.ytmp
            mlstm_mix(k, g, r, q_cm, k_cm, v, cst, hm, idle[:, 0:10 * T].rearrange("p (a s n) -> p a s n", a=5, s=2))

            def as_tm(ap):
                return ap.rearrange("p a b -> p (a b)").rearrange("p (t n) -> p t n", t=NT)

            states.close()
            o, work = as_tm(k_cm[:, :, :]), as_tm(q_cm[:, :, :])
            wo = out_chunks(A["ab_w_out"][0], 16)
            project(k, [(cols(O0 + n * BANK, BANK), "tm", gate_tm(o, n * BANK, ACT.Sigmoid)) for n in range(2)], after=wo[:2], cold=True)
            gated_norm(k, hm, o, ML_H, k.pcol[:, 0, 112:120], k.h, work, True)
            project_out(k, lambda n: ycm[:, n, :] if n < KD else k.h[:, n - KD, :], 16, A["ab_w_out"][0], A["norm_g"][0, 1], next_gain, after=after,
                        scratch=work)



def up_slot(k, s):
    return k.ring[:, (k.parity + s) % 2, 0:KD * 2 * P].rearrange("p (t h n) -> p t h n", t=KD, h=2)


def load_up(k, sp, w, s, at):
    wt = w.rearrange("(t p) n -> p t n", p=P)
    for half in range(2):
        sp.dma_start(up_slot(k, s)[:, :, half, :], wt[:, :, bass.ds(at + half * FFN, P)]).then_inc(k.up_loaded[s].sem, 16)


def ffn_first(k, layer):
    def load(sp):
        k.parity = sum(k.asked) % 2
        for s in range(2):
            load_up(k, sp, k.A["ffn_w_up"][layer], s, s * P)
    return load


def ffn_up(k, layer, h_hi, h_lo, g_cm, ybuf, w_hi, w_lo, down):
    nc = k.nc
    w = k.A["ffn_w_up"][layer]
    TURNS = FT // 2
    tap0, tap1 = k.pcol[:, 1 + 2 * layer, 0:2 * FT], k.pcol[:, 1 + 2 * layer, 2 * FT:4 * FT]
    tap2, bias = k.pcol[:, 2 + 2 * layer, 0:2 * FT], k.pcol[:, 2 + 2 * layer, 2 * FT:4 * FT]

    def column(cols, i, s, half):
        at = 2 * i + (s + half * FT)
        return cols[:, at:at + 1] if isinstance(i, int) else cols[:, bass.ds(at, 1)]

    def bank(s, half):
        return k.ps[:, 2 * s + half, :]

    def wait(engine, signal, i, per, more):
        sem, base = signal(0)
        engine.wait_ge(sem, i * per + (base + more))

    with nc.Block(no_gpsimd_drain=True) as block:
        @block.sync
        def _(sp):
            with sp.Fori(1, TURNS) as i:
                for s in range(2):
                    wait(sp, k.w_lo_ready, i, 4, 2 * (s - 1))
                    load_up(k, sp, w, s, i * (2 * P) + s * P)
            sp.wait_ge(*k.w_lo_ready(2 * FT))
            for chunk in down:
                load_weights(k, sp, chunk)

        @block.tensor
        def _(pe):
            def turn(i):
                for s in range(2):
                    wait(pe, k.vb, i, 2, s + 1)
                    for half in range(2):
                        wait(pe, k.w_lo_ready, i, 4, 2 * s + half + 1)
                        for c in range(KD):
                            if isinstance(i, int) and s + half == 0:
                                pe.wait_ge(*k.h_lo_ready(c + 1))
                            last = product(nc, bank(s, half), [part[:, s, half, c, :] for part in (w_hi, w_lo)], [h[:, c, :] for h in (h_hi, h_lo)],
                                           c == 0, c == KD - 1)
                    last.then_inc(k.products.sem, 1)

            turn(0)
            with pe.Fori(1, TURNS) as i:
                turn(i)

        @block.scalar
        def _(act):
            def split(i, s):
                wait(act, k.up_loaded[s], i, 32, 32)
                for half in range(2):
                    nc.scalar.copy(w_hi[:, s, half, :, :], up_slot(k, s)[:, :, half, :]).then_inc(k.w_hi_ready.sem, 1)

            def finish(i, s, ahead):
                wait(act, k.products, i, 2, s + 1)
                for half in range(2):
                    last = nc.scalar.activation(ybuf[:, s, half, :], bank(s, half), ACT.Identity, bias=column(bias, i, s, half),
                                                scale=column(tap1, i, s, half))
                last.then_inc(k.sa.sem, 1)
                if ahead:
                    split(i + 1, s)
                wait(act, k.va, i, 2, s + 1)
                nc.scalar.activation(ybuf[:, s, 0, :], ybuf[:, s, 0, :], ACT.Gelu_apprx_tanh).then_inc(k.sb.sem, 1)

            split(0, 0)
            for c in range(KD):
                nc.scalar.copy(h_hi[:, c, :], k.h[:, c, :]).then_inc(k.h_hi_ready.sem, 1)
            split(0, 1)
            with act.Fori(0, TURNS - 1) as i:
                for s in range(2):
                    finish(i, s, True)
            for s in range(2):
                finish(TURNS - 1, s, False)

        @block.gpsimd
        def _(pool):
            with pool.Fori(0, TURNS) as i:
                for s in range(2):
                    for half in range(2):
                        wait(pool, k.w_hi_ready, i, 4, 2 * s + half + 1)
                        rest(nc.gpsimd, w_lo[:, s, half, :, :], up_slot(k, s)[:, :, half, :], w_hi[:, s, half, :, :]).then_inc(k.w_lo_ready.sem, 1)
            pool.drain()

        @block.vector
        def _(dve):
            nc.vector.sem_inc(k.vb.sem, 2)
            for c in range(KD):
                dve.wait_ge(*k.h_hi_ready(c + 1))
                rest(nc.vector, h_lo[:, c, :], k.h[:, c, :], h_hi[:, c, :]).then_inc(k.h_lo_ready.sem, 1)
            with dve.Fori(0, TURNS) as i:
                for s in range(2):
                    wait(dve, k.sa, i, 2, s + 1)
                    for half in range(2):
                        nc.vector.scalar_tensor_tensor(out=ybuf[:, s, half, 1:T], in0=bank(s, half)[:, 0:T - 1], scalar=column(tap0, i, s, half),
                                                       in1=ybuf[:, s, half, 1:T], op0=ALU.mult, op1=ALU.add)
                    dve.drain()
                    for half in range(2):
                        last = nc.vector.scalar_tensor_tensor(out=ybuf[:, s, half, 0:T - 1], in0=bank(s, half)[:, 1:T], scalar=column(tap2, i, s, half),
                                                              in1=ybuf[:, s, half, 0:T - 1], op0=ALU.mult, op1=ALU.add)
                    last.then_inc(k.va.sem, 1)
                    dve.drain()
                    wait(dve, k.sb, i, 2, s + 1)
                    nc.vector.tensor_tensor(g_cm[:, bass.ds(2 * i + s, 1), :].rearrange("p o t -> p (o t)"), ybuf[:, s, 0, :], ybuf[:, s, 1, :],
                                            ALU.mult).then_inc(k.vb.sem, 1)
    for signal in (k.products, k.sa, k.sb, k.va):
        signal.close(FT)
    k.vb.close(FT + 2)
    k.h_hi_ready.close(KD)
    k.h_lo_ready.close(KD)
    k.w_hi_ready.close(2 * FT)
    k.w_lo_ready.close(2 * FT)
    for s in range(2):
        k.up_loaded[s].close(32 * TURNS)


def ffn(k, layer, gain, next_gain, after):
    with ExitStack() as c:
        g_cm = k.alloc("ffn_g", [P, FT, T], to=c)
        down = out_chunks(k.A["ffn_w_down"][layer], FT)
        with ExitStack() as e:
            ybuf = k.ytmp[:, 0:2, :].rearrange("p s (h t) -> p s h t", h=2)
            h_hi, h_lo = (k.alloc("ffn_h_" + name, [P, KD, T], F32R, e) for name in ("hi", "lo"))
            w_hi, w_lo = (k.alloc("ffn_w_" + name, [P, 2, 2, KD, P], F32R, e) for name in ("hi", "lo"))
            ffn_up(k, layer, h_hi, h_lo, g_cm, ybuf, w_hi, w_lo, down[:2])
        project_out(k, lambda n: g_cm[:, n, :], FT, k.A["ffn_w_down"][layer], gain, next_gain, after=after, scratch=k.ytmp)



def gla_decay(k, glr, w2, bc, restart):
    nc = k.nc
    H = GLA_H
    bias = k.pcol[:, 5, 8:16]
    neg, low = bc.neg, bc.low

    with nc.Block(no_gpsimd_drain=True) as block:
        @block.gpsimd
        def _(pool):
            nc.gpsimd.memset(restart[:, :, :], 1.0)
            pool.drain()
            for d, at in ((0, 0), (1, GLA_L - 1)):
                nc.gpsimd.memset(restart[:, d, :].rearrange("p (c l) -> p c l", l=GLA_L)[:, :, at:at + 1], 0.0)
            pool.drain()
            nc.gpsimd.memset(bc.bar[:, 0:1], 0.0).then_inc(k.ga.sem, 1)
            pool.drain()

        @block.tensor
        def _(pe):
            for n in range(2 * H):
                d, h = n // H, n % H
                nc.tensor.matmul(k.ps[:, n, :], w2[:, d, h * P:(h + 1) * P], glr[:, d, :], start=True, stop=True).then_inc(k.pa.sem, 1)

        @block.scalar
        def _(act):
            for n in range(2 * H):
                act.wait_ge(*k.pa(n + 1))
                nc.scalar.activation(bc.z[:, n, :], k.ps[:, n, :], ACT.Identity, bias=bias[:, n:n + 1]).then_inc(k.sa.sem, 1)
            for n in range(2 * H):
                act.wait_ge(*k.va(n + 1))
                nc.scalar.activation(neg[:, n, :], neg[:, n, :], ACT.Exp)
            act.drain()
            for n in range(2 * H):
                nc.scalar.activation(neg[:, n, :], neg[:, n, :], ACT.Ln, bias=k.ones[:, 0:1]).then_inc(k.sb.sem, 1)

        @block.vector
        def _(dve):
            for n in range(2 * H):
                dve.wait_ge(*k.sa(n + 1))
                nc.vector.scalar_tensor_tensor(out=neg[:, n, :], in0=bc.z[:, n, :], scalar=-1.0, in1=bc.z[:, n, :], op0=ALU.mult, op1=ALU.min)\
                    .then_inc(k.va.sem, 1)
            dve.wait_ge(*k.ga(1))
            for n in range(2 * H):
                dve.wait_ge(*k.sb(n + 1))
                nc.vector.scalar_tensor_tensor(out=low[:, n, :], in0=bc.z[:, n, :], scalar=0.0, in1=neg[:, n, :], op0=ALU.min, op1=ALU.subtract)
                dve.drain()
                way = slice(None) if n < H else slice(None, None, -1)
                nc.vector.tensor_tensor_scan(bc.sum[:, n, :][:, way], restart[:, n // H, :][:, way], low[:, n, :][:, way], 0.0, ALU.mult, ALU.add)
    k.ga.close(1)
    for signal in (k.pa, k.sa, k.sb, k.va):
        signal.close(2 * H)


def gla_scale(k, bc, q_cm, k_cm, q_in, kd, kw, dec):
    nc = k.nc
    H = GLA_H
    S = 1.0 / GLA_TAU
    tiles = [(d, h) for d in range(2) for h in range(H)]

    def chunks(ap):
        return ap.rearrange("p (c l) -> p c l", l=GLA_L)

    with nc.Block(no_gpsimd_drain=True) as block:
        @block.scalar
        def _(act):
            for n, (d, h) in enumerate(tiles):
                nc.scalar.activation(q_in[:, n, :], bc[:, n, :], ACT.Exp, scale=S)
                nc.scalar.activation(kd[:, n, :], bc[:, n, :], ACT.Exp, scale=-S)
                end = chunks(bc[:, n, :])[:, :, GLA_L - 1 if d == 0 else 0]
                nc.scalar.activation(dec[:, n, :], end, ACT.Exp, scale=S)
                act.wait_ge(*k.va(n + 1))
                nc.scalar.activation(kw[:, n, :], kw[:, n, :], ACT.Exp, scale=S).then_inc(k.sa.sem, 1)

        @block.gpsimd
        def _(pool):
            for n, (d, h) in enumerate(tiles):
                pool.wait_ge(*k.sa(n + 1))
                nc.gpsimd.tensor_tensor(q_in[:, n, :], q_in[:, n, :], q_cm[:, h, :], ALU.mult)
            pool.drain()

        @block.vector
        def _(dve):
            for n, (d, h) in enumerate(tiles):
                at = GLA_L - 1 if d == 0 else 0
                end = chunks(bc[:, n, :])[:, :, at:at + 1]
                nc.vector.tensor_tensor(chunks(kw[:, n, :]), spread(end, [P, GC, GLA_L]), chunks(bc[:, n, :]), ALU.subtract).then_inc(k.va.sem, 1)
            for n, (d, h) in enumerate(tiles):
                dve.wait_ge(*k.sa(n + 1))
                nc.vector.tensor_tensor(kd[:, n, :], kd[:, n, :], k_cm[:, h, :], ALU.mult)
                nc.vector.tensor_tensor(kw[:, n, :], kw[:, n, :], k_cm[:, h, :], ALU.mult)
    k.va.close(len(tiles))
    k.sa.close(len(tiles))


def gla_mix(k, q_in, kd, kw, dec, v, o, st, att, kwt, mask):
    nc = k.nc
    H = GLA_H
    W = GLA_DV
    steps = []
    for n in range(GC - 1):
        steps += [(0, n), (1, GC - 1 - n)]

    def tile(d, h):
        return d * H + h

    with nc.Block(no_gpsimd_drain=True) as block:
        @block.gpsimd
        def _(pool):
            for d in range(2):
                nc.gpsimd.tensor_copy(mask.f[:, d, :], k.tri[d][:, :])
            pool.drain()
            nc.gpsimd.memset(mask.f[0:GLA_L, 0, GLA_L:P], 0.0)
            pool.drain()
            nc.gpsimd.memset(mask.f[GLA_L:P, 1, 0:GLA_L], 0.0)
            pool.drain()
            nc.gpsimd.memset(att[:, :, :, :], 0.0)
            nc.gpsimd.memset(st[:, 0, 0, :], 0.0)
            nc.gpsimd.memset(st[:, 1, GC - 1, :], 0.0)
            pool.drain()
            nc.gpsimd.tensor_copy(mask.u[:, :, :], mask.f[:, :, :]).then_inc(k.ga.sem, 1)
            pool.drain()

        @block.tensor
        def _(pe):
            def scores(h):
                for d in range(2):
                    n = tile(d, h)
                    u = 2 * h + d
                    if h >= 1:
                        pe.wait_ge(*k.sa(u - 1))
                    for t in range(NT):
                        last = nc.tensor.transpose(k.ps[:, d, t * P:(t + 1) * P], kw[:, n, t * P:(t + 1) * P], k.ident[:, :])
                    last.then_inc(k.pa.sem, 1)
                    if h >= 1:
                        pe.wait_ge(*k.va(u - 1))
                    for t in range(NT):
                        tok = slice(t * P, (t + 1) * P)
                        last = nc.tensor.matmul(k.ps[:, 2 + d, tok], kd[:, n, tok], q_in[:, n, tok], start=True, stop=True, skip_group_check=True)
                    last.then_inc(k.pb.sem, 1)

            def states(h):
                pe.wait_ge(*k.sa(2 * h + 2))
                for m, (d, c) in enumerate(steps):
                    at = h * len(steps) + m
                    if at >= 2:
                        pe.wait_ge(*k.vb(at - 1))
                    rows = slice((c % 2) * GLA_L, (c % 2 + 1) * GLA_L)
                    nc.tensor.matmul(k.ps[:, 4 + m % 2, 0:W], kwt[rows, h % 2, d, (c // 2) * P:(c // 2 + 1) * P], v[rows, c // 2, h * W:(h + 1) * W],
                                     start=True, stop=True).then_inc(k.pc.sem, 1)

            def outputs(h):
                pe.wait_ge(*k.va(2 * h + 2))
                pe.wait_ge(*k.vb((h + 1) * len(steps)))
                if h >= 1:
                    pe.wait_ge(*k.acc_free(2 * h))
                for t in range(NT):
                    out = k.ps[:, 6 + t // 2, (t % 2) * W:(t % 2 + 1) * W]
                    for d in range(2):
                        nc.tensor.matmul(out, att[:, 2 * (h % 2) + d, t, :], v[:, t, h * W:(h + 1) * W], start=(d == 0), stop=False, skip_group_check=True)
                    for c in (2 * t, 2 * t + 1):
                        half = out[(c % 2) * GLA_L:(c % 2 + 1) * GLA_L, :]
                        for d in range(2):
                            last = nc.tensor.matmul(half, q_in[:, tile(d, h), c * GLA_L:(c + 1) * GLA_L], st[:, d, c, :],
                                                    start=False, stop=True, skip_group_check=True)
                    if t % 2 == 1:
                        last.then_inc(k.acc_ready.sem, 1)

            scores(0)
            for h in range(H):
                states(h)
                if h + 1 < H:
                    scores(h + 1)
                outputs(h)

        @block.scalar
        def _(act):
            def read_o(h):
                for b in range(2):
                    act.wait_ge(*k.acc_ready(2 * h + b + 1))
                    nc.scalar.copy(o[:, 2 * b:2 * b + 2, h * W:(h + 1) * W], k.ps[:, 6 + b, :].rearrange("p (t w) -> p t w", t=2)).then_inc(k.acc_free.sem, 1)

            for h in range(H):
                for d in range(2):
                    u = 2 * h + d
                    act.wait_ge(*k.pa(u + 1))
                    if h >= 2:
                        act.wait_ge(*k.pc((h - 1) * len(steps)))
                    nc.scalar.copy(kwt[:, h % 2, d, :], k.ps[:, d, :]).then_inc(k.sa.sem, 1)
                if h >= 1:
                    read_o(h - 1)
            read_o(H - 1)

        @block.vector
        def _(dve):
            dve.wait_ge(*k.ga(1))

            def masked(h):
                for d in range(2):
                    u = 2 * h + d
                    dve.wait_ge(*k.pb(u + 1))
                    if h >= 2:
                        dve.wait_ge(*k.acc_ready(2 * (h - 1)))
                    nc.vector.copy_predicated(att[:, 2 * (h % 2) + d, :, :], spread(mask.u[:, d, :].rearrange("p (o l) -> p o l", o=1), [P, NT, P]),
                                              k.ps[:, 2 + d, :].rearrange("p (t l) -> p t l", t=NT)).then_inc(k.va.sem, 1)

            masked(0)
            for h in range(H):
                if h >= 1:
                    dve.wait_ge(*k.acc_ready(2 * h))
                for m, (d, c) in enumerate(steps):
                    nxt = c + 1 if d == 0 else c - 1
                    dve.wait_ge(*k.pc(h * len(steps) + m + 1))
                    dve.drain()
                    nc.vector.scalar_tensor_tensor(out=st[:, d, nxt, :], in0=st[:, d, c, :], scalar=dec[:, tile(d, h), c:c + 1],
                                                   in1=k.ps[:, 4 + m % 2, 0:W], op0=ALU.mult, op1=ALU.add).then_inc(k.vb.sem, 1)
                if h + 1 < H:
                    masked(h + 1)
    k.ga.close(1)
    k.pa.close(2 * H)
    k.pb.close(2 * H)
    k.pc.close(H * len(steps))
    k.sa.close(2 * H)
    k.va.close(2 * H)
    k.vb.close(H * len(steps))
    k.acc_ready.close(2 * H)
    k.acc_free.close(2 * H)


GLA_R0 = 3 * D
GLA_JOBS = (0, BANK, D, D + BANK, 2 * D, 2 * D + BANK, GLA_R0, GLA_R0 + GLA_RANK)


def gla_weights(k):
    w = k.A["c_w_in"][0]
    return [w[:, at:at + (BANK if at < GLA_R0 else GLA_RANK)] for at in GLA_JOBS]


def layer1_mixer(k, next_gain, after):
    nc, A, sb = k.nc, k.A, k.alloc
    with ExitStack() as c:
        qk = sb("gla_qk", [P, 2 * GLA_H, T], to=c)
        q_cm, k_cm = qk[:, 0:GLA_H, :], qk[:, GLA_H:2 * GLA_H, :]
        v = sb("gla_v", [P, NT, D], to=c)
        r = sb("gla_r", [P, NT, D], to=c)
        dec = sb("gla_dec", [P, 2 * GLA_H, GC], to=c)
        glr = k.gpost[0:GLA_RANK, :].rearrange("p (d t) -> p d t", d=2)
        outs = [lambda j, b: (q_cm[:, j, :], GLA_DK ** -0.5), lambda j, b: (k_cm[:, j, :], 1.0)]
        for dst in (v, r):
            func = ACT.Silu if dst is r else ACT.Copy
            outs += [(lambda dst, n, func: lambda t, b: (dst[:, t, n * BANK:(n + 1) * BANK], 1.0, func))(dst, n, func) for n in range(2)]
        outs += [(lambda d: lambda j, b: (glr[:, d, :], 1.0))(d) for d in range(2)]
        kinds = ["cm", "cm", "tm", "tm", "tm", "tm", "cm", "cm"]
        wo = out_chunks(A["c_w_out"][0], KD)

        project(k, list(zip(gla_weights(k), kinds, outs)), after=wo[:2])
        scan = c.enter_context(ExitStack())
        q_in = sb("gla_q_in", [P, 2 * GLA_H, T], to=scan)
        kd = sb("gla_kd", [P, 2 * GLA_H, T], to=scan)
        kw = sb("gla_kw", [P, 2 * GLA_H, T], to=scan)
        early = c.enter_context(ExitStack())
        w2 = sb("gla_w2", [GLA_RANK, 2, GLA_H * P], to=early)
        restart = sb("gla_restart", [P, 2, T], to=early)
        bc = Kernel()
        bc.bar = sb("gla_bar", [P, 1], to=early)
        bc.z, bc.neg, bc.low = q_in, kd, kw
        bc.sum = k.ytmp[:, :, :].rearrange("p a b -> p (a b)").rearrange("p (n t) -> p n t", t=T)
        with nc.Block(no_gpsimd_drain=True) as block:
            @block.sync
            def _(sp):
                sp.dma_start(w2[:, :, :], A["c_gate_w2"][0].rearrange("d r n -> r d n")).then_inc(k.param_loaded.sem, 16)
                sp.wait_ge(*k.param_loaded(16))
        k.param_loaded.close(16)
        gla_decay(k, glr, w2, bc, restart)
        early.close()
        gla_scale(k, bc.sum, q_cm, k_cm, q_in, kd, kw, dec)
        with ExitStack() as e:
            att = sb("gla_att", [P, 4, NT, P], to=e)
            kwt = sb("gla_kwt", [P, 2, 2, T], to=e)
            mask = Kernel()
            mask.f = sb("gla_mask", [P, 2, P], to=e)
            mask.u = sb("gla_mask_u", [P, 2, P], U32, to=e)
            st = qk[:, :, :].rearrange("p a b -> p (a b)").rearrange("p (d c w) -> p d c w", d=2, c=GC)
            gla_mix(k, q_in, kd, kw, dec, v, k.ytmp, st, att, kwt, mask)
        work = kd[:, :, :].rearrange("p a b -> p (a b)").rearrange("p (t n) -> p t n", t=NT)
        gated_norm(k, k.ytmp, r, GLA_H, k.pcol[:, 5, 0:8], k.h, work, False)
        scan.close()
        project_out(k, lambda n: k.h[:, n, :], KD, A["c_w_out"][0], A["norm_g"][1, 1], next_gain, after=after, scratch=k.ytmp)



def turn(k, src, dst, tiles):
    nc = k.nc
    with nc.Block(no_gpsimd_drain=True) as block:
        @block.tensor
        def _(pe):
            for c in range(tiles):
                for t in range(NT):
                    last = nc.tensor.transpose(k.ps[:, c % NBANKS, t * P:(t + 1) * P], src[:, t, c * P:(c + 1) * P], k.ident[:, :])
                last.then_inc(k.pa.sem, 1)

        @block.scalar
        def _(act):
            for c in range(0, tiles, 2):
                act.wait_ge(*k.pa(c + 1))
                nc.scalar.copy(dst[:, c, :], k.ps[:, c, :])

        @block.vector
        def _(dve):
            for c in range(1, tiles, 2):
                dve.wait_ge(*k.pa(c + 1))
                nc.vector.tensor_copy(dst[:, c, :], k.ps[:, c, :])
    k.pa.close(tiles)


def head_norm_tm(k, src, dst, tiles, heads, width, gain, sq):
    nc = k.nc
    ms, root, rstd = (k.stat[:, n, 0:tiles * heads].rearrange("p (t h) -> p t h", h=heads) for n in range(3))

    def per_head(ap):
        return ap.rearrange("p (h e) -> p h e", h=heads)

    with nc.Block(no_gpsimd_drain=True) as block:
        @block.vector
        def _(dve):
            for t in range(tiles):
                nc.vector.tensor_tensor(sq[:, t, 0:heads * width], src[:, t, 0:heads * width], src[:, t, 0:heads * width], ALU.mult)
            dve.drain()
            for t in range(tiles):
                nc.vector.tensor_reduce(ms[:, t, :], per_head(sq[:, t, 0:heads * width]), AX.X, ALU.add)
            dve.drain()
            nc.vector.tensor_scalar(ms, ms, 1.0 / width, EPS, ALU.mult, ALU.add).then_inc(k.mean_ready.sem, 1)
            dve.wait_ge(*k.root_ready(1))
            nc.vector.reciprocal(rstd, root)
            dve.drain()
            for t in range(tiles):
                nc.vector.tensor_tensor(per_head(dst[:, t, 0:heads * width]), per_head(src[:, t, 0:heads * width]),
                                        spread(rstd[:, t, :].rearrange("p (h o) -> p h o", o=1), [P, heads, width]), ALU.mult)
            dve.drain()
            for t in range(tiles):
                nc.vector.tensor_tensor(per_head(dst[:, t, 0:heads * width]), per_head(dst[:, t, 0:heads * width]),
                                        spread(gain.rearrange("p (o e) -> p o e", o=1), [P, heads, width]), ALU.mult)

        @block.scalar
        def _(act):
            act.wait_ge(*k.mean_ready(1))
            nc.scalar.activation(root, ms, ACT.Sqrt).then_inc(k.root_ready.sem, 1)
    k.mean_ready.close(1)
    k.root_ready.close(1)


def attend(k, heads, query, key, keys_of, bias, value, width, scale, o, buf):
    nc = k.nc
    units = [(t, h) for t in range(NT) for h in range(heads)]
    s, pt = buf
    SB, TB, VB = 0, 4, 6
    top, ntop, total, rtotal = (k.stat[:, n, 0:NT * heads].rearrange("p (t h) -> p t h", h=heads) for n in range(4))

    with nc.Block(no_gpsimd_drain=True) as block:
        @block.tensor
        def _(pe):
            def scores(n):
                t, h = units[n]
                if n >= 4:
                    pe.wait_ge(*k.va(n - 3))
                nc.tensor.matmul(k.ps[:, SB + n % 4, 0:keys_of(t)], query(t, h), key(h, keys_of(t)), start=True, stop=True).then_inc(k.pa.sem, 1)

            def turned(n):
                t, h = units[n]
                pe.wait_ge(*k.sa(n + 1))
                if n >= 2:
                    pe.wait_ge(*k.sb(n - 1))
                for b in range(keys_of(t) // P):
                    last = nc.tensor.transpose(k.ps[:, TB + n % 2, b * P:(b + 1) * P], s[:, n % 4, b * P:(b + 1) * P], k.ident[:, :])
                last.then_inc(k.pb.sem, 1)

            def values(n):
                t, h = units[n]
                pe.wait_ge(*k.sb(n + 1))
                if h == 0 and t >= 2:
                    pe.wait_ge(*k.vb(t - 1))
                nb = keys_of(t) // P
                for b in range(nb):
                    last = nc.tensor.matmul(k.ps[:, VB + t % 2, h * width:(h + 1) * width], pt[:, n % 2, b * P:(b + 1) * P], value(h, b),
                                            start=(b == 0), stop=(b == nb - 1), skip_group_check=True)
                last.then_inc(k.pc.sem, 1)

            scores(0)
            scores(1)
            for n in range(len(units)):
                if n + 2 < len(units):
                    scores(n + 2)
                if n >= 1:
                    turned(n - 1)
                if n >= 2:
                    values(n - 2)
            turned(len(units) - 1)
            values(len(units) - 2)
            values(len(units) - 1)

        @block.vector
        def _(dve):
            def largest(n):
                t, h = units[n]
                ps = k.ps[:, SB + n % 4, 0:keys_of(t)]
                dve.wait_ge(*k.pa(n + 1))
                if n >= 4:
                    dve.wait_ge(*k.pb(n - 3))
                if bias is None:
                    nc.vector.tensor_reduce(top[:, t, h:h + 1], ps, AX.X, ALU.max)
                    nc.vector.tensor_copy(s[:, n % 4, 0:keys_of(t)], ps)
                else:
                    nc.vector.tensor_tensor_reduce(out=s[:, n % 4, 0:keys_of(t)], in0=ps, in1=bias(t, keys_of(t)), scale=1.0, scalar=-3e38,
                                                   op0=ALU.add, op1=ALU.max, accum_out=top[:, t, h:h + 1])
                dve.drain()
                nc.vector.tensor_scalar(ntop[:, t, h:h + 1], top[:, t, h:h + 1], -scale, None, ALU.mult).then_inc(k.va.sem, 1)

            def read_out(t):
                dve.wait_ge(*k.sa((t + 1) * heads))
                nc.vector.reciprocal(rtotal[:, t, :], total[:, t, :])
                dve.wait_ge(*k.pc((t + 1) * heads))
                dve.drain()
                nc.vector.tensor_tensor(o[:, t, :].rearrange("p (h e) -> p h e", h=heads), k.ps[:, VB + t % 2, 0:heads * width].rearrange("p (h e) -> p h e", h=heads),
                                        spread(rtotal[:, t, :].rearrange("p (h o) -> p h o", o=1), [P, heads, width]), ALU.mult).then_inc(k.vb.sem, 1)

            for n, (t, h) in enumerate(units):
                largest(n)
                if h == heads - 1 and t >= 1:
                    read_out(t - 1)
            read_out(NT - 1)

        @block.scalar
        def _(act):
            def out(n):
                t, h = units[n]
                act.wait_ge(*k.pb(n + 1))
                if n >= 2:
                    act.wait_ge(*k.pc(n - 1))
                nc.scalar.copy(pt[:, n % 2, 0:keys_of(t)], k.ps[:, TB + n % 2, 0:keys_of(t)]).then_inc(k.sb.sem, 1)

            for n, (t, h) in enumerate(units):
                act.wait_ge(*k.va(n + 1))
                nc.scalar.activation(s[:, n % 4, 0:keys_of(t)], s[:, n % 4, 0:keys_of(t)], ACT.Exp, bias=ntop[:, t, h:h + 1], scale=scale,
                                     accum_out=total[:, t, h:h + 1]).then_inc(k.sa.sem, 1)
                if n >= 1:
                    out(n - 1)
            out(len(units) - 1)
    n = len(units)
    for sg in (k.pa, k.pb, k.pc, k.va, k.sa, k.sb):
        sg.close(n)
    k.vb.close(NT)



QK_HEADS = NQ + NKV
ROT = QK_HEADS + NIDX + 1


def rotated(h):
    return QA0 + h * HD if h < QK_HEADS else QI0 + (h - QK_HEADS) * HD


def rope(k, dve, att, tab, tmp):
    nc = k.nc
    half = HD // 2
    for t in range(0, NT, 2):
        turns = []
        for h0, n, at in ((0, QK_HEADS, QA0), (QK_HEADS, NIDX + 1, QI0)):
            x = att[:, t:t + 2, at:at + n * HD].rearrange("p t (h s e) -> p t h s e", h=n, s=2)
            cos, sin = (spread(tab[:, t:t + 2, f * half:(f + 1) * half].rearrange("p t (o e) -> p t o e", o=1), [P, 2, n, half]) for f in range(2))
            turns.append((x[:, :, :, 0, :], x[:, :, :, 1, :], cos, sin, tmp[:, 0, :, h0:h0 + n, :], tmp[:, 1, :, h0:h0 + n, :]))
        for x1, x2, cos, sin, y1, y2 in turns:
            nc.vector.tensor_tensor(y1, x2, sin, ALU.mult)
            nc.vector.tensor_tensor(y2, x1, sin, ALU.mult)
        dve.drain()
        for x1, x2, cos, sin, y1, y2 in turns:
            nc.vector.tensor_tensor(x1, x1, cos, ALU.mult)
            nc.vector.tensor_tensor(x2, x2, cos, ALU.mult)
        dve.drain()
        for x1, x2, cos, sin, y1, y2 in turns:
            nc.vector.tensor_tensor(x1, x1, y1, ALU.subtract)
            nc.vector.tensor_tensor(x2, x2, y2, ALU.add)
        dve.drain()


def heads_of(ap, heads):
    return ap.rearrange("p t (h e) -> p t h e", h=heads)


def per_head_stat(k, row, at, heads):
    return k.stat[:, row, at:at + NT * heads].rearrange("p (t h o) -> p t h o", t=NT, o=1)


def head_squares(k, dve, groups, scratch):
    nc = k.nc
    for x, heads, _, at in groups:
        sq = scratch[:, 0:NT * x.shape[2]].rearrange("p (t n) -> p t n", t=NT)
        nc.vector.tensor_tensor(sq, x, x, ALU.mult)
        dve.drain()
        nc.vector.tensor_reduce(per_head_stat(k, 0, at, heads), heads_of(sq, heads), AX.X, ALU.add)
        dve.drain()


def head_scale(k, dve, groups):
    nc = k.nc
    for x, heads, gain, at in groups:
        nc.vector.reciprocal(per_head_stat(k, 2, at, heads), per_head_stat(k, 1, at, heads))
    dve.drain()
    for x, heads, gain, at in groups:
        width = x.shape[2] // heads
        nc.vector.tensor_tensor(heads_of(x, heads), heads_of(x, heads), spread(per_head_stat(k, 2, at, heads), [P, NT, heads, width]), ALU.mult)
    dve.drain()
    for x, heads, gain, at in groups:
        width = x.shape[2] // heads
        nc.vector.tensor_tensor(heads_of(x, heads), heads_of(x, heads), spread(gain.rearrange("p (a b e) -> p a b e", a=1, b=1), [P, NT, heads, width]), ALU.mult)
    dve.drain()


PAIR_K, PAIR_QI, PAIR_KI = NQ // 2, NQ // 2 + NKV, NQ // 2 + NKV + NIDX // 2
PAIRS = PAIR_KI + 1


def turn_heads(k, rot, cm, twice):
    nc = k.nc
    doubled = [(PAIR_K, NQ), (PAIR_K + 1, NQ + 1), (PAIR_KI, QK_HEADS + NIDX)]
    with nc.Block(no_gpsimd_drain=True) as block:
        @block.vector
        def _(dve):
            for n, (_, h) in enumerate(doubled):
                for half in range(2):
                    last = nc.vector.tensor_copy(twice[:, n, :, half * HD:(half + 1) * HD], rot[:, :, rotated(h):rotated(h) + HD])
            last.then_inc(k.va.sem, 1)
            for c in range(1, PAIRS, 2):
                dve.wait_ge(*k.pa(c + 1))
                nc.vector.tensor_copy(cm[:, c, :], k.ps[:, c % NBANKS, :]).then_inc(k.vb.sem, 1)

        @block.tensor
        def _(pe):
            pe.wait_ge(*k.va(1))
            for c in range(PAIRS):
                if c >= NBANKS:
                    if c % 2:
                        pe.wait_ge(*k.vb((c - NBANKS) // 2 + 1))
                    else:
                        pe.wait_ge(*k.sa((c - NBANKS) // 2 + 1))
                found = [n for n, (pair, _) in enumerate(doubled) if pair == c]
                for t in range(NT):
                    if found:
                        src = twice[:, found[0], t, :]
                    else:
                        h = 2 * c if c < PAIR_K else QK_HEADS + 2 * (c - PAIR_QI)
                        src = rot[:, t, rotated(h):rotated(h) + 2 * HD]
                    last = nc.tensor.transpose(k.ps[:, c % NBANKS, t * P:(t + 1) * P], src, k.ident[:, :])
                last.then_inc(k.pa.sem, 1)

        @block.scalar
        def _(act):
            for c in range(0, PAIRS, 2):
                act.wait_ge(*k.pa(c + 1))
                nc.scalar.copy(cm[:, c, :], k.ps[:, c % NBANKS, :]).then_inc(k.sa.sem, 1)
    k.va.close(1)
    k.pa.close(PAIRS)
    k.vb.close(PAIRS // 2)
    k.sa.close((PAIRS + 1) // 2)


def index_scores(k, cm, w_idx, score, relu, between):
    nc = k.nc
    units = [(t, h) for t in range(1, NT) for h in range(NIDX)]
    with nc.Block(no_gpsimd_drain=True) as block:
        @block.tensor
        def _(pe):
            for n, (t, h) in enumerate(units):
                rows = slice((h % 2) * HD, (h % 2 + 1) * HD)
                if n >= 4:
                    pe.wait_ge(*k.sa(n - 3))
                nc.tensor.matmul(k.ps[:, n % 4, 0:(t + 1) * P], cm[rows, PAIR_QI + h // 2, t * P:(t + 1) * P], cm[rows, PAIR_KI, 0:(t + 1) * P],
                                 start=True, stop=True).then_inc(k.pa.sem, 1)

        @block.scalar
        def _(act):
            for n, (t, h) in enumerate(units):
                act.wait_ge(*k.pa(n + 1))
                if n >= 4:
                    act.wait_ge(*k.va(n - 3))
                nc.scalar.activation(relu[:, n % 4, 0:(t + 1) * P], k.ps[:, n % 4, 0:(t + 1) * P], ACT.Relu, scale=HD ** -0.5).then_inc(k.sa.sem, 1)

        @block.vector
        def _(dve):
            nc.vector.tensor_scalar(w_idx, w_idx, NIDX ** -0.5, None, ALU.mult)
            dve.drain()
            for n, (t, h) in enumerate(units):
                dve.wait_ge(*k.sa(n + 1))
                out, r, w = score[:, t, 0:(t + 1) * P], relu[:, n % 4, 0:(t + 1) * P], w_idx[:, t, h:h + 1]
                if h == 0:
                    nc.vector.tensor_scalar(out, r, w, None, ALU.mult).then_inc(k.va.sem, 1)
                else:
                    nc.vector.scalar_tensor_tensor(out=out, in0=r, scalar=w, in1=out, op0=ALU.mult, op1=ALU.add).then_inc(k.va.sem, 1)
                between(n)
                dve.drain()

        @block.gpsimd
        def _(pool):
            for t in range(1, NT):
                pool.wait_ge(*k.va(t * NIDX))
                nc.gpsimd.affine_select(out=score[:, t, t * P:(t + 1) * P], in_=score[:, t, t * P:(t + 1) * P], compare_op=ALU.is_ge, fill=-BIG, base=0,
                                        pattern=[[-1, P]], channel_multiplier=1)
            pool.drain()
    n = len(units)
    k.pa.close(n)
    k.sa.close(n)
    k.va.close(n)


TAKEN = -3e38


def choose(k, dve, score, eight):
    nc = k.nc
    tiles = range(1, NT)
    for step in range(TOPK // 8):
        for t in tiles:
            nc.vector.max(eight[:, t, :], score[:, t, 0:(t + 1) * P])
        dve.drain()
        for t in tiles:
            nc.vector.match_replace(score[:, t, 0:(t + 1) * P], eight[:, t, :], score[:, t, 0:(t + 1) * P], TAKEN)
        dve.drain()
    for t in tiles:
        nc.vector.tensor_scalar(score[:, t, 0:(t + 1) * P], score[:, t, 0:(t + 1) * P], -2 * BIG, BIG, ALU.is_lt, ALU.mult)
    nc.vector.tensor_scalar(score[:, 0, 0:P], k.tri[1][:, :], BIG, None, ALU.mult)
    dve.drain()
    for t in range(NT):
        nc.vector.tensor_scalar(score[:, t, 0:(t + 1) * P], score[:, t, 0:(t + 1) * P], -BIG, None, ALU.add)



def conv_gate(k, u, gate):
    nc = k.nc
    with nc.Block(no_gpsimd_drain=True) as block:
        @block.scalar
        def _(act):
            nc.scalar.activation(gate[:, :, :], gate[:, :, :], ACT.Sigmoid).then_inc(k.sa.sem, 1)

        @block.vector
        def _(dve):
            nc.vector.memset(u[:, :, 0:CONV_W - 1], 0.0)
            dve.wait_ge(*k.sa(1))
            for j in range(CT):
                nc.vector.tensor_tensor(u[:, j, CONV_W - 1:], u[:, j, CONV_W - 1:], gate[:, j, :], ALU.mult)
    k.sa.close(1)


def conv_tap(k, u, y, n):
    nc = k.nc
    tap, bias = k.pcol[:, 6, :], k.pcol[:, 5, 40:44]
    i, j = n // CT, n % CT
    if i == 0:
        nc.vector.tensor_scalar(y[:, j, :], u[:, j, 0:T], tap[:, j:j + 1], bias[:, j:j + 1], ALU.mult, ALU.add)
    else:
        nc.vector.scalar_tensor_tensor(out=y[:, j, :], in0=u[:, j, i:i + T], scalar=tap[:, n:n + 1], in1=y[:, j, :], op0=ALU.mult, op1=ALU.add)


def conv_taps(k, dve, u, y, first):
    for n in range(first, CONV_W * CT):
        if n % CT == 0:
            dve.drain()
        conv_tap(k, u, y, n)


def conv_norm(k, y, ob, y_tm, sq):
    nc = k.nc
    gain, shift = k.pcol[:, 5, 44:48], k.pcol[:, 5, 48:52]
    mean, var, root, rstd = (k.stat[:, n, 0:NT] for n in range(4))
    with nc.Block(no_gpsimd_drain=True) as block:
        @block.tensor
        def _(pe):
            for t in range(NT):
                for j in range(CT):
                    last = nc.tensor.transpose(k.ps[:, t, j * P:(j + 1) * P], y[:, j, t * P:(t + 1) * P], k.ident[:, :])
                last.then_inc(k.pa.sem, 1)
            pe.wait_ge(*k.va(1))
            for j in range(CT):
                for t in range(NT):
                    last = nc.tensor.transpose(k.ps[:, 4 + j, t * P:(t + 1) * P], y_tm[:, t, j * P:(j + 1) * P], k.ident[:, :])
                last.then_inc(k.pb.sem, 1)

        @block.vector
        def _(dve):
            for t in range(NT):
                dve.wait_ge(*k.pa(t + 1))
                nc.vector.tensor_reduce(mean[:, t:t + 1], k.ps[:, t, :], AX.X, ALU.add)
            dve.drain()
            nc.vector.tensor_scalar(mean, mean, 1.0 / CONV_C, None, ALU.mult)
            dve.drain()
            for t in range(NT):
                nc.vector.tensor_scalar(y_tm[:, t, :], k.ps[:, t, :], mean[:, t:t + 1], None, ALU.subtract)
            dve.drain()
            for t in range(NT):
                nc.vector.tensor_tensor_reduce(out=sq[:, t, :], in0=y_tm[:, t, :], in1=y_tm[:, t, :], scale=1.0, scalar=0.0, op0=ALU.mult, op1=ALU.add,
                                               accum_out=var[:, t:t + 1])
            dve.drain()
            nc.vector.tensor_scalar(var, var, 1.0 / CONV_C, EPS, ALU.mult, ALU.add).then_inc(k.mean_ready.sem, 1)
            dve.wait_ge(*k.root_ready(1))
            nc.vector.reciprocal(rstd, root)
            dve.drain()
            for t in range(NT):
                last = nc.vector.tensor_scalar(y_tm[:, t, :], y_tm[:, t, :], rstd[:, t:t + 1], None, ALU.mult)
            last.then_inc(k.va.sem, 1)

        @block.scalar
        def _(act):
            act.wait_ge(*k.mean_ready(1))
            nc.scalar.activation(root, var, ACT.Sqrt).then_inc(k.root_ready.sem, 1)
            for j in range(CT):
                act.wait_ge(*k.pb(j + 1))
                nc.scalar.activation(ob[:, j, :], k.ps[:, 4 + j, :], ACT.Silu, bias=shift[:, j:j + 1], scale=gain[:, j:j + 1])
    k.pa.close(NT)
    k.pb.close(CT)
    k.va.close(1)
    k.mean_ready.close(1)
    k.root_ready.close(1)



def merge(k, branches, weights, gates, bgate, m, tmp, after):
    nc = k.nc
    NB = len(branches)
    STEPS = 2 + NT
    pieces = [(b, c) for b in range(NB) for c in range(CT)]
    landed = []
    for _ in range(NB):
        s = sum(k.taken) % 2
        k.taken[s] += 1
        landed.append((s, 16 * k.taken[s]))

    def used(p):
        b, c = pieces[p]
        return STEPS * b + (c + 1 if c < CT - 2 else STEPS)

    def raw(p):
        b, c = pieces[p]
        return k.ring[:, landed[b][0], c * D:(c + 1) * D]

    with ExitStack() as own:
        w_hi, w_lo = (k.alloc("wb_" + name, [P, PIECES, D], F32R, own) for name in ("hi", "lo"))
        l_hi, l_lo = (k.alloc("branch_" + name, [P, PIECES, T], F32R, own) for name in ("hi", "lo"))
        block = own.enter_context(nc.Block(no_gpsimd_drain=True))

        @block.sync
        def _(sp):
            for n, w in enumerate([weights[2], after[0], after[1]]):
                sp.wait_ge(*k.w_lo_ready(CT * (n + 1)))
                load_weights(k, sp, w)

        @block.tensor
        def _(pe):
            def tile(p, t):
                c = pieces[p][1]
                for half in range(2):
                    last = product(nc, k.ps[:, 2 * t + half, :], [h[:, p % PIECES, t * P:(t + 1) * P] for h in (l_hi, l_lo)],
                                   [h[:, p % PIECES, half * BANK:(half + 1) * BANK] for h in (w_hi, w_lo)], c == 0, c == CT - 1, skip_group_check=True)
                return last

            for p, (b, c) in enumerate(pieces):
                pe.wait_ge(*k.w_lo_ready(p + 1))
                if c >= CT - 2:
                    continue
                for t in range(NT):
                    if c == 0 and b >= 1:
                        pe.wait_ge(*k.acc_free(NT * (b - 1) + t + 1))
                    last = tile(p, t)
                last.then_inc(k.products.sem, 1)
                if c == CT - 3:
                    pe.wait_ge(*k.w_lo_ready(p + 3))
                    for t in range(NT):
                        tile(p + 1, t)
                        tile(p + 2, t).then_inc(k.products.sem, 1)

        @block.gpsimd
        def _(pool):
            for p, (b, c) in enumerate(pieces):
                pool.wait_ge(*k.w_hi_ready(p + 1))
                rest(nc.gpsimd, l_lo[:, p % PIECES, :], branches[b][:, c, :], l_hi[:, p % PIECES, :])
                rest(nc.gpsimd, w_lo[:, p % PIECES, :], raw(p), w_hi[:, p % PIECES, :]).then_inc(k.w_lo_ready.sem, 1)
            pool.drain()

        @block.vector
        def _(dve):
            for b in range(NB):
                for t in range(NT):
                    g = gates[b][:, t, :]
                    nc.vector.tensor_tensor(g, g, bgate[:, b * D:(b + 1) * D], ALU.add).then_inc(k.va.sem, 1)
            for b in range(NB):
                for t in range(NT):
                    n = b * NT + t
                    dve.wait_ge(*k.sa(n + 1))
                    dve.wait_ge(*k.products(STEPS * b + 2 + t + 1))
                    acc = k.ps[:, 2 * t:2 * t + 2, :].rearrange("p a b -> p (a b)")
                    dst = m[:, t, :] if b == 0 else tmp[:, n % 2, :]
                    nc.vector.tensor_tensor(dst, gates[b][:, t, :], acc, ALU.mult).then_inc(k.acc_free.sem, 1)
                    dve.drain()
                    if b > 0:
                        nc.vector.tensor_tensor(m[:, t, :], m[:, t, :], tmp[:, n % 2, :], ALU.add)
                        dve.drain()

        @block.scalar
        def _(act):
            def sigmoids(b):
                for t in range(NT):
                    act.wait_ge(*k.va(NT * b + t + 1))
                    g = gates[b][:, t, :]
                    nc.scalar.activation(g, g, ACT.Sigmoid).then_inc(k.sa.sem, 1)

            for p, (b, c) in enumerate(pieces):
                if c == 0:
                    act.wait_ge(k.loaded[landed[b][0]].sem, landed[b][1])
                if p >= PIECES:
                    act.wait_ge(*k.products(used(p - PIECES)))
                nc.scalar.copy(l_hi[:, p % PIECES, :], branches[b][:, c, :])
                nc.scalar.copy(w_hi[:, p % PIECES, :], raw(p)).then_inc(k.w_hi_ready.sem, 1)
                if p == PIECES - 1:
                    sigmoids(0)
                if c == CT - 1 and b + 1 < NB:
                    sigmoids(b + 1)
    k.products.close(STEPS * NB)
    k.w_hi_ready.close(len(pieces))
    k.w_lo_ready.close(len(pieces))
    k.acc_free.close(NB * NT)
    k.va.close(NB * NT)
    k.sa.close(NB * NT)


def block2_weights(k):
    w = k.A["w_in_2"][0]
    cuts = [(QA0, BANK), (QA0 + BANK, BANK), (QA0 + 2 * BANK, ATT - 2 * BANK), (CI0, BANK), (CI0 + BANK, BANK), (QM0, BANK)]
    return [w[:, at:at + n] for at, n in cuts]


def memory_weights(k):
    return [k.A["w_mem_kv_2"][0][:, n * BANK:(n + 1) * BANK] for n in range(2)]


def mixers2(k, next_gain, after):
    nc, A, sb = k.nc, k.A, k.alloc
    w = A["w_in_2"][0]

    def into_tm(dst, at, n):
        return lambda t, b: (dst[:, t, at:at + n], 1.0)

    with ExitStack() as c:
        km_cm = k.gpost[:, :].rearrange("p (h n) -> p h n", h=MH)
        vm = sb("vm_tm", [P, MT, MH * MD], to=c)
        qm = sb("qm_tm", [P, NT, MH * MD], to=c)
        u = sb("conv_u", [P, CT, T + CONV_W - 1], to=c)
        gate = sb("conv_gate", [P, CT, T], to=c)
        cm = sb("heads_cm", [P, PAIRS, T], to=c)
        va = k.pcol[:, 1:1 + NT, :]
        widx = sb("widx", [P, NT, NIDX], to=c)
        with ExitStack() as e:
            mem = sb("mem_tm", [P, MT, D], to=e)
            mcm = sb("mem_cm", [P, KD, MEM], to=e)
            kvw = memory_weights(k)
            with nc.Block(no_gpsimd_drain=True) as block:
                @block.sync
                def _(sp):
                    sp.dma_start(mem[:, :, :], A["mem_2"].rearrange("o (t p) d -> p (o t) d", p=P)).then_inc(k.param_loaded.sem, 16)
                    sp.wait_ge(*k.param_loaded(16))
            k.param_loaded.close(16)
            norm_to_cm(k, mem, k.pcol[:, 5, 32:40], mcm, k.ytmp, tiles=MT)
            km = k.ytmp
            proj = block2_weights(k)
            project(k, [(kvw[0], "tm", into_tm(km, 0, BANK)), (kvw[1], "tm", into_tm(vm, 0, BANK))], src=mcm, tiles=MT, after=proj[:2])
            head_norm_tm(k, km, km, MT, MH, MD, k.b["g_km_2"], mem)
            with nc.Block(no_gpsimd_drain=True) as block:
                @block.tensor
                def _(pe):
                    for h in range(MH):
                        for t in range(MT):
                            last = nc.tensor.transpose(k.ps[:, h, t * P:(t + 1) * P], km[:, t, h * MD:(h + 1) * MD], k.ident[:, :])
                        last.then_inc(k.pa.sem, 1)

                @block.scalar
                def _(act):
                    for h in range(MH):
                        act.wait_ge(*k.pa(h + 1))
                        nc.scalar.copy(km_cm[:, h, :], k.ps[:, h, 0:MEM])
            k.pa.close(MH)
        gw = [w[:, GT0 + n * BANK:GT0 + (n + 1) * BANK] for n in range(6)]
        with ExitStack() as e:
            att = sb("att_tm", [P, NT, ATT], to=e)
            tab = sb("rope_tab", [P, NT, HD], to=e)
            proj[4:6] = proj[5], proj[4]
            outs = [into_tm(att, 0, BANK), into_tm(att, BANK, BANK), into_tm(att, 2 * BANK, ATT - 2 * BANK),
                    lambda j, b: (u[:, j, CONV_W - 1:], 1.0), into_tm(qm, 0, BANK), lambda j, b: (gate[:, j, :], 1.0)]
            kinds = ["tm", "tm", "tm", "cm", "tm", "cm"]
            ATT_ACCS, QM_ACCS = 3 * NT, 3 * NT + CT + NT
            scratch = k.ytmp[:, :, :].rearrange("p a b -> p (a b)")
            att_groups = [(att[:, :, QA0:QA0 + NQ * HD], NQ, k.b["g_qa_2"], 0), (att[:, :, KA0:KA0 + NKV * HD], NKV, k.b["g_ka_2"], NT * NQ),
                          (att[:, :, KI0:KI0 + HD], 1, k.b["g_idx_k_2"], NT * (NQ + NKV))]
            ATT_SUMS = NT * (NQ + NKV + 1)
            qm_groups = [(qm[:, :, :], MH, k.b["g_qm_2"], ATT_SUMS)]

            def table(sp):
                sp.dma_start(tab[:, :, :], A["rope_table"].rearrange("(t p) e -> p t e", p=P)).then_inc(k.param_loaded.sem, 16)

            def heads(dve):
                dve.wait_ge(*k.acc_free(ATT_ACCS))
                head_squares(k, dve, att_groups, scratch)
                nc.vector.sem_inc(k.mean_ready.sem, 1)
                dve.wait_ge(*k.root_ready(1))
                head_scale(k, dve, att_groups)
                dve.wait_ge(*k.param_loaded(16))
                rope(k, dve, att, tab, scratch[:, 0:4 * ROT * HD // 2].rearrange("p (f t h e) -> p f t h e", f=2, t=2, h=ROT))
                dve.wait_ge(*k.acc_free(QM_ACCS))
                head_squares(k, dve, qm_groups, scratch)
                nc.vector.sem_inc(k.mean_ready.sem, 1)
                dve.wait_ge(*k.root_ready(2))
                head_scale(k, dve, qm_groups)

            def roots(n, at, to, width):
                def run(act):
                    act.wait_ge(*k.mean_ready(n))
                    nc.scalar.activation(k.stat[:, 1, at:to], k.stat[:, 0, at:to], ACT.Sqrt, bias=k.eps[:, 0:1], scale=1.0 / width).then_inc(k.root_ready.sem, 1)
                return run

            project(k, list(zip(proj, kinds, outs)), after=gw[:2], depth=2, load=table, vector=heads,
                    scalar={ATT_ACCS + 2: roots(1, 0, ATT_SUMS, HD), QM_ACCS + 2: roots(2, ATT_SUMS, ATT_SUMS + NT * MH, MD)})
            k.param_loaded.close(16)
            k.mean_ready.close(2)
            k.root_ready.close(2)
            with nc.Block(no_gpsimd_drain=True) as block:
                @block.scalar
                def _(act):
                    nc.scalar.copy(va[:, :, :], att[:, :, VA0:VA0 + NKV * HD])
                    nc.scalar.copy(widx[:, :, :], att[:, :, WI0:WI0 + NIDX])
            twice = k.ytmp[:, 0:2, :].rearrange("p a b -> p (a b)")[:, 0:3 * NT * P].rearrange("p (n t e) -> p n t e", n=3, t=NT)
            turn_heads(k, att, cm, twice)
        score = sb("score", [P, NT, T], to=c)
        eight = sb("eight", [P, NT, 8], to=c)
        conv_gate(k, u, gate)
        index_scores(k, cm, widx[:, :, :], score, k.ytmp[:, :, 0:T], lambda n: conv_tap(k, u, gate, n))
        gates = [k.ytmp, k.h[:, :, :].rearrange("p a b -> p (a b)").rearrange("p (t d) -> p t d", t=NT), sb("gates_tm", [P, NT, D], to=c)]

        def meanwhile(dve):
            choose(k, dve, score, eight)
            conv_taps(k, dve, u, gate, (NT - 1) * NIDX)
        brw = [A[n][0] for n in ("w_br_a_2", "w_br_b_2", "w_br_m_2")]
        project(k, [(gw[n], "tm", into_tm(gates[n // 2], n % 2 * BANK, BANK)) for n in range(6)], after=brw[:2], vector=meanwhile, depth=2)
        late = c.enter_context(ExitStack())
        scratch = sb("scratch", [P, NT * D], to=late)
        halves = [scratch[:, n * 2 * D:(n + 1) * 2 * D].rearrange("p (t n) -> p t n", t=NT) for n in range(2)]
        conv_norm(k, gate, gate, *halves)
        spare = [scratch[:, 0:4 * T].rearrange("p (s n) -> p s n", s=4), scratch[:, 4 * T:6 * T].rearrange("p (s n) -> p s n", s=2)]
        o_tm, oa, om = u[:, :, 0:T], cm[:, 0:CT, :], qm
        attend(k, NQ, lambda t, h: cm[(h % 2) * HD:(h % 2 + 1) * HD, h // 2, t * P:(t + 1) * P],
               lambda h, n: cm[(h % 2) * HD:(h % 2 + 1) * HD, PAIR_K + h // (NQ // NKV), 0:n], lambda t: (t + 1) * P,
               lambda t, n: score[:, t, 0:n], lambda h, b: va[:, b, (h // (NQ // NKV)) * HD:(h // (NQ // NKV) + 1) * HD], HD, HD ** -0.5, o_tm, spare)
        turn(k, o_tm, oa, CT)
        qm_cm = score
        turn(k, qm, qm_cm, CT)
        attend(k, MH, lambda t, h: qm_cm[:, h, t * P:(t + 1) * P], lambda h, n: km_cm[:, h, 0:n], lambda t: MEM, None,
               lambda h, b: vm[:, b, h * MD:(h + 1) * MD], MD, MD ** -0.5, o_tm, spare)
        turn(k, o_tm, om, CT)
        wo = out_chunks(A["w_o_2"][0], KD)
        bgate = cm[:, CT:CT + 3 * D // T, :].rearrange("p a b -> p (a b)")
        products = u[:, :, :].rearrange("p a b -> p (a b)")[:, 0:2 * D].rearrange("p (n d) -> p n d", n=2)
        with nc.Block(no_gpsimd_drain=True) as block:
            @block.sync
            def _(sp):
                sp.dma_start(bgate, everywhere(A["b_gate_2"][0], 3 * D)).then_inc(k.param_loaded.sem, 16)
                sp.wait_ge(*k.param_loaded(16))
        k.param_loaded.close(16)
        late.close()
        merge(k, [oa, gate, om], brw, gates, bgate, k.ytmp, products, wo)
    turn(k, k.ytmp, k.h, KD)
    project_out(k, lambda n: k.h[:, n, :], KD, A["w_o_2"][0], None, next_gain, after=after, scratch=k.ytmp)



def route(k, wr, r, rows, rows_dram):
    nc = k.nc
    n = NG + NE
    lg, ex, oneg, m1, m2, one1, one2, tmp, desc = r.lg, r.ex, r.oneg, r.m1, r.m2, r.one1, r.one2, r.tmp, r.desc

    def each(ap, w):
        return spread(ap, [P, NT, w])

    with nc.Block(no_gpsimd_drain=True) as block:
        @block.sync
        def _(sp):
            sp.dma_start(rows_dram.rearrange("(t p) d -> p t d", p=P), rows).then_inc(k.param_loaded.sem, 16)
            sp.wait_ge(*k.param_loaded(16))

        @block.gpsimd
        def _(pool):
            for e in range(NE):
                nc.gpsimd.memset(desc[:, e:e + 1], float(NE - e))
            pool.drain()
            nc.gpsimd.memset(r.bar[:, 0:1], 0.0).then_inc(k.ga.sem, 1)
            pool.drain()

        @block.tensor
        def _(pe):
            pe.wait_ge(*k.weights_loaded(32))
            for t in range(NT):
                for c in range(KD):
                    last = nc.tensor.matmul(k.ps[:, 0, t * n:(t + 1) * n], k.h[:, c, t * P:(t + 1) * P], wr[:, c, :], start=(c == 0), stop=(c == KD - 1),
                                            skip_group_check=True)
            last.then_inc(k.pa.sem, 1)

        @block.vector
        def _(dve):
            def first(out, values, top, w, fall):
                nc.vector.tensor_tensor(out, values, each(top, w), ALU.is_equal)
                dve.drain()
                nc.vector.tensor_tensor(out, out, spread(fall.rearrange("p (o e) -> p o e", o=1), [P, NT, w]), ALU.mult)
                dve.drain()
                nc.vector.tensor_reduce(tmp[:, :, 0:1], out, AX.X, ALU.max)
                dve.drain()
                nc.vector.tensor_tensor(out, out, each(tmp[:, :, 0:1], w), ALU.is_equal)
                dve.drain()

            dve.wait_ge(*k.pa(1))
            dve.wait_ge(*k.ga(1))
            bias = k.brow[:, r.bias_at:r.bias_at + n]
            nc.vector.tensor_tensor(lg[:, :, :], k.ps[:, 0, 0:NT * n].rearrange("p (t e) -> p t e", t=NT),
                                    spread(bias.rearrange("p (o e) -> p o e", o=1), [P, NT, n]), ALU.add)
            dve.drain()
            gl, el = lg[:, :, 0:NG], lg[:, :, NG:n]
            nc.vector.tensor_reduce(m1[:, :, :], gl, AX.X, ALU.max)
            dve.drain()
            nc.vector.tensor_tensor(ex[:, :, 0:NG], gl, each(m1[:, :, :], NG), ALU.subtract).then_inc(k.va.sem, 1)
            first(oneg[:, :, :], gl, m1[:, :, :], NG, desc[:, 0:NG])
            per = "p t (g e) -> p t g e"
            for t in range(NT):
                nc.vector.tensor_tensor(el[:, t, :].rearrange("p (g e) -> p g e", g=NG), el[:, t, :].rearrange("p (g e) -> p g e", g=NG),
                                        spread(oneg[:, t, :].rearrange("p (g o) -> p g o", o=1), [P, NG, EPG]), ALU.mult)
            dve.drain()
            nc.vector.tensor_scalar(oneg[:, :, :], oneg[:, :, :], -1.0, BIG, ALU.add, ALU.mult)
            dve.drain()
            for t in range(NT):
                nc.vector.tensor_tensor(el[:, t, :].rearrange("p (g e) -> p g e", g=NG), el[:, t, :].rearrange("p (g e) -> p g e", g=NG),
                                        spread(oneg[:, t, :].rearrange("p (g o) -> p g o", o=1), [P, NG, EPG]), ALU.add)
            dve.drain()
            nc.vector.tensor_reduce(m1[:, :, :], el, AX.X, ALU.max)
            dve.drain()
            first(one1[:, :, :], el, m1[:, :, :], NE, desc[:, :])
            nc.vector.scalar_tensor_tensor(out=el, in0=one1[:, :, :], scalar=-4 * BIG, in1=el, op0=ALU.mult, op1=ALU.add)
            dve.drain()
            nc.vector.tensor_reduce(m2[:, :, :], el, AX.X, ALU.max)
            dve.drain()
            first(one2[:, :, :], el, m2[:, :, :], NE, desc[:, :])
            nc.vector.tensor_tensor(m2[:, :, :], m2[:, :, :], m1[:, :, :], ALU.subtract).then_inc(k.va.sem, 1)
            dve.wait_ge(*k.sa(2))
            nc.vector.tensor_reduce(tmp[:, :, 0:1], ex[:, :, 0:NG], AX.X, ALU.add)
            nc.vector.tensor_scalar(tmp[:, :, 1:2], m2[:, :, :], 1.0, None, ALU.add)
            dve.drain()
            nc.vector.tensor_tensor(tmp[:, :, 0:1], tmp[:, :, 0:1], tmp[:, :, 1:2], ALU.mult)
            dve.drain()
            nc.vector.reciprocal(m1[:, :, :], tmp[:, :, 0:1])
            dve.drain()
            nc.vector.tensor_tensor(m2[:, :, :], m2[:, :, :], m1[:, :, :], ALU.mult)
            nc.vector.tensor_tensor(r.both[:, :, :], one1[:, :, :], one2[:, :, :], ALU.add)

        @block.scalar
        def _(act):
            act.wait_ge(*k.va(1))
            nc.scalar.activation(ex[:, :, 0:NG], ex[:, :, 0:NG], ACT.Exp).then_inc(k.sa.sem, 1)
            act.wait_ge(*k.va(2))
            nc.scalar.activation(m2[:, :, :], m2[:, :, :], ACT.Exp).then_inc(k.sa.sem, 1)
    k.ga.close(1)
    k.pa.close(1)
    k.va.close(2)
    k.sa.close(2)
    k.param_loaded.close(16)
    k.weights_loaded.close(32)


SLOTS = 2 * T
NB = 2 * -(-((SLOTS + NE * (P - 1)) // P) // 2)
FTE = EF // P


def place(k, r, zeros):
    nc = k.nc
    with nc.Block(no_gpsimd_drain=True) as block:
        @block.tensor
        def _(pe):
            ps = k.ps[:, 0, :]
            for t in range(NT):
                for before in range(t):
                    nc.tensor.matmul(ps[:, t * NE:(t + 1) * NE], k.ones[:, :], r.both[:, before, :], start=(before == 0), stop=False, skip_group_check=True)
                nc.tensor.matmul(ps[:, t * NE:(t + 1) * NE], k.tri[0][:, :], r.both[:, t, :], start=(t == 0), stop=True, skip_group_check=True)
            for t in range(NT):
                nc.tensor.matmul(ps[:, NT * NE:(NT + 1) * NE], k.ones[:, :], r.both[:, t, :], start=(t == 0), stop=(t == NT - 1), skip_group_check=True)
            nc.tensor.matmul(ps[:, (NT + 1) * NE:(NT + 1) * NE + 1], k.tri[0][:, :], k.ones[:, 0:1], start=True, stop=True,
                             skip_group_check=True).then_inc(k.pa.sem, 1)
            pe.wait_ge(*k.va(1))
            for n in range(2 * NT):
                last = nc.tensor.matmul(k.ps[:, 1, 0:NB], r.is_slot[:, n, :], r.is_block[:, n, :], start=(n == 0), stop=(n == 2 * NT - 1))
            last.then_inc(k.pb.sem, 1)

        @block.vector
        def _(dve):
            nc.vector.memset(zeros[:, :], 0.0)
            ps = k.ps[:, 0, :]
            upto = ps[:, 0:NT * NE].rearrange("p (t e) -> p t e", t=NT)
            count = ps[:, NT * NE:(NT + 1) * NE]
            nc.vector.tensor_tensor_scan(r.iota[:, :], k.ones[:, :], k.ones[:, :], 0.0, ALU.mult, ALU.add)
            dve.drain()
            nc.vector.tensor_scalar(r.iota[:, :], r.iota[:, :], -1.0, None, ALU.add)
            dve.wait_ge(*k.pa(1))
            nc.vector.tensor_scalar(r.blocks[:, :], count, 0.0, None, ALU.is_gt)
            for n in range(1, T // P):
                dve.drain()
                nc.vector.scalar_tensor_tensor(out=r.blocks[:, :], in0=count, scalar=float(n * P), in1=r.blocks[:, :], op0=ALU.is_gt, op1=ALU.add)
            dve.drain()
            nc.vector.tensor_tensor_scan(r.end[:, :], k.ones[:, 0:NE], r.blocks[:, :], 0.0, ALU.mult, ALU.add)
            dve.drain()
            nc.vector.tensor_tensor(r.start[:, :], r.end[:, :], r.blocks[:, :], ALU.subtract)
            dve.drain()
            for s, one in enumerate((r.one1, r.one2)):
                nc.vector.tensor_tensor(r.pick[:, 2 * s, :, :], one[:, :, :], upto, ALU.mult)
                nc.vector.tensor_tensor(r.pick[:, 2 * s + 1, :, :], one[:, :, :], spread(r.start.rearrange("p (o e) -> p o e", o=1), [P, NT, NE]), ALU.mult)
            dve.drain()
            nc.vector.tensor_reduce(r.picked[:, :, :, :], r.pick[:, :, :, :], AX.X, ALU.add)
            dve.drain()
            rank = [r.picked[:, 2 * s, :, 0] for s in range(2)]
            first = [r.picked[:, 2 * s + 1, :, 0] for s in range(2)]
            for s in range(2):
                sl = slice(s * NT, (s + 1) * NT)
                nc.vector.tensor_scalar(r.rank[:, sl], rank[s], -1.0, None, ALU.add)
                nc.vector.tensor_copy(r.block[:, sl], first[s])
            dve.drain()
            nc.vector.scalar_tensor_tensor(out=r.row_f[:, :], in0=r.block[:, :], scalar=float(P), in1=r.rank[:, :], op0=ALU.mult, op1=ALU.add)
            nc.vector.tensor_scalar(r.full[:, :], r.rank[:, :], float(P), None, ALU.is_ge)
            for n in range(2, T // P):
                dve.drain()
                nc.vector.scalar_tensor_tensor(out=r.full[:, :], in0=r.rank[:, :], scalar=float(n * P), in1=r.full[:, :], op0=ALU.is_ge, op1=ALU.add)
            dve.drain()
            nc.vector.tensor_tensor(r.block[:, :], r.block[:, :], r.full[:, :], ALU.add)
            nc.vector.scalar_tensor_tensor(out=r.rank[:, :], in0=r.full[:, :], scalar=-float(P), in1=r.rank[:, :], op0=ALU.mult, op1=ALU.add)
            nc.vector.tensor_copy(r.row[:, :], r.row_f[:, :])
            for t in range(NT):
                nc.vector.tensor_scalar(r.token_id[:, t:t + 1], ps[:, (NT + 1) * NE:(NT + 1) * NE + 1], float(t * P - 1), None, ALU.add)
            dve.drain()
            for n in range(2 * NT):
                nc.vector.tensor_scalar(r.is_slot[:, n, :], r.iota[:, :], r.rank[:, n:n + 1], None, ALU.is_equal)
                nc.vector.tensor_scalar(r.is_block[:, n, :], r.iota[:, 0:NB], r.block[:, n:n + 1], r.token_id[:, n % NT:n % NT + 1], ALU.is_equal, ALU.mult)
            dve.drain()
            nc.vector.tensor_tensor(r.ended[:, :, :], spread(r.end.rearrange("p (o e) -> p o e", o=1), [P, NB, NE]),
                                    spread(r.iota[:, 0:NB].rearrange("p (b o) -> p b o", o=1), [P, NB, NE]), ALU.is_le).then_inc(k.va.sem, 1)
            dve.drain()
            nc.vector.tensor_reduce(r.expert_f[:, :, :], r.ended[:, :, :], AX.X, ALU.add)
            dve.drain()
            nc.vector.tensor_scalar(r.pairs[:, :], r.iota[:, 0:NB // 2], 2.0, r.end[:, NE - 1:NE], ALU.mult, ALU.is_lt)
            dve.drain()
            nc.vector.tensor_reduce(r.count[:, :], r.pairs[:, 1:], AX.X, ALU.add)
            dve.drain()
            nc.vector.tensor_scalar(r.before_last[:, :], r.count[:, :], -1.0, None, ALU.add)
            nc.vector.tensor_scalar(r.expert[:, :], r.expert_f[:, :, 0], float(NE - 1), None, ALU.min)
            dve.wait_ge(*k.pb(1))
            nc.vector.tensor_copy(r.token[:, :], k.ps[:, 1, 0:NB])
    k.pa.close(1)
    k.va.close(1)
    k.pb.close(1)


def at_block(n, times=1, more=0):
    if isinstance(n, tuple):
        return n[0] * (2 * times) + (n[1] * times + more)
    return n * times + more


def experts(k, r, rows_dram, y_dram, up, dn, e):
    nc, A = k.nc, k.A
    wu = A["w_up_2"][0].rearrange("e (t p) n -> e p t n", p=P)
    wd = A["w_down_2"][0].rearrange("e (t p) n -> e p t n", p=P)
    XB, UB, HB, YB = 0, 2, 4, 5

    def side(n):
        return n[1] % 2 if isinstance(n, tuple) else n % 2

    def early(n, before):
        return not isinstance(n, tuple) and n < before

    def pair(n, per):
        return n[0] * per + (n[1] // 2 + 1) * per if isinstance(n, tuple) else (n // 2 + 1) * per

    def pair_before_last(queue):
        return queue.value_load(r.before_last[0:1, 0:1], min_val=0, max_val=NB // 2 - 2)

    def each_block(engine, before, step):
        step(0)
        step(1)
        with engine.Fori(1, NB // 2 - 1) as i:
            with engine.If(i <= before):
                step((i, 0, NB))
                step((i, 1, NB))
        step((before, 2, 4))
        step((before, 3, 4))

    def later(n, d):
        return (n[0], n[1] + d, n[2]) if isinstance(n, tuple) else n + d

    def inside(n, d):
        return n[1] + d < n[2] if isinstance(n, tuple) else n + d >= 0

    with nc.Block(no_gpsimd_drain=True) as block:
        @block.sync
        def _(sp):
            def expert_of(n):
                at = at_block(n)
                one = r.expert[0:1, bass.ds(at, 1)] if isinstance(n, tuple) else r.expert[0:1, at:at + 1]
                return nc.sync.value_load(one, min_val=0, max_val=NE - 1)

            def load_up(n, expert):
                sp.dma_start(up[side(n)], wu[bass.ds(expert, 1)].rearrange("o p t n -> p (o t) n")).then_inc(e.up_loaded[side(n)], 16)

            def load_down(n, expert):
                sp.dma_start(dn[side(n)], wd[bass.ds(expert, 1)].rearrange("o p t n -> p (o t) n")).then_inc(e.down_loaded[side(n)], 16)

            def of_last_pair(n):
                return isinstance(n, tuple) and n[1] >= 2 and n[2] == 4

            def store(n):
                sp.wait_ge(e.y_ready, at_block(n, 1, 1))
                sp.dma_start(y_dram[bass.ds(at_block(n, P), P), :] if isinstance(n, tuple) else y_dram[n * P:(n + 1) * P, :],
                             e.y[:, side(n), :]).then_inc(e.y_ended if of_last_pair(n) else e.y_stored[side(n)], 16)

            def step(n):
                if inside(n, 2):
                    expert = expert_of(later(n, 2))
                    sp.wait_ge(e.up_done, at_block(n, 1, 1))
                    load_up(later(n, 2), expert)
                if inside(n, -1):
                    if inside(n, 1):
                        expert = expert_of(later(n, 1))
                        sp.wait_ge(e.down_done, at_block(n))
                        load_down(later(n, 1), expert)
                    store(later(n, -1))

            for n in range(2):
                expert = expert_of(n)
                load_up(n, expert)
                load_down(n, expert)
            before = pair_before_last(nc.sync)
            with sp.Fori(0, NB // 2 - 1) as i:
                with sp.If(before < i):
                    sp.dma_start(y_dram[bass.ds(i * (2 * P) + 2 * P, 2 * P), :].rearrange("(s p) d -> p s d", p=P),
                                 e.zeros[:, :].rearrange("p (o d) -> p o d", o=1).to_broadcast([P, 2, D])).then_inc(e.y_zeroed, 16)
                with sp.If(i <= before):
                    sp.sem_inc(e.y_zeroed, 16)
            each_block(sp, before, step)
            store((before, 3, 4))
            sp.wait_ge(e.y_ended, 32)
            sp.wait_ge(e.y_zeroed, 16 * (NB // 2 - 1))

        @block.gpsimd
        def _(pool):
            def step(n):
                s = side(n)
                if not early(n, 2):
                    pool.wait_ge(e.turned, at_block(n, 1, -1))
                nc.gpsimd.tensor_copy(e.slot_token[:, s:s + 1], r.token[:, bass.ds(at_block(n), 1)] if isinstance(n, tuple) else r.token[:, n:n + 1])
                pool.drain()
                nc.gpsimd.indirect_dma_start(e.rows[:, s, :], None, rows_dram, bass.IndirectOffsetOnAxis(ap=e.slot_token[:, s:s + 1], axis=0))\
                    .then_inc(e.gathered[s], 16)

            each_block(pool, pair_before_last(nc.gpsimd), step)
            pool.drain()

        @block.tensor
        def _(pe):
            def turn_rows(n):
                s = side(n)
                pe.wait_ge(e.gathered[s], pair(n, 16))
                if not early(n, 1):
                    pe.wait_ge(e.x_ready, at_block(n))
                for c in range(KD):
                    last = nc.tensor.transpose(k.ps[:, XB + c // NT, (c % NT) * P:(c % NT + 1) * P], e.rows[:, s, c * P:(c + 1) * P], k.ident[:, :])
                last.then_inc(e.turned, 1)

            def first(n):
                s = side(n)
                pe.wait_ge(e.x_ready, at_block(n, 1, 1))
                pe.wait_ge(e.up_loaded[s], pair(n, 16))
                if not early(n, 2):
                    pe.wait_ge(e.hidden, at_block(n, 1, -1))
                for c in range(KD):
                    last = nc.tensor.matmul(k.ps[:, UB + s, :], e.x[:, s, c, :], up[s][:, c, :], start=(c == 0), stop=(c == KD - 1))
                last.then_inc(e.up_done, 1)

            def turn_hidden(n):
                s = side(n)
                pe.wait_ge(e.hidden, at_block(n, 1, 1))
                if not early(n, 1):
                    pe.wait_ge(e.hid_ready, at_block(n))
                for j in range(FTE):
                    last = nc.tensor.transpose(k.ps[:, HB, j * P:(j + 1) * P], e.hid[:, s, j * P:(j + 1) * P], k.ident[:, :])
                last.then_inc(e.hid_turned, 1)

            def second(n):
                s = side(n)
                pe.wait_ge(e.hid_ready, at_block(n, 1, 1))
                pe.wait_ge(e.down_loaded[s], pair(n, 16))
                if not early(n, 1):
                    pe.wait_ge(e.y_ready, at_block(n))
                for half in range(2):
                    for j in range(FTE):
                        last = nc.tensor.matmul(k.ps[:, YB + half, :], e.hid_cm[:, s, j, :], dn[s][:, j, half * BANK:(half + 1) * BANK],
                                                start=(j == 0), stop=(j == FTE - 1))
                last.then_inc(e.down_done, 1)

            def step(n):
                if inside(n, 1):
                    first(later(n, 1))
                turn_hidden(n)
                if inside(n, 2):
                    turn_rows(later(n, 2))
                second(n)

            turn_rows(0)
            first(0)
            turn_rows(1)
            each_block(pe, pair_before_last(nc.tensor), step)

        @block.scalar
        def _(act):
            def silu(n):
                s = side(n)
                act.wait_ge(e.up_done, at_block(n, 1, 1))
                if not early(n, 2):
                    act.wait_ge(e.hidden, at_block(n, 1, -1))
                nc.scalar.activation(e.silu[:, s, :], k.ps[:, UB + s, 0:EF], ACT.Silu).then_inc(e.silu_ready, 1)

            def step(n):
                s = side(n)
                if inside(n, 1):
                    silu(later(n, 1))
                act.wait_ge(e.hid_turned, at_block(n, 1, 1))
                if not early(n, 2):
                    act.wait_ge(e.down_done, at_block(n, 1, -1))
                nc.scalar.copy(e.hid_cm[:, s, :, :], k.ps[:, HB, 0:EF].rearrange("p (j m) -> p j m", j=FTE)).then_inc(e.hid_ready, 1)
                act.wait_ge(e.down_done, at_block(n, 1, 1))
                if not early(n, 2):
                    act.wait_ge(e.y_stored[s], at_block_pairs(n))
                for half in range(2):
                    last = nc.scalar.copy(e.y[:, s, half * BANK:(half + 1) * BANK], k.ps[:, YB + half, :])
                last.then_inc(e.y_ready, 1)

            def at_block_pairs(n):
                return n[0] * 16 + 16 * (n[1] // 2) if isinstance(n, tuple) else 16 * (n // 2)

            silu(0)
            each_block(act, pair_before_last(nc.scalar), step)

        @block.vector
        def _(dve):
            def columns(n):
                s = side(n)
                dve.wait_ge(e.turned, at_block(n, 1, 1))
                if not early(n, 2):
                    dve.wait_ge(e.up_done, at_block(n, 1, -1))
                for half in range(2):
                    c = slice(half * NT, (half + 1) * NT)
                    last = nc.vector.tensor_copy(e.x[:, s, c, :], k.ps[:, XB + half, :].rearrange("p (c m) -> p c m", c=NT))
                last.then_inc(e.x_ready, 1)

            def gated(n):
                s = side(n)
                dve.wait_ge(e.silu_ready, at_block(n, 1, 1))
                if not early(n, 2):
                    dve.wait_ge(e.hid_turned, at_block(n, 1, -1))
                nc.vector.tensor_tensor(e.hid[:, s, :], e.silu[:, s, :], k.ps[:, UB + s, EF:2 * EF], ALU.mult).then_inc(e.hidden, 1)

            def step(n):
                if inside(n, 1):
                    gated(later(n, 1))
                if inside(n, 2):
                    columns(later(n, 2))

            columns(0)
            gated(0)
            columns(1)
            each_block(dve, pair_before_last(nc.vector), step)


def combine(k, r, y_dram, picked, out):
    nc = k.nc
    tiles = out.rearrange("o (t p) d -> p (o t) d", p=P)
    with nc.Block(no_gpsimd_drain=True) as block:
        @block.gpsimd
        def _(pool):
            for n in range(2 * NT):
                at = (n % 2) * NT + n // 2
                nc.gpsimd.indirect_dma_start(picked[:, n, :], None, y_dram, bass.IndirectOffsetOnAxis(ap=r.row[:, at:at + 1], axis=0))\
                    .then_inc(r.row_picked[n], 16)
            for n in range(2 * NT):
                pool.wait_ge(r.row_picked[n], 16)
            pool.drain()

        @block.vector
        def _(dve):
            for t in range(NT):
                for s, share in enumerate((r.m1, r.m2)):
                    dve.wait_ge(r.row_picked[2 * t + s], 16)
                    last = nc.vector.scalar_tensor_tensor(out=k.x[:, t, :], in0=picked[:, 2 * t + s, :], scalar=share[:, t, 0:1], in1=k.x[:, t, :],
                                                          op0=ALU.mult, op1=ALU.add)
                    dve.drain()
                nc.vector.sem_inc(k.va.sem, 1)

        @block.sync
        def _(sp):
            for t in range(NT):
                sp.wait_ge(*k.va(t + 1))
                sp.dma_start(tiles[:, t, :], k.x[:, t, :]).then_inc(k.param_loaded.sem, 16)
            sp.wait_ge(*k.param_loaded(16 * NT))


def router_place(k):
    return k.gpost[:, 0:KD * (NG + NE)].rearrange("p (t n) -> p t n", t=KD)


def load_router(k):
    wr = router_place(k)

    def load(sp):
        sp.dma_start(wr[:, :, 0:NG], k.A["w_rg_2"][0].rearrange("(t p) n -> p t n", p=P)).then_inc(k.weights_loaded.sem, 16)
        sp.dma_start(wr[:, :, NG:], k.A["w_re_2"][0].rearrange("(t p) n -> p t n", p=P)).then_inc(k.weights_loaded.sem, 16)
    return load


def moe(k, out):
    nc, A, sb = k.nc, k.A, k.alloc
    with ExitStack() as c:
        wr = router_place(k)
        r = Kernel()
        r.bias_at = k.router_bias_at
        r.lg, r.ex, r.oneg, r.m1, r.m2, r.one1, r.one2, r.tmp, r.both = (
            sb("moe_" + name, [P, NT, w], to=c) for name, w in (("logits", NG + NE), ("ex", NG), ("group", NG), ("share1", 1), ("share2", 1),
                                                                ("one1", NE), ("one2", NE), ("tmp", 2), ("both", NE)))
        r.desc = sb("moe_desc", [P, NE], to=c)
        r.bar = sb("moe_bar", [P, 1], to=c)
        r.iota = sb("moe_iota", [P, P], to=c)
        r.blocks, r.end, r.start = (sb("moe_" + name, [P, NE], to=c) for name in ("blocks", "block_end", "block_start"))
        r.pick = sb("moe_pick", [P, 4, NT, NE], to=c)
        r.picked = sb("moe_picked", [P, 4, NT, 1], to=c)
        r.rank, r.block, r.full, r.row_f = (sb("moe_" + name, [P, 2 * NT], to=c) for name in ("rank", "block", "full", "row_f"))
        r.row = sb("moe_row", [P, 2 * NT], I32, to=c)
        r.token_id = sb("moe_token_id", [P, NT], to=c)
        r.is_slot = sb("moe_is_slot", [P, 2 * NT, P], to=c)
        r.is_block = sb("moe_is_block", [P, 2 * NT, NB], to=c)
        r.ended = sb("moe_ended", [P, NB, NE], to=c)
        r.expert_f = sb("moe_expert_f", [P, NB, 1], to=c)
        r.expert = sb("moe_expert", [P, NB], I32, to=c)
        r.pairs = sb("moe_pairs", [P, NB // 2], to=c)
        r.count = sb("moe_count", [P, 1], to=c)
        r.before_last = sb("moe_before_last", [P, 1], I32, to=c)
        r.token = sb("moe_token", [P, NB], I32, to=c)
        r.row_picked = [k.new_count(f"row_picked{n}").sem for n in range(2 * NT)]
        e = Kernel()
        e.rows = sb("expert_rows", [P, 2, D], to=c)
        e.x = sb("expert_x", [P, 2, KD, P], to=c)
        e.silu = sb("expert_silu", [P, 2, EF], to=c)
        e.hid = sb("expert_hid", [P, 2, EF], to=c)
        e.hid_cm = sb("expert_hid_cm", [P, 2, FTE, P], to=c)
        e.zeros = sb("zeros", [P, D], to=c)
        e.y = sb("expert_y", [P, 2, D], to=c)
        e.slot_token = sb("expert_slot_token", [P, 2], I32, to=c)
        e.up_loaded, e.down_loaded, e.gathered, e.y_stored = (
            [k.new_count(f"{name}{s}").sem for s in range(2)] for name in ("expert_up_loaded", "expert_down_loaded", "rows_gathered", "y_stored"))
        e.y_zeroed, e.y_ended = (k.new_count(name).sem for name in ("y_zeroed", "y_ended"))
        e.turned, e.x_ready, e.up_done, e.silu_ready, e.hidden, e.hid_turned, e.hid_ready, e.down_done, e.y_ready = (
            k.new_count(name).sem for name in ("rows_turned", "columns_ready", "up_done", "silu_ready", "hidden_ready", "hidden_turned", "hidden_cm_ready",
                                               "down_done", "y_ready"))
        down = sb("moe_down", [P, 2, FTE, D], to=c)
        up = [k.ring[:, s, :].rearrange("p (t n) -> p t n", t=KD) for s in range(2)]
        dn = [down[:, s, :, :] for s in range(2)]
        rows_dram = nc.dram_tensor("normalised_rows", (T, D), F32, kind="Internal").ap()
        y_dram = nc.dram_tensor("expert_results", (NB * P, D), F32, kind="Internal").ap()
        route(k, wr, r, k.ytmp[:, :, :], rows_dram)
        place(k, r, e.zeros)
        experts(k, r, rows_dram, y_dram, up, dn, e)
        picked = k.ring[:, :, :].rearrange("p s n -> p (s n)").rearrange("p (n d) -> p n d", n=2 * NT)
        combine(k, r, y_dram, picked, out)




def build(nc, A, out):
    with ExitStack() as ctx:
        k = open_kernel(nc, ctx, A)
        k.ytmp = k.alloc("y_tmp", [P, NT, D])
        w = A["ab_w_in"][0]
        setup(k, [w[:, XBC0:XBC0 + BANK], w[:, DT0:DT0 + 2 * SSD_H]], k.ytmp)
        norm_to_cm(k, k.x, k.pcol[:, 0, 0:8], k.h, k.ytmp, rows_done=True)
        layer0_mixer(k, A["norm_g"][0, 2], [ffn_first(k, 0)])
        ffn(k, 0, A["norm_g"][0, 3], A["norm_g"][1, 0], gla_weights(k)[:2])
        layer1_mixer(k, A["norm_g"][1, 2], [ffn_first(k, 1)])
        ffn(k, 1, A["norm_g"][1, 3], A["g_mix_2"][0], memory_weights(k))
        mixers2(k, A["g_ffn_2"][0], [load_router(k)])
        moe(k, out)


def constants():
    half = HD // 2
    inv = np.float32(10000.0) ** (-np.arange(half, dtype=np.float32) / np.float32(half))
    angle = np.arange(T, dtype=np.float32)[:, None] * inv[None, :]
    return {"rope_table": np.concatenate([np.cos(angle), np.sin(angle)], axis=1).astype(np.float32)}


_OUT = ((1, T, D), "float32")


def kernel(**inputs):
    import concourse.bacc as _bacc
    from concourse.bass_utils import run_bass_kernel_spmd as _run

    nc = _bacc.Bacc("TRN2", target_bir_lowering=False, num_devices=1)
    arrays, handles = {}, {}
    for name, value in {**inputs, **constants()}.items():
        a = np.ascontiguousarray(value)
        arrays[f"in_{name}"] = a
        handles[name] = nc.dram_tensor(f"in_{name}", a.shape, mybir.dt.from_np(a.dtype), kind="ExternalInput").ap()
    out = nc.dram_tensor("out", _OUT[0], F32, kind="ExternalOutput").ap()
    build(nc, handles, out)
    r = _run(nc, [arrays], core_ids=[0])
    return r.results[0]["out"]
```
